# Optimizing a Trainium2 kernel written in Bass

```python
import functools
import jax
import jax.numpy as jnp
from jax import lax
import numpy as np

D_MODEL = 1024
BATCH = 1
SEQ = 1024
DEPTH = 2
DEC_BATCH = 8
DEC_SEQ = 8
PAST_LEN = 8192
PAGE_SIZE = 128

N_AB_LAYERS = (DEPTH + 1) // 2
N_C_LAYERS = DEPTH // 2

GLA_HEADS = 4
GLA_DK = D_MODEL // 16
GLA_DV = D_MODEL // 8
GLA_LOWRANK = 16
GLA_GATE_NORM = 16.0
GLA_CHUNK = 64

NSA_HEAD_DIM = 64
NSA_HEADS = (D_MODEL // 2) // NSA_HEAD_DIM
NSA_KV_HEADS = 2
NSA_HPG = NSA_HEADS // NSA_KV_HEADS
NSA_BLOCK = 64
NSA_TOP_K = 16
NSA_WINDOW = 512
NSA_CMP_HIDDEN = 2 * NSA_HEAD_DIM
NSA_Q_BLOCK = 32
FORCED_SCORE = 1000.0

GDN_HEADS = 8
GDN_DK = D_MODEL // GDN_HEADS
GDN_DV = D_MODEL // GDN_HEADS
GDN_CONV = 4
GDN_CHUNK = 64

FF_HIDDEN = ((8 * D_MODEL + 3 * 256 - 1) // (3 * 256)) * 256
DEEPNORM_ALPHA = (2.0 * DEPTH) ** 0.25
DEEPNORM_BETA = (8.0 * DEPTH) ** -0.25
LN_EPS = 1e-5
RMS_EPS = 1e-6
L2_EPS = 1e-6

GLA_KEY_W = GLA_HEADS * GLA_DK
GLA_VAL_W = GLA_HEADS * GLA_DV
NSA_Q_W = NSA_HEADS * NSA_HEAD_DIM
NSA_KV_W = NSA_KV_HEADS * NSA_HEAD_DIM
AB_SIZES = (GLA_KEY_W, GLA_KEY_W, GLA_VAL_W, GLA_VAL_W, GLA_LOWRANK, NSA_Q_W, 6 * NSA_KV_W, 3 * NSA_HEADS)
AB_IN = sum(AB_SIZES)
AB_OUT = GLA_VAL_W + NSA_Q_W
GDN_KEY_W = GDN_HEADS * GDN_DK
GDN_VAL_W = GDN_HEADS * GDN_DV
GDN_CONV_CH = 2 * GDN_KEY_W + GDN_VAL_W
C_SIZES = (GDN_CONV_CH, GDN_HEADS, GDN_HEADS, GDN_VAL_W)
C_IN = sum(C_SIZES)

F32 = jnp.float32
NEG = -1e30

kernel_name = 'hybrid_gla_nsa_gdn_decode_step'

def _split(x, sizes):
    return jnp.split(x, [int(s) for s in np.cumsum(sizes)[:-1]], axis=-1)

def _layernorm(x, g, b):
    mu = jnp.mean(x, -1, keepdims=True)
    var = jnp.mean(jnp.square(x - mu), -1, keepdims=True)
    return (x - mu) * lax.rsqrt(var + LN_EPS) * g.astype(F32) + b.astype(F32)

def _rmsnorm(x, g):
    return x * lax.rsqrt(jnp.mean(jnp.square(x), -1, keepdims=True) + RMS_EPS) * g.astype(F32)

def _l2norm(x):
    return x * lax.rsqrt(jnp.sum(jnp.square(x), -1, keepdims=True) + L2_EPS)

def _masked_softmax(s, mask):
    s = jnp.where(mask, s, NEG)
    e = jnp.exp(s - jnp.max(s, -1, keepdims=True)) * mask
    return e / jnp.maximum(jnp.sum(e, -1, keepdims=True), 1e-30)

def _alibi_slopes():
    return jnp.exp2(-8.0 * jnp.arange(1, NSA_HEADS + 1, dtype=F32) / NSA_HEADS)

def _adaln(c, w, b):
    return _split(jax.nn.silu(c) @ w + b, [D_MODEL] * 6)

def _modulate(x, shift, scale):
    return x * (1 + scale[:, None, :]) + shift[:, None, :]

def _post_norm(x, gate, o, g, b):
    z = DEEPNORM_ALPHA * x.astype(F32) + gate[:, None, :].astype(F32) * o.astype(F32)
    return _layernorm(z, g, b).astype(x.dtype)

def _swiglu(h, w_in, w_out):
    a, u = jnp.split(h @ w_in, 2, axis=-1)
    return (jax.nn.silu(a) * u) @ w_out

def _pad_chunks(x, chunk, t_pad):
    x = jnp.pad(x.astype(F32), [(0, 0), (0, t_pad - x.shape[1])] + [(0, 0)] * (x.ndim - 2))
    return jnp.moveaxis(x.reshape((x.shape[0], t_pad // chunk, chunk) + x.shape[2:]), 1, 0)

def _gla(q, k, v, log_a, s0):
    B, T, H, _ = q.shape
    C = min(GLA_CHUNK, T)
    t_pad = -(-T // C) * C
    xs = tuple(_pad_chunks(a, C, t_pad) for a in (q, k, v, log_a))
    causal = jnp.tril(jnp.ones((C, C), dtype=bool))[None, :, :, None, None]

    def step(S, inp):
        qc, kc, vc, ac = inp
        b = jnp.cumsum(ac, axis=1)
        decay = jnp.exp(jnp.where(causal, b[:, :, None] - b[:, None, :], -jnp.inf))
        scores = jnp.einsum('bihk,bjhk,bijhk->bhij', qc, kc, decay)
        o = jnp.einsum('bihk,bhkv->bihv', qc * jnp.exp(b), S) + jnp.einsum('bhij,bjhv->bihv', scores, vc)
        b_last = b[:, -1]
        S = S * jnp.exp(b_last)[..., None] + jnp.einsum('bjhk,bjhv->bhkv', kc * jnp.exp(b_last[:, None] - b), vc)
        return S, o

    S, o = lax.scan(step, s0.astype(F32), xs)
    return jnp.moveaxis(o, 0, 1).reshape(B, t_pad, H, -1)[:, :T], S

def _gdn(q, k, v, g, beta, s0):
    B, T, H, _ = q.shape
    C = min(GDN_CHUNK, T)
    t_pad = -(-T // C) * C
    xs = tuple(_pad_chunks(a, C, t_pad) for a in (q, k, v, g, beta))
    causal = jnp.tril(jnp.ones((C, C), dtype=bool))
    strict = jnp.tril(jnp.ones((C, C), dtype=F32), -1)
    eye = jnp.eye(C, dtype=F32)

    def step(S, inp):
        qc, kc, vc, gc, bc = inp
        d = jnp.moveaxis(jnp.cumsum(gc, axis=1), 1, 2)
        decay = jnp.exp(jnp.where(causal, d[..., :, None] - d[..., None, :], -jnp.inf))
        qh = jnp.moveaxis(qc, 1, 2)
        kh = jnp.moveaxis(kc, 1, 2)
        bh = jnp.moveaxis(bc, 1, 2)[..., None]
        vh = jnp.moveaxis(vc, 1, 2)
        kb = kh * bh
        t_mat = jnp.einsum('bhik,bhjk->bhij', kb, kh) * decay * strict + eye
        u = lax.linalg.triangular_solve(t_mat, vh * bh, left_side=True, lower=True, unit_diagonal=True)
        w = lax.linalg.triangular_solve(t_mat, kb * jnp.exp(d)[..., None], left_side=True, lower=True, unit_diagonal=True)
        v_new = u - jnp.einsum('bhck,bhkv->bhcv', w, S)
        o = (jnp.einsum('bhck,bhkv->bhcv', qh * jnp.exp(d)[..., None], S)
             + jnp.einsum('bhij,bhjv->bhiv', jnp.einsum('bhik,bhjk->bhij', qh, kh) * decay, v_new))
        d_last = d[..., -1]
        S = S * jnp.exp(d_last)[..., None, None] + jnp.einsum('bhck,bhcv->bhkv', kh * jnp.exp(d_last[..., None] - d)[..., None], v_new)
        return S, o

    S, o = lax.scan(step, s0.astype(F32), xs)
    return jnp.transpose(o, (1, 0, 3, 2, 4)).reshape(B, t_pad, H, -1)[:, :T], S

def _compress(kx, pe, w1, w2):
    B, L, G, HD = kx.shape
    n_cmp = L // NSA_BLOCK
    blocks = kx[:, :n_cmp * NSA_BLOCK].astype(F32).reshape(B, n_cmp, NSA_BLOCK, G, HD) + pe.astype(F32)[:, None, :]
    flat = jnp.moveaxis(blocks, 3, 2).reshape(B, n_cmp, G, NSA_BLOCK * HD)
    return jax.nn.silu(flat @ w1) @ w2

def _to_blocks(kx):
    B, L, G, HD = kx.shape
    n_sel = -(-L // NSA_BLOCK)
    kx = jnp.pad(kx, ((0, 0), (0, n_sel * NSA_BLOCK - L), (0, 0), (0, 0)))
    return jnp.transpose(kx.reshape(B, n_sel, NSA_BLOCK, G, HD), (0, 3, 1, 2, 4))

def _nsa_query_block(q, gates, qpos, kc, vc, ks_blk, vs_blk, kw, vw, kwpos):
    B, Tq = q.shape[:2]
    G, HPG, HD, BLK = NSA_KV_HEADS, NSA_HPG, NSA_HEAD_DIM, NSA_BLOCK
    qg = q.astype(F32).reshape(B, Tq, G, HPG, HD) * HD ** -0.5
    slopes = _alibi_slopes().reshape(1, G, HPG, 1, 1)
    tq = qpos.astype(F32)
    n_cmp = kc.shape[1]
    blk = jnp.arange(n_cmp)
    cmp_center = (blk * BLK).astype(F32) + 0.5 * (BLK - 1)
    cmp_mask = (blk * BLK + BLK - 1)[None, :] <= qpos[:, None]
    s_c = jnp.einsum('btghd,bngd->bghtn', qg, kc.astype(F32)) - slopes * (tq[:, None] - cmp_center[None, :])
    p_c = _masked_softmax(s_c, cmp_mask)
    o_c = jnp.einsum('bghtn,bngd->btghd', p_c, vc.astype(F32))
    n_sel = ks_blk.shape[2]
    k_sel = min(NSA_TOP_K, n_sel)
    score = jnp.pad(jnp.sum(p_c, axis=2), ((0, 0), (0, 0), (0, 0), (0, n_sel - n_cmp)))
    sel = jnp.arange(n_sel)[None, :]
    cur = (qpos // BLK)[:, None]
    forced = (sel == 0) | (sel == cur) | (sel == cur - 1)
    visible = sel * BLK <= qpos[:, None]
    score = jnp.where(visible, jnp.where(forced, FORCED_SCORE, score), -1.0)
    _, idx = lax.top_k(score, k_sel)
    bi = jnp.arange(B)[:, None, None, None]
    gi = jnp.arange(G)[None, :, None, None]
    k_g = ks_blk[bi, gi, idx].astype(F32)
    v_g = vs_blk[bi, gi, idx].astype(F32)
    dist_s = qpos[:, None, None] - (idx[..., None] * BLK + jnp.arange(BLK))
    s_s = jnp.einsum('btghd,bgtkpd->bghtkp', qg, k_g) - slopes[..., None] * dist_s[:, :, None].astype(F32)
    p_s = _masked_softmax(s_s.reshape(B, G, HPG, Tq, k_sel * BLK),
                          (dist_s >= 0).reshape(B, G, 1, Tq, k_sel * BLK))
    o_s = jnp.einsum('bghtkp,bgtkpd->btghd', p_s.reshape(B, G, HPG, Tq, k_sel, BLK), v_g)
    dist_w = qpos[:, None] - kwpos[None, :]
    win_mask = (kwpos[None, :] >= 0) & (dist_w >= 0) & (dist_w <= NSA_WINDOW)
    s_w = jnp.einsum('btghd,bsgd->bghts', qg, kw.astype(F32)) - slopes * dist_w.astype(F32)
    p_w = _masked_softmax(s_w, win_mask)
    o_w = jnp.einsum('bghts,bsgd->btghd', p_w, vw.astype(F32))
    gt = gates.astype(F32).reshape(B, Tq, G, HPG, 3, 1)
    o = gt[..., 0, :] * o_c + gt[..., 1, :] * o_s + gt[..., 2, :] * o_w
    return o.reshape(B, Tq, G * HPG * HD)

def _ab_mixer(h, weights, gla_s0, past):
    w_in, w_gk2, b_gk, gla_norm, cmp_pe, cmp_w1, cmp_w2, w_out = weights
    B, T, _ = h.shape
    q_a, k_a, v_a, r_a, gk_a, q_b, kv_b, gate_b = _split((h @ w_in).astype(F32), AB_SIZES)
    log_a = jax.nn.log_sigmoid(gk_a @ w_gk2 + b_gk) / GLA_GATE_NORM
    heads = lambda x, d: x.reshape(B, T, GLA_HEADS, d)
    if gla_s0 is None:
        gla_s0 = jnp.zeros((B, GLA_HEADS, GLA_DK, GLA_DV), F32)
    o_a, s_a = _gla(heads(q_a, GLA_DK) * GLA_DK ** -0.5, heads(k_a, GLA_DK), heads(v_a, GLA_DV), heads(log_a, GLA_DK), gla_s0)
    o_a = (_rmsnorm(o_a, gla_norm) * jax.nn.silu(heads(r_a, GLA_DV))).reshape(B, T, GLA_VAL_W)
    kv = kv_b.reshape(B, T, 6, NSA_KV_HEADS, NSA_HEAD_DIM)
    k_cmp, v_cmp, k_sel, v_sel, k_win, v_win = [kv[:, :, j] for j in range(6)]
    q_n = q_b.reshape(B, T, NSA_HEADS, NSA_HEAD_DIM)
    gates = jax.nn.sigmoid(gate_b).reshape(B, T, NSA_HEADS, 3)
    if past is None:
        kc_f = _compress(k_cmp, cmp_pe[0], cmp_w1[0], cmp_w2[0])
        vc_f = _compress(v_cmp, cmp_pe[1], cmp_w1[1], cmp_w2[1])
        ks_blk, vs_blk = _to_blocks(k_sel), _to_blocks(v_sel)
        pad_w = ((0, 0), (NSA_WINDOW, 0), (0, 0), (0, 0))
        kw_pad, vw_pad = jnp.pad(k_win, pad_w), jnp.pad(v_win, pad_w)
        n_qb = T // NSA_Q_BLOCK
        to_qb = lambda x: jnp.moveaxis(x.reshape((B, n_qb, NSA_Q_BLOCK) + x.shape[2:]), 1, 0)

        def body(args):
            qb, gb, s0 = args
            qpos = s0 + jnp.arange(NSA_Q_BLOCK)
            kwb = lax.dynamic_slice_in_dim(kw_pad, s0, NSA_WINDOW + NSA_Q_BLOCK, axis=1)
            vwb = lax.dynamic_slice_in_dim(vw_pad, s0, NSA_WINDOW + NSA_Q_BLOCK, axis=1)
            kwpos = s0 - NSA_WINDOW + jnp.arange(NSA_WINDOW + NSA_Q_BLOCK)
            return _nsa_query_block(qb, gb, qpos, kc_f, vc_f, ks_blk, vs_blk, kwb, vwb, kwpos)

        o_b = lax.map(body, (to_qb(q_n), to_qb(gates), jnp.arange(n_qb) * NSA_Q_BLOCK))
        o_b = jnp.moveaxis(o_b, 0, 1).reshape(B, T, NSA_Q_W)
        n_keep = min(NSA_WINDOW, T)
        win_k_new, win_v_new = k_win[:, T - n_keep:], v_win[:, T - n_keep:]
    else:
        page_table, pk_c, pv_c, pk_s, pv_s, buf_k, buf_v = past
        past_len = page_table.shape[1] * PAGE_SIZE

        def gather(pool, new):
            rows = pool[page_table].reshape(B, past_len, NSA_KV_HEADS, NSA_HEAD_DIM)
            return jnp.concatenate([rows.astype(F32), new], axis=1)

        kc_f = _compress(gather(pk_c, k_cmp), cmp_pe[0], cmp_w1[0], cmp_w2[0])
        vc_f = _compress(gather(pv_c, v_cmp), cmp_pe[1], cmp_w1[1], cmp_w2[1])
        ks_blk, vs_blk = _to_blocks(gather(pk_s, k_sel)), _to_blocks(gather(pv_s, v_sel))
        kw = jnp.concatenate([buf_k.astype(F32), k_win], axis=1)
        vw = jnp.concatenate([buf_v.astype(F32), v_win], axis=1)
        n_buf = buf_k.shape[1]
        kwpos = past_len - n_buf + jnp.arange(n_buf + T)
        qpos = past_len + jnp.arange(T)
        o_b = _nsa_query_block(q_n, gates, qpos, kc_f, vc_f, ks_blk, vs_blk, kw, vw, kwpos)
        win_k_new, win_v_new = kw[:, T:], vw[:, T:]
    out = jnp.concatenate([o_a, o_b], axis=-1) @ w_out
    return out, (k_cmp, v_cmp, k_sel, v_sel, win_k_new, win_v_new, s_a)

def _c_mixer(h, weights, gdn_s0, conv_buf):
    w_in, conv_w, a_log, dt_bias, norm_g, w_out = weights
    B, T, _ = h.shape
    qkv, b_, a_, z = _split((h @ w_in).astype(F32), C_SIZES)
    if conv_buf is None:
        conv_buf = jnp.zeros((B, GDN_CONV - 1, GDN_CONV_CH), F32)
        gdn_s0 = jnp.zeros((B, GDN_HEADS, GDN_DK, GDN_DV), F32)
    xpad = jnp.concatenate([conv_buf.astype(F32), qkv], axis=1)
    y = lax.conv_general_dilated(xpad, conv_w.astype(F32)[:, None, :], window_strides=(1,), padding='VALID',
                                 dimension_numbers=('NWC', 'WIO', 'NWC'), feature_group_count=GDN_CONV_CH)
    q, k, v = _split(jax.nn.silu(y), (GDN_KEY_W, GDN_KEY_W, GDN_VAL_W))
    q = _l2norm(q.reshape(B, T, GDN_HEADS, GDN_DK)) * GDN_DK ** -0.5
    k = _l2norm(k.reshape(B, T, GDN_HEADS, GDN_DK))
    v = v.reshape(B, T, GDN_HEADS, GDN_DV)
    beta = jax.nn.sigmoid(b_)
    g = -jnp.exp(a_log.astype(F32)) * jax.nn.softplus(a_ + dt_bias.astype(F32))
    o, S = _gdn(q, k, v, g, beta, gdn_s0)
    o = _rmsnorm(o, norm_g) * jax.nn.silu(z.reshape(B, T, GDN_HEADS, GDN_DV))
    out = o.reshape(B, T, GDN_VAL_W) @ w_out
    return out, (S, xpad[:, -(GDN_CONV - 1):])

def _layer(x, mod, mixer, ln_g, ln_b, w_ffn_in, w_ffn_out):
    shift1, scale1, gate1, shift2, scale2, gate2 = mod
    o, st = mixer(_modulate(x, shift1, scale1))
    x = _post_norm(x, gate1, o, ln_g[0], ln_b[0])
    f = _swiglu(_modulate(x, shift2, scale2), w_ffn_in, w_ffn_out)
    x = _post_norm(x, gate2, f, ln_g[1], ln_b[1])
    return x, st

def setup_inputs(seed: int = 0) -> dict:
    key = jax.random.key(seed)
    keys = iter(jax.random.split(key, 48))
    nrm = lambda shape, scale: jax.random.normal(next(keys), shape, F32) * scale
    n_pages = PAST_LEN // PAGE_SIZE
    n_used = DEC_BATCH * n_pages
    n_pool = n_used + -(-n_used // 4)
    win_buf = min(NSA_WINDOW, PAST_LEN)
    pool_shape = (N_AB_LAYERS, n_pool, PAGE_SIZE, NSA_KV_HEADS, NSA_HEAD_DIM)
    win_shape = (N_AB_LAYERS, DEC_BATCH, win_buf, NSA_KV_HEADS, NSA_HEAD_DIM)
    page_table = jax.random.permutation(next(keys), n_pool)[:n_used].reshape(DEC_BATCH, n_pages).astype(jnp.int32)
    dt = jnp.exp(jax.random.uniform(next(keys), (N_C_LAYERS, GDN_HEADS), F32, np.log(1e-3), np.log(1e-1)))
    return {
        'x_prompt': nrm((BATCH, SEQ, D_MODEL), 1.0),
        'x_sample': nrm((DEC_BATCH, DEC_SEQ, D_MODEL), 1.0),
        'c_prompt': nrm((BATCH, D_MODEL), 1.0),
        'c_sample': nrm((DEC_BATCH, D_MODEL), 1.0),
        'page_table': page_table,
        'cache_cmp_k': nrm(pool_shape, 1.0),
        'cache_cmp_v': nrm(pool_shape, 1.0),
        'cache_sel_k': nrm(pool_shape, 1.0),
        'cache_sel_v': nrm(pool_shape, 1.0),
        'state_win_k': nrm(win_shape, 1.0),
        'state_win_v': nrm(win_shape, 1.0),
        'state_gla': nrm((N_AB_LAYERS, DEC_BATCH, GLA_HEADS, GLA_DK, GLA_DV), 0.5),
        'state_gdn': nrm((N_C_LAYERS, DEC_BATCH, GDN_HEADS, GDN_DK, GDN_DV), 0.1),
        'state_gdn_conv': nrm((N_C_LAYERS, DEC_BATCH, GDN_CONV - 1, GDN_CONV_CH), 1.0),
        'w_ada': nrm((DEPTH, D_MODEL, 6 * D_MODEL), 0.5 * D_MODEL ** -0.5),
        'b_ada': nrm((DEPTH, 6 * D_MODEL), 0.01),
        'ln_g': 1.0 + nrm((DEPTH, 2, D_MODEL), 0.01),
        'ln_b': nrm((DEPTH, 2, D_MODEL), 0.01),
        'w_ffn_in': nrm((DEPTH, D_MODEL, 2 * FF_HIDDEN), D_MODEL ** -0.5),
        'w_ffn_out': nrm((DEPTH, FF_HIDDEN, D_MODEL), DEEPNORM_BETA * FF_HIDDEN ** -0.5),
        'ab_w_in': nrm((N_AB_LAYERS, D_MODEL, AB_IN), D_MODEL ** -0.5),
        'ab_w_gk2': nrm((N_AB_LAYERS, GLA_LOWRANK, GLA_KEY_W), GLA_LOWRANK ** -0.5),
        'ab_b_gk': nrm((N_AB_LAYERS, GLA_KEY_W), 0.1),
        'ab_gla_norm': 1.0 + nrm((N_AB_LAYERS, GLA_DV), 0.01),
        'ab_cmp_pe': nrm((N_AB_LAYERS, 2, NSA_BLOCK, NSA_HEAD_DIM), 0.1),
        'ab_cmp_w1': nrm((N_AB_LAYERS, 2, NSA_BLOCK * NSA_HEAD_DIM, NSA_CMP_HIDDEN), (NSA_BLOCK * NSA_HEAD_DIM) ** -0.5),
        'ab_cmp_w2': nrm((N_AB_LAYERS, 2, NSA_CMP_HIDDEN, NSA_HEAD_DIM), NSA_CMP_HIDDEN ** -0.5),
        'ab_w_out': nrm((N_AB_LAYERS, AB_OUT, D_MODEL), DEEPNORM_BETA * AB_OUT ** -0.5),
        'c_w_in': nrm((N_C_LAYERS, D_MODEL, C_IN), D_MODEL ** -0.5),
        'c_conv_w': nrm((N_C_LAYERS, GDN_CONV, GDN_CONV_CH), GDN_CONV ** -0.5),
        'c_a_log': jnp.log(jax.random.uniform(next(keys), (N_C_LAYERS, GDN_HEADS), F32, 1.0, 16.0)),
        'c_dt_bias': dt + jnp.log(-jnp.expm1(-dt)),
        'c_norm': 1.0 + nrm((N_C_LAYERS, GDN_DV), 0.01),
        'c_w_out': nrm((N_C_LAYERS, GDN_VAL_W, D_MODEL), DEEPNORM_BETA * GDN_VAL_W ** -0.5),
    }

def reference(x_prompt, x_sample, c_prompt, c_sample, page_table,
              cache_cmp_k, cache_cmp_v, cache_sel_k, cache_sel_v, state_win_k, state_win_v,
              state_gla, state_gdn, state_gdn_conv,
              w_ada, b_ada, ln_g, ln_b, w_ffn_in, w_ffn_out,
              ab_w_in, ab_w_gk2, ab_b_gk, ab_gla_norm, ab_cmp_pe, ab_cmp_w1, ab_cmp_w2, ab_w_out,
              c_w_in, c_conv_w, c_a_log, c_dt_bias, c_norm, c_w_out):
    xp, xs = x_prompt, x_sample
    ab_p, ab_s, c_p, c_s = [], [], [], []
    for layer in range(DEPTH):
        ffn = (ln_g[layer], ln_b[layer], w_ffn_in[layer], w_ffn_out[layer])
        mod_p = _adaln(c_prompt, w_ada[layer], b_ada[layer])
        mod_s = _adaln(c_sample, w_ada[layer], b_ada[layer])
        if layer % 2 == 0:
            i = layer // 2
            w = (ab_w_in[i], ab_w_gk2[i], ab_b_gk[i], ab_gla_norm[i], ab_cmp_pe[i], ab_cmp_w1[i], ab_cmp_w2[i], ab_w_out[i])
            past = (page_table, cache_cmp_k[i], cache_cmp_v[i], cache_sel_k[i], cache_sel_v[i], state_win_k[i], state_win_v[i])
            xp, st_p = _layer(xp, mod_p, functools.partial(_ab_mixer, weights=w, gla_s0=None, past=None), *ffn)
            xs, st_s = _layer(xs, mod_s, functools.partial(_ab_mixer, weights=w, gla_s0=state_gla[i], past=past), *ffn)
            ab_p.append(st_p)
            ab_s.append(st_s)
        else:
            i = layer // 2
            w = (c_w_in[i], c_conv_w[i], c_a_log[i], c_dt_bias[i], c_norm[i], c_w_out[i])
            xp, st_p = _layer(xp, mod_p, functools.partial(_c_mixer, weights=w, gdn_s0=None, conv_buf=None), *ffn)
            xs, st_s = _layer(xs, mod_s, functools.partial(_c_mixer, weights=w, gdn_s0=state_gdn[i], conv_buf=state_gdn_conv[i]), *ffn)
            c_p.append(st_p)
            c_s.append(st_s)
    p_cmp_k, p_cmp_v, p_sel_k, p_sel_v, p_win_k, p_win_v, p_gla = [jnp.stack(z) for z in zip(*ab_p)]
    s_cmp_k, s_cmp_v, s_sel_k, s_sel_v, s_win_k, s_win_v, s_gla = [jnp.stack(z) for z in zip(*ab_s)]
    p_gdn, p_conv = [jnp.stack(z) for z in zip(*c_p)]
    s_gdn, s_conv = [jnp.stack(z) for z in zip(*c_s)]
    return (xp, xs, p_cmp_k, p_cmp_v, p_sel_k, p_sel_v, p_win_k, p_win_v, p_gla, p_gdn, p_conv,
            s_cmp_k, s_cmp_v, s_sel_k, s_sel_v, s_win_k, s_win_v, s_gla, s_gdn, s_conv)


_drawn_inputs = setup_inputs


def setup_inputs(seed=0):
    import zlib

    import numpy as np

    out = dict(_drawn_inputs(seed))
    spreads = {}
    factors = {'cache_cmp_k': 8.0,
     'cache_cmp_v': 3.185,
     'cache_sel_k': 8.0,
     'cache_sel_v': 7.283,
     'ln_b': 2.847,
     'ab_gla_norm': 8.0,
     'ab_cmp_pe': 8.0,
     'c_norm': 8.0}
    for name, (base, spread) in spreads.items():
        noise = np.random.default_rng([zlib.crc32(name.encode()), seed]).standard_normal(out[name].shape)
        drawn = base * np.exp(spread * noise) if base else spread * noise
        out[name] = jnp.asarray(drawn.astype(out[name].dtype))
    for name, factor in factors.items():
        out[name] = (out[name] * factor).astype(out[name].dtype)
    return out
```

```python
from contextlib import ExitStack, contextmanager

import numpy as np

import concourse.bass as bass
from concourse import mybir

F32 = mybir.dt.float32
I32 = mybir.dt.int32
ALU = mybir.AluOpType
ACT = mybir.ActivationFunctionType
AX = mybir.AxisListType.X

P = 128
D = 1024
KD = D // P
SEQ = 1024
NS, TS = 8, 8
SROWS = NS * TS
T = SEQ + SROWS
MT = SEQ // P
TILES = MT + 1
ROWS = [P] * MT + [SROWS]
FF = 2816
FT = FF // P
CHUNK = 64
ALPHA = (2.0 * 2) ** 0.25
LN_EPS, RMS_EPS, L2_EPS = 1e-5, 1e-6, 1e-6
PAGES = 64
NPOOL = 640
PAST = 8192
NEG = -1e30
MODS = 9

GH, GK, GV = 4, 64, 128
NH, HD, BLK, WIN = 8, 64, 64, 512
Q_A, K_A, V_A, R_A, GK_A = 0, 256, 512, 1024, 1536
Q_B, KV_B, GATE_B, AB_IN = 1552, 2064, 2832, 2856
K_CMP, V_CMP, K_SEL, V_SEL, K_WIN, V_WIN = [KV_B + 128 * j for j in range(6)]
NCH = 3072
C_BA, C_Z, C_IN = 3072, 3088, 4112
DH = 8


def shape_constants():
    f = np.float32
    i = np.arange(P)
    c = {"ident": np.eye(P, dtype=f), "ones": np.ones((P, P), f)}
    j, k = np.meshgrid(np.arange(CHUNK), np.arange(CHUNK), indexing="ij")
    c["tri"] = (j <= k).astype(f)
    c["tri_mid"] = ((j <= k).astype(f) - (j < CHUNK // 2)).astype(f)
    c["tri_end"] = (j > k).astype(f)
    slopes = np.exp2(-8.0 * np.arange(1, NH + 1) / NH)
    x = np.arange(1024)[None, :] - 896
    c["dist_sel"] = np.where(x <= i[:, None], x - i[:, None], NEG).astype(f)
    x = np.arange(640)[None, :] - 512
    dist = i[:, None] - x
    c["dist_win"] = np.where((dist >= 0) & (dist <= WIN), -dist, NEG).astype(f)
    q = (np.arange(MT)[None, :, None] * P + i[:, None, None])
    b = np.arange(16)[None, None, :]
    seen = b * BLK + BLK - 1 <= q
    c["dist_cmp"] = np.where(seen, b * BLK + 0.5 * (BLK - 1) - q, NEG).astype(f)
    c["seen_cmp"] = seen.astype(f)
    c["slopes8"] = np.broadcast_to((8 * slopes).reshape(4, 1, 2), (4, P, 2)).astype(f)
    row = slopes[:, None] * np.ones((1, TS))
    t = np.arange(TS)[None, :]
    pos = np.arange(PAST).reshape(PAGES, P).T
    c["alibi_page"] = (row[None, None] * (pos[:, :, None, None] - PAST - t[None, None])).reshape(P, PAGES * 64).astype(f)
    wpos = (PAST - WIN + np.arange(WIN)).reshape(4, P).T
    dw = PAST + t[None, None] - wpos[:, :, None, None]
    c["alibi_win"] = np.where(dw <= WIN, -row[None, None] * dw, NEG).reshape(P, 4 * 64).astype(f)
    tok = np.arange(TS)[:, None, None]
    c["alibi_new"] = np.where(tok <= t[None], row[None] * (tok - t[None]), NEG).reshape(TS, 64).astype(f)
    cen = np.arange(P) * BLK + 0.5 * (BLK - 1)
    c["alibi_cmp"] = (row.reshape(64, 1) * (cen[None, :] - PAST - np.tile(np.arange(TS), NH)[:, None])).astype(f)
    c["sel_mod_p"] = (np.arange(MODS)[:, None] == 0).astype(f) * np.ones((1, P), f)
    c["sel_mod_s"] = (np.arange(MODS)[:, None] == 1 + np.arange(SROWS)[None, :] // TS).astype(f)
    r = np.arange(64)
    target = (r // 32) * 8 + r % 8
    c["head_sum"] = (np.arange(NS)[None, :, None] * 16 + target[:, None, None] == np.arange(P)[None, None, :]).reshape(64, NS * P).astype(f)
    c["half"] = (np.arange(2)[:, None] == i[None, :] // 64).astype(f)
    return c


@contextmanager
def phase(nc, *names):
    before = nc.snapshot_sems()
    sems = [nc.alloc_semaphore(f"{name}_{nc.next_id()}") for name in names]
    nums = [s.num for s in sems]
    with nc.Block() as block:
        yield (block, *sems)
    nc.all_engine_barrier(sems_to_clear=range(min(nums), max(nums) + 1))
    nc.restore_sems(before)


def banks(ctx, nc, name, shape):
    n = int(np.prod(shape[1:]))
    whole = -(-n // 512) * 512
    t = ctx.enter_context(nc.psum_tensor(f"{name}_{nc.next_id()}", [P, whole], F32))
    ap = t[0:shape[0], 0:n]
    if len(shape) == 3:
        ap = ap.rearrange("p (a b) -> p a b", a=shape[1])
    if len(shape) == 4:
        ap = ap.rearrange("p (a b c) -> p a b c", a=shape[1], b=shape[2])
    return ap


class InOrder:

    def __init__(self, eng, sem):
        self.eng, self.sem, self.n = eng, sem, 0

    def __call__(self, ins):
        self.n += 1
        ins.then_inc(self.sem, 1)
        self.eng.wait_ge(self.sem, self.n)


def load_all(nc, pairs):
    with phase(nc, "loaded") as (block, loaded):
        @block.sync
        def _(sp):
            for dst, src in pairs:
                sp.dma_start(dst, src).then_inc(loaded, 16)
            sp.wait_ge(loaded, 16 * len(pairs))


def gemm_rows(nc, lhsT, rows, kt, w, out_rows, width, steps, bias=None, tag=""):
    slots = 2 if steps >= 2 else 1
    loops = steps // slots
    n_m = len(rows)
    ring = 3 if (slots * n_m) % 3 == 0 else slots
    wr = w.rearrange("(k p) n -> p k n", p=P)
    per = slots * n_m
    with ExitStack() as ctx:
        ws = [ctx.enter_context(nc.sbuf_tensor(f"w{tag}{s}_{nc.next_id()}", [P, kt, width], F32)) for s in range(slots)]
        bs = [ctx.enter_context(nc.sbuf_tensor(f"b{tag}{s}_{nc.next_id()}", [rows[0], width], F32)) for s in range(slots)] if bias is not None else None
        stage = [ctx.enter_context(nc.sbuf_tensor(f"st{tag}{s}_{nc.next_id()}", [P, width], F32)) for s in range(ring)]
        psum = [ctx.enter_context(nc.psum_tensor(f"pp{tag}{s}_{nc.next_id()}", [P, 512], F32)) for s in range(ring)]
        names = ([f"w_loaded{s}" for s in range(slots)] + [f"w_free{s}" for s in range(slots)]
                 + ["product_ready", "psum_free", "evacuated"] + [f"stage_free{r}" for r in range(ring)])
        with phase(nc, *names) as (block, *sems):
            w_loaded, w_free = sems[:slots], sems[slots:2 * slots]
            product_ready, psum_free, evacuated = sems[2 * slots:2 * slots + 3]
            stage_free = sems[2 * slots + 3:]
            readers = 2 if bias is not None else 1
            dmas_per_slot = 16 * (2 if bias is not None else 1)

            @block.sync
            def _(sp):
                def body(i):
                    for s in range(slots):
                        sp.wait_ge(w_free[s], i * readers + readers)
                        cols = bass.ds(i * (slots * width) + s * width, width)
                        sp.dma_start(ws[s][:], wr[:, :, cols]).then_inc(w_loaded[s], 16)
                        if bias is not None:
                            sp.dma_start(bs[s][:], bias[:, cols]).then_inc(w_loaded[s], 16)
                if loops > 1:
                    with sp.Fori(0, loops) as i:
                        body(i)
                else:
                    body(0)

            @block.tensor
            def _(pe):
                for s in range(slots):
                    pe.sem_inc(w_free[s], 1)

                def body(i):
                    for s in range(slots):
                        pe.wait_ge(w_loaded[s], i * dmas_per_slot + dmas_per_slot)
                        for m in range(n_m):
                            n = s * n_m + m
                            pe.wait_ge(psum_free, i * per + n + 1)
                            for k in range(kt):
                                last = pe.matmul(psum[n % ring][0:rows[m], 0:width], lhsT(m, k), ws[s][:, k, :],
                                                 start=(k == 0), stop=(k == kt - 1))
                            last.then_inc(product_ready, 1)
                        pe.wait_ge(product_ready, i * per + (s + 1) * n_m)
                        pe.sem_inc(w_free[s], 1)
                if loops > 1:
                    with pe.Fori(0, loops) as i:
                        body(i)
                else:
                    body(0)

            @block.vector
            def _(dve):
                dve.sem_inc(psum_free, ring)
                if bias is not None:
                    for s in range(slots):
                        dve.sem_inc(w_free[s], 1)

                def body(i):
                    for n in range(per):
                        m, r = n % n_m, rows[n % n_m]
                        dve.wait_ge(product_ready, i * per + n + 1)
                        dve.wait_ge(stage_free[n % ring], i * (16 * (per // ring)) + 16 * (n // ring) + 16)
                        if bias is None:
                            ins = dve.tensor_copy(stage[n % ring][0:r, :], psum[n % ring][0:r, 0:width])
                        else:
                            ins = dve.tensor_tensor(stage[n % ring][0:r, :], psum[n % ring][0:r, 0:width],
                                                    bs[n // n_m][0:r, :], ALU.add)
                        ins.then_inc(evacuated, 1)
                        dve.wait_ge(evacuated, i * per + n + 1)
                        dve.sem_inc(psum_free, 1)
                        if bias is not None and n % n_m == n_m - 1:
                            dve.sem_inc(w_free[n // n_m], 1)
                if loops > 1:
                    with dve.Fori(0, loops) as i:
                        body(i)
                else:
                    body(0)

            @block.scalar
            def _(act):
                for r in range(ring):
                    act.sem_inc(stage_free[r], 16)

                def body(i):
                    for n in range(per):
                        s, m = divmod(n, n_m)
                        act.wait_ge(evacuated, i * per + n + 1)
                        cols = bass.ds(i * (slots * width) + s * width, width)
                        dst, src = out_rows(m, cols), stage[n % ring][0:rows[m], :]
                        act.dma_start(dst, src).then_inc(stage_free[n % ring], 16)
                if loops > 1:
                    with act.Fori(0, loops) as i:
                        body(i)
                else:
                    body(0)
                for r in range(ring):
                    act.wait_ge(stage_free[r], 16 * (1 + loops * per // ring))


def transpose_rows(nc, src, hT, ident, mod=None, tiles=TILES, loads=(), tag=""):
    with ExitStack() as ctx:
        ps = [ctx.enter_context(nc.psum_tensor(f"tp{s}_{nc.next_id()}", [P, KD, P], F32)) for s in range(2)]
        with phase(nc, "loaded", "turned", "even_out", "odd_out", "sample_steps") as (
                block, loaded, turned, even_out, odd_out, sample_steps):
            @block.sync
            def _(sp):
                for dst, s in loads:
                    sp.dma_start(dst, s).then_inc(loaded, 16)

            @block.tensor
            def _(pe):
                if loads:
                    pe.wait_ge(loaded, 16 * len(loads))
                for m in range(tiles):
                    if m >= 2:
                        pe.wait_ge(even_out, m - 1)
                        pe.wait_ge(odd_out, m - 1)
                    for k in range(KD):
                        last = pe.transpose(ps[m % 2][:, k, 0:ROWS[m]], src[0:ROWS[m], m, k * P:(k + 1) * P],
                                            ident[0:ROWS[m], 0:ROWS[m]])
                    last.then_inc(turned, 1)

            @block.scalar
            def _(act):
                for m in range(tiles):
                    act.wait_ge(turned, m + 1)
                    r = ROWS[m]
                    if mod is None:
                        act.copy(hT[:, 0:4, m * P:m * P + r], ps[m % 2][:, 0:4, 0:r]).then_inc(even_out, 1)
                    elif m < MT:
                        for k in range(4):
                            last = act.activation(hT[:, k, m * P:m * P + r], ps[m % 2][:, k, 0:r], ACT.Identity,
                                                  bias=mod[0][:, k, 0:1], scale=mod[1][:, k, 0:1])
                        last.then_inc(even_out, 1)
                    else:
                        act.sem_inc(even_out, 1)

            @block.vector
            def _(dve):
                for m in range(tiles):
                    dve.wait_ge(turned, m + 1)
                    r = ROWS[m]
                    if mod is None:
                        dve.tensor_copy(hT[:, 4:8, m * P:m * P + r], ps[m % 2][:, 4:8, 0:r]).then_inc(odd_out, 1)
                    elif m < MT:
                        for k in range(4, KD):
                            last = dve.tensor_scalar(hT[:, k, m * P:m * P + r], ps[m % 2][:, k, 0:r],
                                                     mod[1][:, k, 0:1], mod[0][:, k, 0:1], ALU.mult, ALU.add)
                        last.then_inc(odd_out, 1)
                    else:
                        step = InOrder(dve, sample_steps)
                        for k in range(KD):
                            o = hT[:, k, SEQ:T].rearrange("p (s t) -> p s t", t=TS)
                            step(dve.tensor_tensor(o, ps[m % 2][:, k, 0:r].rearrange("p (s t) -> p s t", t=TS),
                                                   mod[1][:, k, 1:MODS].unsqueeze(2).broadcast_to([P, NS, TS]), ALU.mult))
                            step(dve.tensor_tensor(o, o, mod[0][:, k, 1:MODS].unsqueeze(2).broadcast_to([P, NS, TS]), ALU.add))
                        dve.sem_inc(odd_out, 1)


def post_norm(nc, X, y, gate, ln_g, ln_b, c, out=None):
    with ExitStack() as ctx:
        sb = lambda n, s: ctx.enter_context(nc.sbuf_tensor(f"{n}_{nc.next_id()}", s, F32))
        ys = [sb("y", [P, D]) for _ in range(3)]
        gates, gate_p, gate_s = sb("gates", [MODS, D]), sb("gate_p", [P, D]), sb("gate_s", [SROWS, D])
        gB, bB = sb("gB", [P, D]), sb("bB", [P, D])
        stats, mv, rstd = sb("stats", [P, TILES, 2, 6]), sb("mv", [P, TILES, 2]), sb("rstd", [P, TILES])
        eps = sb("eps", [P, 1])
        ps = [ctx.enter_context(nc.psum_tensor(f"pg{s}_{nc.next_id()}", [P, D], F32)) for s in range(2)]
        with phase(nc, "params", "y0", "y1", "y2", "y_used", "gate_ready", "gate_out", "dve_steps", "act_steps", "rstd_ready",
                   "x_ready", "stored") as (
                block, params, y0, y1, y2, y_used, gate_ready, gate_out, dve_steps, act_steps, rstd_ready, x_ready, stored):
            y_loaded = [y0, y1, y2]

            @block.sync
            def _(sp):
                sp.dma_start(gates[:], gate).then_inc(params, 16)
                for m in range(TILES):
                    if m >= 3:
                        sp.wait_ge(y_used, m - 2)
                    sp.dma_start(ys[m % 3][0:ROWS[m], :], y[m * P:m * P + ROWS[m], :]).then_inc(y_loaded[m % 3], 16)
                if out is not None:
                    for m in range(TILES):
                        sp.wait_ge(x_ready, m + 1)
                        dst = out[0][m * P:(m + 1) * P, :] if m < MT else out[1]
                        sp.dma_start(dst, X[0:ROWS[m], m, :]).then_inc(stored, 16)
                    sp.wait_ge(stored, 16 * TILES)

            @block.tensor
            def _(pe):
                pe.wait_ge(params, 48)
                for n in range(2):
                    cols = slice(n * 512, n * 512 + 512)
                    pe.matmul(ps[0][:, cols], c["sel_mod_p"][:], gates[:, cols], start=True, stop=True)
                    last = pe.matmul(ps[1][0:SROWS, cols], c["sel_mod_s"][:], gates[:, cols], start=True, stop=True)
                last.then_inc(gate_ready, 1)

            @block.gpsimd
            def _(pool):
                pool.memset(mv[:], 1.0).then_inc(gate_out, 1)
                pool.memset(eps[:], LN_EPS).then_inc(gate_out, 1)

            @block.scalar
            def _(act):
                act.dma_start(gB[:], ln_g.partition_broadcast(P)).then_inc(params, 16)
                act.dma_start(bB[:], ln_b.partition_broadcast(P)).then_inc(params, 16)
                act.wait_ge(gate_ready, 1)
                act.copy(gate_p[:], ps[0][:]).then_inc(gate_out, 1)
                act.copy(gate_s[:], ps[1][0:SROWS, :]).then_inc(gate_out, 1)
                act.wait_ge(rstd_ready, 1)
                step = InOrder(act, act_steps)
                step(act.activation(rstd[:], mv[:, :, 1], ACT.Ln, bias=eps[:, 0:1]))
                act.activation(rstd[:], rstd[:], ACT.Exp, scale=-0.5).then_inc(rstd_ready, 1)

            @block.vector
            def _(dve):
                step = InOrder(dve, dve_steps)
                dve.wait_ge(gate_out, 4)
                dve.wait_ge(params, 48)
                for m in range(TILES):
                    r = ROWS[m]
                    dve.wait_ge(y_loaded[m % 3], 16 * (m // 3 + 1))
                    yt = ys[m % 3][0:r, :]
                    step(dve.tensor_tensor(yt, yt, (gate_p if m < MT else gate_s)[0:r, :], ALU.mult))
                    step(dve.scalar_tensor_tensor(X[0:r, m, :], X[0:r, m, :], ALPHA, yt, ALU.mult, ALU.add))
                    dve.sem_inc(y_used, 1)
                    for n in range(2):
                        step(dve.bn_stats(stats[0:r, m, n, :], X[0:r, m, n * 512:(n + 1) * 512]))
                    step(dve.bn_aggr(mv[0:r, m, :], stats[0:r, m, :, :].rearrange("p a b -> p (a b)")))
                dve.sem_inc(rstd_ready, 1)
                dve.wait_ge(rstd_ready, 2)
                for m in range(TILES):
                    r = ROWS[m]
                    x = X[0:r, m, :]
                    step(dve.tensor_scalar(x, x, mv[0:r, m, 0:1], rstd[0:r, m:m + 1], ALU.subtract, ALU.mult))
                    step(dve.tensor_tensor(x, x, gB[0:r, :], ALU.mult))
                    dve.tensor_tensor(x, x, bB[0:r, :], ALU.add).then_inc(x_ready, 1)


def swiglu_hidden(nc, hT, hid, w_in):
    wr = w_in.rearrange("(k p) (two n) -> p two k n", p=P, two=2)
    chunks = [(0, 512), (512, 512), (1024, SROWS)]
    NB = 3
    with ExitStack() as ctx:
        sb = lambda n, s: ctx.enter_context(nc.sbuf_tensor(f"{n}_{nc.next_id()}", s, F32))
        ws = [sb("wf", [P, 2, KD, P]) for _ in range(2)]
        e = [sb("e", [P, 512]) for _ in range(NB)]
        ps = [ctx.enter_context(nc.psum_tensor(f"pf{s}_{nc.next_id()}", [P, 2, 512], F32)) for s in range(NB)]
        with phase(nc, "w_loaded0", "w_loaded1", "w_free0", "w_free1", "pair_ready", "exp_ready", "pair_used", "dve_steps") as (
                block, w_loaded0, w_loaded1, w_free0, w_free1, pair_ready, exp_ready, pair_used, dve_steps):
            w_loaded, w_free = [w_loaded0, w_loaded1], [w_free0, w_free1]

            @block.sync
            def _(sp):
                with sp.Fori(0, FT // 2) as i:
                    for s in range(2):
                        sp.wait_ge(w_free[s], i + 1)
                        for two in range(2):
                            sp.dma_start(ws[s][:, two], wr[:, two, :, bass.ds(i * 256 + s * P, P)]).then_inc(w_loaded[s], 16)

            @block.tensor
            def _(pe):
                pe.sem_inc(w_free0, 1)
                pe.sem_inc(w_free1, 1)
                with pe.Fori(0, FT // 2) as i:
                    for s in range(2):
                        pe.wait_ge(w_loaded[s], i * 32 + 32)
                        for j, (t0, tn) in enumerate(chunks):
                            n = s * 3 + j
                            pe.wait_ge(pair_used, i * 6 + n + 1)
                            for two in range(2):
                                for k in range(KD):
                                    last = pe.matmul(ps[n % NB][:, two, 0:tn], ws[s][:, two, k, :], hT[:, k, t0:t0 + tn],
                                                     start=(k == 0), stop=(k == KD - 1))
                            last.then_inc(pair_ready, 1)
                        pe.wait_ge(pair_ready, i * 6 + s * 3 + 3)
                        pe.sem_inc(w_free[s], 1)

            @block.scalar
            def _(act):
                with act.Fori(0, FT // 2) as i:
                    for s in range(2):
                        for j, (t0, tn) in enumerate(chunks):
                            n = s * 3 + j
                            act.wait_ge(pair_ready, i * 6 + n + 1)
                            act.activation(e[n % NB][:, 0:tn], ps[n % NB][:, 0, 0:tn], ACT.Exp, scale=-1.0).then_inc(exp_ready, 1)

            @block.vector
            def _(dve):
                dve.sem_inc(pair_used, NB)
                with dve.Fori(0, FT // 2) as i:
                    for s in range(2):
                        for j, (t0, tn) in enumerate(chunks):
                            n = s * 3 + j
                            et, pt = e[n % NB][:, 0:tn], ps[n % NB]
                            dve.wait_ge(exp_ready, i * 6 + n + 1)
                            base = i * 24 + n * 4
                            dve.tensor_scalar(et, et, 1.0, None, ALU.add).then_inc(dve_steps, 1)
                            dve.wait_ge(dve_steps, base + 1)
                            dve.reciprocal(et, et).then_inc(dve_steps, 1)
                            dve.wait_ge(dve_steps, base + 2)
                            dve.tensor_tensor(et, et, pt[:, 0, 0:tn], ALU.mult).then_inc(dve_steps, 1)
                            dve.wait_ge(dve_steps, base + 3)
                            dve.tensor_tensor(hid[:, bass.ds(i * (2 * T) + s * T + t0, tn)], et, pt[:, 1, 0:tn], ALU.mult).then_inc(dve_steps, 1)
                            dve.wait_ge(dve_steps, base + 4)
                            dve.sem_inc(pair_used, 1)


def adaln_mods(nc, A, c, modT, mod_rows):
    with ExitStack() as ctx:
        sb = lambda n, s: ctx.enter_context(nc.sbuf_tensor(f"{n}_{nc.next_id()}", s, F32))
        cond, ex, cT = sb("cond", [MODS, D]), sb("ex", [MODS, D]), sb("cT", [P, KD, MODS])
        ps = ctx.enter_context(nc.psum_tensor("cond_ps", [P, KD, MODS], F32))
        with phase(nc, "loaded", "exp_ready", "dve_steps", "silu_ready", "turned") as (
                block, loaded, exp_ready, dve_steps, silu_ready, turned):
            @block.sync
            def _(sp):
                sp.dma_start(cond[0:1, :], A["c_prompt"]).then_inc(loaded, 16)
                sp.dma_start(cond[1:MODS, :], A["c_sample"]).then_inc(loaded, 16)

            @block.scalar
            def _(act):
                act.wait_ge(loaded, 32)
                act.activation(ex[:], cond[:], ACT.Exp, scale=-1.0).then_inc(exp_ready, 1)

            @block.vector
            def _(dve):
                step = InOrder(dve, dve_steps)
                dve.wait_ge(exp_ready, 1)
                step(dve.tensor_scalar(ex[:], ex[:], 1.0, None, ALU.add))
                step(dve.reciprocal(ex[:], ex[:]))
                dve.tensor_tensor(cond[:], cond[:], ex[:], ALU.mult).then_inc(silu_ready, 1)
                dve.wait_ge(turned, 1)
                dve.tensor_copy(cT[:], ps[:]).then_inc(dve_steps, 1)

            @block.tensor
            def _(pe):
                pe.wait_ge(silu_ready, 1)
                for k in range(KD):
                    last = pe.transpose(ps[:, k, :], cond[:, k * P:(k + 1) * P], c["ident"][0:MODS, 0:MODS])
                last.then_inc(turned, 1)

        for layer in range(2):
            gemm_rows(nc, lambda m, k: cT[:, k, :], [MODS], KD, A["w_ada"][layer],
                      lambda m, cols, l=layer: mod_rows[:, l].rearrange("s n -> s n")[:, cols], 512, 12,
                      bias=A["b_ada"][layer].partition_broadcast(MODS), tag="ada")
        rows = sb("mod_rows_sb", [MODS, 2, 6, D])
        pm = [ctx.enter_context(nc.psum_tensor(f"pm{s}", [P, 2, 4, KD, 4], F32)) for s in range(0)]
        pt = [ctx.enter_context(nc.psum_tensor(f"pmt{l}", [P, 4, KD, MODS], F32)) for l in range(2)]
        with phase(nc, "loaded", "turned", "copied") as (block, loaded, turned, copied):
            @block.sync
            def _(sp):
                sp.dma_start(rows[:], mod_rows.rearrange("s l (c n) -> s l c n", c=6)).then_inc(loaded, 16)

            @block.tensor
            def _(pe):
                pe.wait_ge(loaded, 16)
                for l in range(2):
                    for n, chunk in enumerate((0, 1, 3, 4)):
                        for k in range(KD):
                            last = pe.transpose(pt[l][:, n, k, :], rows[:, l, chunk, k * P:(k + 1) * P],
                                                c["ident"][0:MODS, 0:MODS])
                last.then_inc(turned, 1)

            @block.vector
            def _(dve):
                dve.wait_ge(turned, 1)
                for l in range(2):
                    for n in range(4):
                        dve.tensor_scalar(modT[:, l, n], pt[l][:, n], float(n % 2), None, ALU.add).then_inc(copied, 1)


def ffn(nc, A, c, X, layer, modT, mod_rows, y, out=None):
    with ExitStack() as outer:
        hid = outer.enter_context(nc.sbuf_tensor(f"hid_{nc.next_id()}", [P, FT * T], F32))
        with nc.sbuf_tensor(f"hT_{nc.next_id()}", [P, KD, T], F32) as hT:
            transpose_rows(nc, X, hT, c["ident"], (modT[:, layer, 2], modT[:, layer, 3]))
            swiglu_hidden(nc, hT, hid, A["w_ffn_in"][layer])
        gemm_rows(nc, lambda m, k: hid[:, k * T + m * P:k * T + m * P + ROWS[m]], ROWS, FT, A["w_ffn_out"][layer],
                  lambda m, cols: y[m * P:m * P + ROWS[m], cols], 256, 4, tag="f2")
    post_norm(nc, X, y, mod_rows[:, layer, 5 * D:6 * D], A["ln_g"][layer, 1], A["ln_b"][layer, 1], c, out)


def gla_gates(nc, A, c, proj, log_a):
    W = GH * GK
    with ExitStack() as ctx:
        sb = lambda n, s: ctx.enter_context(nc.sbuf_tensor(f"{n}_{nc.next_id()}", s, F32))
        gk, gkT = sb("gk", [P, TILES, 16]), sb("gkT", [16, T])
        w2, bias = sb("w_gk2", [16, W]), sb("b_gk", [P, W])
        x, e = sb("gate_x", [P, TILES, W]), sb("gate_e", [P, TILES, W])
        pt = [ctx.enter_context(nc.psum_tensor(f"gkt{i}", [16, 512], F32)) for i in range(3)]
        px = [ctx.enter_context(nc.psum_tensor(f"gx{i}", [P, 2, W], F32)) for i in range(5)]
        with phase(nc, "loaded", "turned", "copied", "product", "dve_steps", "abs_ready", "log_ready", "act_steps", "done", "stored") as (
                block, loaded, turned, copied, product, dve_steps, abs_ready, log_ready, act_steps, done, stored):
            @block.sync
            def _(sp):
                g = proj[:, GK_A:GK_A + 16]
                sp.dma_start(gk[:, 0:MT, :], g[0:SEQ].rearrange("(m p) k -> p m k", p=P)).then_inc(loaded, 16)
                sp.dma_start(gk[0:SROWS, MT, :], g[SEQ:T]).then_inc(loaded, 16)
                sp.dma_start(w2[:], A["ab_w_gk2"][0]).then_inc(loaded, 16)
                sp.dma_start(bias[:], A["ab_b_gk"][0].partition_broadcast(P)).then_inc(loaded, 16)
                sp.wait_ge(done, 1)
                sp.dma_start(log_a[0:SEQ].rearrange("(m p) k -> p m k", p=P), x[:, 0:MT, :]).then_inc(stored, 16)
                sp.dma_start(log_a[SEQ:T], x[0:SROWS, MT, :]).then_inc(stored, 16)
                sp.wait_ge(stored, 32)

            @block.tensor
            def _(pe):
                pe.wait_ge(loaded, 64)
                for m in range(TILES):
                    last = pe.transpose(pt[m // 4][:, (m % 4) * P:(m % 4) * P + ROWS[m]], gk[0:ROWS[m], m, :], c["ident"][0:ROWS[m], 0:ROWS[m]])
                last.then_inc(turned, 1)
                pe.wait_ge(copied, 3)
                for m in range(TILES):
                    last = pe.matmul(px[m // 2][0:ROWS[m], m % 2, :], gkT[:, m * P:m * P + ROWS[m]], w2[:], start=True, stop=True)
                last.then_inc(product, 1)

            @block.scalar
            def _(act):
                step = InOrder(act, act_steps)
                act.wait_ge(abs_ready, 1)
                step(act.activation(e[:], e[:], ACT.Exp, scale=-1.0))
                act.activation(e[:], e[:], ACT.Ln, bias=1.0).then_inc(log_ready, 1)

            @block.vector
            def _(dve):
                step = InOrder(dve, dve_steps)
                dve.wait_ge(turned, 1)
                for i in range(3):
                    w = min(512, T - i * 512)
                    dve.tensor_copy(gkT[:, i * 512:i * 512 + w], pt[i][:, 0:w]).then_inc(copied, 1)
                dve.wait_ge(product, 1)
                step(dve.memset(x[:, MT, :], 0.0))
                for m in range(TILES):
                    step(dve.tensor_tensor(x[0:ROWS[m], m, :], px[m // 2][0:ROWS[m], m % 2, :], bias[0:ROWS[m], :], ALU.add))
                dve.scalar_tensor_tensor(e[:], x[:], -1.0, x[:], ALU.mult, ALU.max).then_inc(abs_ready, 1)
                step(dve.tensor_scalar(x[:], x[:], 0.0, None, ALU.min))
                dve.wait_ge(log_ready, 1)
                step(dve.tensor_tensor(x[:], x[:], e[:], ALU.subtract))
                dve.tensor_scalar(x[:], x[:], 1.0 / 16.0, None, ALU.mult).then_inc(done, 1)


def gla_chunk(nc, c, C, gnorm, src, la_src, dst, S, state_in=None, state_out=None):
    W = GH * GK
    V = GH * GV
    with ExitStack() as ctx:
        sb = lambda n, s: ctx.enter_context(nc.sbuf_tensor(f"{n}_{nc.next_id()}", s, F32))
        ps = lambda n, s: banks(ctx, nc, n, s)
        row, la = sb("row", [C, 1536]), sb("la", [C, W])
        e_in, e_mid, e_neg, e_end, e_last = [sb(n, [C, W]) for n in ("e_in", "e_mid", "e_neg", "e_end")] + [sb("e_last", [GK, GH])]
        qs, q2, k2, k4 = [sb(n, [C, W]) for n in ("qs", "q2", "k2", "k4")]
        tr, pT = sb("tr", [GK, 12, C]), sb("pT", [C, GH, C])
        o, sq, er = sb("o", [C, GH, GV]), sb("sq", [C, GH, GV]), sb("er", [C, V])
        ss, eps = sb("ss", [C, GH]), sb("eps", [C, 1])
        pa, pb = ps("pa", [C, 512]), ps("pb", [C, 512])
        pl, pt = pb[:, W:W + GH] if C == GK else ps("pl", [GK, GH]), ps("pt", [GK, 2, 8, CHUNK])[:, :, 0:6, :]
        psc, po, pkv = ps("psc", [C, GH, C]), ps("po", [C, GH, GV]), ps("pkv", [GK, GH, GV])
        tri, tri_mid, tri_end, ones = c["tri"], c["tri_mid"], c["tri_end"], c["ones"]
        with phase(nc, "loaded", "state_loaded", "sums", "exps", "scaled", "turned", "turned_out", "scores", "masked", "products",
                   "o_out", "square", "ln", "stored", "dve_steps", "act_steps") as (
                block, loaded, state_loaded, sums, exps, scaled, turned, turned_out, scores, masked, products, o_out, square,
                ln, stored, dve_steps, act_steps):
            @block.sync
            def _(sp):
                sp.dma_start(la[:], la_src).then_inc(loaded, 16)
                sp.dma_start(row[:], src).then_inc(loaded, 16)
                if state_in is not None:
                    sp.dma_start(S[:], state_in).then_inc(state_loaded, 16)
                sp.wait_ge(o_out, 2)
                sp.dma_start(dst, o[:].rearrange("p h v -> p (h v)")).then_inc(stored, 16)
                if state_out is not None:
                    sp.dma_start(state_out, S[:]).then_inc(stored, 16)
                sp.wait_ge(stored, 16 * (2 if state_out is not None else 1))

            @block.tensor
            def _(pe):
                pe.wait_ge(loaded, 32)
                pe.matmul(pa[:, 0:W], tri[0:C, 0:C], la[:], start=True, stop=True)
                pe.matmul(pa[:, W:2 * W], tri_mid[0:C, 0:C], la[:], start=True, stop=True)
                pe.matmul(pb[:, 0:W], tri_end[0:C, 0:C], la[:], start=True, stop=True)
                for h in range(GH):
                    last = pe.matmul(pl[:, h:h + 1], la[:, h * GK:(h + 1) * GK], ones[0:C, 0:1], start=True, stop=True)
                last.then_inc(sums, 1)
                pe.wait_ge(scaled, 3)
                for n, x in enumerate((qs, q2, k2)):
                    for h in range(GH):
                        last = pe.transpose(pt[:, (4 * n + h) // 6, (4 * n + h) % 6, 0:C], x[:, h * GK:(h + 1) * GK], c["ident"][0:C, 0:C])
                last.then_inc(turned, 1)
                pe.wait_ge(turned_out, 1)
                for h in range(GH):
                    last = pe.matmul(psc[:, h, :], tr[:, 8 + h, :], tr[:, 4 + h, :], start=True, stop=True)
                last.then_inc(scores, 1)
                if state_in is not None:
                    pe.wait_ge(state_loaded, 16)
                pe.wait_ge(scaled, 4)
                pe.wait_ge(masked, 1)
                for h in range(GH):
                    v = row[:, 512 + h * GV:512 + (h + 1) * GV]
                    pe.matmul(po[:, h, :], tr[:, h, :], S[:, h, :], start=True, stop=False)
                    pe.matmul(po[:, h, :], pT[:, h, :], v, start=False, stop=True)
                    last = pe.matmul(pkv[:, h, :], k4[:, h * GK:(h + 1) * GK], v, start=True, stop=True)
                last.then_inc(products, 1)

            @block.scalar
            def _(act):
                step = InOrder(act, act_steps)
                act.wait_ge(sums, 1)
                act.activation(e_in[:], pa[:, 0:W], ACT.Exp).then_inc(exps, 1)
                act.activation(e_mid[:], pa[:, W:2 * W], ACT.Exp).then_inc(exps, 1)
                act.activation(e_neg[:], pa[:, W:2 * W], ACT.Exp, scale=-1.0).then_inc(exps, 1)
                act.activation(e_end[:], pb[:, 0:W], ACT.Exp).then_inc(exps, 1)
                act.activation(e_last[:], pl, ACT.Exp).then_inc(exps, 1)
                act.activation(er[:], row[:, R_A:R_A + V], ACT.Exp, scale=-1.0).then_inc(exps, 1)
                act.wait_ge(square, 1)
                step(act.activation(ss[:], ss[:], ACT.Ln, scale=1.0 / GV, bias=eps[:, 0:1]))
                act.activation(ss[:], ss[:], ACT.Exp, scale=-0.5).then_inc(ln, 1)

            @block.vector
            def _(dve):
                step = InOrder(dve, dve_steps)
                step(dve.memset(eps[:], RMS_EPS))
                dve.wait_ge(exps, 1)
                dve.scalar_tensor_tensor(qs[:], e_in[:], GK ** -0.5, row[:, Q_A:Q_A + W], ALU.mult, ALU.mult).then_inc(scaled, 1)
                dve.wait_ge(exps, 3)
                dve.scalar_tensor_tensor(q2[:], e_mid[:], GK ** -0.5, row[:, Q_A:Q_A + W], ALU.mult, ALU.mult).then_inc(scaled, 1)
                dve.tensor_tensor(k2[:], e_neg[:], row[:, K_A:K_A + W], ALU.mult).then_inc(scaled, 1)
                dve.wait_ge(exps, 4)
                dve.tensor_tensor(k4[:], e_end[:], row[:, K_A:K_A + W], ALU.mult).then_inc(scaled, 1)
                dve.wait_ge(turned, 1)
                dve.tensor_copy(tr[:].rearrange("p (a b) i -> p a b i", a=2), pt[:, :, :, 0:C]).then_inc(turned_out, 1)
                dve.wait_ge(exps, 6)
                step(dve.tensor_scalar(er[:], er[:], 1.0, None, ALU.add))
                step(dve.reciprocal(er[:], er[:]))
                step(dve.tensor_tensor(er[:], er[:], row[:, R_A:R_A + V], ALU.mult))
                step(dve.tensor_tensor(er[:].rearrange("p (h v) -> p h v", h=GH), er[:].rearrange("p (h v) -> p h v", h=GH),
                                       gnorm[0:C, :].unsqueeze(1).broadcast_to([C, GH, GV]), ALU.mult))
                dve.wait_ge(scores, 1)
                dve.tensor_tensor(pT[:], psc[:], tri[0:C, 0:C].unsqueeze(1).broadcast_to([C, GH, C]), ALU.mult).then_inc(masked, 1)
                dve.wait_ge(products, 1)
                step(dve.tensor_tensor(S[:], S[:], e_last[:].unsqueeze(2).broadcast_to([GK, GH, GV]), ALU.mult))
                step(dve.tensor_tensor(S[:], S[:], pkv, ALU.add))
                dve.sem_inc(o_out, 1)
                step(dve.tensor_copy(o[:], po[:]))
                step(dve.tensor_tensor(sq[:], o[:], o[:], ALU.mult))
                dve.tensor_reduce(ss[:], sq[:], AX, ALU.add).then_inc(square, 1)
                dve.wait_ge(ln, 1)
                step(dve.tensor_tensor(o[:], o[:], ss[:].unsqueeze(2).broadcast_to([C, GH, GV]), ALU.mult))
                dve.tensor_tensor(o[:].rearrange("p h v -> p (h v)"), o[:].rearrange("p h v -> p (h v)"), er[:], ALU.mult).then_inc(o_out, 1)


def gla(nc, A, O, c, proj, log_a, mixed):
    with ExitStack() as ctx:
        S = ctx.enter_context(nc.sbuf_tensor("gla_state", [GK, GH, GV], F32))
        gnorm = ctx.enter_context(nc.sbuf_tensor("gla_norm", [CHUNK, GV], F32))
        load_all(nc, [(gnorm[:], A["ab_gla_norm"][0].partition_broadcast(CHUNK))])
        with phase(nc, "cleared") as (block, cleared):
            @block.vector
            def _(dve):
                dve.memset(S[:], 0.0).then_inc(cleared, 1)
        with nc.Fori(0, SEQ // CHUNK) as i:
            rows = bass.ds(i * CHUNK, CHUNK)
            gla_chunk(nc, c, CHUNK, gnorm, proj[rows, 0:1536], log_a[rows, :], mixed[rows, 0:512], S)
        with phase(nc, "stored") as (block, stored):
            @block.sync
            def _(sp):
                sp.dma_start(O["p_gla"][0, 0].rearrange("h k v -> k h v"), S[:]).then_inc(stored, 16)
                sp.wait_ge(stored, 16)
        with nc.Fori(0, NS) as i:
            rows = bass.ds(i * TS + SEQ, TS)
            gla_chunk(nc, c, TS, gnorm, proj[rows, 0:1536], log_a[rows, :], mixed[rows, 0:512], S,
                      state_in=A["state_gla"][0, bass.ds(i, 1)].rearrange("b h k v -> k (b h) v"),
                      state_out=O["s_gla"][0, bass.ds(i, 1)].rearrange("b h k v -> k (b h) v"))


def project_in(nc, A, hT, proj):
    gemm_rows(nc, lambda m, k: hT[:, k, m * P:m * P + ROWS[m]], ROWS, KD, A["ab_w_in"][0],
              lambda m, cols: proj[m * P:m * P + ROWS[m], cols], 476, 6, tag="ab")


def conv_tile(nc, r, cw, eps, taps, dst):
    QK = 2 * DH
    with ExitStack() as ctx:
        sb = lambda n, s: ctx.enter_context(nc.sbuf_tensor(f"{n}_{nc.next_id()}", s, F32))
        x = [sb(f"tap{j}", [r, NCH]) for j in range(4)]
        sq, ss = sb("sq", [r, D]), sb("ss", [r, QK])
        with phase(nc, "l0", "l1", "l2", "l3", "loaded3", "pool_steps", "pool_done", "act_steps", "silu_done", "dve_steps", "conv_done", "sums_done",
                   "ln_done", "done", "stored") as (block, l0, l1, l2, l3, loaded3, pool_steps, pool_done, act_steps, silu_done, dve_steps, conv_done,
                                          sums_done, ln_done, done, stored):
            tap_loaded = [l0, l1, l2, l3]

            @block.sync
            def _(sp):
                for j in range(4):
                    sp.dma_start(x[j][:], taps[j]).then_inc(tap_loaded[j], 16)
                for n in range(3):
                    if n < 2:
                        sp.wait_ge(done, n + 1)
                    else:
                        sp.wait_ge(silu_done, 3)
                    sp.dma_start(dst[:, n * D:(n + 1) * D], x[0][:, n * D:(n + 1) * D]).then_inc(stored, 16)
                sp.wait_ge(stored, 48)

            @block.gpsimd
            def _(pool):
                for j in (3, 2):
                    pool.wait_ge(tap_loaded[j], 16)
                    pool.tensor_tensor(x[j][:], x[j][:], cw[0:r, j, :], ALU.mult).then_inc(pool_done, 1)

            @block.vector
            def _(dve):
                step = InOrder(dve, dve_steps)
                for j in (0, 1):
                    dve.wait_ge(tap_loaded[j], 16)
                    step(dve.tensor_tensor(x[j][:], x[j][:], cw[0:r, j, :], ALU.mult))
                step(dve.tensor_tensor(x[0][:], x[0][:], x[1][:], ALU.add))
                for j in (3, 2):
                    dve.wait_ge(pool_done, 4 - j)
                    step(dve.tensor_tensor(x[0][:], x[0][:], x[j][:], ALU.add))
                dve.sem_inc(conv_done, 1)
                for n in range(2):
                    dve.wait_ge(silu_done, n + 1)
                    step(dve.tensor_tensor(sq[:], x[0][:, n * D:(n + 1) * D], x[0][:, n * D:(n + 1) * D], ALU.mult))
                    step(dve.tensor_reduce(ss[:, n * DH:(n + 1) * DH], sq[:].rearrange("p (h k) -> p h k", h=DH), AX, ALU.add))
                dve.sem_inc(sums_done, 1)
                dve.wait_ge(ln_done, 1)
                for n in range(2):
                    v = x[0][:, n * D:(n + 1) * D].rearrange("p (h k) -> p h k", h=DH)
                    s = ss[:, n * DH:(n + 1) * DH].unsqueeze(2).broadcast_to([r, DH, P])
                    if n == 0:
                        step(dve.tensor_scalar(ss[:, 0:DH], ss[:, 0:DH], P ** -0.5, None, ALU.mult))
                    dve.tensor_tensor(v, v, s, ALU.mult).then_inc(done, 1)

            @block.scalar
            def _(act):
                step = InOrder(act, act_steps)
                act.wait_ge(conv_done, 1)
                for n in range(3):
                    act.activation(x[0][:, n * D:(n + 1) * D], x[0][:, n * D:(n + 1) * D], ACT.Silu).then_inc(silu_done, 1)
                act.wait_ge(sums_done, 1)
                step(act.activation(ss[:], ss[:], ACT.Ln, bias=eps[0:r, 0:1]))
                act.activation(ss[:], ss[:], ACT.Exp, scale=-0.5).then_inc(ln_done, 1)


def gdn_gates(nc, A, ba, gb):
    with ExitStack() as ctx:
        sb = lambda n, s: ctx.enter_context(nc.sbuf_tensor(f"{n}_{nc.next_id()}", s, F32))
        x, e, y = sb("ba", [P, TILES, 2, DH]), sb("ba_e", [P, TILES, 2, DH]), sb("gb", [P, TILES, 2, DH])
        al, dt = sb("a_log", [P, DH]), sb("dt_bias", [P, DH])
        with phase(nc, "zeroed", "loaded", "dve_steps", "abs_ready", "exp_ready", "act_steps", "ln_ready", "done", "stored") as (
                block, zeroed, loaded, dve_steps, abs_ready, exp_ready, act_steps, ln_ready, done, stored):
            @block.sync
            def _(sp):
                sp.wait_ge(zeroed, 1)
                sp.dma_start(x[:, 0:MT], ba[0:SEQ].rearrange("(m p) (c h) -> p m c h", p=P, c=2)).then_inc(loaded, 16)
                sp.dma_start(x[0:SROWS, MT], ba[SEQ:T].rearrange("p (c h) -> p c h", c=2)).then_inc(loaded, 16)
                sp.dma_start(al[:], A["c_a_log"][0].partition_broadcast(P)).then_inc(loaded, 16)
                sp.dma_start(dt[:], A["c_dt_bias"][0].partition_broadcast(P)).then_inc(loaded, 16)
                sp.wait_ge(done, 1)
                sp.dma_start(gb[0:SEQ].rearrange("(m p) (c h) -> p m c h", p=P, c=2), y[:, 0:MT]).then_inc(stored, 16)
                sp.dma_start(gb[SEQ:T].rearrange("p (c h) -> p c h", c=2), y[0:SROWS, MT]).then_inc(stored, 16)
                sp.wait_ge(stored, 32)

            @block.vector
            def _(dve):
                step = InOrder(dve, dve_steps)
                dve.memset(x[:], 0.0).then_inc(zeroed, 1)
                dve.wait_ge(loaded, 64)
                b, a = x[:, :, 0, :], x[:, :, 1, :]
                step(dve.tensor_tensor(a, a, dt[:].unsqueeze(1).broadcast_to([P, TILES, DH]), ALU.add))
                step(dve.scalar_tensor_tensor(e[:, :, 1, :], a, -1.0, a, ALU.mult, ALU.min))
                dve.tensor_scalar(e[:, :, 0, :], b, -1.0, None, ALU.mult).then_inc(abs_ready, 1)
                dve.wait_ge(exp_ready, 2)
                step(dve.tensor_scalar(e[:, :, 0, :], e[:, :, 0, :], 1.0, None, ALU.add))
                step(dve.reciprocal(y[:, :, 1, :], e[:, :, 0, :]))
                dve.wait_ge(ln_ready, 1)
                step(dve.scalar_tensor_tensor(y[:, :, 0, :], a, 0.0, e[:, :, 1, :], ALU.max, ALU.add))
                step(dve.tensor_scalar(y[:, :, 0, :], y[:, :, 0, :], -1.0, None, ALU.mult))
                dve.tensor_tensor(y[:, :, 0, :], y[:, :, 0, :], al[:].unsqueeze(1).broadcast_to([P, TILES, DH]), ALU.mult).then_inc(done, 1)

            @block.scalar
            def _(act):
                step = InOrder(act, act_steps)
                act.wait_ge(loaded, 64)
                act.activation(al[:], al[:], ACT.Exp).then_inc(exp_ready, 1)
                act.wait_ge(abs_ready, 1)
                act.activation(e[:], e[:], ACT.Exp).then_inc(exp_ready, 1)
                act.wait_ge(exp_ready, 2)
                act.activation(e[:, :, 1, :], e[:, :, 1, :], ACT.Ln, bias=1.0).then_inc(ln_ready, 1)


def gdn_chunk(nc, c, C, cnorm, qkv_src, z_src, gb_src, dst, S, state_in=None, state_out=None):
    doublings = {64: 5, 8: 2}[C]
    HC = [C, DH, C]
    with ExitStack() as ctx:
        sb = lambda n, s: ctx.enter_context(nc.sbuf_tensor(f"{n}_{nc.next_id()}", s, F32))
        row, z, gb = sb("qkv", [C, 3, DH, P]), sb("z", [C, DH, P]), sb("gbc", [C, 2, DH])
        gm, bm = sb("gm", HC), sb("bm", HC)
        E, bs, MTr, M, Z, PT = sb("E", HC), sb("bs", HC), sb("MT", HC), sb("M", HC), sb("ZT", HC), sb("PT", HC)
        ed, eend, elast, bd = sb("ed", [C, DH]), sb("eend", [C, DH]), sb("elast", [P, DH]), sb("bd", [C, DH])
        kT, qT, wT = sb("kT", [P, DH, C]), sb("qT", [P, DH, C]), sb("wT", [P, DH, C])
        vb, kbd, kl, vn, o = [sb(n, [C, DH, P]) for n in ("vb", "kbd", "kl", "vn", "o")]
        ss, eps = sb("ss", [C, DH]), sb("eps", [C, 1])
        b0, b1, b2 = [banks(ctx, nc, n, [P, 1024]) for n in ("b0", "b1", "b2")]
        b3, b4 = banks(ctx, nc, "b3", [P, 512]), banks(ctx, nc, "b4", [P, 512])
        tri, strict, ones = c["tri"][0:C, 0:C], c["tri_end"][0:C, 0:C], c["ones"]
        sq = lambda b: b[0:C, 0:DH * C].rearrange("p (h i) -> p h i", h=DH)
        wide = lambda b, r=C: b[0:r, 0:1024].rearrange("p (h v) -> p h v", h=DH)
        two = lambda b: b[:, 0:1024].rearrange("p (h i) -> p h i", h=DH)
        with phase(nc, "loaded", "state_loaded", "gm_ready", "sums", "exps", "turned", "turned_out", "kk", "at_ready", "a_turned",
                   "squared", "m_out", "mt_out", "z_out", "wt_ready", "wt_out", "rhs_ready", "vn_ready", "vn_out", "o_ready", "s_ready",
                   "done", "sum_ready", "ln_ready", "stored", "dve_steps", "act_steps") as (
                block, loaded, state_loaded, gm_ready, sums, exps, turned, turned_out, kk, at_ready, a_turned,
                squared, m_out, mt_out, z_out, wt_ready, wt_out, rhs_ready, vn_ready, vn_out, o_ready, s_ready,
                done, sum_ready, ln_ready, stored, dve_steps, act_steps):
            @block.sync
            def _(sp):
                sp.dma_start(gb[:], gb_src).then_inc(loaded, 16)
                sp.dma_start(row[:], qkv_src).then_inc(loaded, 16)
                sp.dma_start(z[:], z_src).then_inc(loaded, 16)
                if state_in is not None:
                    sp.dma_start(S[:], state_in).then_inc(state_loaded, 16)
                sp.wait_ge(done, 2)
                sp.dma_start(dst, o[:]).then_inc(stored, 16)
                if state_out is not None:
                    sp.dma_start(state_out, S[:]).then_inc(stored, 16)
                sp.wait_ge(stored, 16 * (2 if state_out is not None else 1))

            @block.tensor
            def _(pe):
                pe.wait_ge(loaded, 48)
                for h in range(DH):
                    pe.transpose(b0[:, h * C:(h + 1) * C], row[:, 0, h, :], c["ident"][0:C, 0:C])
                for h in range(DH):
                    last = pe.transpose(b0[:, 512 + h * C:512 + (h + 1) * C], row[:, 1, h, :], c["ident"][0:C, 0:C])
                last.then_inc(turned, 1)
                pe.wait_ge(gm_ready, 2)
                pe.matmul(sq(b1), strict, gm[:], start=True, stop=True)
                pe.matmul(b1[0:C, 512:512 + DH * C], strict, bm[:], start=True, stop=True)
                pe.matmul(b3[0:C, 0:DH], tri, gb[:, 0, :], start=True, stop=True)
                pe.matmul(b3[0:C, DH:2 * DH], strict, gb[:, 0, :], start=True, stop=True)
                pe.matmul(b3[:, 2 * DH:3 * DH], ones[0:C, :], gb[:, 0, :], start=True, stop=True).then_inc(sums, 1)
                pe.wait_ge(turned_out, 2)
                for h in range(DH):
                    pe.matmul(sq(b2)[:, h, :], kT[:, h, :], kT[:, h, :], start=True, stop=True)
                for h in range(DH):
                    last = pe.matmul(b2[0:C, 512 + h * C:512 + (h + 1) * C], kT[:, h, :], qT[:, h, :], start=True, stop=True)
                last.then_inc(kk, 1)
                pe.wait_ge(at_ready, 1)
                for h in range(DH):
                    last = pe.transpose(sq(b4)[:, h, :], MTr[:, h, :], c["ident"][0:C, 0:C])
                last.then_inc(a_turned, 1)
                for s in range(doublings):
                    pe.wait_ge(m_out, s + 1)
                    if s:
                        pe.wait_ge(mt_out, s)
                        pe.wait_ge(z_out, s)
                    for h in range(DH):
                        pe.matmul(sq(b3)[:, h, :], MTr[:, h, :], M[:, h, :], start=True, stop=True)
                    for h in range(DH):
                        last = pe.matmul(sq(b4)[:, h, :], M[:, h, :], MTr[:, h, :], start=True, stop=True)
                    last.then_inc(squared, 1)
                    pe.wait_ge(m_out, s + 2)
                    for h in range(DH):
                        last = pe.matmul(sq(b0)[:, h, :], M[:, h, :], Z[:, h, :], start=True, stop=True)
                    last.then_inc(squared, 1)
                pe.wait_ge(z_out, doublings)
                pe.wait_ge(rhs_ready, 3)
                for h in range(DH):
                    last = pe.matmul(b3[:, h * C:(h + 1) * C], kbd[:, h, :], Z[:, h, :], start=True, stop=True)
                last.then_inc(wt_ready, 1)
                pe.wait_ge(wt_out, 1)
                if state_in is not None:
                    pe.wait_ge(state_loaded, 16)
                for h in range(DH):
                    pe.matmul(wide(b1)[:, h, :], Z[:, h, :], vb[:, h, :], start=True, stop=False)
                    last = pe.matmul(wide(b1)[:, h, :], wT[:, h, :], S[:, h, :], start=False, stop=True)
                last.then_inc(vn_ready, 1)
                for h in range(DH):
                    last = pe.matmul(wide(b2)[:, h, :], qT[:, h, :], S[:, h, :], start=True, stop=True)
                last.then_inc(o_ready, 1)
                pe.wait_ge(vn_out, 1)
                for h in range(DH):
                    last = pe.matmul(two(b0)[:, h, :], kl[:, h, :], vn[:, h, :], start=True, stop=True)
                last.then_inc(s_ready, 1)
                for h in range(DH):
                    last = pe.matmul(wide(b1)[:, h, :], PT[:, h, :], vn[:, h, :], start=True, stop=True)
                last.then_inc(o_ready, 1)

            @block.scalar
            def _(act):
                step = InOrder(act, act_steps)
                act.wait_ge(turned, 1)
                act.copy(qT[:], b0[:, 0:DH * C].rearrange("p (h i) -> p h i", h=DH)).then_inc(turned_out, 1)
                act.copy(kT[:], b0[:, 512:512 + DH * C].rearrange("p (h i) -> p h i", h=DH)).then_inc(turned_out, 1)
                act.wait_ge(sums, 1)
                act.activation(E[:], sq(b1), ACT.Exp).then_inc(exps, 1)
                act.copy(bs[:], b1[0:C, 512:512 + DH * C].rearrange("p (h i) -> p h i", h=DH)).then_inc(exps, 1)
                act.activation(ed[:], b3[0:C, 0:DH], ACT.Exp).then_inc(exps, 1)
                act.activation(eend[:], b3[0:C, DH:2 * DH], ACT.Exp).then_inc(exps, 1)
                act.activation(elast[:], b3[:, 2 * DH:3 * DH], ACT.Exp).then_inc(exps, 1)
                act.wait_ge(a_turned, 1)
                act.copy(M[:], sq(b4)).then_inc(m_out, 1)
                for s in range(doublings):
                    act.wait_ge(squared, 2 * s + 1)
                    if s == 0:
                        act.wait_ge(rhs_ready, 1)
                    act.copy(M[:], sq(b3)).then_inc(m_out, 1)
                    if s < doublings - 1:
                        act.copy(MTr[:], sq(b4)).then_inc(mt_out, 1)
                act.wait_ge(wt_ready, 1)
                act.copy(wT[:], b3[:, 0:DH * C].rearrange("p (h i) -> p h i", h=DH)).then_inc(wt_out, 1)
                act.wait_ge(vn_ready, 1)
                act.copy(vn[:], wide(b1)).then_inc(vn_out, 1)
                act.wait_ge(sum_ready, 1)
                step(act.activation(ss[:], ss[:], ACT.Ln, scale=1.0 / P, bias=eps[:, 0:1]))
                act.activation(ss[:], ss[:], ACT.Exp, scale=-0.5).then_inc(ln_ready, 1)
                act.activation(z[:], z[:], ACT.Silu).then_inc(ln_ready, 1)

            @block.vector
            def _(dve):
                step = InOrder(dve, dve_steps)
                step(dve.memset(eps[:], RMS_EPS))
                dve.wait_ge(loaded, 48)
                g, beta = gb[:, 0, :], gb[:, 1, :]
                over_i = lambda x: x.unsqueeze(2).broadcast_to(HC)
                over_v = lambda x, r=C: x.unsqueeze(2).broadcast_to([r, DH, P])
                over_h = lambda x: x.unsqueeze(1).broadcast_to(HC)
                dve.tensor_tensor(gm[:], over_i(g), over_h(tri), ALU.mult).then_inc(gm_ready, 1)
                dve.tensor_tensor(bm[:], over_i(beta), over_h(c["ident"][0:C, 0:C]), ALU.mult).then_inc(gm_ready, 1)
                step(dve.tensor_tensor(vb[:], row[:, 2], over_v(beta), ALU.mult))
                dve.wait_ge(exps, 5)
                step(dve.tensor_tensor(E[:], E[:], over_h(tri), ALU.mult))
                dve.wait_ge(kk, 1)
                step(dve.tensor_tensor(MTr[:], sq(b2), E[:], ALU.mult))
                dve.tensor_tensor(MTr[:], MTr[:], bs[:], ALU.mult).then_inc(at_ready, 1)
                dve.wait_ge(at_ready, 1)
                dve.tensor_tensor(Z[:], over_h(c["ident"][0:C, 0:C]), MTr[:], ALU.subtract).then_inc(rhs_ready, 1)
                step(dve.tensor_tensor(PT[:], b2[0:C, 512:512 + DH * C].rearrange("p (h i) -> p h i", h=DH), E[:], ALU.mult))
                step(dve.scalar_tensor_tensor(bd[:], ed[:], -1.0, beta, ALU.mult, ALU.mult))
                dve.tensor_tensor(kbd[:], row[:, 1], over_v(bd[:]), ALU.mult).then_inc(rhs_ready, 1)
                dve.tensor_tensor(kl[:], row[:, 1], over_v(eend[:]), ALU.mult).then_inc(rhs_ready, 1)
                dve.wait_ge(rhs_ready, 1)
                for s in range(doublings):
                    dve.wait_ge(squared, 2 * s + 2)
                    dve.tensor_tensor(Z[:], Z[:], sq(b0), ALU.add).then_inc(z_out, 1)
                    dve.wait_ge(z_out, s + 1)
                dve.wait_ge(o_ready, 1)
                step(dve.tensor_tensor(o[:], wide(b2), over_v(ed[:]), ALU.mult))
                step(dve.tensor_tensor(S[:], S[:], over_v(elast[:], P), ALU.mult))
                dve.wait_ge(s_ready, 1)
                dve.tensor_tensor(S[:], S[:], two(b0), ALU.add).then_inc(done, 1)
                dve.wait_ge(o_ready, 2)
                step(dve.tensor_tensor(o[:], o[:], wide(b1), ALU.add))
                step(dve.tensor_tensor(vb[:], o[:], o[:], ALU.mult))
                dve.tensor_reduce(ss[:], vb[:], AX, ALU.add).then_inc(sum_ready, 1)
                dve.wait_ge(ln_ready, 2)
                step(dve.tensor_tensor(o[:], o[:], over_v(ss[:]), ALU.mult))
                step(dve.tensor_tensor(z[:], z[:], cnorm[0:C, :].unsqueeze(1).broadcast_to([C, DH, P]), ALU.mult))
                dve.tensor_tensor(o[:], o[:], z[:], ALU.mult).then_inc(done, 1)


def gdn(nc, A, O, c, xp, xs, z, ba, qkv, gb, mixed):
    with ExitStack() as ctx:
        sb = lambda n, s: ctx.enter_context(nc.sbuf_tensor(f"{n}_{nc.next_id()}", s, F32))
        with phase(nc, "stored") as (block, stored):
            @block.sync
            def _(sp):
                sp.dma_start(O["p_conv"][0, 0], xp[SEQ:SEQ + 3]).then_inc(stored, 16)
                sp.dma_start(O["s_conv"][0], xs[:, TS:TS + 3]).then_inc(stored, 16)
                sp.wait_ge(stored, 32)
        with ExitStack() as inner:
            cw = inner.enter_context(nc.sbuf_tensor("conv_w", [P, 4, NCH], F32))
            eps = inner.enter_context(nc.sbuf_tensor("l2_eps", [P, 1], F32))
            load_all(nc, [(cw[:], A["c_conv_w"][0].partition_broadcast(P))])
            with phase(nc, "filled") as (block, filled):
                @block.vector
                def _(dve):
                    dve.memset(eps[:], L2_EPS).then_inc(filled, 1)
            with nc.Fori(0, MT) as i:
                conv_tile(nc, P, cw, eps, [xp[bass.ds(i * P + j, P)] for j in range(4)], qkv[bass.ds(i * P, P)])
            conv_tile(nc, SROWS, cw, eps, [xs[:, j:j + TS] for j in range(4)], qkv[SEQ:T])
        gdn_gates(nc, A, ba, gb)
        S, cnorm = sb("gdn_state", [P, DH, P]), sb("c_norm", [CHUNK, P])
        load_all(nc, [(cnorm[:], A["c_norm"][0].partition_broadcast(CHUNK))])
        with phase(nc, "cleared") as (block, cleared):
            @block.vector
            def _(dve):
                dve.memset(S[:], 0.0).then_inc(cleared, 1)

        def sources(rows):
            return (qkv[rows].rearrange("t (n h k) -> t n h k", n=3, h=DH), z[rows].rearrange("t (h k) -> t h k", h=DH),
                    gb[rows].rearrange("t (n h) -> t n h", n=2), mixed[rows].rearrange("t (h k) -> t h k", h=DH))
        with nc.Fori(0, SEQ // CHUNK) as i:
            gdn_chunk(nc, c, CHUNK, cnorm, *sources(bass.ds(i * CHUNK, CHUNK)), S)
        with phase(nc, "stored") as (block, stored):
            @block.sync
            def _(sp):
                sp.dma_start(O["p_gdn"][0, 0].rearrange("h k v -> k h v"), S[:]).then_inc(stored, 16)
                sp.wait_ge(stored, 16)
        with nc.Fori(0, NS) as i:
            gdn_chunk(nc, c, TS, cnorm, *sources(bass.ds(i * TS + SEQ, TS)), S,
                      state_in=A["state_gdn"][0, bass.ds(i, 1)].rearrange("b h k v -> k (b h) v"),
                      state_out=O["s_gdn"][0, bass.ds(i, 1)].rearrange("b h k v -> k (b h) v"))


def cache_rows(nc, A, O, proj):
    pairs = []
    for name, col in (("cmp_k", K_CMP), ("cmp_v", V_CMP), ("sel_k", K_SEL), ("sel_v", V_SEL)):
        pairs.append((O["p_" + name][0, 0].rearrange("t g d -> t (g d)"), proj[0:SEQ, col:col + P]))
        pairs.append((O["s_" + name][0].rearrange("b t g d -> (b t) (g d)"), proj[SEQ:T, col:col + P]))
    for name, col in (("win_k", K_WIN), ("win_v", V_WIN)):
        pairs.append((O["p_" + name][0, 0].rearrange("t g d -> t (g d)"), proj[SEQ - WIN:SEQ, col:col + P]))
        flat = O["s_" + name][0].rearrange("b t g d -> b t (g d)")
        pairs.append((flat[:, 0:WIN - TS], A["state_" + name][0, :, TS:WIN].rearrange("b t g d -> b t (g d)")))
        pairs.append((flat[:, WIN - TS:WIN], proj[SEQ:T, col:col + P].rearrange("(b t) c -> b t c", t=TS)))
    with phase(nc, "stored_sp", "stored_act") as (block, stored_sp, stored_act):
        @block.sync
        def _(sp):
            for dst, src in pairs[::2]:
                sp.dma_start(dst, src).then_inc(stored_sp, 16)
            sp.wait_ge(stored_sp, 16 * len(pairs[::2]))

        @block.scalar
        def _(act):
            for dst, src in pairs[1::2]:
                act.dma_start(dst, src).then_inc(stored_act, 16)
            act.wait_ge(stored_act, 16 * len(pairs[1::2]))


def turn_queries(nc, c, proj, qk_turned):
    with ExitStack() as ctx:
        rows = ctx.enter_context(nc.sbuf_tensor("qk_rows", [P, MT, D], F32))
        qkT = ctx.enter_context(nc.sbuf_tensor("qkT", [P, KD, SEQ], F32))
        tok = lambda col, n: proj[0:SEQ, col:col + n].rearrange("(m p) c -> p m c", p=P)
        loads = [(rows[:, :, 0:512], tok(Q_B, 512))]
        for j, col in enumerate((K_SEL, K_SEL + HD, K_WIN, K_WIN + HD)):
            for half in range(2):
                at = 512 + j * P + half * HD
                loads.append((rows[:, :, at:at + HD], tok(col, HD)))
        transpose_rows(nc, rows, qkT, c["ident"], tiles=MT, loads=loads)
        with phase(nc, "stored") as (block, stored):
            @block.sync
            def _(sp):
                sp.dma_start(qk_turned.rearrange("n p t -> p n t"), qkT[:]).then_inc(stored, 16)
                sp.wait_ge(stored, 16)


def turn_sample(nc, c, proj, q_diag, k_new):
    with ExitStack() as ctx:
        sb = lambda n, s: ctx.enter_context(nc.sbuf_tensor(f"{n}_{nc.next_id()}", s, F32))
        rows, kn = sb("s_rows", [SROWS, 6, P]), sb("k_new_sb", [P, 2, SROWS])
        qd = sb("q_diag_sb", [P, NS, 2, 4, TS])
        pt = [banks(ctx, nc, f"qs{i}", [P, 4, SROWS]) for i in range(2)]
        with phase(nc, "loaded", "turned", "zeroed", "copied", "stored") as (block, loaded, turned, zeroed, copied, stored):
            @block.sync
            def _(sp):
                q = proj[SEQ:T, Q_B:Q_B + 512].rearrange("r (g h d) -> r g h d", g=2, h=4)
                for g in range(2):
                    sp.dma_start(rows[:, 0:4, g * HD:(g + 1) * HD], q[:, g]).then_inc(loaded, 16)
                sp.dma_start(rows[:, 4, :], proj[SEQ:T, K_SEL:K_SEL + P]).then_inc(loaded, 16)
                sp.dma_start(rows[:, 5, :], proj[SEQ:T, K_WIN:K_WIN + P]).then_inc(loaded, 16)
                sp.wait_ge(copied, 9)
                sp.dma_start(q_diag.rearrange("b p c -> p b c"), qd[:].rearrange("p b g h t -> p b (g h t)")).then_inc(stored, 16)
                for n in range(2):
                    sp.dma_start(k_new[n].rearrange("b p t -> p b t"), kn[:, n].rearrange("p (b t) -> p b t", t=TS)).then_inc(stored, 16)
                sp.wait_ge(stored, 48)

            @block.tensor
            def _(pe):
                pe.wait_ge(loaded, 64)
                for n in range(6):
                    last = pe.transpose(pt[n // 4][:, n % 4, :], rows[:, n, :], c["ident"][0:SROWS, 0:SROWS])
                last.then_inc(turned, 1)

            @block.vector
            def _(dve):
                dve.memset(qd[:], 0.0).then_inc(zeroed, 1)
                dve.wait_ge(zeroed, 1)
                dve.wait_ge(turned, 1)
                for g in range(2):
                    lo = g * HD
                    for h in range(4):
                        dve.tensor_copy(qd[lo:lo + HD, :, g, h, :],
                                        pt[0][lo:lo + HD, h, :].rearrange("p (b t) -> p b t", t=TS)).then_inc(copied, 1)
                dve.tensor_copy(kn[:], pt[1][:, 0:2, :]).then_inc(copied, 1)


def compress_weights(nc, A, W1, W2, pe_bias):
    with ExitStack() as ctx:
        pe_sb = ctx.enter_context(nc.sbuf_tensor("cmp_pe_sb", [BLK, 2, HD], F32))
        pb = [banks(ctx, nc, f"pe{n}", [P, 1]) for n in range(2)]
        with phase(nc, "loaded", "summed", "copied") as (block, loaded, summed, copied):
            @block.sync
            def _(sp):
                for n in range(2):
                    for half in range(2):
                        sp.dma_start(W1[n][half * 64:half * 64 + 64],
                                     A["ab_cmp_w1"][0, n].rearrange("(t d) h -> t d h", d=HD)).then_inc(loaded, 16)
                    sp.dma_start(W2[n][:], A["ab_cmp_w2"][0, n]).then_inc(loaded, 16)
                    sp.dma_start(pe_sb[:, n, :], A["ab_cmp_pe"][0, n]).then_inc(loaded, 16)

            @block.tensor
            def _(pe):
                pe.wait_ge(loaded, 16 * 8)
                for n in range(2):
                    for d in range(HD):
                        last = pe.matmul(pb[n], W1[n][0:64, d, :], pe_sb[:, n, d:d + 1], start=(d == 0), stop=(d == HD - 1))
                    last.then_inc(summed, 1)

            @block.vector
            def _(dve):
                for n in range(2):
                    dve.wait_ge(summed, n + 1)
                    dve.tensor_copy(pe_bias[n][:], pb[n]).then_inc(copied, 1)


def hidden_products(pe, pages, W1, out, signal):
    x = pages.rearrange("p m (g d) -> p (m g) d", d=HD)
    for d in range(HD):
        for half in range(2):
            lo = half * 64
            last = pe.matmul(out[half], W1[lo:lo + 64, d, :], x[lo:lo + 64, :, d], start=(d == 0), stop=(d == HD - 1))
    last.then_inc(signal, 1)


def compress_prompt(nc, A, proj, W1, W2, pe_bias, kc_turned, vc_rows):
    NB = SEQ // BLK
    with ExitStack() as ctx:
        sb = lambda n, s: ctx.enter_context(nc.sbuf_tensor(f"{n}_{nc.next_id()}", s, F32))
        src = [sb("cmp_src", [P, MT, P]) for _ in range(2)]
        hid = [sb("cmp_hid", [P, 2, MT, 2]) for _ in range(2)]
        kc, vc = sb("kc_p", [P, 2, NB]), sb("vc_p", [NB, 2, HD])
        ph = [[banks(ctx, nc, f"ph{n}{half}", [P, MT * 2]) for half in range(2)] for n in range(2)]
        pk, pv = banks(ctx, nc, "pk", [P, 2, NB]), banks(ctx, nc, "pv", [NB, 2, HD])
        with phase(nc, "loaded", "hidden", "silu_done", "product", "copied", "stored") as (
                block, loaded, hidden, silu_done, product, copied, stored):
            @block.sync
            def _(sp):
                for n, col in enumerate((K_CMP, V_CMP)):
                    sp.dma_start(src[n][:], proj[0:SEQ, col:col + P].rearrange("(m p) c -> p m c", p=P)).then_inc(loaded, 16)
                sp.wait_ge(copied, 2)
                sp.dma_start(kc_turned.rearrange("g p n -> p g n"), kc[:]).then_inc(stored, 16)
                sp.dma_start(vc_rows.rearrange("g n d -> n g d"), vc[:]).then_inc(stored, 16)
                sp.wait_ge(stored, 32)

            @block.tensor
            def _(pe):
                pe.wait_ge(loaded, 32)
                for n in range(2):
                    hidden_products(pe, src[n][:], W1[n], ph[n], hidden)
                pe.wait_ge(silu_done, 4)
                for g in range(2):
                    flat = lambda n: hid[n][:, g].rearrange("p m two -> p (m two)")
                    for half in range(2):
                        pe.matmul(pk[half * 64:half * 64 + 64, g, :], W2[0][:], flat(0), start=True, stop=True)
                    last = pe.matmul(pv[:, g, :], flat(1), W2[1][:], start=True, stop=True)
                last.then_inc(product, 1)

            @block.scalar
            def _(act):
                for n in range(2):
                    act.wait_ge(hidden, n + 1)
                    for half in range(2):
                        act.activation(hid[n][:, :, :, half], ph[n][half].rearrange("p (m g) -> p g m", g=2), ACT.Silu,
                                       bias=pe_bias[n][:, 0:1]).then_inc(silu_done, 1)

            @block.vector
            def _(dve):
                dve.wait_ge(product, 1)
                dve.tensor_copy(kc[:], pk).then_inc(copied, 1)
                dve.tensor_copy(vc[:], pv).then_inc(copied, 1)


def prompt_attention(nc, c, A, proj, qk_turned, kc_turned, vc_rows, mixed):
    HP = 2
    units = [(m, h) for m in range(MT) for h in range(HP)]
    NB = SEQ // BLK
    NP = 14
    with ExitStack() as ctx:
        sb = lambda n, s: ctx.enter_context(nc.sbuf_tensor(f"{n}_{nc.next_id()}", s, F32))
        qT, ks, kw, kc = sb("qT", [P, SEQ]), sb("ks", [P, SEQ]), sb("kw", [P, SEQ]), sb("kc", [P, NB])
        vs, vw, vc = sb("vs", [P, MT, HD]), sb("vw", [P, MT, HD]), sb("vc", [NB, HD])
        gates, slopes = sb("gates", [P, MT, HP, 3]), sb("slopes", [P, HP])
        dist_sel, dist_win = sb("dist_sel", [P, 1024]), sb("dist_win", [P, 640])
        dist_cmp, seen = sb("dist_cmp", [P, MT, NB]), sb("seen", [P, MT, NB])
        s_sel, s_win, s_cmp = [[sb(n, [P, w]) for _ in range(2)] for n, w in (("s_sel", 1024), ("s_win", 640), ("s_cmp", NB))]
        top, neg, den, wgt = [[sb(n, [P, 3]) for _ in range(2)] for n in ("top", "neg", "den", "wgt")]
        pT = [sb("pT", [P, NP, P]) for _ in range(2)]
        o = sb("o_pair", [P, MT, HP, HD])
        p_sel, p_win = banks(ctx, nc, "p_sel", [P, 1024]), banks(ctx, nc, "p_win", [P, 1024])
        p_tr = [banks(ctx, nc, f"p_tr{i}", [P, 4, P]) for i in range(2)]
        p_o = [banks(ctx, nc, f"p_o{i}", [P, 3, HD]) for i in range(2)]
        load_all(nc, [(dist_sel[:], A["c_dist_sel"]), (dist_win[:], A["c_dist_win"]), (dist_cmp[:], A["c_dist_cmp"]), (seen[:], A["c_seen_cmp"])])
        tok = lambda col, n: proj[0:SEQ, col].rearrange("(m p) c -> p m c", p=P)

        def key_tiles(m):
            n_sel, w0 = m + 1, max(0, m - 4)
            slots = [("s", k) for k in range(n_sel)] + [("w", k) for k in range(w0, m + 1)] + [("c", 0)]
            return n_sel, w0, [slots[i:i + 4] for i in range(0, len(slots), 4)]
        groups_before = [0]
        for m, h in units:
            groups_before.append(groups_before[-1] + len(key_tiles(m)[2]))

        def pair_phase(g, pr, pair):
            with phase(nc, "loaded", "gates_ready", "scores", "scores_out", "neg_ready", "probs", "cmp_masked", "turned", "turned_out",
                       "values", "o_ready", "act_steps", "dve_steps", "stored") as (
                    block, loaded, gates_ready, scores, scores_out, neg_ready, probs, cmp_masked, turned, turned_out,
                    values, o_ready, act_steps, dve_steps, stored):
                @block.sync
                def _(sp):
                    lone = lambda x: x.rearrange("a p t -> p (a t)")
                    sp.dma_start(qT[:], lone(qk_turned[bass.ds(pair, 1)])).then_inc(loaded, 16)
                    sp.dma_start(ks[:], lone(qk_turned[bass.ds(g + 4, 1)])).then_inc(loaded, 16)
                    sp.dma_start(kw[:], lone(qk_turned[bass.ds(g + 6, 1)])).then_inc(loaded, 16)
                    sp.dma_start(kc[:], lone(kc_turned[bass.ds(g, 1)])).then_inc(loaded, 16)
                    sp.dma_start(vc[:], lone(vc_rows[bass.ds(g, 1)])).then_inc(loaded, 16)
                    sp.dma_start(vs[:], tok(bass.ds(g * HD + V_SEL, HD), HD)).then_inc(loaded, 16)
                    sp.dma_start(vw[:], tok(bass.ds(g * HD + V_WIN, HD), HD)).then_inc(loaded, 16)
                    sp.dma_start(gates[:].rearrange("p m h b -> p m (h b)"), tok(bass.ds(pair * 6 + GATE_B, 6), 6)).then_inc(loaded, 16)
                    sp.dma_start(slopes[:], lone(A["c_slopes8"][bass.ds(pair, 1)])).then_inc(loaded, 16)
                    sp.wait_ge(o_ready, len(units))
                    sp.dma_start(mixed[0:SEQ, bass.ds(pair * P + 512, P)].rearrange("(m p) c -> p m c", p=P),
                                 o[:].rearrange("p m h d -> p m (h d)")).then_inc(stored, 16)
                    sp.wait_ge(stored, 16)

                @block.tensor
                def _(pe):
                    def score(u):
                        m, h = units[u]
                        n_sel, w0, _ = key_tiles(m)
                        q = qT[h * HD:(h + 1) * HD, m * P:(m + 1) * P]
                        lo = slice(h * HD, (h + 1) * HD)
                        if u:
                            pe.wait_ge(scores_out, u)
                        for a in range(0, n_sel * P, 512):
                            b = min(a + 512, n_sel * P)
                            pe.matmul(p_sel[:, a:b], q, ks[lo, a:b], start=True, stop=True)
                        nw = (m + 1 - w0) * P
                        for a in range(0, nw, 512):
                            b = min(a + 512, nw)
                            pe.matmul(p_win[:, a:b], q, kw[lo, w0 * P + a:w0 * P + b], start=True, stop=True)
                        pe.matmul(p_win[:, 1024 - NB:1024], q, kc[lo, :], start=True, stop=True).then_inc(scores, 1)

                    pe.wait_ge(loaded, 16 * 9)
                    score(0)
                    for u, (m, h) in enumerate(units):
                        if u + 1 < len(units):
                            score(u + 1)
                        n_sel, w0, groups = key_tiles(m)
                        for n, group in enumerate(groups):
                            done = groups_before[u] + n
                            if done >= 2:
                                pe.wait_ge(turned_out, done - 1)
                            if n == 0:
                                pe.wait_ge(probs, u + 1)
                                pe.wait_ge(cmp_masked, u + 1)
                            for j, (kind, k) in enumerate(group):
                                if kind == "s":
                                    last = pe.transpose(p_tr[done % 2][:, j, :], s_sel[u % 2][:, k * P:(k + 1) * P], c["ident"][:])
                                elif kind == "w":
                                    last = pe.transpose(p_tr[done % 2][:, j, :], s_win[u % 2][:, (k - w0) * P:(k - w0 + 1) * P], c["ident"][:])
                                else:
                                    last = pe.transpose(p_tr[done % 2][0:NB, j, :], s_cmp[u % 2][:], c["ident"][:])
                            last.then_inc(turned, 1)
                        pe.wait_ge(turned_out, groups_before[u + 1])
                        if u >= 2:
                            pe.wait_ge(o_ready, u - 1)
                        slot = 0
                        for k in range(n_sel):
                            pe.matmul(p_o[u % 2][:, 1, :], pT[u % 2][:, slot, :], vs[:, k, :], start=(k == 0), stop=(k == n_sel - 1))
                            slot += 1
                        for k in range(w0, m + 1):
                            pe.matmul(p_o[u % 2][:, 2, :], pT[u % 2][:, slot, :], vw[:, k, :], start=(k == w0), stop=(k == m))
                            slot += 1
                        pe.matmul(p_o[u % 2][:, 0, :], pT[u % 2][0:NB, slot, :], vc[:], start=True, stop=True).then_inc(values, 1)

                @block.scalar
                def _(act):
                    act.wait_ge(loaded, 16 * 9)
                    act.activation(gates[:], gates[:], ACT.Exp, scale=-1.0).then_inc(gates_ready, 1)

                    def probabilities(u):
                        m, h = units[u]
                        n_sel, w0, _ = key_tiles(m)
                        act.wait_ge(neg_ready, u + 1)
                        for n, (s, w) in enumerate(((s_cmp[u % 2], NB), (s_sel[u % 2], n_sel * P), (s_win[u % 2], (m + 1 - w0) * P))):
                            ins = act.activation(s[:, 0:w], s[:, 0:w], ACT.Exp, bias=neg[u % 2][:, n:n + 1], scale=HD ** -0.5,
                                                 accum_out=den[u % 2][:, n:n + 1])
                        ins.then_inc(probs, 1)
                    probabilities(0)
                    for u, (m, h) in enumerate(units):
                        if u + 1 < len(units):
                            probabilities(u + 1)
                        _, _, groups = key_tiles(m)
                        slot = 0
                        if u >= 2:
                            act.wait_ge(values, u - 1)
                        for n, group in enumerate(groups):
                            done = groups_before[u] + n
                            act.wait_ge(turned, done + 1)
                            full = len(group) - (group[-1][0] == "c")
                            ins = None
                            if full:
                                ins = act.copy(pT[u % 2][:, slot:slot + full, :], p_tr[done % 2][:, 0:full, :])
                            if full < len(group):
                                ins = act.copy(pT[u % 2][0:NB, slot + full, :], p_tr[done % 2][0:NB, full, :])
                            ins.then_inc(turned_out, 1)
                            slot += len(group)

                @block.vector
                def _(dve):
                    step = InOrder(dve, dve_steps)
                    dve.wait_ge(gates_ready, 1)
                    step(dve.tensor_scalar(gates[:], gates[:], 1.0, None, ALU.add))
                    step(dve.reciprocal(gates[:], gates[:]))

                    def finish_scores(u):
                        m, h = units[u]
                        n_sel, w0, _ = key_tiles(m)
                        b, nw = u % 2, (m + 1 - w0) * P
                        dve.wait_ge(scores, u + 1)
                        if u >= 2:
                            dve.wait_ge(values, u - 1)
                        slope = slopes[:, h:h + 1]
                        add = lambda out, dist, ps: dve.scalar_tensor_tensor(out, dist, slope, ps, ALU.mult, ALU.add)
                        add(s_sel[b][:, 0:n_sel * P], dist_sel[:, 896 - m * P:1024], p_sel[:, 0:n_sel * P])
                        add(s_win[b][:, 0:nw], dist_win[:, 640 - nw:640], p_win[:, 0:nw])
                        step(add(s_cmp[b][:], dist_cmp[:, m, :], p_win[:, 1024 - NB:1024]))
                        dve.sem_inc(scores_out, 1)
                        dve.reduce_max(top[b][:, 0:1], s_cmp[b][:], AX)
                        dve.reduce_max(top[b][:, 1:2], s_sel[b][:, 0:n_sel * P], AX)
                        step(dve.reduce_max(top[b][:, 2:3], s_win[b][:, 0:nw], AX))
                        dve.tensor_scalar(neg[b][:], top[b][:], -(HD ** -0.5), None, ALU.mult).then_inc(neg_ready, 1)
                    finish_scores(0)
                    for u, (m, h) in enumerate(units):
                        if u + 1 < len(units):
                            finish_scores(u + 1)
                        b = u % 2
                        dve.wait_ge(probs, u + 1)
                        dve.tensor_tensor(s_cmp[b][:], s_cmp[b][:], seen[:, m, :], ALU.mult).then_inc(cmp_masked, 1)
                        dve.wait_ge(cmp_masked, u + 1)
                        step(dve.reduce_sum(den[b][:, 0:1], s_cmp[b][:], AX))
                        step(dve.tensor_scalar(den[b][:], den[b][:], 1e-30, None, ALU.max))
                        step(dve.reciprocal(wgt[b][:], den[b][:]))
                        step(dve.tensor_tensor(wgt[b][:], wgt[b][:], gates[:, m, h, :], ALU.mult))
                        dve.wait_ge(values, u + 1)
                        out = o[:, m, h, :]
                        step(dve.tensor_scalar(out, p_o[b][:, 0, :], wgt[b][:, 0:1], None, ALU.mult))
                        step(dve.scalar_tensor_tensor(out, p_o[b][:, 1, :], wgt[b][:, 1:2], out, ALU.mult, ALU.add))
                        dve.scalar_tensor_tensor(out, p_o[b][:, 2, :], wgt[b][:, 2:3], out, ALU.mult, ALU.add).then_inc(o_ready, 1)

        with nc.Fori(0, 2) as g:
            with nc.Fori(0, 2) as pr:
                pair_phase(g, pr, g * 2 + pr)


def load_pages(eng, pool, ids, pages, loaded):
    for p in range(PAGES):
        page = eng.value_load(ids[0:1, p:p + 1], min_val=0, max_val=NPOOL - 1)
        eng.dma_start(pages[:, p, :], pool[0, bass.ds(page, 1)].rearrange("a t g d -> t (a g d)")).then_inc(loaded, 16)


def sample_compressed(nc, c, A, W1, W2, pe_bias, q_diag, importance, o_cmp):
    with ExitStack() as ctx:
        sb = lambda n, s, d=F32: ctx.enter_context(nc.sbuf_tensor(f"{n}_{nc.next_id()}", s, d))
        pages = [sb(f"pages{n}", [P, PAGES, P]) for n in range(2)]
        hid = [sb("hid_s", [P, 2, PAGES, 2]) for _ in range(2)]
        ids, q, hsum, alibi = sb("ids", [1, PAGES], I32), sb("q", [P, 64]), sb("hsum", [64, P]), sb("alibi_cmp", [64, P])
        kc, vc, s, pT, o = sb("kc_s", [P, P]), sb("vc_s", [P, P]), sb("s_c", [64, P]), sb("pT_c", [P, 64]), sb("o_c", [64, HD])
        top, den = sb("top_c", [64, 1]), sb("den_c", [64, 1])
        ph = [[banks(ctx, nc, f"ph{n}{half}", [P, PAGES * 2]) for half in range(2)] for n in range(2)]
        pk, pv, ps, po = [banks(ctx, nc, n, [P, P]) for n in ("pk", "pv", "ps", "po")]
        load_all(nc, [(alibi[:], A["c_alibi_cmp"])])
        with phase(nc, "zeroed") as (block, zeroed):
            @block.vector
            def _(dve):
                dve.memset(importance[:], 0.0).then_inc(zeroed, 1)
        with nc.Fori(0, NS) as b:
            with phase(nc, "ids_loaded", "small_loaded", "k_loaded", "v_loaded", "hidden", "silu_done", "k_ready", "k_out", "v_ready", "v_out",
                       "scores", "neg_ready", "probs", "p_ready", "turned", "pT_out", "sums", "values", "o_ready", "dve_steps", "stored") as (
                    block, ids_loaded, small_loaded, k_loaded, v_loaded, hidden, silu_done, k_ready, k_out, v_ready, v_out,
                    scores, neg_ready, probs, p_ready, turned, pT_out, sums, values, o_ready, dve_steps, stored):
                @block.sync
                def _(sp):
                    lone = lambda x: x.rearrange("a p t -> p (a t)")
                    sp.dma_start(ids[:], A["page_table"][bass.ds(b, 1), :]).then_inc(ids_loaded, 16)
                    sp.dma_start(q[:], lone(q_diag[bass.ds(b, 1)])).then_inc(small_loaded, 16)
                    sp.dma_start(hsum[:], A["c_head_sum"][:, bass.ds(b * P, P)]).then_inc(small_loaded, 16)
                    sp.wait_ge(ids_loaded, 16)
                    load_pages(sp, A["cache_cmp_k"], ids, pages[0], k_loaded)
                    sp.wait_ge(o_ready, 2)
                    sp.dma_start(o_cmp[bass.ds(b, 1)].rearrange("a c d -> c (a d)"), o[:]).then_inc(stored, 16)
                    sp.wait_ge(stored, 16)

                @block.tensor
                def _(pe):
                    pe.wait_ge(k_loaded, 16 * PAGES)
                    hidden_products(pe, pages[0][:], W1[0], ph[0], hidden)
                    pe.wait_ge(v_loaded, 16 * PAGES)
                    hidden_products(pe, pages[1][:], W1[1], ph[1], hidden)
                    flat = lambda n, g: hid[n][:, g].rearrange("p m two -> p (m two)")
                    pe.wait_ge(silu_done, 2)
                    for g in range(2):
                        last = pe.matmul(pk[g * 64:g * 64 + 64, :], W2[0][:], flat(0, g), start=True, stop=True)
                    last.then_inc(k_ready, 1)
                    pe.wait_ge(silu_done, 4)
                    for g in range(2):
                        last = pe.matmul(pv[:, g * HD:(g + 1) * HD], flat(1, g), W2[1][:], start=True, stop=True)
                    last.then_inc(v_ready, 1)
                    pe.wait_ge(small_loaded, 32)
                    pe.wait_ge(k_out, 1)
                    pe.matmul(ps[0:64, :], q[:], kc[:], start=True, stop=True).then_inc(scores, 1)
                    pe.wait_ge(p_ready, 1)
                    pe.transpose(pk[:, 0:64], s[:], c["ident"][0:64, 0:64]).then_inc(turned, 1)
                    pe.matmul(ps[:], hsum[:], s[:], start=True, stop=True).then_inc(sums, 1)
                    pe.wait_ge(pT_out, 1)
                    pe.wait_ge(v_out, 1)
                    pe.matmul(po[0:64, :], pT[:], vc[:], start=True, stop=True).then_inc(values, 1)

                @block.scalar
                def _(act):
                    act.wait_ge(ids_loaded, 16)
                    load_pages(act, A["cache_cmp_v"], ids, pages[1], v_loaded)
                    for n in range(2):
                        act.wait_ge(hidden, n + 1)
                        for half in range(2):
                            act.activation(hid[n][:, :, :, half], ph[n][half].rearrange("p (m g) -> p g m", g=2), ACT.Silu,
                                           bias=pe_bias[n][:, 0:1]).then_inc(silu_done, 1)
                    act.wait_ge(neg_ready, 1)
                    act.activation(s[:], s[:], ACT.Exp, bias=top[:], accum_out=den[:]).then_inc(probs, 1)

                @block.vector
                def _(dve):
                    step = InOrder(dve, dve_steps)
                    dve.wait_ge(k_ready, 1)
                    dve.tensor_copy(kc[:], pk).then_inc(k_out, 1)
                    dve.wait_ge(v_ready, 1)
                    dve.tensor_copy(vc[:], pv).then_inc(v_out, 1)
                    dve.wait_ge(scores, 1)
                    step(dve.scalar_tensor_tensor(s[:], ps[0:64, :], HD ** -0.5, alibi[:], ALU.mult, ALU.add))
                    step(dve.reduce_max(top[:], s[:], AX))
                    dve.tensor_scalar(top[:], top[:], -1.0, None, ALU.mult).then_inc(neg_ready, 1)
                    dve.wait_ge(probs, 1)
                    step(dve.tensor_scalar(den[:], den[:], 1e-30, None, ALU.max))
                    step(dve.reciprocal(den[:], den[:]))
                    dve.tensor_scalar(s[:], s[:], den[:, 0:1], None, ALU.mult).then_inc(p_ready, 1)
                    dve.wait_ge(turned, 1)
                    dve.tensor_copy(pT[:], pk[:, 0:64]).then_inc(pT_out, 1)
                    dve.wait_ge(sums, 1)
                    step(dve.tensor_tensor(importance[:], importance[:], ps, ALU.add))
                    dve.wait_ge(values, 1)
                    for g in range(2):
                        dve.tensor_copy(o[g * 32:g * 32 + 32, :], po[g * 32:g * 32 + 32, g * HD:(g + 1) * HD]).then_inc(o_ready, 1)


def choose_blocks(nc, importance, block_mask):
    TAKEN = -2.0
    with ExitStack() as ctx:
        sb = lambda n, s: ctx.enter_context(nc.sbuf_tensor(f"{n}_{nc.next_id()}", s, F32))
        left, rest, top, mask = sb("left", [P, P]), sb("rest", [P, P]), sb("top8", [P, 8]), sb("mask", [P, 2, PAGES])
        with phase(nc, "dve_steps", "done", "stored") as (block, dve_steps, done, stored):
            @block.vector
            def _(dve):
                step = InOrder(dve, dve_steps)
                step(dve.memset(importance[:, 0:1], 1000.0))
                step(dve.memset(importance[:, P - 1:P], 1000.0))
                step(dve.max(top[:], importance[:]))
                step(dve.match_replace(left[:], top[:], importance[:], TAKEN))
                step(dve.max(top[:], left[:]))
                step(dve.memset(top[:, 7:8], TAKEN))
                step(dve.match_replace(rest[:], top[:], left[:], TAKEN))
                dve.tensor_scalar(mask[:], rest[:].rearrange("p (m two) -> p two m", two=2), TAKEN, NEG,
                                  ALU.not_equal, ALU.mult).then_inc(done, 1)

            @block.sync
            def _(sp):
                sp.wait_ge(done, 1)
                for b in range(NS):
                    sp.dma_start(block_mask[b].rearrange("two c m -> c two m"), mask[b * 16:(b + 1) * 16]).then_inc(stored, 16)
                sp.wait_ge(stored, 16 * NS)


def sample_selected(nc, c, A, proj, q_diag, k_new, block_mask, o_cmp, mixed):
    COLS = 64
    branches = [(0, PAGES), (1, 4)]
    with ExitStack() as ctx:
        sb = lambda n, s, d=F32: ctx.enter_context(nc.sbuf_tensor(f"{n}_{nc.next_id()}", s, d))
        kp, vp = sb("k_pages", [P, PAGES, P]), sb("v_pages", [P, PAGES, P])
        kw, vw = sb("k_win", [P, 4, P]), sb("v_win", [P, 4, P])
        kn, vn = sb("k_new", [P, 2, TS]), sb("v_new", [TS, 2, P])
        E = [sb("e_sel", [P, PAGES + 1, COLS]), sb("e_win", [P, 5, COLS])]
        alibi = [sb("alibi_page", [P, PAGES, COLS]), sb("alibi_win", [P, 4, COLS])]
        alibi_new = sb("alibi_new", [TS, COLS])
        kT = [sb("kT", [P, 4, P]) for _ in range(2)]
        ids, q, half, mask = sb("ids2", [1, PAGES], I32), sb("q2", [P, COLS]), sb("half", [2, P]), sb("mask_b", [2, 16, PAGES])
        cm, diag, mB = sb("cm", [P, 2, COLS]), sb("diag", [P, P]), sb("mB", [P, 2, COLS])
        mcol = sb("mcol", [P, 1])
        rs, gates, oc = sb("rs", [P, 2, COLS]), sb("gates_s", [COLS, 3]), sb("oc", [COLS, HD])
        w = sb("w_s", [COLS, 2])
        p_tr = [banks(ctx, nc, f"st{i}", [P, 4, P]) for i in range(2)]
        p_s = [banks(ctx, nc, f"ss{i}", [P, 8, COLS]) for i in range(2)]
        p_mask = banks(ctx, nc, "smask", [P, 16, PAGES])
        p_a, p_o = banks(ctx, nc, "sa", [P, P]), banks(ctx, nc, "so", [COLS, 4, P])
        load_all(nc, [(alibi[0][:].rearrange("p m c -> p (m c)"), A["c_alibi_page"]), (alibi[1][:].rearrange("p m c -> p (m c)"), A["c_alibi_win"]),
                      (alibi_new[:], A["c_alibi_new"]), (half[:], A["c_half"])])
        SG = PAGES // 4 + 1
        with nc.Fori(0, NS) as b:
            with phase(nc, "ids_loaded", "small", "k_loaded", "v_loaded", "filled", "turned", "kT_out", "scores", "scores_out", "masks",
                       "max_ready", "max_turned", "diag_ready", "max_spread", "shifted", "probs", "summed", "values", "dve_steps",
                       "act_steps", "gates_exp", "o_ready", "stored") as (
                    block, ids_loaded, small, k_loaded, v_loaded, filled, turned, kT_out, scores, scores_out, masks,
                    max_ready, max_turned, diag_ready, max_spread, shifted, probs, summed, values, dve_steps,
                    act_steps, gates_exp, o_ready, stored):
                lone = lambda x: x.rearrange("a p t -> p (a t)")
                srow = lambda col, n: proj[bass.ds(b * TS + SEQ, TS), col:col + n]

                @block.sync
                def _(sp):
                    sp.dma_start(ids[:], A["page_table"][bass.ds(b, 1), :]).then_inc(ids_loaded, 16)
                    sp.dma_start(q[:], lone(q_diag[bass.ds(b, 1)])).then_inc(small, 16)
                    sp.dma_start(kw[:], A["state_win_k"][0, bass.ds(b, 1)].rearrange("a (m p) g d -> p (a m) (g d)", p=P)).then_inc(small, 16)
                    sp.dma_start(vw[:], A["state_win_v"][0, bass.ds(b, 1)].rearrange("a (m p) g d -> p (a m) (g d)", p=P)).then_inc(small, 16)
                    sp.dma_start(mask[:], block_mask[bass.ds(b, 1)].rearrange("a two c m -> two (a c) m")).then_inc(small, 16)
                    sp.dma_start(oc[:], lone(o_cmp[bass.ds(b, 1)])).then_inc(small, 16)
                    for n in range(2):
                        sp.dma_start(kn[:, n, :], lone(k_new[n, bass.ds(b, 1)])).then_inc(small, 16)
                        sp.dma_start(vn[:, n, :], srow((V_SEL, V_WIN)[n], P)).then_inc(small, 16)
                    for h in range(NH):
                        sp.dma_start(gates[h * TS:(h + 1) * TS, :], srow(GATE_B + 3 * h, 3)).then_inc(small, 16)
                    sp.wait_ge(ids_loaded, 16)
                    load_pages(sp, A["cache_sel_k"], ids, kp, k_loaded)
                    sp.wait_ge(o_ready, 1)
                    for h in range(NH):
                        sp.dma_start(mixed[bass.ds(b * TS + SEQ, TS), 512 + h * HD:512 + (h + 1) * HD], oc[h * TS:(h + 1) * TS, :]).then_inc(stored, 16)
                    sp.wait_ge(stored, 16 * NH)

                @block.tensor
                def _(pe):
                    pe.wait_ge(small, 16 * 17)
                    for n in range(2):
                        last = pe.matmul(p_mask[:, n * 8:(n + 1) * 8, :], half[:], mask[:, n * 8:(n + 1) * 8, :], start=True, stop=True)
                    last.then_inc(masks, 1)
                    for n in range(SG + 1):
                        if n < SG:
                            if n == 1:
                                pe.wait_ge(k_loaded, 16 * PAGES)
                            if n >= 2:
                                pe.wait_ge(kT_out, n - 1)
                            for j in range(4):
                                page = kw[:, j, :] if n == 0 else kp[:, 4 * (n - 1) + j, :]
                                last = pe.transpose(p_tr[n % 2][:, j, :], page, c["ident"][:])
                            last.then_inc(turned, 1)
                        if n >= 1:
                            s = n - 1
                            pe.wait_ge(kT_out, s + 1)
                            if s >= 2:
                                pe.wait_ge(scores_out, s - 1)
                            for j in range(4):
                                last = pe.matmul(p_s[s % 2][:, j, :], kT[s % 2][:, j, :], q[:], start=True, stop=True)
                            if s == 0:
                                for k in range(2):
                                    last = pe.matmul(p_s[0][0:TS, 4 + k, :], kn[:, k, :], q[:], start=True, stop=True)
                            last.then_inc(scores, 1)
                    pe.wait_ge(max_ready, 1)
                    pe.transpose(p_a, cm[:].rearrange("p n c -> p (n c)"), c["ident"][:]).then_inc(max_turned, 1)
                    pe.wait_ge(diag_ready, 1)
                    pe.matmul(p_a, c["ones"][:], diag[:], start=True, stop=True).then_inc(max_spread, 1)
                    pe.wait_ge(probs, 2)
                    pe.wait_ge(v_loaded, 16 * PAGES)
                    for n, count in branches:
                        for k in range(count):
                            pe.matmul(p_o[:, n, :], E[n][:, k, :], (vp if n == 0 else vw)[:, k, :], start=(k == 0), stop=False)
                        pe.matmul(p_o[:, n, :], E[n][0:TS, count, :], vn[:, n, :], start=False, stop=True)
                    pe.wait_ge(summed, 2)
                    for n in range(2):
                        last = pe.matmul(p_o[:, 2, n:n + 1], rs[:, n, :], c["ones"][:, 0:1], start=True, stop=True)
                    last.then_inc(values, 1)

                @block.scalar
                def _(act):
                    act.wait_ge(ids_loaded, 16)
                    load_pages(act, A["cache_sel_v"], ids, vp, v_loaded)
                    act.wait_ge(small, 16 * 17)
                    act.activation(gates[:], gates[:], ACT.Exp, scale=-1.0).then_inc(gates_exp, 1)
                    for n in range(SG):
                        act.wait_ge(turned, n + 1)
                        if n >= 2:
                            act.wait_ge(scores, n - 1)
                        act.copy(kT[n % 2][:], p_tr[n % 2]).then_inc(kT_out, 1)
                    for n in range(2):
                        act.wait_ge(shifted, n + 1)
                        act.activation(E[n][:], E[n][:], ACT.Exp).then_inc(probs, 1)

                @block.vector
                def _(dve):
                    step = InOrder(dve, dve_steps)
                    dve.wait_ge(small, 16 * 17)
                    for n, count in branches:
                        step(dve.memset(E[n][:, count, :], NEG))
                    for s in range(SG):
                        dve.wait_ge(scores, s + 1)
                        ps = p_s[s % 2]
                        if s == 0:
                            for n, count in branches:
                                dve.scalar_tensor_tensor(E[n][0:TS, count, :], ps[0:TS, 4 + n, :], HD ** -0.5, alibi_new[:], ALU.mult, ALU.add)
                            out, al = E[1][:, 0:4, :], alibi[1][:]
                        else:
                            out, al = E[0][:, 4 * s - 4:4 * s, :], alibi[0][:, 4 * s - 4:4 * s, :]
                        step(dve.scalar_tensor_tensor(out, ps[:, 0:4, :], HD ** -0.5, al, ALU.mult, ALU.add))
                        dve.sem_inc(scores_out, 1)
                    dve.wait_ge(masks, 1)
                    for g in range(2):
                        v = E[0][:, 0:PAGES, g * 32:(g + 1) * 32].rearrange("p m (h t) -> p h t m", h=4)
                        step(dve.tensor_tensor(v, v, p_mask[:, g * 8:(g + 1) * 8, :].unsqueeze(1).broadcast_to([P, 4, TS, PAGES]), ALU.add))
                    for n, count in branches:
                        step(dve.reduce_max(cm[:, n, :], E[n][:].rearrange("p m c -> p c m"), AX))
                    dve.sem_inc(max_ready, 1)
                    dve.wait_ge(max_turned, 1)
                    step(dve.reduce_max(mcol[:], p_a, AX))
                    dve.tensor_scalar(diag[:], c["ident"][:], mcol[:, 0:1], None, ALU.mult).then_inc(diag_ready, 1)
                    dve.wait_ge(max_spread, 1)
                    step(dve.tensor_copy(mB[:].rearrange("p n c -> p (n c)"), p_a))
                    for n, count in branches:
                        dve.tensor_tensor(E[n][:], E[n][:], mB[:, n, :].unsqueeze(1).broadcast_to([P, count + 1, COLS]), ALU.subtract).then_inc(shifted, 1)
                    dve.wait_ge(gates_exp, 1)
                    step(dve.tensor_scalar(gates[:], gates[:], 1.0, None, ALU.add))
                    step(dve.reciprocal(gates[:], gates[:]))
                    for n, count in branches:
                        dve.wait_ge(probs, n + 1)
                        dve.reduce_sum(rs[:, n, :], E[n][:].rearrange("p m c -> p c m"), AX).then_inc(summed, 1)
                    dve.wait_ge(values, 1)
                    step(dve.tensor_scalar(w[:], p_o[:, 2, 0:2], 1e-30, None, ALU.max))
                    step(dve.reciprocal(w[:], w[:]))
                    step(dve.tensor_tensor(w[:], w[:], gates[:, 1:3], ALU.mult))
                    step(dve.tensor_scalar(oc[:], oc[:], gates[:, 0:1], None, ALU.mult))
                    for n in range(2):
                        for g in range(2):
                            r = slice(g * 32, g * 32 + 32)
                            step(dve.scalar_tensor_tensor(oc[r, :], p_o[r, n, g * HD:(g + 1) * HD], w[r, n:n + 1], oc[r, :], ALU.mult, ALU.add))
                    dve.sem_inc(o_ready, 1)


BASE = ("ident", "ones", "tri", "tri_mid", "tri_end", "sel_mod_p", "sel_mod_s")


def hybrid_decoder(nc, A, O):
    scratch = lambda n, s: nc.dram_tensor("scratch_" + n, s, F32, kind="Internal").ap()
    mod_rows = scratch("mod_rows", [MODS, 2, 6 * D])
    y, mixed = scratch("y", [T, D]), scratch("mixed", [T, D])
    row_tile = lambda x, m, cols: x[m * P:m * P + ROWS[m], cols]
    with ExitStack() as top:
        sb = lambda n, s, st=top: st.enter_context(nc.sbuf_tensor(n, s, F32))
        c = {k: sb("c_" + k, list(A["c_" + k].shape)) for k in BASE}
        X, modT = sb("X", [P, TILES, D]), sb("modT", [P, 2, 4, KD, MODS])
        load_all(nc, [(c[k][:], A["c_" + k]) for k in BASE]
                 + [(X[:, 0:MT, :], A["x_prompt"][0].rearrange("(m p) d -> p m d", p=P)),
                    (X[0:SROWS, MT, :], A["x_sample"].rearrange("b t d -> (b t) d"))])
        adaln_mods(nc, A, c, modT, mod_rows)

        def project_out(w):
            with ExitStack() as ctx:
                hT = ctx.enter_context(nc.sbuf_tensor(f"mT_{nc.next_id()}", [P, KD, T], F32))
                with nc.sbuf_tensor(f"mrows_{nc.next_id()}", [P, TILES, D], F32) as rows:
                    loads = [(rows[:, 0:MT, :], mixed[0:SEQ].rearrange("(m p) d -> p m d", p=P)), (rows[0:SROWS, MT, :], mixed[SEQ:T])]
                    transpose_rows(nc, rows, hT, c["ident"], loads=loads)
                gemm_rows(nc, lambda m, k: hT[:, k, m * P:m * P + ROWS[m]], ROWS, KD, w, lambda m, cols: row_tile(y, m, cols), 512, 2, tag="out")

        proj = scratch("proj", [T, AB_IN])
        with nc.sbuf_tensor("hT_ab", [P, KD, T], F32) as hT:
            transpose_rows(nc, X, hT, c["ident"], (modT[:, 0, 0], modT[:, 0, 1]))
            project_in(nc, A, hT, proj)
        cache_rows(nc, A, O, proj)
        log_a = scratch("log_a", [T, GH * GK])
        gla_gates(nc, A, c, proj, log_a)
        gla(nc, A, O, c, proj, log_a, mixed)
        qk_turned, q_diag, k_new = scratch("qk", [8, P, SEQ]), scratch("q_diag", [NS, P, 64]), scratch("k_new", [2, NS, P, TS])
        kc_turned, vc_rows = scratch("kc", [2, P, SEQ // BLK]), scratch("vc", [2, SEQ // BLK, HD])
        o_cmp, block_mask = scratch("o_cmp", [NS, 64, HD]), scratch("block_mask", [NS, 2, 16, PAGES])
        turn_queries(nc, c, proj, qk_turned)
        turn_sample(nc, c, proj, q_diag, k_new)
        with nc.sbuf_tensor("importance", [P, P], F32) as importance:
            with ExitStack() as ctx:
                W1 = [sb(f"cmp_w1_{n}", [P, HD, P], ctx) for n in range(2)]
                W2 = [sb(f"cmp_w2_{n}", [P, HD], ctx) for n in range(2)]
                pe_bias = [sb(f"pe_bias_{n}", [P, 1], ctx) for n in range(2)]
                compress_weights(nc, A, W1, W2, pe_bias)
                compress_prompt(nc, A, proj, W1, W2, pe_bias, kc_turned, vc_rows)
                sample_compressed(nc, c, A, W1, W2, pe_bias, q_diag, importance, o_cmp)
            choose_blocks(nc, importance, block_mask)
        prompt_attention(nc, c, A, proj, qk_turned, kc_turned, vc_rows, mixed)
        sample_selected(nc, c, A, proj, q_diag, k_new, block_mask, o_cmp, mixed)
        project_out(A["ab_w_out"][0])
        post_norm(nc, X, y, mod_rows[:, 0, 2 * D:3 * D], A["ln_g"][0, 0], A["ln_b"][0, 0], c)
        ffn(nc, A, c, X, 0, modT, mod_rows, y)

        xp, xs = scratch("xp", [3 + SEQ, NCH]), scratch("xs", [NS, 3 + TS, NCH])
        z, ba, qkv, gb = scratch("z", [T, D]), scratch("ba", [T, 16]), scratch("qkv", [T, NCH]), scratch("gb", [T, 16])
        with ExitStack() as ctx:
            hT = sb("hT_c", [P, KD, T], ctx)
            zero = sb("zero3", [3, NCH], ctx)
            transpose_rows(nc, X, hT, c["ident"], (modT[:, 1, 0], modT[:, 1, 1]))
            with phase(nc, "zeroed", "stored") as (block, zeroed, stored):
                @block.vector
                def _(dve):
                    dve.memset(zero[:], 0.0).then_inc(zeroed, 1)

                @block.sync
                def _(sp):
                    sp.wait_ge(zeroed, 1)
                    sp.dma_start(xp[0:3], zero[:]).then_inc(stored, 16)
                    sp.dma_start(xs[:, 0:3], A["state_gdn_conv"][0]).then_inc(stored, 16)
                    sp.wait_ge(stored, 32)
            lhsT = lambda m, k: hT[:, k, m * P:m * P + ROWS[m]]

            def conv_rows(m, cols):
                return xp[3 + m * P:3 + (m + 1) * P, cols] if m < MT else xs[:, 3:3 + TS, cols]
            w = A["c_w_in"][0]
            gemm_rows(nc, lhsT, ROWS, KD, w[:, 0:NCH], conv_rows, 512, 6, tag="c")
            gemm_rows(nc, lhsT, ROWS, KD, w[:, C_BA:C_Z], lambda m, cols: row_tile(ba, m, cols), 16, 1, tag="cb")
            gemm_rows(nc, lhsT, ROWS, KD, w[:, C_Z:C_IN], lambda m, cols: row_tile(z, m, cols), 512, 2, tag="cz")
        gdn(nc, A, O, c, xp, xs, z, ba, qkv, gb, mixed)
        project_out(A["c_w_out"][0])
        post_norm(nc, X, y, mod_rows[:, 1, 2 * D:3 * D], A["ln_g"][1, 0], A["ln_b"][1, 0], c)
        ffn(nc, A, c, X, 1, modT, mod_rows, y, (O["y_prompt"][0], O["y_sample"].rearrange("b t d -> (b t) d")))


_INS = ["x_prompt", "x_sample", "c_prompt", "c_sample", "page_table", "cache_cmp_k", "cache_cmp_v", "cache_sel_k", "cache_sel_v",
        "state_win_k", "state_win_v", "state_gla", "state_gdn", "state_gdn_conv", "w_ada", "b_ada", "ln_g", "ln_b", "w_ffn_in",
        "w_ffn_out", "ab_w_in", "ab_w_gk2", "ab_b_gk", "ab_gla_norm", "ab_cmp_pe", "ab_cmp_w1", "ab_cmp_w2", "ab_w_out", "c_w_in",
        "c_conv_w", "c_a_log", "c_dt_bias", "c_norm", "c_w_out"]
_ROWS_P, _ROWS_S = (1, 1, SEQ, 2, HD), (1, NS, TS, 2, HD)
_OUTS = {"y_prompt": (1, SEQ, D), "y_sample": (NS, TS, D),
         "p_cmp_k": _ROWS_P, "p_cmp_v": _ROWS_P, "p_sel_k": _ROWS_P, "p_sel_v": _ROWS_P,
         "p_win_k": (1, 1, WIN, 2, HD), "p_win_v": (1, 1, WIN, 2, HD),
         "p_gla": (1, 1, GH, GK, GV), "p_gdn": (1, 1, DH, P, P), "p_conv": (1, 1, 3, NCH),
         "s_cmp_k": _ROWS_S, "s_cmp_v": _ROWS_S, "s_sel_k": _ROWS_S, "s_sel_v": _ROWS_S,
         "s_win_k": (1, NS, WIN, 2, HD), "s_win_v": (1, NS, WIN, 2, HD),
         "s_gla": (1, NS, GH, GK, GV), "s_gdn": (1, NS, DH, P, P), "s_conv": (1, NS, 3, NCH)}


def kernel(**inputs):
    import numpy as _np
    import concourse.bacc as _bacc
    from concourse import mybir as _mybir
    from concourse.bass_utils import run_bass_kernel_spmd as _run

    nc = _bacc.Bacc("TRN2", target_bir_lowering=False, num_devices=1)
    arrays, A, O = {}, {}, {}
    given = {name: inputs[name] for name in _INS}
    given.update({"c_" + name: a for name, a in shape_constants().items()})
    for name, a in given.items():
        a = _np.ascontiguousarray(a)
        arrays[f"in_{name}"] = a
        A[name] = nc.dram_tensor(f"in_{name}", a.shape, _mybir.dt.from_np(a.dtype), kind="ExternalInput").ap()
    for name, shape in _OUTS.items():
        O[name] = nc.dram_tensor(f"out_{name}", shape, _mybir.dt.float32, kind="ExternalOutput").ap()
    hybrid_decoder(nc, A, O)
    r = _run(nc, [arrays], core_ids=[0])
    return tuple(r.results[0][f"out_{name}"] for name in _OUTS)
```

```python
from contextlib import ExitStack, contextmanager

import numpy as np

import concourse.bass as bass
from concourse import mybir

F32 = mybir.dt.float32
I32 = mybir.dt.int32
ALU = mybir.AluOpType
ACT = mybir.ActivationFunctionType
AX = mybir.AxisListType.X

P = 128
D = 1024
KD = D // P
SEQ = 1024
NS, TS = 8, 8
SROWS = NS * TS
T = SEQ + SROWS
MT = SEQ // P
TILES = MT + 1
ROWS = [P] * MT + [SROWS]
FF = 2816
FT = FF // P
CHUNK = 64
ALPHA = (2.0 * 2) ** 0.25
LN_EPS, RMS_EPS, L2_EPS = 1e-5, 1e-6, 1e-6
PAGES = 64
NPOOL = 640
PAST = 8192
NEG = -1e30
MODS = 9

GH, GK, GV = 4, 64, 128
NH, HD, BLK, WIN = 8, 64, 64, 512
Q_A, K_A, V_A, R_A, GK_A = 0, 256, 512, 1024, 1536
Q_B, KV_B, GATE_B, AB_IN = 1552, 2064, 2832, 2856
K_CMP, V_CMP, K_SEL, V_SEL, K_WIN, V_WIN = [KV_B + 128 * j for j in range(6)]
NCH = 3072
C_BA, C_Z, C_IN = 3072, 3088, 4112
DH = 8


def shape_constants():
    f = np.float32
    i = np.arange(P)
    c = {"ident": np.eye(P, dtype=f), "ones": np.ones((P, P), f)}
    j, k = np.meshgrid(np.arange(CHUNK), np.arange(CHUNK), indexing="ij")
    c["tri"] = (j <= k).astype(f)
    c["tri_mid"] = ((j <= k).astype(f) - (j < CHUNK // 2)).astype(f)
    c["tri_end"] = (j > k).astype(f)
    slopes = np.exp2(-8.0 * np.arange(1, NH + 1) / NH)
    x = np.arange(1024)[None, :] - 896
    c["dist_sel"] = np.where(x <= i[:, None], x - i[:, None], NEG).astype(f)
    x = np.arange(640)[None, :] - 512
    dist = i[:, None] - x
    c["dist_win"] = np.where((dist >= 0) & (dist <= WIN), -dist, NEG).astype(f)
    q = (np.arange(MT)[None, :, None] * P + i[:, None, None])
    b = np.arange(16)[None, None, :]
    seen = b * BLK + BLK - 1 <= q
    c["dist_cmp"] = np.where(seen, b * BLK + 0.5 * (BLK - 1) - q, NEG).astype(f)
    c["seen_cmp"] = seen.astype(f)
    c["slopes8"] = np.broadcast_to((8 * slopes).reshape(4, 1, 2), (4, P, 2)).astype(f)
    row = slopes[:, None] * np.ones((1, TS))
    t = np.arange(TS)[None, :]
    pos = np.arange(PAST).reshape(PAGES, P).T
    c["alibi_page"] = (row[None, None] * (pos[:, :, None, None] - PAST - t[None, None])).reshape(P, PAGES * 64).astype(f)
    wpos = (PAST - WIN + np.arange(WIN)).reshape(4, P).T
    dw = PAST + t[None, None] - wpos[:, :, None, None]
    c["alibi_win"] = np.where(dw <= WIN, -row[None, None] * dw, NEG).reshape(P, 4 * 64).astype(f)
    tok = np.arange(TS)[:, None, None]
    c["alibi_new"] = np.where(tok <= t[None], row[None] * (tok - t[None]), NEG).reshape(TS, 64).astype(f)
    cen = np.arange(P) * BLK + 0.5 * (BLK - 1)
    c["alibi_cmp"] = (row.reshape(64, 1) * (cen[None, :] - PAST - np.tile(np.arange(TS), NH)[:, None])).astype(f)
    c["sel_mod_p"] = (np.arange(MODS)[:, None] == 0).astype(f) * np.ones((1, P), f)
    c["sel_mod_s"] = (np.arange(MODS)[:, None] == 1 + np.arange(SROWS)[None, :] // TS).astype(f)
    r = np.arange(64)
    target = (r // 32) * 8 + r % 8
    c["head_sum"] = (np.arange(NS)[None, :, None] * 16 + target[:, None, None] == np.arange(P)[None, None, :]).reshape(64, NS * P).astype(f)
    c["half"] = (np.arange(2)[:, None] == i[None, :] // 64).astype(f)
    return c


@contextmanager
def phase(nc, *names):
    before = nc.snapshot_sems()
    sems = [nc.alloc_semaphore(f"{name}_{nc.next_id()}") for name in names]
    nums = [s.num for s in sems]
    with nc.Block() as block:
        yield (block, *sems)
    nc.all_engine_barrier(sems_to_clear=range(min(nums), max(nums) + 1))
    nc.restore_sems(before)


def banks(ctx, nc, name, shape):
    n = int(np.prod(shape[1:]))
    whole = -(-n // 512) * 512
    t = ctx.enter_context(nc.psum_tensor(f"{name}_{nc.next_id()}", [P, whole], F32))
    ap = t[0:shape[0], 0:n]
    if len(shape) == 3:
        ap = ap.rearrange("p (a b) -> p a b", a=shape[1])
    if len(shape) == 4:
        ap = ap.rearrange("p (a b c) -> p a b c", a=shape[1], b=shape[2])
    return ap


class InOrder:

    def __init__(self, eng, sem):
        self.eng, self.sem, self.n = eng, sem, 0

    def __call__(self, ins):
        self.n += 1
        ins.then_inc(self.sem, 1)
        self.eng.wait_ge(self.sem, self.n)


def load_all(nc, pairs):
    with phase(nc, "loaded") as (block, loaded):
        @block.sync
        def _(sp):
            for dst, src in pairs:
                sp.dma_start(dst, src).then_inc(loaded, 16)
            sp.wait_ge(loaded, 16 * len(pairs))


def gemm_rows(nc, lhsT, rows, kt, w, out_rows, width, steps, bias=None, tag=""):
    slots = 2 if steps >= 2 else 1
    loops = steps // slots
    n_m = len(rows)
    ring = 3 if (slots * n_m) % 3 == 0 else slots
    wr = w.rearrange("(k p) n -> p k n", p=P)
    per = slots * n_m
    with ExitStack() as ctx:
        ws = [ctx.enter_context(nc.sbuf_tensor(f"w{tag}{s}_{nc.next_id()}", [P, kt, width], F32)) for s in range(slots)]
        bs = [ctx.enter_context(nc.sbuf_tensor(f"b{tag}{s}_{nc.next_id()}", [rows[0], width], F32)) for s in range(slots)] if bias is not None else None
        stage = [ctx.enter_context(nc.sbuf_tensor(f"st{tag}{s}_{nc.next_id()}", [P, width], F32)) for s in range(ring)]
        psum = [ctx.enter_context(nc.psum_tensor(f"pp{tag}{s}_{nc.next_id()}", [P, 512], F32)) for s in range(ring)]
        names = ([f"w_loaded{s}" for s in range(slots)] + [f"w_free{s}" for s in range(slots)]
                 + ["product_ready", "psum_free", "evacuated"] + [f"stage_free{r}" for r in range(ring)])
        with phase(nc, *names) as (block, *sems):
            w_loaded, w_free = sems[:slots], sems[slots:2 * slots]
            product_ready, psum_free, evacuated = sems[2 * slots:2 * slots + 3]
            stage_free = sems[2 * slots + 3:]
            readers = 2 if bias is not None else 1
            dmas_per_slot = 16 * (2 if bias is not None else 1)

            @block.sync
            def _(sp):
                def body(i):
                    for s in range(slots):
                        sp.wait_ge(w_free[s], i * readers + readers)
                        cols = bass.ds(i * (slots * width) + s * width, width)
                        sp.dma_start(ws[s][:], wr[:, :, cols]).then_inc(w_loaded[s], 16)
                        if bias is not None:
                            sp.dma_start(bs[s][:], bias[:, cols]).then_inc(w_loaded[s], 16)
                if loops > 1:
                    with sp.Fori(0, loops) as i:
                        body(i)
                else:
                    body(0)

            @block.tensor
            def _(pe):
                for s in range(slots):
                    pe.sem_inc(w_free[s], 1)

                def body(i):
                    for s in range(slots):
                        pe.wait_ge(w_loaded[s], i * dmas_per_slot + dmas_per_slot)
                        for m in range(n_m):
                            n = s * n_m + m
                            pe.wait_ge(psum_free, i * per + n + 1)
                            for k in range(kt):
                                last = pe.matmul(psum[n % ring][0:rows[m], 0:width], lhsT(m, k), ws[s][:, k, :],
                                                 start=(k == 0), stop=(k == kt - 1))
                            last.then_inc(product_ready, 1)
                        pe.wait_ge(product_ready, i * per + (s + 1) * n_m)
                        pe.sem_inc(w_free[s], 1)
                if loops > 1:
                    with pe.Fori(0, loops) as i:
                        body(i)
                else:
                    body(0)

            @block.vector
            def _(dve):
                dve.sem_inc(psum_free, ring)
                if bias is not None:
                    for s in range(slots):
                        dve.sem_inc(w_free[s], 1)

                def body(i):
                    for n in range(per):
                        m, r = n % n_m, rows[n % n_m]
                        dve.wait_ge(product_ready, i * per + n + 1)
                        dve.wait_ge(stage_free[n % ring], i * (16 * (per // ring)) + 16 * (n // ring) + 16)
                        if bias is None:
                            ins = dve.tensor_copy(stage[n % ring][0:r, :], psum[n % ring][0:r, 0:width])
                        else:
                            ins = dve.tensor_tensor(stage[n % ring][0:r, :], psum[n % ring][0:r, 0:width],
                                                    bs[n // n_m][0:r, :], ALU.add)
                        ins.then_inc(evacuated, 1)
                        dve.wait_ge(evacuated, i * per + n + 1)
                        dve.sem_inc(psum_free, 1)
                        if bias is not None and n % n_m == n_m - 1:
                            dve.sem_inc(w_free[n // n_m], 1)
                if loops > 1:
                    with dve.Fori(0, loops) as i:
                        body(i)
                else:
                    body(0)

            @block.scalar
            def _(act):
                for r in range(ring):
                    act.sem_inc(stage_free[r], 16)

                def body(i):
                    for n in range(per):
                        s, m = divmod(n, n_m)
                        act.wait_ge(evacuated, i * per + n + 1)
                        cols = bass.ds(i * (slots * width) + s * width, width)
                        dst, src = out_rows(m, cols), stage[n % ring][0:rows[m], :]
                        act.dma_start(dst, src).then_inc(stage_free[n % ring], 16)
                if loops > 1:
                    with act.Fori(0, loops) as i:
                        body(i)
                else:
                    body(0)
                for r in range(ring):
                    act.wait_ge(stage_free[r], 16 * (1 + loops * per // ring))


def transpose_rows(nc, src, hT, ident, mod=None, tiles=TILES, loads=(), tag=""):
    with ExitStack() as ctx:
        ps = [ctx.enter_context(nc.psum_tensor(f"tp{s}_{nc.next_id()}", [P, KD, P], F32)) for s in range(2)]
        with phase(nc, "loaded", "turned", "even_out", "odd_out", "sample_steps") as (
                block, loaded, turned, even_out, odd_out, sample_steps):
            @block.sync
            def _(sp):
                for dst, s in loads:
                    sp.dma_start(dst, s).then_inc(loaded, 16)

            @block.tensor
            def _(pe):
                if loads:
                    pe.wait_ge(loaded, 16 * len(loads))
                for m in range(tiles):
                    if m >= 2:
                        pe.wait_ge(even_out, m - 1)
                        pe.wait_ge(odd_out, m - 1)
                    for k in range(KD):
                        last = pe.transpose(ps[m % 2][:, k, 0:ROWS[m]], src[0:ROWS[m], m, k * P:(k + 1) * P],
                                            ident[0:ROWS[m], 0:ROWS[m]])
                    last.then_inc(turned, 1)

            @block.scalar
            def _(act):
                for m in range(tiles):
                    act.wait_ge(turned, m + 1)
                    r = ROWS[m]
                    if mod is None:
                        act.copy(hT[:, 0:4, m * P:m * P + r], ps[m % 2][:, 0:4, 0:r]).then_inc(even_out, 1)
                    elif m < MT:
                        for k in range(4):
                            last = act.activation(hT[:, k, m * P:m * P + r], ps[m % 2][:, k, 0:r], ACT.Identity,
                                                  bias=mod[0][:, k, 0:1], scale=mod[1][:, k, 0:1])
                        last.then_inc(even_out, 1)
                    else:
                        act.sem_inc(even_out, 1)

            @block.vector
            def _(dve):
                for m in range(tiles):
                    dve.wait_ge(turned, m + 1)
                    r = ROWS[m]
                    if mod is None:
                        dve.tensor_copy(hT[:, 4:8, m * P:m * P + r], ps[m % 2][:, 4:8, 0:r]).then_inc(odd_out, 1)
                    elif m < MT:
                        for k in range(4, KD):
                            last = dve.tensor_scalar(hT[:, k, m * P:m * P + r], ps[m % 2][:, k, 0:r],
                                                     mod[1][:, k, 0:1], mod[0][:, k, 0:1], ALU.mult, ALU.add)
                        last.then_inc(odd_out, 1)
                    else:
                        step = InOrder(dve, sample_steps)
                        for k in range(KD):
                            o = hT[:, k, SEQ:T].rearrange("p (s t) -> p s t", t=TS)
                            step(dve.tensor_tensor(o, ps[m % 2][:, k, 0:r].rearrange("p (s t) -> p s t", t=TS),
                                                   mod[1][:, k, 1:MODS].unsqueeze(2).broadcast_to([P, NS, TS]), ALU.mult))
                            step(dve.tensor_tensor(o, o, mod[0][:, k, 1:MODS].unsqueeze(2).broadcast_to([P, NS, TS]), ALU.add))
                        dve.sem_inc(odd_out, 1)


def post_norm(nc, X, y, gate, ln_g, ln_b, c, out=None):
    with ExitStack() as ctx:
        sb = lambda n, s: ctx.enter_context(nc.sbuf_tensor(f"{n}_{nc.next_id()}", s, F32))
        ys = [sb("y", [P, D]) for _ in range(3)]
        gates, gate_p, gate_s = sb("gates", [MODS, D]), sb("gate_p", [P, D]), sb("gate_s", [SROWS, D])
        gB, bB = sb("gB", [P, D]), sb("bB", [P, D])
        stats, mv, rstd = sb("stats", [P, TILES, 2, 6]), sb("mv", [P, TILES, 2]), sb("rstd", [P, TILES])
        eps = sb("eps", [P, 1])
        ps = [ctx.enter_context(nc.psum_tensor(f"pg{s}_{nc.next_id()}", [P, D], F32)) for s in range(2)]
        with phase(nc, "params", "y0", "y1", "y2", "y_used", "gate_ready", "gate_out", "dve_steps", "act_steps", "rstd_ready",
                   "x_ready", "stored") as (
                block, params, y0, y1, y2, y_used, gate_ready, gate_out, dve_steps, act_steps, rstd_ready, x_ready, stored):
            y_loaded = [y0, y1, y2]

            @block.sync
            def _(sp):
                sp.dma_start(gates[:], gate).then_inc(params, 16)
                for m in range(TILES):
                    if m >= 3:
                        sp.wait_ge(y_used, m - 2)
                    sp.dma_start(ys[m % 3][0:ROWS[m], :], y[m * P:m * P + ROWS[m], :]).then_inc(y_loaded[m % 3], 16)
                if out is not None:
                    for m in range(TILES):
                        sp.wait_ge(x_ready, m + 1)
                        dst = out[0][m * P:(m + 1) * P, :] if m < MT else out[1]
                        sp.dma_start(dst, X[0:ROWS[m], m, :]).then_inc(stored, 16)
                    sp.wait_ge(stored, 16 * TILES)

            @block.tensor
            def _(pe):
                pe.wait_ge(params, 48)
                for n in range(2):
                    cols = slice(n * 512, n * 512 + 512)
                    pe.matmul(ps[0][:, cols], c["sel_mod_p"][:], gates[:, cols], start=True, stop=True)
                    last = pe.matmul(ps[1][0:SROWS, cols], c["sel_mod_s"][:], gates[:, cols], start=True, stop=True)
                last.then_inc(gate_ready, 1)

            @block.gpsimd
            def _(pool):
                pool.memset(mv[:], 1.0).then_inc(gate_out, 1)
                pool.memset(eps[:], LN_EPS).then_inc(gate_out, 1)

            @block.scalar
            def _(act):
                act.dma_start(gB[:], ln_g.partition_broadcast(P)).then_inc(params, 16)
                act.dma_start(bB[:], ln_b.partition_broadcast(P)).then_inc(params, 16)
                act.wait_ge(gate_ready, 1)
                act.copy(gate_p[:], ps[0][:]).then_inc(gate_out, 1)
                act.copy(gate_s[:], ps[1][0:SROWS, :]).then_inc(gate_out, 1)
                act.wait_ge(rstd_ready, 1)
                step = InOrder(act, act_steps)
                step(act.activation(rstd[:], mv[:, :, 1], ACT.Ln, bias=eps[:, 0:1]))
                act.activation(rstd[:], rstd[:], ACT.Exp, scale=-0.5).then_inc(rstd_ready, 1)

            @block.vector
            def _(dve):
                step = InOrder(dve, dve_steps)
                dve.wait_ge(gate_out, 4)
                dve.wait_ge(params, 48)
                for m in range(TILES):
                    r = ROWS[m]
                    dve.wait_ge(y_loaded[m % 3], 16 * (m // 3 + 1))
                    yt = ys[m % 3][0:r, :]
                    step(dve.tensor_tensor(yt, yt, (gate_p if m < MT else gate_s)[0:r, :], ALU.mult))
                    step(dve.scalar_tensor_tensor(X[0:r, m, :], X[0:r, m, :], ALPHA, yt, ALU.mult, ALU.add))
                    dve.sem_inc(y_used, 1)
                    for n in range(2):
                        step(dve.bn_stats(stats[0:r, m, n, :], X[0:r, m, n * 512:(n + 1) * 512]))
                    step(dve.bn_aggr(mv[0:r, m, :], stats[0:r, m, :, :].rearrange("p a b -> p (a b)")))
                dve.sem_inc(rstd_ready, 1)
                dve.wait_ge(rstd_ready, 2)
                for m in range(TILES):
                    r = ROWS[m]
                    x = X[0:r, m, :]
                    step(dve.tensor_scalar(x, x, mv[0:r, m, 0:1], rstd[0:r, m:m + 1], ALU.subtract, ALU.mult))
                    step(dve.tensor_tensor(x, x, gB[0:r, :], ALU.mult))
                    dve.tensor_tensor(x, x, bB[0:r, :], ALU.add).then_inc(x_ready, 1)


def swiglu_hidden(nc, hT, hid, w_in):
    wr = w_in.rearrange("(k p) (two n) -> p two k n", p=P, two=2)
    chunks = [(0, 512), (512, 512), (1024, SROWS)]
    NB = 3
    with ExitStack() as ctx:
        sb = lambda n, s: ctx.enter_context(nc.sbuf_tensor(f"{n}_{nc.next_id()}", s, F32))
        ws = [sb("wf", [P, 2, KD, P]) for _ in range(2)]
        e = [sb("e", [P, 512]) for _ in range(NB)]
        ps = [ctx.enter_context(nc.psum_tensor(f"pf{s}_{nc.next_id()}", [P, 2, 512], F32)) for s in range(NB)]
        with phase(nc, "w_loaded0", "w_loaded1", "w_free0", "w_free1", "pair_ready", "silu_ready", "pair_used", "dve_steps") as (
                block, w_loaded0, w_loaded1, w_free0, w_free1, pair_ready, silu_ready, pair_used, dve_steps):
            w_loaded, w_free = [w_loaded0, w_loaded1], [w_free0, w_free1]

            @block.sync
            def _(sp):
                with sp.Fori(0, FT // 2) as i:
                    for s in range(2):
                        sp.wait_ge(w_free[s], i + 1)
                        for two in range(2):
                            sp.dma_start(ws[s][:, two], wr[:, two, :, bass.ds(i * 256 + s * P, P)]).then_inc(w_loaded[s], 16)

            @block.tensor
            def _(pe):
                pe.sem_inc(w_free0, 1)
                pe.sem_inc(w_free1, 1)
                with pe.Fori(0, FT // 2) as i:
                    for s in range(2):
                        pe.wait_ge(w_loaded[s], i * 32 + 32)
                        for j, (t0, tn) in enumerate(chunks):
                            n = s * 3 + j
                            pe.wait_ge(pair_used, i * 6 + n + 1)
                            for two in range(2):
                                for k in range(KD):
                                    last = pe.matmul(ps[n % NB][:, two, 0:tn], ws[s][:, two, k, :], hT[:, k, t0:t0 + tn],
                                                     start=(k == 0), stop=(k == KD - 1))
                            last.then_inc(pair_ready, 1)
                        pe.wait_ge(pair_ready, i * 6 + s * 3 + 3)
                        pe.sem_inc(w_free[s], 1)

            @block.scalar
            def _(act):
                with act.Fori(0, FT // 2) as i:
                    for s in range(2):
                        for j, (t0, tn) in enumerate(chunks):
                            n = s * 3 + j
                            act.wait_ge(pair_ready, i * 6 + n + 1)
                            act.activation(e[n % NB][:, 0:tn], ps[n % NB][:, 0, 0:tn], ACT.Silu).then_inc(silu_ready, 1)

            @block.vector
            def _(dve):
                dve.sem_inc(pair_used, NB)
                with dve.Fori(0, FT // 2) as i:
                    for s in range(2):
                        for j, (t0, tn) in enumerate(chunks):
                            n = s * 3 + j
                            et, pt = e[n % NB][:, 0:tn], ps[n % NB]
                            dve.wait_ge(silu_ready, i * 6 + n + 1)
                            dve.tensor_tensor(hid[:, bass.ds(i * (2 * T) + s * T + t0, tn)], et, pt[:, 1, 0:tn], ALU.mult).then_inc(dve_steps, 1)
                            dve.wait_ge(dve_steps, i * 6 + n + 1)
                            dve.sem_inc(pair_used, 1)


def adaln_mods(nc, A, c, modT, mod_rows):
    with ExitStack() as ctx:
        sb = lambda n, s: ctx.enter_context(nc.sbuf_tensor(f"{n}_{nc.next_id()}", s, F32))
        cond, ex, cT = sb("cond", [MODS, D]), sb("ex", [MODS, D]), sb("cT", [P, KD, MODS])
        ps = ctx.enter_context(nc.psum_tensor("cond_ps", [P, KD, MODS], F32))
        with phase(nc, "loaded", "exp_ready", "dve_steps", "silu_ready", "turned") as (
                block, loaded, exp_ready, dve_steps, silu_ready, turned):
            @block.sync
            def _(sp):
                sp.dma_start(cond[0:1, :], A["c_prompt"]).then_inc(loaded, 16)
                sp.dma_start(cond[1:MODS, :], A["c_sample"]).then_inc(loaded, 16)

            @block.scalar
            def _(act):
                act.wait_ge(loaded, 32)
                act.activation(ex[:], cond[:], ACT.Exp, scale=-1.0).then_inc(exp_ready, 1)

            @block.vector
            def _(dve):
                step = InOrder(dve, dve_steps)
                dve.wait_ge(exp_ready, 1)
                step(dve.tensor_scalar(ex[:], ex[:], 1.0, None, ALU.add))
                step(dve.reciprocal(ex[:], ex[:]))
                dve.tensor_tensor(cond[:], cond[:], ex[:], ALU.mult).then_inc(silu_ready, 1)
                dve.wait_ge(turned, 1)
                dve.tensor_copy(cT[:], ps[:]).then_inc(dve_steps, 1)

            @block.tensor
            def _(pe):
                pe.wait_ge(silu_ready, 1)
                for k in range(KD):
                    last = pe.transpose(ps[:, k, :], cond[:, k * P:(k + 1) * P], c["ident"][0:MODS, 0:MODS])
                last.then_inc(turned, 1)

        for layer in range(2):
            gemm_rows(nc, lambda m, k: cT[:, k, :], [MODS], KD, A["w_ada"][layer],
                      lambda m, cols, l=layer: mod_rows[:, l].rearrange("s n -> s n")[:, cols], 512, 12,
                      bias=A["b_ada"][layer].partition_broadcast(MODS), tag="ada")
        rows = sb("mod_rows_sb", [MODS, 2, 6, D])
        pm = [ctx.enter_context(nc.psum_tensor(f"pm{s}", [P, 2, 4, KD, 4], F32)) for s in range(0)]
        pt = [ctx.enter_context(nc.psum_tensor(f"pmt{l}", [P, 4, KD, MODS], F32)) for l in range(2)]
        with phase(nc, "loaded", "turned", "copied") as (block, loaded, turned, copied):
            @block.sync
            def _(sp):
                sp.dma_start(rows[:], mod_rows.rearrange("s l (c n) -> s l c n", c=6)).then_inc(loaded, 16)

            @block.tensor
            def _(pe):
                pe.wait_ge(loaded, 16)
                for l in range(2):
                    for n, chunk in enumerate((0, 1, 3, 4)):
                        for k in range(KD):
                            last = pe.transpose(pt[l][:, n, k, :], rows[:, l, chunk, k * P:(k + 1) * P],
                                                c["ident"][0:MODS, 0:MODS])
                last.then_inc(turned, 1)

            @block.vector
            def _(dve):
                dve.wait_ge(turned, 1)
                for l in range(2):
                    for n in range(4):
                        dve.tensor_scalar(modT[:, l, n], pt[l][:, n], float(n % 2), None, ALU.add).then_inc(copied, 1)


def ffn(nc, A, c, X, layer, modT, mod_rows, y, out=None):
    with ExitStack() as outer:
        hid = outer.enter_context(nc.sbuf_tensor(f"hid_{nc.next_id()}", [P, FT * T], F32))
        with nc.sbuf_tensor(f"hT_{nc.next_id()}", [P, KD, T], F32) as hT:
            transpose_rows(nc, X, hT, c["ident"], (modT[:, layer, 2], modT[:, layer, 3]))
            swiglu_hidden(nc, hT, hid, A["w_ffn_in"][layer])
        gemm_rows(nc, lambda m, k: hid[:, k * T + m * P:k * T + m * P + ROWS[m]], ROWS, FT, A["w_ffn_out"][layer],
                  lambda m, cols: y[m * P:m * P + ROWS[m], cols], 256, 4, tag="f2")
    post_norm(nc, X, y, mod_rows[:, layer, 5 * D:6 * D], A["ln_g"][layer, 1], A["ln_b"][layer, 1], c, out)


def gla_gates(nc, A, c, proj, log_a):
    W = GH * GK
    with ExitStack() as ctx:
        sb = lambda n, s: ctx.enter_context(nc.sbuf_tensor(f"{n}_{nc.next_id()}", s, F32))
        gk, gkT = sb("gk", [P, TILES, 16]), sb("gkT", [16, T])
        w2, bias = sb("w_gk2", [16, W]), sb("b_gk", [P, W])
        x, e = sb("gate_x", [P, TILES, W]), sb("gate_e", [P, TILES, W])
        pt = [ctx.enter_context(nc.psum_tensor(f"gkt{i}", [16, 512], F32)) for i in range(3)]
        px = [ctx.enter_context(nc.psum_tensor(f"gx{i}", [P, 2, W], F32)) for i in range(5)]
        with phase(nc, "loaded", "turned", "copied", "product", "dve_steps", "abs_ready", "log_ready", "act_steps", "done", "stored") as (
                block, loaded, turned, copied, product, dve_steps, abs_ready, log_ready, act_steps, done, stored):
            @block.sync
            def _(sp):
                g = proj[:, GK_A:GK_A + 16]
                sp.dma_start(gk[:, 0:MT, :], g[0:SEQ].rearrange("(m p) k -> p m k", p=P)).then_inc(loaded, 16)
                sp.dma_start(gk[0:SROWS, MT, :], g[SEQ:T]).then_inc(loaded, 16)
                sp.dma_start(w2[:], A["ab_w_gk2"][0]).then_inc(loaded, 16)
                sp.dma_start(bias[:], A["ab_b_gk"][0].partition_broadcast(P)).then_inc(loaded, 16)
                sp.wait_ge(done, 1)
                sp.dma_start(log_a[0:SEQ].rearrange("(m p) k -> p m k", p=P), x[:, 0:MT, :]).then_inc(stored, 16)
                sp.dma_start(log_a[SEQ:T], x[0:SROWS, MT, :]).then_inc(stored, 16)
                sp.wait_ge(stored, 32)

            @block.tensor
            def _(pe):
                pe.wait_ge(loaded, 64)
                for m in range(TILES):
                    last = pe.transpose(pt[m // 4][:, (m % 4) * P:(m % 4) * P + ROWS[m]], gk[0:ROWS[m], m, :], c["ident"][0:ROWS[m], 0:ROWS[m]])
                last.then_inc(turned, 1)
                pe.wait_ge(copied, 3)
                for m in range(TILES):
                    last = pe.matmul(px[m // 2][0:ROWS[m], m % 2, :], gkT[:, m * P:m * P + ROWS[m]], w2[:], start=True, stop=True)
                last.then_inc(product, 1)

            @block.scalar
            def _(act):
                step = InOrder(act, act_steps)
                act.wait_ge(abs_ready, 1)
                step(act.activation(e[:], e[:], ACT.Exp, scale=-1.0))
                act.activation(e[:], e[:], ACT.Ln, bias=1.0).then_inc(log_ready, 1)

            @block.vector
            def _(dve):
                step = InOrder(dve, dve_steps)
                dve.wait_ge(turned, 1)
                for i in range(3):
                    w = min(512, T - i * 512)
                    dve.tensor_copy(gkT[:, i * 512:i * 512 + w], pt[i][:, 0:w]).then_inc(copied, 1)
                dve.wait_ge(product, 1)
                step(dve.memset(x[:, MT, :], 0.0))
                for m in range(TILES):
                    step(dve.tensor_tensor(x[0:ROWS[m], m, :], px[m // 2][0:ROWS[m], m % 2, :], bias[0:ROWS[m], :], ALU.add))
                dve.scalar_tensor_tensor(e[:], x[:], -1.0, x[:], ALU.mult, ALU.max).then_inc(abs_ready, 1)
                step(dve.tensor_scalar(x[:], x[:], 0.0, None, ALU.min))
                dve.wait_ge(log_ready, 1)
                step(dve.tensor_tensor(x[:], x[:], e[:], ALU.subtract))
                dve.tensor_scalar(x[:], x[:], 1.0 / 16.0, None, ALU.mult).then_inc(done, 1)


def gla_chunk(nc, c, C, gnorm, src, la_src, dst, S, state_in=None, state_out=None):
    W = GH * GK
    V = GH * GV
    with ExitStack() as ctx:
        sb = lambda n, s: ctx.enter_context(nc.sbuf_tensor(f"{n}_{nc.next_id()}", s, F32))
        ps = lambda n, s: banks(ctx, nc, n, s)
        row, la = sb("row", [C, 1536]), sb("la", [C, W])
        e_in, e_mid, e_neg, e_end, e_last = [sb(n, [C, W]) for n in ("e_in", "e_mid", "e_neg", "e_end")] + [sb("e_last", [GK, GH])]
        qs, q2, k2, k4 = [sb(n, [C, W]) for n in ("qs", "q2", "k2", "k4")]
        tr, pT = sb("tr", [GK, 12, C]), sb("pT", [C, GH, C])
        o, sq, er = sb("o", [C, GH, GV]), sb("sq", [C, GH, GV]), sb("er", [C, V])
        ss, eps = sb("ss", [C, GH]), sb("eps", [C, 1])
        pa, pb = ps("pa", [C, 512]), ps("pb", [C, 512])
        pl, pt = pb[:, W:W + GH] if C == GK else ps("pl", [GK, GH]), ps("pt", [GK, 2, 8, CHUNK])[:, :, 0:6, :]
        psc, po, pkv = ps("psc", [C, GH, C]), ps("po", [C, GH, GV]), ps("pkv", [GK, GH, GV])
        tri, tri_mid, tri_end, ones = c["tri"], c["tri_mid"], c["tri_end"], c["ones"]
        with phase(nc, "loaded", "state_loaded", "sums", "exps", "scaled", "turned", "turned_out", "scores", "masked", "products",
                   "o_out", "square", "ln", "stored", "dve_steps", "act_steps") as (
                block, loaded, state_loaded, sums, exps, scaled, turned, turned_out, scores, masked, products, o_out, square,
                ln, stored, dve_steps, act_steps):
            @block.sync
            def _(sp):
                sp.dma_start(la[:], la_src).then_inc(loaded, 16)
                sp.dma_start(row[:], src).then_inc(loaded, 16)
                if state_in is not None:
                    sp.dma_start(S[:], state_in).then_inc(state_loaded, 16)
                sp.wait_ge(o_out, 2)
                sp.dma_start(dst, o[:].rearrange("p h v -> p (h v)")).then_inc(stored, 16)
                if state_out is not None:
                    sp.dma_start(state_out, S[:]).then_inc(stored, 16)
                sp.wait_ge(stored, 16 * (2 if state_out is not None else 1))

            @block.tensor
            def _(pe):
                pe.wait_ge(loaded, 32)
                pe.matmul(pa[:, 0:W], tri[0:C, 0:C], la[:], start=True, stop=True)
                pe.matmul(pa[:, W:2 * W], tri_mid[0:C, 0:C], la[:], start=True, stop=True)
                pe.matmul(pb[:, 0:W], tri_end[0:C, 0:C], la[:], start=True, stop=True)
                for h in range(GH):
                    last = pe.matmul(pl[:, h:h + 1], la[:, h * GK:(h + 1) * GK], ones[0:C, 0:1], start=True, stop=True)
                last.then_inc(sums, 1)
                pe.wait_ge(scaled, 3)
                for n, x in enumerate((qs, q2, k2)):
                    for h in range(GH):
                        last = pe.transpose(pt[:, (4 * n + h) // 6, (4 * n + h) % 6, 0:C], x[:, h * GK:(h + 1) * GK], c["ident"][0:C, 0:C])
                last.then_inc(turned, 1)
                pe.wait_ge(turned_out, 1)
                for h in range(GH):
                    last = pe.matmul(psc[:, h, :], tr[:, 8 + h, :], tr[:, 4 + h, :], start=True, stop=True)
                last.then_inc(scores, 1)
                if state_in is not None:
                    pe.wait_ge(state_loaded, 16)
                pe.wait_ge(scaled, 4)
                pe.wait_ge(masked, 1)
                for h in range(GH):
                    v = row[:, 512 + h * GV:512 + (h + 1) * GV]
                    pe.matmul(po[:, h, :], tr[:, h, :], S[:, h, :], start=True, stop=False)
                    pe.matmul(po[:, h, :], pT[:, h, :], v, start=False, stop=True)
                    last = pe.matmul(pkv[:, h, :], k4[:, h * GK:(h + 1) * GK], v, start=True, stop=True)
                last.then_inc(products, 1)

            @block.scalar
            def _(act):
                step = InOrder(act, act_steps)
                act.wait_ge(sums, 1)
                act.activation(e_in[:], pa[:, 0:W], ACT.Exp).then_inc(exps, 1)
                act.activation(e_mid[:], pa[:, W:2 * W], ACT.Exp).then_inc(exps, 1)
                act.activation(e_neg[:], pa[:, W:2 * W], ACT.Exp, scale=-1.0).then_inc(exps, 1)
                act.activation(e_end[:], pb[:, 0:W], ACT.Exp).then_inc(exps, 1)
                act.activation(e_last[:], pl, ACT.Exp).then_inc(exps, 1)
                act.activation(er[:], row[:, R_A:R_A + V], ACT.Silu).then_inc(exps, 1)
                act.wait_ge(square, 1)
                step(act.activation(ss[:], ss[:], ACT.Ln, scale=1.0 / GV, bias=eps[:, 0:1]))
                act.activation(ss[:], ss[:], ACT.Exp, scale=-0.5).then_inc(ln, 1)

            @block.vector
            def _(dve):
                step = InOrder(dve, dve_steps)
                step(dve.memset(eps[:], RMS_EPS))
                dve.wait_ge(exps, 1)
                dve.scalar_tensor_tensor(qs[:], e_in[:], GK ** -0.5, row[:, Q_A:Q_A + W], ALU.mult, ALU.mult).then_inc(scaled, 1)
                dve.wait_ge(exps, 3)
                dve.scalar_tensor_tensor(q2[:], e_mid[:], GK ** -0.5, row[:, Q_A:Q_A + W], ALU.mult, ALU.mult).then_inc(scaled, 1)
                dve.tensor_tensor(k2[:], e_neg[:], row[:, K_A:K_A + W], ALU.mult).then_inc(scaled, 1)
                dve.wait_ge(exps, 4)
                dve.tensor_tensor(k4[:], e_end[:], row[:, K_A:K_A + W], ALU.mult).then_inc(scaled, 1)
                dve.wait_ge(turned, 1)
                dve.tensor_copy(tr[:].rearrange("p (a b) i -> p a b i", a=2), pt[:, :, :, 0:C]).then_inc(turned_out, 1)
                dve.wait_ge(exps, 6)
                step(dve.tensor_tensor(er[:].rearrange("p (h v) -> p h v", h=GH), er[:].rearrange("p (h v) -> p h v", h=GH),
                                       gnorm[0:C, :].unsqueeze(1).broadcast_to([C, GH, GV]), ALU.mult))
                dve.wait_ge(scores, 1)
                dve.tensor_tensor(pT[:], psc[:], tri[0:C, 0:C].unsqueeze(1).broadcast_to([C, GH, C]), ALU.mult).then_inc(masked, 1)
                dve.wait_ge(products, 1)
                step(dve.tensor_tensor(S[:], S[:], e_last[:].unsqueeze(2).broadcast_to([GK, GH, GV]), ALU.mult))
                step(dve.tensor_tensor(S[:], S[:], pkv, ALU.add))
                dve.sem_inc(o_out, 1)
                step(dve.tensor_copy(o[:], po[:]))
                step(dve.tensor_tensor(sq[:], o[:], o[:], ALU.mult))
                dve.tensor_reduce(ss[:], sq[:], AX, ALU.add).then_inc(square, 1)
                dve.wait_ge(ln, 1)
                step(dve.tensor_tensor(o[:], o[:], ss[:].unsqueeze(2).broadcast_to([C, GH, GV]), ALU.mult))
                dve.tensor_tensor(o[:].rearrange("p h v -> p (h v)"), o[:].rearrange("p h v -> p (h v)"), er[:], ALU.mult).then_inc(o_out, 1)


def gla(nc, A, O, c, proj, log_a, mixed):
    with ExitStack() as ctx:
        S = ctx.enter_context(nc.sbuf_tensor("gla_state", [GK, GH, GV], F32))
        gnorm = ctx.enter_context(nc.sbuf_tensor("gla_norm", [CHUNK, GV], F32))
        load_all(nc, [(gnorm[:], A["ab_gla_norm"][0].partition_broadcast(CHUNK))])
        with phase(nc, "cleared") as (block, cleared):
            @block.vector
            def _(dve):
                dve.memset(S[:], 0.0).then_inc(cleared, 1)
        with nc.Fori(0, SEQ // CHUNK) as i:
            rows = bass.ds(i * CHUNK, CHUNK)
            gla_chunk(nc, c, CHUNK, gnorm, proj[rows, 0:1536], log_a[rows, :], mixed[rows, 0:512], S)
        with phase(nc, "stored") as (block, stored):
            @block.sync
            def _(sp):
                sp.dma_start(O["p_gla"][0, 0].rearrange("h k v -> k h v"), S[:]).then_inc(stored, 16)
                sp.wait_ge(stored, 16)
        with nc.Fori(0, NS) as i:
            rows = bass.ds(i * TS + SEQ, TS)
            gla_chunk(nc, c, TS, gnorm, proj[rows, 0:1536], log_a[rows, :], mixed[rows, 0:512], S,
                      state_in=A["state_gla"][0, bass.ds(i, 1)].rearrange("b h k v -> k (b h) v"),
                      state_out=O["s_gla"][0, bass.ds(i, 1)].rearrange("b h k v -> k (b h) v"))


def project_in(nc, A, hT, proj):
    gemm_rows(nc, lambda m, k: hT[:, k, m * P:m * P + ROWS[m]], ROWS, KD, A["ab_w_in"][0],
              lambda m, cols: proj[m * P:m * P + ROWS[m], cols], 476, 6, tag="ab")


def conv_tile(nc, r, cw, eps, taps, dst):
    QK = 2 * DH
    with ExitStack() as ctx:
        sb = lambda n, s: ctx.enter_context(nc.sbuf_tensor(f"{n}_{nc.next_id()}", s, F32))
        x = [sb(f"tap{j}", [r, NCH]) for j in range(4)]
        sq, ss = sb("sq", [r, D]), sb("ss", [r, QK])
        with phase(nc, "l0", "l1", "l2", "l3", "loaded3", "pool_steps", "pool_done", "act_steps", "silu_done", "dve_steps", "conv_done", "sums_done",
                   "ln_done", "done", "stored") as (block, l0, l1, l2, l3, loaded3, pool_steps, pool_done, act_steps, silu_done, dve_steps, conv_done,
                                          sums_done, ln_done, done, stored):
            tap_loaded = [l0, l1, l2, l3]

            @block.sync
            def _(sp):
                for j in range(4):
                    sp.dma_start(x[j][:], taps[j]).then_inc(tap_loaded[j], 16)
                for n in range(3):
                    if n < 2:
                        sp.wait_ge(done, n + 1)
                    else:
                        sp.wait_ge(silu_done, 3)
                    sp.dma_start(dst[:, n * D:(n + 1) * D], x[0][:, n * D:(n + 1) * D]).then_inc(stored, 16)
                sp.wait_ge(stored, 48)

            @block.gpsimd
            def _(pool):
                for j in (3, 2):
                    pool.wait_ge(tap_loaded[j], 16)
                    pool.tensor_tensor(x[j][:], x[j][:], cw[0:r, j, :], ALU.mult).then_inc(pool_done, 1)

            @block.vector
            def _(dve):
                step = InOrder(dve, dve_steps)
                for j in (0, 1):
                    dve.wait_ge(tap_loaded[j], 16)
                    step(dve.tensor_tensor(x[j][:], x[j][:], cw[0:r, j, :], ALU.mult))
                step(dve.tensor_tensor(x[0][:], x[0][:], x[1][:], ALU.add))
                for j in (3, 2):
                    dve.wait_ge(pool_done, 4 - j)
                    step(dve.tensor_tensor(x[0][:], x[0][:], x[j][:], ALU.add))
                dve.sem_inc(conv_done, 1)
                for n in range(2):
                    dve.wait_ge(silu_done, n + 1)
                    step(dve.tensor_tensor(sq[:], x[0][:, n * D:(n + 1) * D], x[0][:, n * D:(n + 1) * D], ALU.mult))
                    step(dve.tensor_reduce(ss[:, n * DH:(n + 1) * DH], sq[:].rearrange("p (h k) -> p h k", h=DH), AX, ALU.add))
                dve.sem_inc(sums_done, 1)
                dve.wait_ge(ln_done, 1)
                for n in range(2):
                    v = x[0][:, n * D:(n + 1) * D].rearrange("p (h k) -> p h k", h=DH)
                    s = ss[:, n * DH:(n + 1) * DH].unsqueeze(2).broadcast_to([r, DH, P])
                    if n == 0:
                        step(dve.tensor_scalar(ss[:, 0:DH], ss[:, 0:DH], P ** -0.5, None, ALU.mult))
                    dve.tensor_tensor(v, v, s, ALU.mult).then_inc(done, 1)

            @block.scalar
            def _(act):
                step = InOrder(act, act_steps)
                act.wait_ge(conv_done, 1)
                for n in range(3):
                    act.activation(x[0][:, n * D:(n + 1) * D], x[0][:, n * D:(n + 1) * D], ACT.Silu).then_inc(silu_done, 1)
                act.wait_ge(sums_done, 1)
                step(act.activation(ss[:], ss[:], ACT.Ln, bias=eps[0:r, 0:1]))
                act.activation(ss[:], ss[:], ACT.Exp, scale=-0.5).then_inc(ln_done, 1)


def gdn_gates(nc, A, ba, gb):
    with ExitStack() as ctx:
        sb = lambda n, s: ctx.enter_context(nc.sbuf_tensor(f"{n}_{nc.next_id()}", s, F32))
        x, e, y = sb("ba", [P, TILES, 2, DH]), sb("ba_e", [P, TILES, 2, DH]), sb("gb", [P, TILES, 2, DH])
        al, dt = sb("a_log", [P, DH]), sb("dt_bias", [P, DH])
        with phase(nc, "zeroed", "loaded", "dve_steps", "abs_ready", "exp_ready", "act_steps", "ln_ready", "done", "stored") as (
                block, zeroed, loaded, dve_steps, abs_ready, exp_ready, act_steps, ln_ready, done, stored):
            @block.sync
            def _(sp):
                sp.wait_ge(zeroed, 1)
                sp.dma_start(x[:, 0:MT], ba[0:SEQ].rearrange("(m p) (c h) -> p m c h", p=P, c=2)).then_inc(loaded, 16)
                sp.dma_start(x[0:SROWS, MT], ba[SEQ:T].rearrange("p (c h) -> p c h", c=2)).then_inc(loaded, 16)
                sp.dma_start(al[:], A["c_a_log"][0].partition_broadcast(P)).then_inc(loaded, 16)
                sp.dma_start(dt[:], A["c_dt_bias"][0].partition_broadcast(P)).then_inc(loaded, 16)
                sp.wait_ge(done, 1)
                sp.dma_start(gb[0:SEQ].rearrange("(m p) (c h) -> p m c h", p=P, c=2), y[:, 0:MT]).then_inc(stored, 16)
                sp.dma_start(gb[SEQ:T].rearrange("p (c h) -> p c h", c=2), y[0:SROWS, MT]).then_inc(stored, 16)
                sp.wait_ge(stored, 32)

            @block.vector
            def _(dve):
                step = InOrder(dve, dve_steps)
                dve.memset(x[:], 0.0).then_inc(zeroed, 1)
                dve.wait_ge(loaded, 64)
                b, a = x[:, :, 0, :], x[:, :, 1, :]
                step(dve.tensor_tensor(a, a, dt[:].unsqueeze(1).broadcast_to([P, TILES, DH]), ALU.add))
                step(dve.scalar_tensor_tensor(e[:, :, 1, :], a, -1.0, a, ALU.mult, ALU.min))
                dve.tensor_scalar(e[:, :, 0, :], b, -1.0, None, ALU.mult).then_inc(abs_ready, 1)
                dve.wait_ge(exp_ready, 2)
                step(dve.tensor_scalar(e[:, :, 0, :], e[:, :, 0, :], 1.0, None, ALU.add))
                step(dve.reciprocal(y[:, :, 1, :], e[:, :, 0, :]))
                dve.wait_ge(ln_ready, 1)
                step(dve.scalar_tensor_tensor(y[:, :, 0, :], a, 0.0, e[:, :, 1, :], ALU.max, ALU.add))
                step(dve.tensor_scalar(y[:, :, 0, :], y[:, :, 0, :], -1.0, None, ALU.mult))
                dve.tensor_tensor(y[:, :, 0, :], y[:, :, 0, :], al[:].unsqueeze(1).broadcast_to([P, TILES, DH]), ALU.mult).then_inc(done, 1)

            @block.scalar
            def _(act):
                step = InOrder(act, act_steps)
                act.wait_ge(loaded, 64)
                act.activation(al[:], al[:], ACT.Exp).then_inc(exp_ready, 1)
                act.wait_ge(abs_ready, 1)
                act.activation(e[:], e[:], ACT.Exp).then_inc(exp_ready, 1)
                act.wait_ge(exp_ready, 2)
                act.activation(e[:, :, 1, :], e[:, :, 1, :], ACT.Ln, bias=1.0).then_inc(ln_ready, 1)


def gdn_chunk(nc, c, C, cnorm, qkv_src, z_src, gb_src, dst, S, state_in=None, state_out=None):
    doublings = {64: 5, 8: 2}[C]
    HC = [C, DH, C]
    with ExitStack() as ctx:
        sb = lambda n, s: ctx.enter_context(nc.sbuf_tensor(f"{n}_{nc.next_id()}", s, F32))
        row, z, gb = sb("qkv", [C, 3, DH, P]), sb("z", [C, DH, P]), sb("gbc", [C, 2, DH])
        gm, bm = sb("gm", HC), sb("bm", HC)
        E, bs, MTr, M, Z, PT = sb("E", HC), sb("bs", HC), sb("MT", HC), sb("M", HC), sb("ZT", HC), sb("PT", HC)
        ed, eend, elast, bd = sb("ed", [C, DH]), sb("eend", [C, DH]), sb("elast", [P, DH]), sb("bd", [C, DH])
        kT, qT, wT = sb("kT", [P, DH, C]), sb("qT", [P, DH, C]), sb("wT", [P, DH, C])
        vb, kbd, kl, vn, o = [sb(n, [C, DH, P]) for n in ("vb", "kbd", "kl", "vn", "o")]
        ss, eps = sb("ss", [C, DH]), sb("eps", [C, 1])
        b0, b1, b2 = [banks(ctx, nc, n, [P, 1024]) for n in ("b0", "b1", "b2")]
        b3, b4 = banks(ctx, nc, "b3", [P, 512]), banks(ctx, nc, "b4", [P, 512])
        tri, strict, ones = c["tri"][0:C, 0:C], c["tri_end"][0:C, 0:C], c["ones"]
        sq = lambda b: b[0:C, 0:DH * C].rearrange("p (h i) -> p h i", h=DH)
        wide = lambda b, r=C: b[0:r, 0:1024].rearrange("p (h v) -> p h v", h=DH)
        two = lambda b: b[:, 0:1024].rearrange("p (h i) -> p h i", h=DH)
        with phase(nc, "loaded", "state_loaded", "gm_ready", "sums", "exps", "turned", "turned_out", "kk", "at_ready", "a_turned",
                   "squared", "m_out", "mt_out", "z_out", "wt_ready", "wt_out", "rhs_ready", "vn_ready", "vn_out", "o_ready", "s_ready",
                   "done", "sum_ready", "ln_ready", "stored", "dve_steps", "act_steps") as (
                block, loaded, state_loaded, gm_ready, sums, exps, turned, turned_out, kk, at_ready, a_turned,
                squared, m_out, mt_out, z_out, wt_ready, wt_out, rhs_ready, vn_ready, vn_out, o_ready, s_ready,
                done, sum_ready, ln_ready, stored, dve_steps, act_steps):
            @block.sync
            def _(sp):
                sp.dma_start(gb[:], gb_src).then_inc(loaded, 16)
                sp.dma_start(row[:], qkv_src).then_inc(loaded, 16)
                sp.dma_start(z[:], z_src).then_inc(loaded, 16)
                if state_in is not None:
                    sp.dma_start(S[:], state_in).then_inc(state_loaded, 16)
                sp.wait_ge(done, 2)
                sp.dma_start(dst, o[:]).then_inc(stored, 16)
                if state_out is not None:
                    sp.dma_start(state_out, S[:]).then_inc(stored, 16)
                sp.wait_ge(stored, 16 * (2 if state_out is not None else 1))

            @block.tensor
            def _(pe):
                pe.wait_ge(loaded, 48)
                for h in range(DH):
                    pe.transpose(b0[:, h * C:(h + 1) * C], row[:, 0, h, :], c["ident"][0:C, 0:C])
                for h in range(DH):
                    last = pe.transpose(b0[:, 512 + h * C:512 + (h + 1) * C], row[:, 1, h, :], c["ident"][0:C, 0:C])
                last.then_inc(turned, 1)
                pe.wait_ge(gm_ready, 2)
                pe.matmul(sq(b1), strict, gm[:], start=True, stop=True)
                pe.matmul(b1[0:C, 512:512 + DH * C], strict, bm[:], start=True, stop=True)
                pe.matmul(b3[0:C, 0:DH], tri, gb[:, 0, :], start=True, stop=True)
                pe.matmul(b3[0:C, DH:2 * DH], strict, gb[:, 0, :], start=True, stop=True)
                pe.matmul(b3[:, 2 * DH:3 * DH], ones[0:C, :], gb[:, 0, :], start=True, stop=True).then_inc(sums, 1)
                pe.wait_ge(turned_out, 2)
                for h in range(DH):
                    pe.matmul(sq(b2)[:, h, :], kT[:, h, :], kT[:, h, :], start=True, stop=True)
                for h in range(DH):
                    last = pe.matmul(b2[0:C, 512 + h * C:512 + (h + 1) * C], kT[:, h, :], qT[:, h, :], start=True, stop=True)
                last.then_inc(kk, 1)
                pe.wait_ge(at_ready, 1)
                for h in range(DH):
                    last = pe.transpose(sq(b4)[:, h, :], MTr[:, h, :], c["ident"][0:C, 0:C])
                last.then_inc(a_turned, 1)
                for s in range(doublings):
                    pe.wait_ge(m_out, s + 1)
                    if s:
                        pe.wait_ge(mt_out, s)
                        pe.wait_ge(z_out, s)
                    for h in range(DH):
                        pe.matmul(sq(b3)[:, h, :], MTr[:, h, :], M[:, h, :], start=True, stop=True)
                    for h in range(DH):
                        last = pe.matmul(sq(b4)[:, h, :], M[:, h, :], MTr[:, h, :], start=True, stop=True)
                    last.then_inc(squared, 1)
                    pe.wait_ge(m_out, s + 2)
                    for h in range(DH):
                        last = pe.matmul(sq(b0)[:, h, :], M[:, h, :], Z[:, h, :], start=True, stop=True)
                    last.then_inc(squared, 1)
                pe.wait_ge(z_out, doublings)
                pe.wait_ge(rhs_ready, 3)
                for h in range(DH):
                    last = pe.matmul(b3[:, h * C:(h + 1) * C], kbd[:, h, :], Z[:, h, :], start=True, stop=True)
                last.then_inc(wt_ready, 1)
                pe.wait_ge(wt_out, 1)
                if state_in is not None:
                    pe.wait_ge(state_loaded, 16)
                for h in range(DH):
                    pe.matmul(wide(b1)[:, h, :], Z[:, h, :], vb[:, h, :], start=True, stop=False)
                    last = pe.matmul(wide(b1)[:, h, :], wT[:, h, :], S[:, h, :], start=False, stop=True)
                last.then_inc(vn_ready, 1)
                for h in range(DH):
                    last = pe.matmul(wide(b2)[:, h, :], qT[:, h, :], S[:, h, :], start=True, stop=True)
                last.then_inc(o_ready, 1)
                pe.wait_ge(vn_out, 1)
                for h in range(DH):
                    last = pe.matmul(two(b0)[:, h, :], kl[:, h, :], vn[:, h, :], start=True, stop=True)
                last.then_inc(s_ready, 1)
                for h in range(DH):
                    last = pe.matmul(wide(b1)[:, h, :], PT[:, h, :], vn[:, h, :], start=True, stop=True)
                last.then_inc(o_ready, 1)

            @block.scalar
            def _(act):
                step = InOrder(act, act_steps)
                act.wait_ge(turned, 1)
                act.copy(qT[:], b0[:, 0:DH * C].rearrange("p (h i) -> p h i", h=DH)).then_inc(turned_out, 1)
                act.copy(kT[:], b0[:, 512:512 + DH * C].rearrange("p (h i) -> p h i", h=DH)).then_inc(turned_out, 1)
                act.wait_ge(sums, 1)
                act.activation(E[:], sq(b1), ACT.Exp).then_inc(exps, 1)
                act.copy(bs[:], b1[0:C, 512:512 + DH * C].rearrange("p (h i) -> p h i", h=DH)).then_inc(exps, 1)
                act.activation(ed[:], b3[0:C, 0:DH], ACT.Exp).then_inc(exps, 1)
                act.activation(eend[:], b3[0:C, DH:2 * DH], ACT.Exp).then_inc(exps, 1)
                act.activation(elast[:], b3[:, 2 * DH:3 * DH], ACT.Exp).then_inc(exps, 1)
                act.wait_ge(a_turned, 1)
                act.copy(M[:], sq(b4)).then_inc(m_out, 1)
                for s in range(doublings):
                    act.wait_ge(squared, 2 * s + 1)
                    if s == 0:
                        act.wait_ge(rhs_ready, 1)
                    act.copy(M[:], sq(b3)).then_inc(m_out, 1)
                    if s < doublings - 1:
                        act.copy(MTr[:], sq(b4)).then_inc(mt_out, 1)
                act.wait_ge(wt_ready, 1)
                act.copy(wT[:], b3[:, 0:DH * C].rearrange("p (h i) -> p h i", h=DH)).then_inc(wt_out, 1)
                act.wait_ge(vn_ready, 1)
                act.copy(vn[:], wide(b1)).then_inc(vn_out, 1)
                act.wait_ge(sum_ready, 1)
                step(act.activation(ss[:], ss[:], ACT.Ln, scale=1.0 / P, bias=eps[:, 0:1]))
                act.activation(ss[:], ss[:], ACT.Exp, scale=-0.5).then_inc(ln_ready, 1)
                act.activation(z[:], z[:], ACT.Silu).then_inc(ln_ready, 1)

            @block.vector
            def _(dve):
                step = InOrder(dve, dve_steps)
                step(dve.memset(eps[:], RMS_EPS))
                dve.wait_ge(loaded, 48)
                g, beta = gb[:, 0, :], gb[:, 1, :]
                over_i = lambda x: x.unsqueeze(2).broadcast_to(HC)
                over_v = lambda x, r=C: x.unsqueeze(2).broadcast_to([r, DH, P])
                over_h = lambda x: x.unsqueeze(1).broadcast_to(HC)
                dve.tensor_tensor(gm[:], over_i(g), over_h(tri), ALU.mult).then_inc(gm_ready, 1)
                dve.tensor_tensor(bm[:], over_i(beta), over_h(c["ident"][0:C, 0:C]), ALU.mult).then_inc(gm_ready, 1)
                step(dve.tensor_tensor(vb[:], row[:, 2], over_v(beta), ALU.mult))
                dve.wait_ge(exps, 5)
                step(dve.tensor_tensor(E[:], E[:], over_h(tri), ALU.mult))
                dve.wait_ge(kk, 1)
                step(dve.tensor_tensor(MTr[:], sq(b2), E[:], ALU.mult))
                dve.tensor_tensor(MTr[:], MTr[:], bs[:], ALU.mult).then_inc(at_ready, 1)
                dve.wait_ge(at_ready, 1)
                dve.tensor_tensor(Z[:], over_h(c["ident"][0:C, 0:C]), MTr[:], ALU.subtract).then_inc(rhs_ready, 1)
                step(dve.tensor_tensor(PT[:], b2[0:C, 512:512 + DH * C].rearrange("p (h i) -> p h i", h=DH), E[:], ALU.mult))
                step(dve.scalar_tensor_tensor(bd[:], ed[:], -1.0, beta, ALU.mult, ALU.mult))
                dve.tensor_tensor(kbd[:], row[:, 1], over_v(bd[:]), ALU.mult).then_inc(rhs_ready, 1)
                dve.tensor_tensor(kl[:], row[:, 1], over_v(eend[:]), ALU.mult).then_inc(rhs_ready, 1)
                dve.wait_ge(rhs_ready, 1)
                for s in range(doublings):
                    dve.wait_ge(squared, 2 * s + 2)
                    dve.tensor_tensor(Z[:], Z[:], sq(b0), ALU.add).then_inc(z_out, 1)
                    dve.wait_ge(z_out, s + 1)
                dve.wait_ge(o_ready, 1)
                step(dve.tensor_tensor(o[:], wide(b2), over_v(ed[:]), ALU.mult))
                step(dve.tensor_tensor(S[:], S[:], over_v(elast[:], P), ALU.mult))
                dve.wait_ge(s_ready, 1)
                dve.tensor_tensor(S[:], S[:], two(b0), ALU.add).then_inc(done, 1)
                dve.wait_ge(o_ready, 2)
                step(dve.tensor_tensor(o[:], o[:], wide(b1), ALU.add))
                step(dve.tensor_tensor(vb[:], o[:], o[:], ALU.mult))
                dve.tensor_reduce(ss[:], vb[:], AX, ALU.add).then_inc(sum_ready, 1)
                dve.wait_ge(ln_ready, 2)
                step(dve.tensor_tensor(o[:], o[:], over_v(ss[:]), ALU.mult))
                step(dve.tensor_tensor(z[:], z[:], cnorm[0:C, :].unsqueeze(1).broadcast_to([C, DH, P]), ALU.mult))
                dve.tensor_tensor(o[:], o[:], z[:], ALU.mult).then_inc(done, 1)


def gdn(nc, A, O, c, xp, xs, z, ba, qkv, gb, mixed):
    with ExitStack() as ctx:
        sb = lambda n, s: ctx.enter_context(nc.sbuf_tensor(f"{n}_{nc.next_id()}", s, F32))
        with phase(nc, "stored") as (block, stored):
            @block.sync
            def _(sp):
                sp.dma_start(O["p_conv"][0, 0], xp[SEQ:SEQ + 3]).then_inc(stored, 16)
                sp.dma_start(O["s_conv"][0], xs[:, TS:TS + 3]).then_inc(stored, 16)
                sp.wait_ge(stored, 32)
        with ExitStack() as inner:
            cw = inner.enter_context(nc.sbuf_tensor("conv_w", [P, 4, NCH], F32))
            eps = inner.enter_context(nc.sbuf_tensor("l2_eps", [P, 1], F32))
            load_all(nc, [(cw[:], A["c_conv_w"][0].partition_broadcast(P))])
            with phase(nc, "filled") as (block, filled):
                @block.vector
                def _(dve):
                    dve.memset(eps[:], L2_EPS).then_inc(filled, 1)
            with nc.Fori(0, MT) as i:
                conv_tile(nc, P, cw, eps, [xp[bass.ds(i * P + j, P)] for j in range(4)], qkv[bass.ds(i * P, P)])
            conv_tile(nc, SROWS, cw, eps, [xs[:, j:j + TS] for j in range(4)], qkv[SEQ:T])
        gdn_gates(nc, A, ba, gb)
        S, cnorm = sb("gdn_state", [P, DH, P]), sb("c_norm", [CHUNK, P])
        load_all(nc, [(cnorm[:], A["c_norm"][0].partition_broadcast(CHUNK))])
        with phase(nc, "cleared") as (block, cleared):
            @block.vector
            def _(dve):
                dve.memset(S[:], 0.0).then_inc(cleared, 1)

        def sources(rows):
            return (qkv[rows].rearrange("t (n h k) -> t n h k", n=3, h=DH), z[rows].rearrange("t (h k) -> t h k", h=DH),
                    gb[rows].rearrange("t (n h) -> t n h", n=2), mixed[rows].rearrange("t (h k) -> t h k", h=DH))
        with nc.Fori(0, SEQ // CHUNK) as i:
            gdn_chunk(nc, c, CHUNK, cnorm, *sources(bass.ds(i * CHUNK, CHUNK)), S)
        with phase(nc, "stored") as (block, stored):
            @block.sync
            def _(sp):
                sp.dma_start(O["p_gdn"][0, 0].rearrange("h k v -> k h v"), S[:]).then_inc(stored, 16)
                sp.wait_ge(stored, 16)
        with nc.Fori(0, NS) as i:
            gdn_chunk(nc, c, TS, cnorm, *sources(bass.ds(i * TS + SEQ, TS)), S,
                      state_in=A["state_gdn"][0, bass.ds(i, 1)].rearrange("b h k v -> k (b h) v"),
                      state_out=O["s_gdn"][0, bass.ds(i, 1)].rearrange("b h k v -> k (b h) v"))


def cache_rows(nc, A, O, proj):
    pairs = []
    for name, col in (("cmp_k", K_CMP), ("cmp_v", V_CMP), ("sel_k", K_SEL), ("sel_v", V_SEL)):
        pairs.append((O["p_" + name][0, 0].rearrange("t g d -> t (g d)"), proj[0:SEQ, col:col + P]))
        pairs.append((O["s_" + name][0].rearrange("b t g d -> (b t) (g d)"), proj[SEQ:T, col:col + P]))
    for name, col in (("win_k", K_WIN), ("win_v", V_WIN)):
        pairs.append((O["p_" + name][0, 0].rearrange("t g d -> t (g d)"), proj[SEQ - WIN:SEQ, col:col + P]))
        flat = O["s_" + name][0].rearrange("b t g d -> b t (g d)")
        pairs.append((flat[:, 0:WIN - TS], A["state_" + name][0, :, TS:WIN].rearrange("b t g d -> b t (g d)")))
        pairs.append((flat[:, WIN - TS:WIN], proj[SEQ:T, col:col + P].rearrange("(b t) c -> b t c", t=TS)))
    with phase(nc, "stored_sp", "stored_act") as (block, stored_sp, stored_act):
        @block.sync
        def _(sp):
            for dst, src in pairs[::2]:
                sp.dma_start(dst, src).then_inc(stored_sp, 16)
            sp.wait_ge(stored_sp, 16 * len(pairs[::2]))

        @block.scalar
        def _(act):
            for dst, src in pairs[1::2]:
                act.dma_start(dst, src).then_inc(stored_act, 16)
            act.wait_ge(stored_act, 16 * len(pairs[1::2]))


def turn_queries(nc, c, proj, qk_turned):
    with ExitStack() as ctx:
        rows = ctx.enter_context(nc.sbuf_tensor("qk_rows", [P, MT, D], F32))
        qkT = ctx.enter_context(nc.sbuf_tensor("qkT", [P, KD, SEQ], F32))
        tok = lambda col, n: proj[0:SEQ, col:col + n].rearrange("(m p) c -> p m c", p=P)
        loads = [(rows[:, :, 0:512], tok(Q_B, 512))]
        for j, col in enumerate((K_SEL, K_SEL + HD, K_WIN, K_WIN + HD)):
            for half in range(2):
                at = 512 + j * P + half * HD
                loads.append((rows[:, :, at:at + HD], tok(col, HD)))
        transpose_rows(nc, rows, qkT, c["ident"], tiles=MT, loads=loads)
        with phase(nc, "stored") as (block, stored):
            @block.sync
            def _(sp):
                sp.dma_start(qk_turned.rearrange("n p t -> p n t"), qkT[:]).then_inc(stored, 16)
                sp.wait_ge(stored, 16)


def turn_sample(nc, c, proj, q_diag, k_new):
    with ExitStack() as ctx:
        sb = lambda n, s: ctx.enter_context(nc.sbuf_tensor(f"{n}_{nc.next_id()}", s, F32))
        rows, kn = sb("s_rows", [SROWS, 6, P]), sb("k_new_sb", [P, NS, 2, TS])
        pt = [banks(ctx, nc, f"qs{i}", [P, 4, SROWS]) for i in range(2)]
        with phase(nc, "loaded", "turned", "zeroed", "copied", "stored") as (block, loaded, turned, zeroed, copied, stored):
            @block.sync
            def _(sp):
                q = proj[SEQ:T, Q_B:Q_B + 512].rearrange("r (g h d) -> r g h d", g=2, h=4)
                for g in range(2):
                    sp.dma_start(rows[:, 0:4, g * HD:(g + 1) * HD], q[:, g]).then_inc(loaded, 16)
                sp.dma_start(rows[:, 4, :], proj[SEQ:T, K_SEL:K_SEL + P]).then_inc(loaded, 16)
                sp.dma_start(rows[:, 5, :], proj[SEQ:T, K_WIN:K_WIN + P]).then_inc(loaded, 16)
                sp.wait_ge(copied, 10)
                sp.dma_start(k_new.rearrange("b p n t -> p b n t"), kn[:]).then_inc(stored, 16)
                sp.wait_ge(stored, 16)

            @block.tensor
            def _(pe):
                pe.wait_ge(loaded, 64)
                for n in range(6):
                    last = pe.transpose(pt[n // 4][:, n % 4, :], rows[:, n, :], c["ident"][0:SROWS, 0:SROWS])
                last.then_inc(turned, 1)

            @block.vector
            def _(dve):
                dve.memset(q_diag[:], 0.0).then_inc(zeroed, 1)
                dve.wait_ge(zeroed, 1)
                dve.wait_ge(turned, 1)
                by_seq = lambda x: x.rearrange("p (b t) -> p b t", t=TS)
                for g in range(2):
                    lo = g * HD
                    for h in range(4):
                        at = (g * 4 + h) * TS
                        dve.tensor_copy(q_diag[lo:lo + HD, :, at:at + TS], by_seq(pt[0][lo:lo + HD, h, :])).then_inc(copied, 1)
                for n in range(2):
                    dve.tensor_copy(kn[:, :, n, :], by_seq(pt[1][:, n, :])).then_inc(copied, 1)


def compress_weights(nc, A, n, W1, W2, pe_bias):
    with ExitStack() as ctx:
        pe_sb = ctx.enter_context(nc.sbuf_tensor(f"cmp_pe_sb{n}", [BLK, HD], F32))
        pb = banks(ctx, nc, f"pe{n}", [P, 1])
        with phase(nc, "loaded", "zeroed", "summed", "copied") as (block, loaded, zeroed, summed, copied):
            @block.sync
            def _(sp):
                for half in range(2):
                    sp.dma_start(W1[half * 64:half * 64 + 64, :, half, :],
                                 A["ab_cmp_w1"][0, n].rearrange("(t d) h -> t d h", d=HD)).then_inc(loaded, 16)
                sp.dma_start(W2[:], A["ab_cmp_w2"][0, n]).then_inc(loaded, 16)
                sp.dma_start(pe_sb[:], A["ab_cmp_pe"][0, n]).then_inc(loaded, 16)

            @block.tensor
            def _(pe):
                pe.wait_ge(loaded, 16 * 4)
                for d in range(HD):
                    last = pe.matmul(pb, W1[0:64, d, 0, :], pe_sb[:, d:d + 1], start=(d == 0), stop=(d == HD - 1))
                last.then_inc(summed, 1)

            @block.gpsimd
            def _(pool):
                pool.memset(W1[0:64, :, 1, :], 0.0).then_inc(zeroed, 1)

            @block.vector
            def _(dve):
                dve.memset(W1[64:P, :, 0, :], 0.0).then_inc(zeroed, 1)
                dve.wait_ge(summed, 1)
                dve.tensor_copy(pe_bias[:], pb).then_inc(copied, 1)


def hidden_products(pe, pages, W1, out):
    x = pages.rearrange("p m (g d) -> p (m g) d", d=HD)
    for half in range(2):
        for d in range(HD):
            last = pe.matmul(out[half], W1[:, d, half, :], x[:, :, d], start=(d == 0), stop=(d == HD - 1))
    return last


def compress_prompt(nc, n, proj, W1, W2, pe_bias, out):
    NB = SEQ // BLK
    with ExitStack() as ctx:
        sb = lambda name, s: ctx.enter_context(nc.sbuf_tensor(f"{name}_{nc.next_id()}", s, F32))
        src, hid = sb("cmp_src", [P, MT, P]), sb("cmp_hid", [P, 2, MT, 2])
        ph = [banks(ctx, nc, f"ph{half}", [P, MT * 2]) for half in range(2)]
        r, w = (P, NB) if n == 0 else (NB, HD)
        res, pk = sb("cmp_res", [r, 2, w]), banks(ctx, nc, "pk", [r, 2, w])
        with phase(nc, "loaded", "hidden", "silu_done", "product", "copied", "stored") as (
                block, loaded, hidden, silu_done, product, copied, stored):
            @block.sync
            def _(sp):
                col = (K_CMP, V_CMP)[n]
                sp.dma_start(src[:], proj[0:SEQ, col:col + P].rearrange("(m p) c -> p m c", p=P)).then_inc(loaded, 16)
                sp.wait_ge(copied, 1)
                sp.dma_start(out.rearrange("g p n -> p g n"), res[:]).then_inc(stored, 16)
                sp.wait_ge(stored, 16)

            @block.tensor
            def _(pe):
                pe.wait_ge(loaded, 16)
                hidden_products(pe, src[:], W1, ph).then_inc(hidden, 1)
                pe.wait_ge(silu_done, 2)
                for g in range(2):
                    flat = hid[:, g].rearrange("p m two -> p (m two)")
                    if n == 0:
                        for half in range(2):
                            last = pe.matmul(pk[half * 64:half * 64 + 64, g, :], W2[:], flat, start=True, stop=True)
                    else:
                        last = pe.matmul(pk[:, g, :], flat, W2[:], start=True, stop=True)
                last.then_inc(product, 1)

            @block.scalar
            def _(act):
                act.wait_ge(hidden, 1)
                for half in range(2):
                    act.activation(hid[:, :, :, half], ph[half].rearrange("p (m g) -> p g m", g=2), ACT.Silu,
                                   bias=pe_bias[:, 0:1]).then_inc(silu_done, 1)

            @block.vector
            def _(dve):
                dve.wait_ge(product, 1)
                dve.tensor_copy(res[:], pk).then_inc(copied, 1)


def prompt_attention(nc, c, A, proj, qk_turned, kc_turned, vc_rows, mixed):
    HP = 2
    units = [(m, h) for m in range(MT) for h in range(HP)]
    NB = SEQ // BLK
    NP = 14
    with ExitStack() as ctx:
        sb = lambda n, s: ctx.enter_context(nc.sbuf_tensor(f"{n}_{nc.next_id()}", s, F32))
        qT, ks, kw, kc = sb("qT", [P, SEQ]), sb("ks", [P, SEQ]), sb("kw", [P, SEQ]), sb("kc", [P, NB])
        vs, vw, vc = sb("vs", [P, MT, HD]), sb("vw", [P, MT, HD]), sb("vc", [NB, HD])
        gates, slopes = sb("gates", [P, MT, HP, 3]), sb("slopes", [P, HP])
        dist_sel, dist_win = sb("dist_sel", [P, 1024]), sb("dist_win", [P, 640])
        dist_cmp, seen = sb("dist_cmp", [P, MT, NB]), sb("seen", [P, MT, NB])
        s_sel, s_win, s_cmp = [[sb(n, [P, w]) for _ in range(2)] for n, w in (("s_sel", 1024), ("s_win", 640), ("s_cmp", NB))]
        top, neg, den, wgt = [[sb(n, [P, 3]) for _ in range(2)] for n in ("top", "neg", "den", "wgt")]
        pT = [sb("pT", [P, NP, P]) for _ in range(2)]
        o = sb("o_pair", [P, MT, HP, HD])
        p_sel, p_win = banks(ctx, nc, "p_sel", [P, 1024]), banks(ctx, nc, "p_win", [P, 1024])
        p_tr = [banks(ctx, nc, f"p_tr{i}", [P, 4, P]) for i in range(2)]
        p_o = [banks(ctx, nc, f"p_o{i}", [P, 3, HD]) for i in range(2)]
        load_all(nc, [(dist_sel[:], A["c_dist_sel"]), (dist_win[:], A["c_dist_win"]), (dist_cmp[:], A["c_dist_cmp"]), (seen[:], A["c_seen_cmp"])])
        tok = lambda col, n: proj[0:SEQ, col].rearrange("(m p) c -> p m c", p=P)

        def key_tiles(m):
            n_sel, w0 = m + 1, max(0, m - 4)
            slots = [("s", k) for k in range(n_sel)] + [("w", k) for k in range(w0, m + 1)] + [("c", 0)]
            return n_sel, w0, [slots[i:i + 4] for i in range(0, len(slots), 4)]
        groups_before = [0]
        for m, h in units:
            groups_before.append(groups_before[-1] + len(key_tiles(m)[2]))

        def pair_phase(g, pr, pair):
            with phase(nc, "loaded", "gates_ready", "scores", "scores_out", "neg_ready", "probs", "cmp_masked", "turned", "turned_out",
                       "values", "o_ready", "act_steps", "dve_steps", "stored") as (
                    block, loaded, gates_ready, scores, scores_out, neg_ready, probs, cmp_masked, turned, turned_out,
                    values, o_ready, act_steps, dve_steps, stored):
                @block.sync
                def _(sp):
                    lone = lambda x: x.rearrange("a p t -> p (a t)")
                    sp.dma_start(qT[:], lone(qk_turned[bass.ds(pair, 1)])).then_inc(loaded, 16)
                    sp.dma_start(ks[:], lone(qk_turned[bass.ds(g + 4, 1)])).then_inc(loaded, 16)
                    sp.dma_start(kw[:], lone(qk_turned[bass.ds(g + 6, 1)])).then_inc(loaded, 16)
                    sp.dma_start(kc[:], lone(kc_turned[bass.ds(g, 1)])).then_inc(loaded, 16)
                    sp.dma_start(vc[:], lone(vc_rows[bass.ds(g, 1)])).then_inc(loaded, 16)
                    sp.dma_start(vs[:], tok(bass.ds(g * HD + V_SEL, HD), HD)).then_inc(loaded, 16)
                    sp.dma_start(vw[:], tok(bass.ds(g * HD + V_WIN, HD), HD)).then_inc(loaded, 16)
                    sp.dma_start(gates[:].rearrange("p m h b -> p m (h b)"), tok(bass.ds(pair * 6 + GATE_B, 6), 6)).then_inc(loaded, 16)
                    sp.dma_start(slopes[:], lone(A["c_slopes8"][bass.ds(pair, 1)])).then_inc(loaded, 16)
                    sp.wait_ge(o_ready, len(units))
                    sp.dma_start(mixed[0:SEQ, bass.ds(pair * P + 512, P)].rearrange("(m p) c -> p m c", p=P),
                                 o[:].rearrange("p m h d -> p m (h d)")).then_inc(stored, 16)
                    sp.wait_ge(stored, 16)

                @block.tensor
                def _(pe):
                    def score(u):
                        m, h = units[u]
                        n_sel, w0, _ = key_tiles(m)
                        q = qT[h * HD:(h + 1) * HD, m * P:(m + 1) * P]
                        lo = slice(h * HD, (h + 1) * HD)
                        if u:
                            pe.wait_ge(scores_out, u)
                        for a in range(0, n_sel * P, 512):
                            b = min(a + 512, n_sel * P)
                            pe.matmul(p_sel[:, a:b], q, ks[lo, a:b], start=True, stop=True)
                        nw = (m + 1 - w0) * P
                        for a in range(0, nw, 512):
                            b = min(a + 512, nw)
                            pe.matmul(p_win[:, a:b], q, kw[lo, w0 * P + a:w0 * P + b], start=True, stop=True)
                        pe.matmul(p_win[:, 1024 - NB:1024], q, kc[lo, :], start=True, stop=True).then_inc(scores, 1)

                    pe.wait_ge(loaded, 16 * 9)
                    score(0)
                    for u, (m, h) in enumerate(units):
                        if u + 1 < len(units):
                            score(u + 1)
                        n_sel, w0, groups = key_tiles(m)
                        for n, group in enumerate(groups):
                            done = groups_before[u] + n
                            if done >= 2:
                                pe.wait_ge(turned_out, done - 1)
                            if n == 0:
                                pe.wait_ge(probs, u + 1)
                                pe.wait_ge(cmp_masked, u + 1)
                            for j, (kind, k) in enumerate(group):
                                if kind == "s":
                                    last = pe.transpose(p_tr[done % 2][:, j, :], s_sel[u % 2][:, k * P:(k + 1) * P], c["ident"][:])
                                elif kind == "w":
                                    last = pe.transpose(p_tr[done % 2][:, j, :], s_win[u % 2][:, (k - w0) * P:(k - w0 + 1) * P], c["ident"][:])
                                else:
                                    last = pe.transpose(p_tr[done % 2][0:NB, j, :], s_cmp[u % 2][:], c["ident"][:])
                            last.then_inc(turned, 1)
                        pe.wait_ge(turned_out, groups_before[u + 1])
                        if u >= 2:
                            pe.wait_ge(o_ready, u - 1)
                        slot = 0
                        for k in range(n_sel):
                            pe.matmul(p_o[u % 2][:, 1, :], pT[u % 2][:, slot, :], vs[:, k, :], start=(k == 0), stop=(k == n_sel - 1))
                            slot += 1
                        for k in range(w0, m + 1):
                            pe.matmul(p_o[u % 2][:, 2, :], pT[u % 2][:, slot, :], vw[:, k, :], start=(k == w0), stop=(k == m))
                            slot += 1
                        pe.matmul(p_o[u % 2][:, 0, :], pT[u % 2][0:NB, slot, :], vc[:], start=True, stop=True).then_inc(values, 1)

                @block.scalar
                def _(act):
                    act.wait_ge(loaded, 16 * 9)
                    act.activation(gates[:], gates[:], ACT.Exp, scale=-1.0).then_inc(gates_ready, 1)

                    def probabilities(u):
                        m, h = units[u]
                        n_sel, w0, _ = key_tiles(m)
                        act.wait_ge(neg_ready, u + 1)
                        for n, (s, w) in enumerate(((s_cmp[u % 2], NB), (s_sel[u % 2], n_sel * P), (s_win[u % 2], (m + 1 - w0) * P))):
                            ins = act.activation(s[:, 0:w], s[:, 0:w], ACT.Exp, bias=neg[u % 2][:, n:n + 1], scale=HD ** -0.5,
                                                 accum_out=den[u % 2][:, n:n + 1])
                        ins.then_inc(probs, 1)
                    probabilities(0)
                    for u, (m, h) in enumerate(units):
                        _, _, groups = key_tiles(m)
                        slot = 0
                        if u >= 2:
                            act.wait_ge(values, u - 1)
                        for n, group in enumerate(groups):
                            done = groups_before[u] + n
                            act.wait_ge(turned, done + 1)
                            full = len(group) - (group[-1][0] == "c")
                            ins = None
                            if full:
                                ins = act.copy(pT[u % 2][:, slot:slot + full, :], p_tr[done % 2][:, 0:full, :])
                            if full < len(group):
                                ins = act.copy(pT[u % 2][0:NB, slot + full, :], p_tr[done % 2][0:NB, full, :])
                            ins.then_inc(turned_out, 1)
                            slot += len(group)
                        if u + 1 < len(units):
                            probabilities(u + 1)

                @block.vector
                def _(dve):
                    step = InOrder(dve, dve_steps)
                    dve.wait_ge(gates_ready, 1)
                    step(dve.tensor_scalar(gates[:], gates[:], 1.0, None, ALU.add))
                    step(dve.reciprocal(gates[:], gates[:]))

                    def finish_scores(u):
                        m, h = units[u]
                        n_sel, w0, _ = key_tiles(m)
                        b, nw = u % 2, (m + 1 - w0) * P
                        dve.wait_ge(scores, u + 1)
                        if u >= 2:
                            dve.wait_ge(values, u - 1)
                        slope = slopes[:, h:h + 1]
                        add = lambda out, dist, ps: dve.scalar_tensor_tensor(out, dist, slope, ps, ALU.mult, ALU.add)
                        add(s_sel[b][:, 0:n_sel * P], dist_sel[:, 896 - m * P:1024], p_sel[:, 0:n_sel * P])
                        add(s_win[b][:, 0:nw], dist_win[:, 640 - nw:640], p_win[:, 0:nw])
                        step(add(s_cmp[b][:], dist_cmp[:, m, :], p_win[:, 1024 - NB:1024]))
                        dve.sem_inc(scores_out, 1)
                        dve.reduce_max(top[b][:, 0:1], s_cmp[b][:], AX)
                        dve.reduce_max(top[b][:, 1:2], s_sel[b][:, 0:n_sel * P], AX)
                        step(dve.reduce_max(top[b][:, 2:3], s_win[b][:, 0:nw], AX))
                        dve.tensor_scalar(neg[b][:], top[b][:], -(HD ** -0.5), None, ALU.mult).then_inc(neg_ready, 1)
                    finish_scores(0)
                    for u, (m, h) in enumerate(units):
                        if u + 1 < len(units):
                            finish_scores(u + 1)
                        b = u % 2
                        dve.wait_ge(probs, u + 1)
                        dve.tensor_tensor(s_cmp[b][:], s_cmp[b][:], seen[:, m, :], ALU.mult).then_inc(cmp_masked, 1)
                        dve.wait_ge(cmp_masked, u + 1)
                        step(dve.reduce_sum(den[b][:, 0:1], s_cmp[b][:], AX))
                        step(dve.tensor_scalar(den[b][:], den[b][:], 1e-30, None, ALU.max))
                        step(dve.reciprocal(wgt[b][:], den[b][:]))
                        step(dve.tensor_tensor(wgt[b][:], wgt[b][:], gates[:, m, h, :], ALU.mult))
                        dve.wait_ge(values, u + 1)
                        out = o[:, m, h, :]
                        step(dve.tensor_scalar(out, p_o[b][:, 0, :], wgt[b][:, 0:1], None, ALU.mult))
                        step(dve.scalar_tensor_tensor(out, p_o[b][:, 1, :], wgt[b][:, 1:2], out, ALU.mult, ALU.add))
                        dve.scalar_tensor_tensor(out, p_o[b][:, 2, :], wgt[b][:, 2:3], out, ALU.mult, ALU.add).then_inc(o_ready, 1)

        with nc.Fori(0, 2) as g:
            with nc.Fori(0, 2) as pr:
                pair_phase(g, pr, g * 2 + pr)


HW_PAGES = 40


def load_pages(eng, pool, ids, seq, some, pages, loaded, taken):
    eng.sem_inc(taken, 1)
    for p in some:
        page = eng.value_load(ids[0:1, bass.ds(seq * PAGES + p, 1)], min_val=0, max_val=NPOOL - 1)
        eng.dma_start(pages[:, p, :], pool[0, bass.ds(page, 1)].rearrange("a t g d -> t (a g d)")).then_inc(loaded, 16)


def sample_hidden(nc, pool_rows, ids, W1, pe_bias, hid, software, turn):
    with ExitStack() as ctx:
        pages = [ctx.enter_context(nc.sbuf_tensor(f"pages{i}_{nc.next_id()}", [P, PAGES, P], F32)) for i in range(2)]
        ph = [[banks(ctx, nc, f"ph{i}{half}", [P, PAGES * 2]) for half in range(2)] for i in range(2)]
        with phase(nc, "hw0", "hw1", "free0", "free1", "hidden", "psum_free", "silu_done", "taken", "taken_sw") as (
                block, hw0, hw1, free0, free1, hidden, psum_free, silu_done, taken, taken_sw):
            hw, sw, free = [hw0, hw1], software, [free0, free1]
            sw_pages = PAGES - HW_PAGES
            sw_before = turn * (NS // 2) * 16 * sw_pages

            @block.sync
            def _(sp):
                with sp.Fori(0, NS // 2) as i:
                    for j in range(2):
                        sp.wait_ge(free[j], i + 1)
                        load_pages(sp, pool_rows, ids, i * 2 + j, range(HW_PAGES), pages[j], hw[j], taken)

            @block.gpsimd
            def _(pool):
                with pool.Fori(0, NS // 2) as i:
                    for j in range(2):
                        pool.wait_ge(free[j], i + 1)
                        load_pages(pool, pool_rows, ids, i * 2 + j, range(HW_PAGES, PAGES), pages[j], sw[j], taken_sw)

            @block.tensor
            def _(pe):
                pe.sem_inc(free0, 1)
                pe.sem_inc(free1, 1)
                with pe.Fori(0, NS // 2) as i:
                    for j in range(2):
                        pe.wait_ge(hw[j], i * (16 * HW_PAGES) + 16 * HW_PAGES)
                        pe.wait_ge(sw[j], i * (16 * sw_pages) + (sw_before + 16 * sw_pages))
                        pe.wait_ge(psum_free, i * 2 + j + 1)
                        hidden_products(pe, pages[j][:], W1, ph[j]).then_inc(hidden, 1)
                        pe.wait_ge(hidden, i * 2 + j + 1)
                        pe.sem_inc(free[j], 1)

            @block.scalar
            def _(act):
                act.sem_inc(psum_free, 2)
                with act.Fori(0, NS // 2) as i:
                    for j in range(2):
                        act.wait_ge(hidden, i * 2 + j + 1)
                        for half in range(2):
                            out = hid[:, bass.ds(i * 2 + j, 1), :, :, half].rearrange("p b g m -> p (b g) m")
                            act.activation(out, ph[j][half].rearrange("p (m g) -> p g m", g=2), ACT.Silu,
                                           bias=pe_bias[:, 0:1]).then_inc(silu_done, 1)
                        act.wait_ge(silu_done, i * 4 + 2 * j + 2)
                        act.sem_inc(psum_free, 1)


def sample_importance(nc, c, A, hid, W2, q_diag, p_turned, importance):
    with ExitStack() as ctx:
        sb = lambda n, s, d=F32: ctx.enter_context(nc.sbuf_tensor(f"{n}_{nc.next_id()}", s, d))
        alibi, hsum = sb("alibi_cmp", [64, P]), sb("hsum", [64, NS, P])
        kc, s, top, den = sb("kc_s", [P, NS, P]), sb("s_c", [64, NS, P]), sb("top_c", [64, NS]), sb("den_c", [64, NS])
        pk, ps = banks(ctx, nc, "pk", [P, NS, P]), banks(ctx, nc, "ps", [64, NS, P])
        pt, pi = banks(ctx, nc, "pt", [P, NS, 64]), banks(ctx, nc, "pi", [P, P])
        with phase(nc, "loaded", "keys", "keys_out", "scores", "shifted", "probs", "p_ready", "turned", "sums", "dve_steps", "done") as (
                block, loaded, keys, keys_out, scores, shifted, probs, p_ready, turned, sums, dve_steps, done):
            @block.sync
            def _(sp):
                sp.dma_start(alibi[:], A["c_alibi_cmp"]).then_inc(loaded, 16)
                sp.dma_start(hsum[:].rearrange("p b r -> p (b r)"), A["c_head_sum"]).then_inc(loaded, 16)

            @block.tensor
            def _(pe):
                for b in range(NS):
                    for g in range(2):
                        last = pe.matmul(pk[g * 64:g * 64 + 64, b, :], W2[:], hid[:, b, g].rearrange("p m two -> p (m two)"),
                                         start=True, stop=True)
                last.then_inc(keys, 1)
                pe.wait_ge(keys_out, 1)
                for b in range(NS):
                    last = pe.matmul(ps[:, b, :], q_diag[:, b, :], kc[:, b, :], start=True, stop=True)
                last.then_inc(scores, 1)
                pe.wait_ge(loaded, 32)
                pe.wait_ge(p_ready, 1)
                for b in range(NS):
                    last = pe.transpose(pt[:, b, :], s[:, b, :], c["ident"][0:64, 0:64])
                last.then_inc(turned, 1)
                for b in range(NS):
                    last = pe.matmul(pi, hsum[:, b, :], s[:, b, :], start=(b == 0), stop=(b == NS - 1))
                last.then_inc(sums, 1)

            @block.scalar
            def _(act):
                act.wait_ge(shifted, 1)
                act.activation(s[:], s[:], ACT.Exp).then_inc(probs, 1)

            @block.vector
            def _(dve):
                step = InOrder(dve, dve_steps)
                over = lambda x: x.unsqueeze(2).broadcast_to([64, NS, P])
                dve.wait_ge(keys, 1)
                dve.tensor_copy(kc[:], pk).then_inc(keys_out, 1)
                dve.wait_ge(loaded, 32)
                dve.wait_ge(scores, 1)
                step(dve.scalar_tensor_tensor(s[:], ps, HD ** -0.5, alibi[:].unsqueeze(1).broadcast_to([64, NS, P]), ALU.mult, ALU.add))
                step(dve.reduce_max(top[:], s[:], AX))
                dve.tensor_tensor(s[:], s[:], over(top[:]), ALU.subtract).then_inc(shifted, 1)
                dve.wait_ge(probs, 1)
                step(dve.reduce_sum(den[:], s[:], AX))
                step(dve.tensor_scalar(den[:], den[:], 1e-30, None, ALU.max))
                step(dve.reciprocal(den[:], den[:]))
                dve.tensor_tensor(s[:], s[:], over(den[:]), ALU.mult).then_inc(p_ready, 1)
                dve.wait_ge(turned, 1)
                dve.tensor_copy(p_turned[:], pt).then_inc(done, 1)
                dve.wait_ge(sums, 1)
                dve.tensor_copy(importance[:], pi).then_inc(done, 1)


def sample_compressed_values(nc, hid, W2, p_turned, o_cmp):
    with ExitStack() as ctx:
        vc = ctx.enter_context(nc.sbuf_tensor("vc_s", [P, NS, P], F32))
        pv, po = banks(ctx, nc, "pv", [P, NS, P]), banks(ctx, nc, "po", [64, NS, P])
        with phase(nc, "rows_ready", "rows_out", "values", "done") as (block, rows_ready, rows_out, values, done):
            @block.tensor
            def _(pe):
                for b in range(NS):
                    for g in range(2):
                        last = pe.matmul(pv[:, b, g * HD:(g + 1) * HD], hid[:, b, g].rearrange("p m two -> p (m two)"), W2[:],
                                         start=True, stop=True)
                last.then_inc(rows_ready, 1)
                pe.wait_ge(rows_out, 1)
                for b in range(NS):
                    last = pe.matmul(po[:, b, :], p_turned[:, b, :], vc[:, b, :], start=True, stop=True)
                last.then_inc(values, 1)

            @block.vector
            def _(dve):
                dve.wait_ge(rows_ready, 1)
                dve.tensor_copy(vc[:], pv).then_inc(rows_out, 1)
                dve.wait_ge(values, 1)
                for g in range(2):
                    r = slice(g * 32, g * 32 + 32)
                    dve.tensor_copy(o_cmp[r, :, :], po[r, :, g * HD:(g + 1) * HD]).then_inc(done, 1)


def choose_blocks(nc, importance, block_mask):
    TAKEN = -2.0
    with ExitStack() as ctx:
        sb = lambda n, s: ctx.enter_context(nc.sbuf_tensor(f"{n}_{nc.next_id()}", s, F32))
        left, rest, top, mask = sb("left", [P, P]), sb("rest", [P, P]), sb("top8", [P, 8]), sb("mask", [P, 2, PAGES])
        with phase(nc, "dve_steps", "done", "stored") as (block, dve_steps, done, stored):
            @block.vector
            def _(dve):
                step = InOrder(dve, dve_steps)
                step(dve.memset(importance[:, 0:1], 1000.0))
                step(dve.memset(importance[:, P - 1:P], 1000.0))
                step(dve.max(top[:], importance[:]))
                step(dve.match_replace(left[:], top[:], importance[:], TAKEN))
                step(dve.max(top[:], left[:]))
                step(dve.memset(top[:, 7:8], TAKEN))
                step(dve.match_replace(rest[:], top[:], left[:], TAKEN))
                dve.tensor_scalar(mask[:], rest[:].rearrange("p (m two) -> p two m", two=2), TAKEN, NEG,
                                  ALU.not_equal, ALU.mult).then_inc(done, 1)

            @block.sync
            def _(sp):
                sp.wait_ge(done, 1)
                for b in range(NS):
                    sp.dma_start(block_mask[b].rearrange("two c m -> c two m"), mask[b * 16:(b + 1) * 16]).then_inc(stored, 16)
                sp.wait_ge(stored, 16 * NS)


def sample_selected(nc, c, A, proj, ids, q_diag, k_new, block_mask, o_cmp, mixed, k_sw, v_sw):
    COLS = 64
    branches = [(0, PAGES), (1, 4)]
    with ExitStack() as ctx:
        sb = lambda n, s, d=F32: ctx.enter_context(nc.sbuf_tensor(f"{n}_{nc.next_id()}", s, d))
        kp, vp = sb("k_pages", [P, PAGES, P]), sb("v_pages", [P, PAGES, P])
        kw, vw = sb("k_win", [P, 4, P]), sb("v_win", [P, 4, P])
        kn, vn = sb("k_new", [P, 2, TS]), sb("v_new", [TS, 2, P])
        E = [sb("e_sel", [P, PAGES + 1, COLS]), sb("e_win", [P, 5, COLS])]
        alibi = [sb("alibi_page", [P, PAGES, COLS]), sb("alibi_win", [P, 4, COLS])]
        alibi_new = sb("alibi_new", [TS, COLS])
        kT = [sb("kT", [P, 4, P]) for _ in range(2)]
        half, mask = sb("half", [2, P]), sb("mask_b", [2, 16, PAGES])
        cm, diag, mB = sb("cm", [P, 2, COLS]), sb("diag", [P, P]), sb("mB", [P, 2, COLS])
        mcol = sb("mcol", [P, 1])
        rs, gates, o = sb("rs", [P, 2, COLS]), sb("gates_s", [COLS, NS, 3]), sb("o_s", [COLS, NS, HD])
        w = sb("w_s", [COLS, 2])
        p_tr = [banks(ctx, nc, f"st{i}", [P, 4, P]) for i in range(2)]
        p_s = [banks(ctx, nc, f"ss{i}", [P, 8, COLS]) for i in range(2)]
        p_mask = banks(ctx, nc, "smask", [P, 16, PAGES])
        p_a, p_o = banks(ctx, nc, "sa", [P, P]), banks(ctx, nc, "so", [COLS, 4, P])
        g_rows = [(gates[h * TS:(h + 1) * TS], proj[SEQ:T, GATE_B + 3 * h:GATE_B + 3 * h + 3].rearrange("(b t) c -> t b c", t=TS)) for h in range(NH)]
        load_all(nc, [(alibi[0][:].rearrange("p m c -> p (m c)"), A["c_alibi_page"]), (alibi[1][:].rearrange("p m c -> p (m c)"), A["c_alibi_win"]),
                      (alibi_new[:], A["c_alibi_new"]), (half[:], A["c_half"])] + g_rows)
        SG = PAGES // 4 + 1
        SMALL = 5
        STEPS = 2 + SG + 2 + 2 + 1 + 1 + 3 + 4
        with phase(nc, "k_hw", "v_hw", "taken", "taken_sw", "k_free", "v_free", "small", "small_free", "turned", "kT_out", "scores",
                   "scores_out", "masks", "max_ready", "max_turned", "diag_ready", "max_spread", "shifted", "probs", "summed",
                   "values", "dve_steps", "gates_exp", "gates_done", "o_ready", "stored") as (
                block, k_hw, v_hw, taken, taken_sw, k_free, v_free, small, small_free, turned, kT_out, scores,
                scores_out, masks, max_ready, max_turned, diag_ready, max_spread, shifted, probs, summed,
                values, dve_steps, gates_exp, gates_done, o_ready, stored):
            lone = lambda x: x.rearrange("a p n t -> p (a n) t")
            SW = PAGES - HW_PAGES

            @block.sync
            def _(sp):
                with sp.Fori(0, NS) as b:
                    sp.wait_ge(k_free, b + 1)
                    load_pages(sp, A["cache_sel_k"], ids, b, range(HW_PAGES), kp, k_hw, taken)
                    sp.wait_ge(small_free, b + 1)
                    sp.dma_start(kw[:], A["state_win_k"][0, bass.ds(b, 1)].rearrange("a (m p) g d -> p (a m) (g d)", p=P)).then_inc(small, 16)
                    sp.dma_start(vw[:], A["state_win_v"][0, bass.ds(b, 1)].rearrange("a (m p) g d -> p (a m) (g d)", p=P)).then_inc(small, 16)
                    sp.dma_start(mask[:], block_mask[bass.ds(b, 1)].rearrange("a two c m -> two (a c) m")).then_inc(small, 16)
                    sp.dma_start(kn[:], lone(k_new[bass.ds(b, 1)])).then_inc(small, 16)
                    sp.dma_start(vn[:], proj[bass.ds(b * TS + SEQ, TS), V_SEL:V_SEL + 3 * P].rearrange("t (n c) -> t n c", c=P)[:, 0:3:2, :]).then_inc(small, 16)
                    sp.wait_ge(v_free, b + 1)
                    load_pages(sp, A["cache_sel_v"], ids, b, range(HW_PAGES), vp, v_hw, taken)
                sp.wait_ge(o_ready, NS)
                for h in range(NH):
                    sp.dma_start(mixed[SEQ:T, 512 + h * HD:512 + (h + 1) * HD].rearrange("(b t) d -> t b d", t=TS), o[h * TS:(h + 1) * TS]).then_inc(stored, 16)
                sp.wait_ge(stored, 16 * NH)

            @block.gpsimd
            def _(pool):
                with pool.Fori(0, NS) as b:
                    pool.wait_ge(k_free, b + 1)
                    load_pages(pool, A["cache_sel_k"], ids, b, range(HW_PAGES, PAGES), kp, k_sw, taken_sw)
                    pool.wait_ge(v_free, b + 1)
                    load_pages(pool, A["cache_sel_v"], ids, b, range(HW_PAGES, PAGES), vp, v_sw, taken_sw)

            @block.tensor
            def _(pe):
                pe.sem_inc(k_free, 1)
                pe.sem_inc(v_free, 1)
                with pe.Fori(0, NS) as b:
                    q = q_diag[:, bass.ds(b, 1), :].rearrange("p b c -> p (b c)")
                    pe.wait_ge(k_hw, b * (16 * HW_PAGES) + 16 * HW_PAGES)
                    pe.wait_ge(k_sw, b * (16 * SW) + 16 * SW)
                    for n in range(SG + 1):
                        if n < SG:
                            pe.wait_ge(kT_out, b * SG + n + 1)
                            if n == SG - 1:
                                pe.wait_ge(small, b * (16 * SMALL) + 16 * SMALL)
                            for j in range(4):
                                page = kw[:, j, :] if n == SG - 1 else kp[:, 4 * n + j, :]
                                last = pe.transpose(p_tr[n % 2][:, j, :], page, c["ident"][:])
                            last.then_inc(turned, 1)
                            if n == SG - 2:
                                pe.wait_ge(turned, b * SG + n + 1)
                                pe.sem_inc(k_free, 1)
                        if n >= 1:
                            s = n - 1
                            pe.wait_ge(kT_out, b * SG + s + 3)
                            pe.wait_ge(scores_out, b * SG + s + 1)
                            for j in range(4):
                                last = pe.matmul(p_s[s % 2][:, j, :], kT[s % 2][:, j, :], q, start=True, stop=True)
                            if s == SG - 1:
                                for k in range(2):
                                    last = pe.matmul(p_s[s % 2][0:TS, 4 + k, :], kn[:, k, :], q_diag[:, bass.ds(b, 1), :].rearrange("p b c -> p (b c)"), start=True, stop=True)
                            last.then_inc(scores, 1)
                    for n in range(2):
                        last = pe.matmul(p_mask[:, n * 8:(n + 1) * 8, :], half[:], mask[:, n * 8:(n + 1) * 8, :], start=True, stop=True)
                    last.then_inc(masks, 1)
                    pe.wait_ge(max_ready, b + 1)
                    pe.transpose(p_a, cm[:].rearrange("p n c -> p (n c)"), c["ident"][:]).then_inc(max_turned, 1)
                    pe.wait_ge(diag_ready, b + 1)
                    pe.matmul(p_a, c["ones"][:], diag[:], start=True, stop=True).then_inc(max_spread, 1)
                    pe.wait_ge(v_hw, b * (16 * HW_PAGES) + 16 * HW_PAGES)
                    pe.wait_ge(v_sw, b * (16 * SW) + 16 * SW)
                    for n, count in branches:
                        pe.wait_ge(probs, b * 2 + n + 1)
                        for k in range(count):
                            pe.matmul(p_o[:, n, :], E[n][:, k, :], (vp if n == 0 else vw)[:, k, :], start=(k == 0), stop=False)
                        pe.matmul(p_o[:, n, :], E[n][0:TS, count, :], vn[:, n, :], start=False, stop=True)
                    pe.wait_ge(summed, b * 2 + 2)
                    for n in range(2):
                        last = pe.matmul(p_o[:, 2, n:n + 1], rs[:, n, :], c["ones"][:, 0:1], start=True, stop=True)
                    last.then_inc(values, 1)
                    pe.wait_ge(values, b + 1)
                    pe.sem_inc(v_free, 1)

            @block.scalar
            def _(act):
                act.activation(gates[:], gates[:], ACT.Exp, scale=-1.0).then_inc(gates_exp, 1)
                act.sem_inc(kT_out, 2)
                with act.Fori(0, NS) as b:
                    for n in range(SG):
                        act.wait_ge(turned, b * SG + n + 1)
                        if n >= 2:
                            act.wait_ge(scores, b * SG + n - 1)
                        act.copy(kT[n % 2][:], p_tr[n % 2]).then_inc(kT_out, 1)
                    for n in range(2):
                        act.wait_ge(shifted, b * 2 + n + 1)
                        act.activation(E[n][:], E[n][:], ACT.Exp).then_inc(probs, 1)

            @block.vector
            def _(dve):
                dve.wait_ge(gates_exp, 1)
                dve.tensor_scalar(gates[:], gates[:], 1.0, None, ALU.add).then_inc(gates_done, 1)
                dve.wait_ge(gates_done, 1)
                dve.reciprocal(gates[:], gates[:]).then_inc(gates_done, 1)
                dve.wait_ge(gates_done, 2)
                dve.tensor_tensor(o[:], o_cmp[:], gates[:, :, 0:1].broadcast_to([COLS, NS, HD]), ALU.mult).then_inc(gates_done, 1)
                dve.wait_ge(gates_done, 3)
                dve.sem_inc(small_free, 1)
                dve.sem_inc(scores_out, 2)
                with dve.Fori(0, NS) as b:
                    done = [0]

                    def step(ins):
                        done[0] += 1
                        ins.then_inc(dve_steps, 1)
                        dve.wait_ge(dve_steps, b * STEPS + done[0])
                    for n, count in branches:
                        step(dve.memset(E[n][:, count, :], NEG))
                    for s in range(SG):
                        dve.wait_ge(scores, b * SG + s + 1)
                        ps = p_s[s % 2]
                        if s == SG - 1:
                            for n, count in branches:
                                dve.scalar_tensor_tensor(E[n][0:TS, count, :], ps[0:TS, 4 + n, :], HD ** -0.5, alibi_new[:], ALU.mult, ALU.add)
                            out, al = E[1][:, 0:4, :], alibi[1][:]
                        else:
                            out, al = E[0][:, 4 * s:4 * s + 4, :], alibi[0][:, 4 * s:4 * s + 4, :]
                        step(dve.scalar_tensor_tensor(out, ps[:, 0:4, :], HD ** -0.5, al, ALU.mult, ALU.add))
                        dve.sem_inc(scores_out, 1)
                    dve.wait_ge(masks, b + 1)
                    for g in range(2):
                        v = E[0][:, 0:PAGES, g * 32:(g + 1) * 32].rearrange("p m (h t) -> p h t m", h=4)
                        step(dve.tensor_tensor(v, v, p_mask[:, g * 8:(g + 1) * 8, :].unsqueeze(1).broadcast_to([P, 4, TS, PAGES]), ALU.add))
                    for n, count in branches:
                        step(dve.reduce_max(cm[:, n, :], E[n][:].rearrange("p m c -> p c m"), AX))
                    dve.sem_inc(max_ready, 1)
                    dve.wait_ge(max_turned, b + 1)
                    step(dve.reduce_max(mcol[:], p_a, AX))
                    dve.tensor_scalar(diag[:], c["ident"][:], mcol[:, 0:1], None, ALU.mult).then_inc(diag_ready, 1)
                    dve.wait_ge(max_spread, b + 1)
                    step(dve.tensor_copy(mB[:].rearrange("p n c -> p (n c)"), p_a))
                    for n, count in branches:
                        dve.tensor_tensor(E[n][:], E[n][:], mB[:, n, :].unsqueeze(1).broadcast_to([P, count + 1, COLS]), ALU.subtract).then_inc(shifted, 1)
                    for n, count in branches:
                        dve.wait_ge(probs, b * 2 + n + 1)
                        dve.reduce_sum(rs[:, n, :], E[n][:].rearrange("p m c -> p c m"), AX).then_inc(summed, 1)
                    dve.wait_ge(values, b + 1)
                    g_b = gates[:, bass.ds(b, 1), 1:3].rearrange("p b n -> p (b n)")
                    step(dve.tensor_scalar(w[:], p_o[:, 2, 0:2], 1e-30, None, ALU.max))
                    step(dve.reciprocal(w[:], w[:]))
                    step(dve.tensor_tensor(w[:], w[:], g_b, ALU.mult))
                    for n in range(2):
                        for g in range(2):
                            r = slice(g * 32, g * 32 + 32)
                            ob = o[r, bass.ds(b, 1), :].rearrange("p b d -> p (b d)")
                            step(dve.scalar_tensor_tensor(ob, p_o[r, n, g * HD:(g + 1) * HD], w[r, n:n + 1], ob, ALU.mult, ALU.add))
                    dve.sem_inc(o_ready, 1)
                    dve.sem_inc(small_free, 1)
                    assert done[0] == STEPS


def sample_nsa_cache(nc, c, A, proj, kc_turned, vc_rows, ids, q_diag, importance, o_cmp, software):
    with ExitStack() as ctx:
        sb = lambda n, s: ctx.enter_context(nc.sbuf_tensor(n, s, F32))
        W1, W2, pe_bias = sb("cmp_w1", [P, HD, 2, P]), sb("cmp_w2", [P, HD]), sb("pe_bias", [P, 1])
        p_turned = sb("p_turned", [P, NS, 64])
        for n in range(2):
            compress_weights(nc, A, n, W1, W2, pe_bias)
            compress_prompt(nc, n, proj, W1, W2, pe_bias, (kc_turned, vc_rows)[n])
            with nc.sbuf_tensor(f"cmp_hid_all{n}", [P, NS, 2, PAGES, 2], F32) as hid:
                sample_hidden(nc, A[("cache_cmp_k", "cache_cmp_v")[n]], ids, W1, pe_bias, hid, software, n)
                if n == 0:
                    sample_importance(nc, c, A, hid, W2, q_diag, p_turned, importance)
                else:
                    sample_compressed_values(nc, hid, W2, p_turned, o_cmp)


BASE = ("ident", "ones", "tri", "tri_mid", "tri_end", "sel_mod_p", "sel_mod_s")


def hybrid_decoder(nc, A, O):
    scratch = lambda n, s: nc.dram_tensor("scratch_" + n, s, F32, kind="Internal").ap()
    mod_rows = scratch("mod_rows", [MODS, 2, 6 * D])
    y, mixed = scratch("y", [T, D]), scratch("mixed", [T, D])
    software = [nc.alloc_semaphore(f"software_dma{i}") for i in range(4)]
    row_tile = lambda x, m, cols: x[m * P:m * P + ROWS[m], cols]
    with ExitStack() as top:
        sb = lambda n, s, st=top: st.enter_context(nc.sbuf_tensor(n, s, F32))
        c = {k: sb("c_" + k, list(A["c_" + k].shape)) for k in BASE}
        X, modT = sb("X", [P, TILES, D]), sb("modT", [P, 2, 4, KD, MODS])
        load_all(nc, [(c[k][:], A["c_" + k]) for k in BASE]
                 + [(X[:, 0:MT, :], A["x_prompt"][0].rearrange("(m p) d -> p m d", p=P)),
                    (X[0:SROWS, MT, :], A["x_sample"].rearrange("b t d -> (b t) d"))])
        adaln_mods(nc, A, c, modT, mod_rows)

        def project_out(w):
            with ExitStack() as ctx:
                hT = ctx.enter_context(nc.sbuf_tensor(f"mT_{nc.next_id()}", [P, KD, T], F32))
                with nc.sbuf_tensor(f"mrows_{nc.next_id()}", [P, TILES, D], F32) as rows:
                    loads = [(rows[:, 0:MT, :], mixed[0:SEQ].rearrange("(m p) d -> p m d", p=P)), (rows[0:SROWS, MT, :], mixed[SEQ:T])]
                    transpose_rows(nc, rows, hT, c["ident"], loads=loads)
                gemm_rows(nc, lambda m, k: hT[:, k, m * P:m * P + ROWS[m]], ROWS, KD, w, lambda m, cols: row_tile(y, m, cols), 512, 2, tag="out")

        proj = scratch("proj", [T, AB_IN])
        with nc.sbuf_tensor("hT_ab", [P, KD, T], F32) as hT:
            transpose_rows(nc, X, hT, c["ident"], (modT[:, 0, 0], modT[:, 0, 1]))
            project_in(nc, A, hT, proj)
        cache_rows(nc, A, O, proj)
        log_a = scratch("log_a", [T, GH * GK])
        gla_gates(nc, A, c, proj, log_a)
        gla(nc, A, O, c, proj, log_a, mixed)
        qk_turned, k_new = scratch("qk", [8, P, SEQ]), scratch("k_new", [NS, P, 2, TS])
        kc_turned, vc_rows = scratch("kc", [2, P, SEQ // BLK]), scratch("vc", [2, SEQ // BLK, HD])
        block_mask = scratch("block_mask", [NS, 2, 16, PAGES])
        turn_queries(nc, c, proj, qk_turned)
        with ExitStack() as ctx:
            importance, q_diag, o_cmp = sb("importance", [P, P], ctx), sb("q_diag", [P, NS, 64], ctx), sb("o_cmp", [64, NS, HD], ctx)
            ids = ctx.enter_context(nc.sbuf_tensor("page_ids", [1, NS * PAGES], I32))
            load_all(nc, [(ids[:], A["page_table"].rearrange("b p -> (b p)").unsqueeze(0))])
            turn_sample(nc, c, proj, q_diag, k_new)
            sample_nsa_cache(nc, c, A, proj, kc_turned, vc_rows, ids, q_diag, importance, o_cmp, software[0:2])
            choose_blocks(nc, importance, block_mask)
            sample_selected(nc, c, A, proj, ids, q_diag, k_new, block_mask, o_cmp, mixed, *software[2:4])
        prompt_attention(nc, c, A, proj, qk_turned, kc_turned, vc_rows, mixed)
        project_out(A["ab_w_out"][0])
        post_norm(nc, X, y, mod_rows[:, 0, 2 * D:3 * D], A["ln_g"][0, 0], A["ln_b"][0, 0], c)
        ffn(nc, A, c, X, 0, modT, mod_rows, y)

        xp, xs = scratch("xp", [3 + SEQ, NCH]), scratch("xs", [NS, 3 + TS, NCH])
        z, ba, qkv, gb = scratch("z", [T, D]), scratch("ba", [T, 16]), scratch("qkv", [T, NCH]), scratch("gb", [T, 16])
        with ExitStack() as ctx:
            hT = sb("hT_c", [P, KD, T], ctx)
            zero = sb("zero3", [3, NCH], ctx)
            transpose_rows(nc, X, hT, c["ident"], (modT[:, 1, 0], modT[:, 1, 1]))
            with phase(nc, "zeroed", "stored") as (block, zeroed, stored):
                @block.vector
                def _(dve):
                    dve.memset(zero[:], 0.0).then_inc(zeroed, 1)

                @block.sync
                def _(sp):
                    sp.wait_ge(zeroed, 1)
                    sp.dma_start(xp[0:3], zero[:]).then_inc(stored, 16)
                    sp.dma_start(xs[:, 0:3], A["state_gdn_conv"][0]).then_inc(stored, 16)
                    sp.wait_ge(stored, 32)
            lhsT = lambda m, k: hT[:, k, m * P:m * P + ROWS[m]]

            def conv_rows(m, cols):
                return xp[3 + m * P:3 + (m + 1) * P, cols] if m < MT else xs[:, 3:3 + TS, cols]
            w = A["c_w_in"][0]
            gemm_rows(nc, lhsT, ROWS, KD, w[:, 0:NCH], conv_rows, 512, 6, tag="c")
            gemm_rows(nc, lhsT, ROWS, KD, w[:, C_BA:C_Z], lambda m, cols: row_tile(ba, m, cols), 16, 1, tag="cb")
            gemm_rows(nc, lhsT, ROWS, KD, w[:, C_Z:C_IN], lambda m, cols: row_tile(z, m, cols), 512, 2, tag="cz")
        gdn(nc, A, O, c, xp, xs, z, ba, qkv, gb, mixed)
        project_out(A["c_w_out"][0])
        post_norm(nc, X, y, mod_rows[:, 1, 2 * D:3 * D], A["ln_g"][1, 0], A["ln_b"][1, 0], c)
        ffn(nc, A, c, X, 1, modT, mod_rows, y, (O["y_prompt"][0], O["y_sample"].rearrange("b t d -> (b t) d")))


_INS = ["x_prompt", "x_sample", "c_prompt", "c_sample", "page_table", "cache_cmp_k", "cache_cmp_v", "cache_sel_k", "cache_sel_v",
        "state_win_k", "state_win_v", "state_gla", "state_gdn", "state_gdn_conv", "w_ada", "b_ada", "ln_g", "ln_b", "w_ffn_in",
        "w_ffn_out", "ab_w_in", "ab_w_gk2", "ab_b_gk", "ab_gla_norm", "ab_cmp_pe", "ab_cmp_w1", "ab_cmp_w2", "ab_w_out", "c_w_in",
        "c_conv_w", "c_a_log", "c_dt_bias", "c_norm", "c_w_out"]
_ROWS_P, _ROWS_S = (1, 1, SEQ, 2, HD), (1, NS, TS, 2, HD)
_OUTS = {"y_prompt": (1, SEQ, D), "y_sample": (NS, TS, D),
         "p_cmp_k": _ROWS_P, "p_cmp_v": _ROWS_P, "p_sel_k": _ROWS_P, "p_sel_v": _ROWS_P,
         "p_win_k": (1, 1, WIN, 2, HD), "p_win_v": (1, 1, WIN, 2, HD),
         "p_gla": (1, 1, GH, GK, GV), "p_gdn": (1, 1, DH, P, P), "p_conv": (1, 1, 3, NCH),
         "s_cmp_k": _ROWS_S, "s_cmp_v": _ROWS_S, "s_sel_k": _ROWS_S, "s_sel_v": _ROWS_S,
         "s_win_k": (1, NS, WIN, 2, HD), "s_win_v": (1, NS, WIN, 2, HD),
         "s_gla": (1, NS, GH, GK, GV), "s_gdn": (1, NS, DH, P, P), "s_conv": (1, NS, 3, NCH)}


def kernel(**inputs):
    import numpy as _np
    import concourse.bacc as _bacc
    from concourse import mybir as _mybir
    from concourse.bass_utils import run_bass_kernel_spmd as _run

    nc = _bacc.Bacc("TRN2", target_bir_lowering=False, num_devices=1)
    arrays, A, O = {}, {}, {}
    given = {name: inputs[name] for name in _INS}
    given.update({"c_" + name: a for name, a in shape_constants().items()})
    for name, a in given.items():
        a = _np.ascontiguousarray(a)
        arrays[f"in_{name}"] = a
        A[name] = nc.dram_tensor(f"in_{name}", a.shape, _mybir.dt.from_np(a.dtype), kind="ExternalInput").ap()
    for name, shape in _OUTS.items():
        O[name] = nc.dram_tensor(f"out_{name}", shape, _mybir.dt.float32, kind="ExternalOutput").ap()
    hybrid_decoder(nc, A, O)
    r = _run(nc, [arrays], core_ids=[0])
    return tuple(r.results[0][f"out_{name}"] for name in _OUTS)
```

```python
from contextlib import ExitStack, contextmanager

import numpy as np

import concourse.bass as bass
from concourse import mybir

F32 = mybir.dt.float32
I32 = mybir.dt.int32
ALU = mybir.AluOpType
ACT = mybir.ActivationFunctionType
AX = mybir.AxisListType.X

P = 128
D = 1024
KD = D // P
SEQ = 1024
NS, TS = 8, 8
SROWS = NS * TS
T = SEQ + SROWS
MT = SEQ // P
TILES = MT + 1
ROWS = [P] * MT + [SROWS]
FF = 2816
FT = FF // P
CHUNK = 64
ALPHA = (2.0 * 2) ** 0.25
LN_EPS, RMS_EPS, L2_EPS = 1e-5, 1e-6, 1e-6
PAGES = 64
NPOOL = 640
PAST = 8192
NEG = -1e30
MODS = 1 + NS

GH, GK, GV = 4, 64, 128
NH, HD, BLK, WIN = 8, 64, 64, 512
Q_A, K_A, V_A, R_A, GK_A = 0, 256, 512, 1024, 1536
Q_B, KV_B, GATE_B, AB_IN = 1552, 2064, 2832, 2856
K_CMP, V_CMP, K_SEL, V_SEL, K_WIN, V_WIN = [KV_B + 128 * j for j in range(6)]
NCH = 3072
C_BA, C_Z, C_IN = 3072, 3088, 4112
DH = 8


def shape_constants():
    f = np.float32
    i = np.arange(P)
    c = {"ident": np.eye(P, dtype=f), "ones": np.ones((P, P), f)}
    j, k = np.meshgrid(np.arange(P), np.arange(P), indexing="ij")
    c["tri_p"], c["strict_p"] = (j <= k).astype(f), (j > k).astype(f)
    half = j // CHUNK == k // CHUNK
    c["inside_p"] = (half & (j <= k)).astype(f)
    c["mid_p"] = c["inside_p"] - (half & (j % CHUNK < CHUNK // 2)).astype(f)
    c["border_p"] = (half & np.where(k < CHUNK, j > k, j <= k)).astype(f)
    j, k = j[:SROWS, :SROWS], k[:SROWS, :SROWS]
    same = j // TS == k // TS
    c["tri_s"], c["strict_s"] = (same & (j <= k)).astype(f), (same & (j > k)).astype(f)
    c["mid_s"] = c["tri_s"] - (same & (j % TS < TS // 2)).astype(f)
    c["seq_mask"] = (np.arange(SROWS)[:, None] // TS == np.arange(NS)[None, :]).astype(f)
    slopes = np.exp2(-8.0 * np.arange(1, NH + 1) / NH)
    x = np.arange(1024)[None, :] - 896
    c["dist_sel"] = np.where(x <= i[:, None], x - i[:, None], NEG).astype(f)
    x = np.arange(640)[None, :] - 512
    dist = i[:, None] - x
    c["dist_win"] = np.where((dist >= 0) & (dist <= WIN), -dist, NEG).astype(f)
    q = (np.arange(MT)[None, :, None] * P + i[:, None, None])
    b = np.arange(16)[None, None, :]
    seen = b * BLK + BLK - 1 <= q
    c["dist_cmp"] = np.where(seen, b * BLK + 0.5 * (BLK - 1) - q, NEG).astype(f)
    c["seen_cmp"] = seen.astype(f)
    c["slopes8"] = np.broadcast_to((8 * slopes).reshape(4, 1, 2), (4, P, 2)).astype(f)
    row = slopes[:, None] * np.ones((1, TS))
    t = np.arange(TS)[None, :]
    pos = np.arange(PAST).reshape(PAGES, P).T
    c["alibi_page"] = (row[None, None] * (pos[:, :, None, None] - PAST - t[None, None])).reshape(P, PAGES * 64).astype(f)
    wpos = (PAST - WIN + np.arange(WIN)).reshape(4, P).T
    dw = PAST + t[None, None] - wpos[:, :, None, None]
    c["alibi_win"] = np.where(dw <= WIN, -row[None, None] * dw, NEG).reshape(P, 4 * 64).astype(f)
    tok = np.arange(TS)[:, None, None]
    c["alibi_new"] = np.where(tok <= t[None], row[None] * (tok - t[None]), NEG).reshape(TS, 64).astype(f)
    cen = np.arange(P) * BLK + 0.5 * (BLK - 1)
    c["alibi_cmp"] = (row.reshape(64, 1) * (cen[None, :] - PAST - np.tile(np.arange(TS), NH)[:, None])).astype(f)
    c["sel_mod_p"] = (np.arange(MODS)[:, None] == 0).astype(f) * np.ones((1, P), f)
    c["sel_mod_s"] = (np.arange(MODS)[:, None] == 1 + np.arange(SROWS)[None, :] // TS).astype(f)
    r = np.arange(64)
    target = (r // 32) * 8 + r % 8
    c["head_sum"] = (np.arange(NS)[None, :, None] * 16 + target[:, None, None] == np.arange(P)[None, None, :]).reshape(64, NS * P).astype(f)
    c["half"] = (np.arange(2)[:, None] == i[None, :] // 64).astype(f)
    return c


@contextmanager
def phase(nc, *names):
    before = nc.snapshot_sems()
    sems = [nc.alloc_semaphore(f"{name}_{nc.next_id()}") for name in names]
    nums = [s.num for s in sems]
    with nc.Block() as block:
        yield (block, *sems)
    nc.all_engine_barrier(sems_to_clear=range(min(nums), max(nums) + 1))
    nc.restore_sems(before)


def banks(ctx, nc, name, shape):
    n = int(np.prod(shape[1:]))
    whole = -(-n // 512) * 512
    t = ctx.enter_context(nc.psum_tensor(f"{name}_{nc.next_id()}", [P, whole], F32))
    ap = t[0:shape[0], 0:n]
    if len(shape) == 3:
        ap = ap.rearrange("p (a b) -> p a b", a=shape[1])
    if len(shape) == 4:
        ap = ap.rearrange("p (a b c) -> p a b c", a=shape[1], b=shape[2])
    return ap


class InOrder:

    def __init__(self, eng, sem):
        self.eng, self.sem, self.n = eng, sem, 0

    def __call__(self, ins):
        self.n += 1
        ins.then_inc(self.sem, 1)
        self.eng.wait_ge(self.sem, self.n)


def pipelined(eng, count, pre, post):
    pre(0, 0)
    with eng.Fori(0, count // 2 - 1) as i:
        t = i * 2
        pre(t + 1, 1)
        post(t, 0)
        pre(t + 2, 0)
        post(t + 1, 1)
    pre(count - 1, 1)
    post(count - 2, 0)
    post(count - 1, 1)


def load_all(nc, pairs):
    with phase(nc, "loaded") as (block, loaded):
        @block.sync
        def _(sp):
            for dst, src in pairs:
                sp.dma_start(dst, src).then_inc(loaded, 16)
            sp.wait_ge(loaded, 16 * len(pairs))


def gemm_rows(nc, lhsT, rows, kt, w, out_rows, width, steps, bias=None, tag=""):
    slots = 2 if steps >= 2 else 1
    loops = steps // slots
    n_m = len(rows)
    ring = 3 if (slots * n_m) % 3 == 0 else slots
    wr = w.rearrange("(k p) n -> p k n", p=P)
    per = slots * n_m
    with ExitStack() as ctx:
        ws = [ctx.enter_context(nc.sbuf_tensor(f"w{tag}{s}_{nc.next_id()}", [P, kt, width], F32)) for s in range(slots)]
        bs = [ctx.enter_context(nc.sbuf_tensor(f"b{tag}{s}_{nc.next_id()}", [rows[0], width], F32)) for s in range(slots)] if bias is not None else None
        stage = [ctx.enter_context(nc.sbuf_tensor(f"st{tag}{s}_{nc.next_id()}", [P, width], F32)) for s in range(ring)]
        psum = [ctx.enter_context(nc.psum_tensor(f"pp{tag}{s}_{nc.next_id()}", [P, 512], F32)) for s in range(ring)]
        names = ([f"w_loaded{s}" for s in range(slots)] + [f"w_free{s}" for s in range(slots)]
                 + ["product_ready", "psum_free", "evacuated"] + [f"stage_free{r}" for r in range(ring)])
        with phase(nc, *names) as (block, *sems):
            w_loaded, w_free = sems[:slots], sems[slots:2 * slots]
            product_ready, psum_free, evacuated = sems[2 * slots:2 * slots + 3]
            stage_free = sems[2 * slots + 3:]
            readers = 2 if bias is not None else 1
            dmas_per_slot = 16 * (2 if bias is not None else 1)

            @block.sync
            def _(sp):
                def body(i):
                    for s in range(slots):
                        sp.wait_ge(w_free[s], i * readers + readers)
                        cols = bass.ds(i * (slots * width) + s * width, width)
                        sp.dma_start(ws[s][:], wr[:, :, cols]).then_inc(w_loaded[s], 16)
                        if bias is not None:
                            sp.dma_start(bs[s][:], bias[:, cols]).then_inc(w_loaded[s], 16)
                if loops > 1:
                    with sp.Fori(0, loops) as i:
                        body(i)
                else:
                    body(0)

            @block.tensor
            def _(pe):
                for s in range(slots):
                    pe.sem_inc(w_free[s], 1)

                def body(i):
                    for s in range(slots):
                        pe.wait_ge(w_loaded[s], i * dmas_per_slot + dmas_per_slot)
                        for m in range(n_m):
                            n = s * n_m + m
                            pe.wait_ge(psum_free, i * per + n + 1)
                            for k in range(kt):
                                last = pe.matmul(psum[n % ring][0:rows[m], 0:width], lhsT(m, k), ws[s][:, k, :],
                                                 start=(k == 0), stop=(k == kt - 1))
                            last.then_inc(product_ready, 1)
                        pe.wait_ge(product_ready, i * per + (s + 1) * n_m)
                        pe.sem_inc(w_free[s], 1)
                if loops > 1:
                    with pe.Fori(0, loops) as i:
                        body(i)
                else:
                    body(0)

            @block.vector
            def _(dve):
                dve.sem_inc(psum_free, ring)
                if bias is not None:
                    for s in range(slots):
                        dve.sem_inc(w_free[s], 1)

                def body(i):
                    for n in range(per):
                        m, r = n % n_m, rows[n % n_m]
                        dve.wait_ge(product_ready, i * per + n + 1)
                        dve.wait_ge(stage_free[n % ring], i * (16 * (per // ring)) + 16 * (n // ring) + 16)
                        if bias is None:
                            ins = dve.tensor_copy(stage[n % ring][0:r, :], psum[n % ring][0:r, 0:width])
                        else:
                            ins = dve.tensor_tensor(stage[n % ring][0:r, :], psum[n % ring][0:r, 0:width],
                                                    bs[n // n_m][0:r, :], ALU.add)
                        ins.then_inc(evacuated, 1)
                        dve.wait_ge(evacuated, i * per + n + 1)
                        dve.sem_inc(psum_free, 1)
                        if bias is not None and n % n_m == n_m - 1:
                            dve.sem_inc(w_free[n // n_m], 1)
                if loops > 1:
                    with dve.Fori(0, loops) as i:
                        body(i)
                else:
                    body(0)

            @block.scalar
            def _(act):
                for r in range(ring):
                    act.sem_inc(stage_free[r], 16)

                def body(i):
                    for n in range(per):
                        s, m = divmod(n, n_m)
                        act.wait_ge(evacuated, i * per + n + 1)
                        cols = bass.ds(i * (slots * width) + s * width, width)
                        dst, src = out_rows(m, cols), stage[n % ring][0:rows[m], :]
                        act.dma_start(dst, src).then_inc(stage_free[n % ring], 16)
                if loops > 1:
                    with act.Fori(0, loops) as i:
                        body(i)
                else:
                    body(0)
                for r in range(ring):
                    act.wait_ge(stage_free[r], 16 * (1 + loops * per // ring))


def transpose_rows(nc, src, hT, ident, mod=None, tiles=TILES, loads=()):
    with ExitStack() as ctx:
        ps = [ctx.enter_context(nc.psum_tensor(f"tp{s}_{nc.next_id()}", [P, KD, P], F32)) for s in range(2)]
        with phase(nc, "loaded", "turned", "even_out", "odd_out", "sample_steps") as (
                block, loaded, turned, even_out, odd_out, sample_steps):
            @block.sync
            def _(sp):
                for dst, s in loads:
                    sp.dma_start(dst, s).then_inc(loaded, 16)

            @block.tensor
            def _(pe):
                if loads:
                    pe.wait_ge(loaded, 16 * len(loads))
                for m in range(tiles):
                    if m >= 2:
                        pe.wait_ge(even_out, m - 1)
                        pe.wait_ge(odd_out, m - 1)
                    for k in range(KD):
                        last = pe.transpose(ps[m % 2][:, k, 0:ROWS[m]], src[0:ROWS[m], m, k * P:(k + 1) * P],
                                            ident[0:ROWS[m], 0:ROWS[m]])
                    last.then_inc(turned, 1)

            @block.scalar
            def _(act):
                for m in range(tiles):
                    act.wait_ge(turned, m + 1)
                    r = ROWS[m]
                    if mod is None:
                        act.copy(hT[:, 0:4, m * P:m * P + r], ps[m % 2][:, 0:4, 0:r]).then_inc(even_out, 1)
                    elif m < MT:
                        for k in range(4):
                            last = act.activation(hT[:, k, m * P:m * P + r], ps[m % 2][:, k, 0:r], ACT.Identity,
                                                  bias=mod[0][:, k, 0:1], scale=mod[1][:, k, 0:1])
                        last.then_inc(even_out, 1)
                    else:
                        act.sem_inc(even_out, 1)

            @block.vector
            def _(dve):
                for m in range(tiles):
                    dve.wait_ge(turned, m + 1)
                    r = ROWS[m]
                    if mod is None:
                        dve.tensor_copy(hT[:, 4:8, m * P:m * P + r], ps[m % 2][:, 4:8, 0:r]).then_inc(odd_out, 1)
                    elif m < MT:
                        for k in range(4, KD):
                            last = dve.tensor_scalar(hT[:, k, m * P:m * P + r], ps[m % 2][:, k, 0:r],
                                                     mod[1][:, k, 0:1], mod[0][:, k, 0:1], ALU.mult, ALU.add)
                        last.then_inc(odd_out, 1)
                    else:
                        step = InOrder(dve, sample_steps)
                        for k in range(KD):
                            o = hT[:, k, SEQ:T].rearrange("p (s t) -> p s t", t=TS)
                            step(dve.tensor_tensor(o, ps[m % 2][:, k, 0:r].rearrange("p (s t) -> p s t", t=TS),
                                                   mod[1][:, k, 1:MODS].unsqueeze(2).broadcast_to([P, NS, TS]), ALU.mult))
                            step(dve.tensor_tensor(o, o, mod[0][:, k, 1:MODS].unsqueeze(2).broadcast_to([P, NS, TS]), ALU.add))
                        dve.sem_inc(odd_out, 1)


def post_norm(nc, X, y, gate, ln_g, ln_b, c, out=None):
    with ExitStack() as ctx:
        sb = lambda n, s: ctx.enter_context(nc.sbuf_tensor(f"{n}_{nc.next_id()}", s, F32))
        ys = [sb("y", [P, D]) for _ in range(3)]
        gates, gate_p, gate_s = sb("gates", [MODS, D]), sb("gate_p", [P, D]), sb("gate_s", [SROWS, D])
        gB, bB = sb("gB", [P, D]), sb("bB", [P, D])
        stats, mv, rstd = sb("stats", [P, TILES, 2, 6]), sb("mv", [P, TILES, 2]), sb("rstd", [P, TILES])
        eps = sb("eps", [P, 1])
        ps = [ctx.enter_context(nc.psum_tensor(f"pg{s}_{nc.next_id()}", [P, D], F32)) for s in range(2)]
        with phase(nc, "params", "y0", "y1", "y2", "y_used", "gate_ready", "gate_out", "dve_steps", "act_steps", "rstd_ready",
                   "x_ready", "stored") as (
                block, params, y0, y1, y2, y_used, gate_ready, gate_out, dve_steps, act_steps, rstd_ready, x_ready, stored):
            y_loaded = [y0, y1, y2]

            @block.sync
            def _(sp):
                sp.dma_start(gates[:], gate).then_inc(params, 16)
                for m in range(TILES):
                    if m >= 3:
                        sp.wait_ge(y_used, m - 2)
                    sp.dma_start(ys[m % 3][0:ROWS[m], :], y[m * P:m * P + ROWS[m], :]).then_inc(y_loaded[m % 3], 16)
                if out is not None:
                    for m in range(TILES):
                        sp.wait_ge(x_ready, m + 1)
                        dst = out[0][m * P:(m + 1) * P, :] if m < MT else out[1]
                        sp.dma_start(dst, X[0:ROWS[m], m, :]).then_inc(stored, 16)
                    sp.wait_ge(stored, 16 * TILES)

            @block.tensor
            def _(pe):
                pe.wait_ge(params, 48)
                for n in range(2):
                    cols = slice(n * 512, n * 512 + 512)
                    pe.matmul(ps[0][:, cols], c["sel_mod_p"][:], gates[:, cols], start=True, stop=True)
                    last = pe.matmul(ps[1][0:SROWS, cols], c["sel_mod_s"][:], gates[:, cols], start=True, stop=True)
                last.then_inc(gate_ready, 1)

            @block.gpsimd
            def _(pool):
                pool.memset(mv[:], 1.0).then_inc(gate_out, 1)
                pool.memset(eps[:], LN_EPS).then_inc(gate_out, 1)

            @block.scalar
            def _(act):
                act.dma_start(gB[:], ln_g.partition_broadcast(P)).then_inc(params, 16)
                act.dma_start(bB[:], ln_b.partition_broadcast(P)).then_inc(params, 16)
                act.wait_ge(gate_ready, 1)
                act.copy(gate_p[:], ps[0][:]).then_inc(gate_out, 1)
                act.copy(gate_s[:], ps[1][0:SROWS, :]).then_inc(gate_out, 1)
                act.wait_ge(rstd_ready, 1)
                step = InOrder(act, act_steps)
                step(act.activation(rstd[:], mv[:, :, 1], ACT.Ln, bias=eps[:, 0:1]))
                act.activation(rstd[:], rstd[:], ACT.Exp, scale=-0.5).then_inc(rstd_ready, 1)

            @block.vector
            def _(dve):
                step = InOrder(dve, dve_steps)
                dve.wait_ge(gate_out, 4)
                dve.wait_ge(params, 48)
                for m in range(TILES):
                    r = ROWS[m]
                    dve.wait_ge(y_loaded[m % 3], 16 * (m // 3 + 1))
                    yt = ys[m % 3][0:r, :]
                    step(dve.tensor_tensor(yt, yt, (gate_p if m < MT else gate_s)[0:r, :], ALU.mult))
                    step(dve.scalar_tensor_tensor(X[0:r, m, :], X[0:r, m, :], ALPHA, yt, ALU.mult, ALU.add))
                    dve.sem_inc(y_used, 1)
                    for n in range(2):
                        step(dve.bn_stats(stats[0:r, m, n, :], X[0:r, m, n * 512:(n + 1) * 512]))
                    step(dve.bn_aggr(mv[0:r, m, :], stats[0:r, m, :, :].rearrange("p a b -> p (a b)")))
                dve.sem_inc(rstd_ready, 1)
                dve.wait_ge(rstd_ready, 2)
                for m in range(TILES):
                    r = ROWS[m]
                    x = X[0:r, m, :]
                    step(dve.tensor_scalar(x, x, mv[0:r, m, 0:1], rstd[0:r, m:m + 1], ALU.subtract, ALU.mult))
                    step(dve.tensor_tensor(x, x, gB[0:r, :], ALU.mult))
                    dve.tensor_tensor(x, x, bB[0:r, :], ALU.add).then_inc(x_ready, 1)


def project_norm(nc, X, hT, w, gate, ln_g, ln_b, c):
    with ExitStack() as ctx:
        sb = lambda n, s: ctx.enter_context(nc.sbuf_tensor(f"{n}_{nc.next_id()}", s, F32))
        ws = [sb("w_out", [P, KD, 512]) for _ in range(2)]
        y = [sb("y", [P, D]) for _ in range(2)]
        gates, gate_p, gate_s = sb("gates", [MODS, D]), sb("gate_p", [P, D]), sb("gate_s", [SROWS, D])
        gB, bB = sb("gB", [P, D]), sb("bB", [P, D])
        stats, mv, rstd, eps = sb("stats", [P, TILES, 2, 6]), sb("mv", [P, TILES, 2]), sb("rstd", [P, TILES]), sb("eps", [P, 1])
        pg = [banks(ctx, nc, f"pg{s}", [P, D]) for s in range(2)]
        py = [banks(ctx, nc, f"py{s}", [P, D]) for s in range(2)]
        with phase(nc, "w0", "w1", "params", "gate_ready", "gate_out", "eps_ready", "product", "taken", "dve_steps", "act_steps",
                   "var_ready", "rstd_ready", "x_ready") as (
                block, w0, w1, params, gate_ready, gate_out, eps_ready, product, taken, dve_steps, act_steps,
                var_ready, rstd_ready, x_ready):
            w_loaded = [w0, w1]

            @block.sync
            def _(sp):
                wr = w.rearrange("(k p) n -> p k n", p=P)
                sp.dma_start(gates[:], gate).then_inc(params, 16)
                for n in range(2):
                    sp.dma_start(ws[n][:], wr[:, :, n * 512:(n + 1) * 512]).then_inc(w_loaded[n], 16)
                sp.dma_start(gB[:], ln_g.partition_broadcast(P)).then_inc(params, 16)
                sp.dma_start(bB[:], ln_b.partition_broadcast(P)).then_inc(params, 16)

            @block.tensor
            def _(pe):
                pe.wait_ge(params, 48)
                for n in range(2):
                    cols = slice(n * 512, n * 512 + 512)
                    pe.matmul(pg[0][:, cols], c["sel_mod_p"][:], gates[:, cols], start=True, stop=True)
                    last = pe.matmul(pg[1][0:SROWS, cols], c["sel_mod_s"][:], gates[:, cols], start=True, stop=True)
                last.then_inc(gate_ready, 1)
                for m in range(TILES):
                    r = ROWS[m]
                    if m >= 2:
                        pe.wait_ge(taken, m - 1)
                    for n in range(2):
                        if m == 0:
                            pe.wait_ge(w_loaded[n], 16)
                        for k in range(KD):
                            last = pe.matmul(py[m % 2][0:r, n * 512:(n + 1) * 512], hT[:, k, m * P:m * P + r], ws[n][:, k, :],
                                             start=(k == 0), stop=(k == KD - 1))
                    last.then_inc(product, 1)

            @block.scalar
            def _(act):
                step = InOrder(act, act_steps)
                act.wait_ge(gate_ready, 1)
                act.copy(gate_p[:], pg[0]).then_inc(gate_out, 1)
                act.copy(gate_s[:], pg[1][0:SROWS, :]).then_inc(gate_out, 1)
                act.wait_ge(eps_ready, 1)
                for m in range(TILES):
                    r = ROWS[m]
                    act.wait_ge(var_ready, m + 1)
                    step(act.activation(rstd[0:r, m:m + 1], mv[0:r, m, 1:2], ACT.Ln, bias=eps[0:r, 0:1]))
                    act.activation(rstd[0:r, m:m + 1], rstd[0:r, m:m + 1], ACT.Exp, scale=-0.5).then_inc(rstd_ready, 1)

            @block.vector
            def _(dve):
                step = InOrder(dve, dve_steps)
                dve.memset(eps[:], LN_EPS).then_inc(eps_ready, 1)
                dve.wait_ge(gate_out, 2)
                dve.wait_ge(params, 48)

                def scaled(m):
                    r, x = ROWS[m], X[0:ROWS[m], m, :]
                    dve.wait_ge(rstd_ready, m + 1)
                    step(dve.tensor_scalar(x, x, mv[0:r, m, 0:1], rstd[0:r, m:m + 1], ALU.subtract, ALU.mult))
                    step(dve.tensor_tensor(x, x, gB[0:r, :], ALU.mult))
                    dve.tensor_tensor(x, x, bB[0:r, :], ALU.add).then_inc(x_ready, 1)
                for m in range(TILES):
                    r, x = ROWS[m], X[0:ROWS[m], m, :]
                    dve.wait_ge(product, m + 1)
                    yt = y[m % 2][0:r, :]
                    step(dve.tensor_tensor(yt, py[m % 2][0:r, :], (gate_p if m < MT else gate_s)[0:r, :], ALU.mult))
                    dve.sem_inc(taken, 1)
                    step(dve.scalar_tensor_tensor(x, x, ALPHA, yt, ALU.mult, ALU.add))
                    for n in range(2):
                        step(dve.bn_stats(stats[0:r, m, n, :], X[0:r, m, n * 512:(n + 1) * 512]))
                    dve.bn_aggr(mv[0:r, m, :], stats[0:r, m, :, :].rearrange("p a b -> p (a b)")).then_inc(var_ready, 1)
                    if m:
                        scaled(m - 1)
                scaled(TILES - 1)


def swiglu_hidden(nc, hT, hid, w_in):
    wr = w_in.rearrange("(k p) (two n) -> p two k n", p=P, two=2)
    chunks = [(0, 512), (512, 512), (1024, SROWS)]
    NB = 3
    with ExitStack() as ctx:
        sb = lambda n, s: ctx.enter_context(nc.sbuf_tensor(f"{n}_{nc.next_id()}", s, F32))
        ws = [sb("wf", [P, 2, KD, P]) for _ in range(2)]
        e = [sb("e", [P, 512]) for _ in range(NB)]
        ps = [ctx.enter_context(nc.psum_tensor(f"pf{s}_{nc.next_id()}", [P, 2, 512], F32)) for s in range(NB)]
        with phase(nc, "w_loaded0", "w_loaded1", "w_free0", "w_free1", "pair_ready", "silu_ready", "pair_used", "dve_steps") as (
                block, w_loaded0, w_loaded1, w_free0, w_free1, pair_ready, silu_ready, pair_used, dve_steps):
            w_loaded, w_free = [w_loaded0, w_loaded1], [w_free0, w_free1]

            @block.sync
            def _(sp):
                with sp.Fori(0, FT // 2) as i:
                    for s in range(2):
                        sp.wait_ge(w_free[s], i + 1)
                        for two in range(2):
                            sp.dma_start(ws[s][:, two], wr[:, two, :, bass.ds(i * 256 + s * P, P)]).then_inc(w_loaded[s], 16)

            @block.tensor
            def _(pe):
                pe.sem_inc(w_free0, 1)
                pe.sem_inc(w_free1, 1)
                with pe.Fori(0, FT // 2) as i:
                    for s in range(2):
                        pe.wait_ge(w_loaded[s], i * 32 + 32)
                        for j, (t0, tn) in enumerate(chunks):
                            n = s * 3 + j
                            pe.wait_ge(pair_used, i * 6 + n + 1)
                            for two in range(2):
                                for k in range(KD):
                                    last = pe.matmul(ps[n % NB][:, two, 0:tn], ws[s][:, two, k, :], hT[:, k, t0:t0 + tn],
                                                     start=(k == 0), stop=(k == KD - 1))
                            last.then_inc(pair_ready, 1)
                        pe.wait_ge(pair_ready, i * 6 + s * 3 + 3)
                        pe.sem_inc(w_free[s], 1)

            @block.scalar
            def _(act):
                with act.Fori(0, FT // 2) as i:
                    for s in range(2):
                        for j, (t0, tn) in enumerate(chunks):
                            n = s * 3 + j
                            act.wait_ge(pair_ready, i * 6 + n + 1)
                            act.activation(e[n % NB][:, 0:tn], ps[n % NB][:, 0, 0:tn], ACT.Silu).then_inc(silu_ready, 1)

            @block.vector
            def _(dve):
                dve.sem_inc(pair_used, NB)
                with dve.Fori(0, FT // 2) as i:
                    for s in range(2):
                        for j, (t0, tn) in enumerate(chunks):
                            n = s * 3 + j
                            et, pt = e[n % NB][:, 0:tn], ps[n % NB]
                            dve.wait_ge(silu_ready, i * 6 + n + 1)
                            dve.tensor_tensor(hid[:, bass.ds(i * (2 * T) + s * T + t0, tn)], et, pt[:, 1, 0:tn], ALU.mult).then_inc(dve_steps, 1)
                            dve.wait_ge(dve_steps, i * 6 + n + 1)
                            dve.sem_inc(pair_used, 1)


def adaln_mods(nc, A, c, modT, mod_rows):
    with ExitStack() as ctx:
        sb = lambda n, s: ctx.enter_context(nc.sbuf_tensor(f"{n}_{nc.next_id()}", s, F32))
        cond, ex, cT = sb("cond", [MODS, D]), sb("ex", [MODS, D]), sb("cT", [P, KD, MODS])
        ps = ctx.enter_context(nc.psum_tensor("cond_ps", [P, KD, MODS], F32))
        with phase(nc, "loaded", "exp_ready", "dve_steps", "silu_ready", "turned") as (
                block, loaded, exp_ready, dve_steps, silu_ready, turned):
            @block.sync
            def _(sp):
                sp.dma_start(cond[0:1, :], A["c_prompt"]).then_inc(loaded, 16)
                sp.dma_start(cond[1:MODS, :], A["c_sample"]).then_inc(loaded, 16)

            @block.scalar
            def _(act):
                act.wait_ge(loaded, 32)
                act.activation(ex[:], cond[:], ACT.Exp, scale=-1.0).then_inc(exp_ready, 1)

            @block.vector
            def _(dve):
                step = InOrder(dve, dve_steps)
                dve.wait_ge(exp_ready, 1)
                step(dve.tensor_scalar(ex[:], ex[:], 1.0, None, ALU.add))
                step(dve.reciprocal(ex[:], ex[:]))
                dve.tensor_tensor(cond[:], cond[:], ex[:], ALU.mult).then_inc(silu_ready, 1)
                dve.wait_ge(turned, 1)
                dve.tensor_copy(cT[:], ps[:]).then_inc(dve_steps, 1)

            @block.tensor
            def _(pe):
                pe.wait_ge(silu_ready, 1)
                for k in range(KD):
                    last = pe.transpose(ps[:, k, :], cond[:, k * P:(k + 1) * P], c["ident"][0:MODS, 0:MODS])
                last.then_inc(turned, 1)

        for layer in range(2):
            gemm_rows(nc, lambda m, k: cT[:, k, :], [MODS], KD, A["w_ada"][layer],
                      lambda m, cols, l=layer: mod_rows[:, l, cols], 512, 12,
                      bias=A["b_ada"][layer].partition_broadcast(MODS), tag="ada")
        rows = sb("mod_rows_sb", [MODS, 2, 6, D])
        pt = [ctx.enter_context(nc.psum_tensor(f"pmt{l}", [P, 4, KD, MODS], F32)) for l in range(2)]
        with phase(nc, "loaded", "turned", "copied") as (block, loaded, turned, copied):
            @block.sync
            def _(sp):
                sp.dma_start(rows[:], mod_rows.rearrange("s l (c n) -> s l c n", c=6)).then_inc(loaded, 16)

            @block.tensor
            def _(pe):
                pe.wait_ge(loaded, 16)
                for l in range(2):
                    for n, chunk in enumerate((0, 1, 3, 4)):
                        for k in range(KD):
                            last = pe.transpose(pt[l][:, n, k, :], rows[:, l, chunk, k * P:(k + 1) * P],
                                                c["ident"][0:MODS, 0:MODS])
                last.then_inc(turned, 1)

            @block.vector
            def _(dve):
                dve.wait_ge(turned, 1)
                for l in range(2):
                    for n in range(4):
                        dve.tensor_scalar(modT[:, l, n], pt[l][:, n], float(n % 2), None, ALU.add).then_inc(copied, 1)


def ffn(nc, A, c, X, layer, modT, mod_rows, y, out=None):
    with ExitStack() as outer:
        hid = outer.enter_context(nc.sbuf_tensor(f"hid_{nc.next_id()}", [P, FT * T], F32))
        with nc.sbuf_tensor(f"hT_{nc.next_id()}", [P, KD, T], F32) as hT:
            transpose_rows(nc, X, hT, c["ident"], (modT[:, layer, 2], modT[:, layer, 3]))
            swiglu_hidden(nc, hT, hid, A["w_ffn_in"][layer])
        gemm_rows(nc, lambda m, k: hid[:, k * T + m * P:k * T + m * P + ROWS[m]], ROWS, FT, A["w_ffn_out"][layer],
                  lambda m, cols: y[m * P:m * P + ROWS[m], cols], 256, 4, tag="f2")
    post_norm(nc, X, y, mod_rows[:, layer, 5 * D:6 * D], A["ln_g"][layer, 1], A["ln_b"][layer, 1], c, out)


def gla_gates(nc, A, c, proj, log_a):
    W = GH * GK
    with ExitStack() as ctx:
        sb = lambda n, s: ctx.enter_context(nc.sbuf_tensor(f"{n}_{nc.next_id()}", s, F32))
        gk, gkT = sb("gk", [P, TILES, 16]), sb("gkT", [16, T])
        w2, bias = sb("w_gk2", [16, W]), sb("b_gk", [P, W])
        x, e = sb("gate_x", [P, TILES, W]), sb("gate_e", [P, TILES, W])
        pt = [ctx.enter_context(nc.psum_tensor(f"gkt{i}", [16, 512], F32)) for i in range(3)]
        px = [ctx.enter_context(nc.psum_tensor(f"gx{i}", [P, 2, W], F32)) for i in range(5)]
        with phase(nc, "loaded", "turned", "copied", "product", "dve_steps", "abs_ready", "log_ready", "act_steps", "done", "stored") as (
                block, loaded, turned, copied, product, dve_steps, abs_ready, log_ready, act_steps, done, stored):
            @block.sync
            def _(sp):
                g = proj[:, GK_A:GK_A + 16]
                sp.dma_start(gk[:, 0:MT, :], g[0:SEQ].rearrange("(m p) k -> p m k", p=P)).then_inc(loaded, 16)
                sp.dma_start(gk[0:SROWS, MT, :], g[SEQ:T]).then_inc(loaded, 16)
                sp.dma_start(w2[:], A["ab_w_gk2"][0]).then_inc(loaded, 16)
                sp.dma_start(bias[:], A["ab_b_gk"][0].partition_broadcast(P)).then_inc(loaded, 16)
                sp.wait_ge(done, 1)
                sp.dma_start(log_a[0:SEQ].rearrange("(m p) k -> p m k", p=P), x[:, 0:MT, :]).then_inc(stored, 16)
                sp.dma_start(log_a[SEQ:T], x[0:SROWS, MT, :]).then_inc(stored, 16)
                sp.wait_ge(stored, 32)

            @block.tensor
            def _(pe):
                pe.wait_ge(loaded, 64)
                for m in range(TILES):
                    last = pe.transpose(pt[m // 4][:, (m % 4) * P:(m % 4) * P + ROWS[m]], gk[0:ROWS[m], m, :], c["ident"][0:ROWS[m], 0:ROWS[m]])
                last.then_inc(turned, 1)
                pe.wait_ge(copied, 3)
                for m in range(TILES):
                    last = pe.matmul(px[m // 2][0:ROWS[m], m % 2, :], gkT[:, m * P:m * P + ROWS[m]], w2[:], start=True, stop=True)
                last.then_inc(product, 1)

            @block.scalar
            def _(act):
                step = InOrder(act, act_steps)
                act.wait_ge(abs_ready, 1)
                step(act.activation(e[:], e[:], ACT.Exp, scale=-1.0))
                act.activation(e[:], e[:], ACT.Ln, bias=1.0).then_inc(log_ready, 1)

            @block.vector
            def _(dve):
                step = InOrder(dve, dve_steps)
                dve.wait_ge(turned, 1)
                for i in range(3):
                    w = min(512, T - i * 512)
                    dve.tensor_copy(gkT[:, i * 512:i * 512 + w], pt[i][:, 0:w]).then_inc(copied, 1)
                dve.wait_ge(product, 1)
                step(dve.memset(x[:, MT, :], 0.0))
                for m in range(TILES):
                    step(dve.tensor_tensor(x[0:ROWS[m], m, :], px[m // 2][0:ROWS[m], m % 2, :], bias[0:ROWS[m], :], ALU.add))
                dve.scalar_tensor_tensor(e[:], x[:], -1.0, x[:], ALU.mult, ALU.max).then_inc(abs_ready, 1)
                step(dve.tensor_scalar(x[:], x[:], 0.0, None, ALU.min))
                dve.wait_ge(log_ready, 1)
                step(dve.tensor_tensor(x[:], x[:], e[:], ALU.subtract))
                dve.tensor_scalar(x[:], x[:], 1.0 / 16.0, None, ALU.mult).then_inc(done, 1)


def gla_block(nc, c, masks, gnorm, held, dst, S, next_src=None, state_in=None, state_out=None):
    samples = state_in is not None
    C, U = (SROWS, 1) if samples else (P, 2)
    BL, W, V = range(U), GH * GK, GH * GV
    row, la = held
    EXPS, TR = (5, 3) if samples else (6, 4)
    ident = c["ident"][0:C, 0:C]
    with ExitStack() as ctx:
        sb = lambda n, s: ctx.enter_context(nc.sbuf_tensor(f"{n}_{nc.next_id()}", s, F32))
        NB = NS if samples else 1
        e_in, e_mid, e_neg, e_end, e_x = [sb(n, [C, U, W]) for n in ("e_in", "e_mid", "e_neg", "e_end", "e_x")]
        e_last = sb("e_last", [GK, U, GH, NB])
        qs, q2, k2, k4, x3 = [sb(n, [C, U, W]) for n in ("qs", "q2", "k2", "k4", "x3")]
        qsT, q2T, k2T, x3T = [sb(n, [GK, U, GH, C]) for n in ("qsT", "q2T", "k2T", "x3T")]
        pT = sb("pT", [C, U, GH, C])
        o, sq, er = [sb(n, [C, U, GH, GV]) for n in ("o", "sq", "er")]
        ss, eps = sb("ss", [C, U, GH]), sb("eps", [C, 1])
        if samples:
            k4m, XT = sb("k4m", [C, NS, W]), sb("XT", [P, GH, C])
        b0, b1, b2, b3 = [[banks(ctx, nc, n, [P, 512]) for _ in BL] for n in ("g0", "g1", "g2", "g3")]
        turn = lambda b: b[0:GK, 0:GH * C].rearrange("p (h i) -> p h i", h=GH)
        sq4 = lambda b: b[0:C, 0:GH * C].rearrange("p (h i) -> p h i", h=GH)
        wide = lambda b, r=C: b[0:r, :].rearrange("p (h v) -> p h v", h=GH)
        last4 = lambda b: b[0:GK, 0:GH * NB].rearrange("p (h n) -> p h n", h=GH)
        with phase(nc, "loaded", "state_loaded", "sums", "exps", "silu_done", "qs_ready", "q2_ready", "k2_ready", "k4_ready", "x3_ready",
                   "k4m_ready", "turned", "turned_out", "scores", "masked", "x_ready", "x_out", "o_ready", "kv_ready", "s_out",
                   "sum_ready", "ln_ready", "er_ready", "done", "stored", "dve_steps", "act_steps") as (
                block, loaded, state_loaded, sums, exps, silu_done, qs_ready, q2_ready, k2_ready, k4_ready, x3_ready,
                k4m_ready, turned, turned_out, scores, masked, x_ready, x_out, o_ready, kv_ready, s_out,
                sum_ready, ln_ready, er_ready, done, stored, dve_steps, act_steps):
            @block.sync
            def _(sp):
                if samples:
                    for b in range(NS):
                        sp.dma_start(S[:, b], state_in[b].rearrange("h k v -> k h v")).then_inc(state_loaded, 16)
                if next_src is not None:
                    sp.wait_ge(x3_ready, U)
                    sp.wait_ge(k4_ready, U)
                    sp.wait_ge(silu_done, 1)
                    sp.wait_ge(sums, U)
                    sp.dma_start(la[:], next_src[1]).then_inc(loaded, 16)
                    sp.wait_ge(kv_ready, U)
                    sp.dma_start(row[:], next_src[0]).then_inc(loaded, 16)
                if samples:
                    for b in range(NS):
                        sp.wait_ge(s_out, b + 1)
                        sp.dma_start(state_out[b].rearrange("h k v -> k h v"), S[:, b]).then_inc(stored, 16)
                for u in BL:
                    sp.wait_ge(done, u + 1)
                    sp.dma_start(dst[u], o[:, u].rearrange("p h v -> p (h v)")).then_inc(stored, 16)
                sp.wait_ge(stored, 16 * (U + (NS if samples else 0)))
                if next_src is not None:
                    sp.wait_ge(loaded, 32)

            @block.tensor
            def _(pe):
                for u in BL:
                    pe.matmul(b0[u][0:C, 0:W], masks["tri"], la[:, u, :], start=True, stop=True)
                    pe.matmul(b0[u][0:C, W:2 * W], masks["mid"], la[:, u, :], start=True, stop=True)
                    pe.matmul(b1[u][0:C, 0:W], masks["strict"], la[:, u, :], start=True, stop=True)
                    if not samples:
                        pe.matmul(b1[u][0:C, W:2 * W], masks["border"], la[:, u, :], start=True, stop=True)
                    for h in range(GH):
                        last = pe.matmul(last4(b3[u])[:, h, :], la[:, u, h * GK:(h + 1) * GK], masks["seq"], start=True, stop=True)
                    last.then_inc(sums, 1)
                for u in BL:
                    pe.wait_ge(exps, EXPS * (u + 1))
                    for x, ready, bank in ((qs, qs_ready, b0), (q2, q2_ready, b1), (k2, k2_ready, b2), (x3, x3_ready, b3)):
                        if x is x3 and samples:
                            continue
                        pe.wait_ge(ready, u + 1)
                        for h in range(GH):
                            last = pe.transpose(turn(bank[u])[:, h, :], x[:, u, h * GK:(h + 1) * GK], ident)
                        last.then_inc(turned, 1)
                for u in BL:
                    pe.wait_ge(turned_out, TR * (u + 1))
                    for h in range(GH):
                        last = pe.matmul(sq4(b2[u])[:, h, :], k2T[:, u, h, :], q2T[:, u, h, :], start=True, stop=True)
                    if not samples:
                        for h in range(GH):
                            last = pe.matmul(sq4(b3[u])[0:CHUNK, h, 0:CHUNK], x3T[:, u, h, 0:CHUNK], x3T[:, u, h, CHUNK:P], start=True, stop=True)
                    last.then_inc(scores, 1)
                if samples:
                    pe.wait_ge(state_loaded, 16 * NS)
                    for h in range(GH):
                        for b in range(NS):
                            t = slice(b * TS, (b + 1) * TS)
                            last = pe.matmul(b3[0][:, h * C + b * TS:h * C + (b + 1) * TS], S[:, b, h, :], qsT[:, 0, h, t], start=True, stop=True)
                    last.then_inc(x_ready, 1)
                    pe.wait_ge(x_out, 1)
                for u in BL:
                    pe.wait_ge(masked, u + 1)
                    if u:
                        pe.wait_ge(s_out, u)
                    for h in range(GH):
                        v = row[:, u, 512 + h * GV:512 + (h + 1) * GV]
                        if samples:
                            pe.matmul(wide(b0[u])[:, h, :], XT[:, h, :], c["ident"][:], start=True, stop=False)
                        else:
                            pe.matmul(wide(b0[u])[:, h, :], qsT[:, u, h, :], S[:, h, :], start=True, stop=False)
                        last = pe.matmul(wide(b0[u])[:, h, :], pT[:, u, h, :], v, start=False, stop=True)
                    last.then_inc(o_ready, 1)
                    if not samples:
                        pe.wait_ge(k4_ready, u + 1)
                        for h in range(GH):
                            v = row[:, u, 512 + h * GV:512 + (h + 1) * GV]
                            last = pe.matmul(wide(b1[u], GK)[:, h, :], k4[:, u, h * GK:(h + 1) * GK], v, start=True, stop=True)
                        last.then_inc(kv_ready, 1)
                if samples:
                    pe.wait_ge(k4m_ready, 1)
                    for b in range(NS):
                        if b >= 2:
                            pe.wait_ge(s_out, b - 1)
                        for h in range(GH):
                            v = row[:, 0, 512 + h * GV:512 + (h + 1) * GV]
                            last = pe.matmul(wide((b1, b2)[b % 2][0], GK)[:, h, :], k4m[:, b, h * GK:(h + 1) * GK], v, start=True, stop=True)
                        last.then_inc(kv_ready, 1)

            @block.scalar
            def _(act):
                step = InOrder(act, act_steps)
                act.activation(er[:].rearrange("p u h v -> p u (h v)"), row[:, :, R_A:R_A + V], ACT.Silu).then_inc(silu_done, 1)
                act.preload_act_table_set("natural_log_exp_and_others")
                for u in BL:
                    act.wait_ge(sums, u + 1)
                    act.activation(e_in[:, u], b0[u][0:C, 0:W], ACT.Exp).then_inc(exps, 1)
                    act.activation(e_mid[:, u], b0[u][0:C, W:2 * W], ACT.Exp).then_inc(exps, 1)
                    act.activation(e_neg[:, u], b0[u][0:C, W:2 * W], ACT.Exp, scale=-1.0).then_inc(exps, 1)
                    act.activation(e_end[:, u], b1[u][0:C, 0:W], ACT.Exp).then_inc(exps, 1)
                    if not samples:
                        act.activation(e_x[:, u], b1[u][0:C, W:2 * W], ACT.Exp).then_inc(exps, 1)
                    act.activation(e_last[:, u], last4(b3[u]), ACT.Exp).then_inc(exps, 1)
                for u in BL:
                    for n, (x, bank) in enumerate(((qsT, b0), (q2T, b1), (k2T, b2), (x3T, b3))[0:TR]):
                        act.wait_ge(turned, TR * u + n + 1)
                        act.copy(x[:, u], turn(bank[u])).then_inc(turned_out, 1)
                if samples:
                    act.wait_ge(x_ready, 1)
                    act.copy(XT[:], b3[0][:, 0:GH * C].rearrange("p (h i) -> p h i", h=GH)).then_inc(x_out, 1)
                for u in BL:
                    act.wait_ge(sum_ready, u + 1)
                    step(act.activation(ss[:, u], ss[:, u], ACT.Ln, scale=1.0 / GV, bias=eps[:, 0:1]))
                    act.activation(ss[:, u], ss[:, u], ACT.Exp, scale=-0.5).then_inc(ln_ready, 1)

            @block.gpsimd
            def _(pool):
                for u in BL:
                    pool.wait_ge(exps, EXPS * u + 4)
                    pool.tensor_tensor(k4[:, u], e_end[:, u], row[:, u, K_A:K_A + W], ALU.mult).then_inc(k4_ready, 1)
                    pool.wait_ge(silu_done, 1)
                    pool.tensor_tensor(er[:, u], er[:, u], gnorm[0:C, :].unsqueeze(1).broadcast_to([C, GH, GV]), ALU.mult).then_inc(er_ready, 1)
                if samples:
                    pool.wait_ge(k4_ready, 1)
                    pool.tensor_tensor(k4m[:], k4[:, 0].unsqueeze(1).broadcast_to([C, NS, W]), masks["seq"].unsqueeze(2).broadcast_to([C, NS, W]),
                                       ALU.mult).then_inc(k4m_ready, 1)

            @block.vector
            def _(dve):
                step = InOrder(dve, dve_steps)
                step(dve.memset(eps[:], RMS_EPS))
                scale = GK ** -0.5
                for u in BL:
                    q, k = row[:, u, Q_A:Q_A + W], row[:, u, K_A:K_A + W]
                    dve.wait_ge(exps, EXPS * u + 1)
                    dve.scalar_tensor_tensor(qs[:, u], e_in[:, u], scale, q, ALU.mult, ALU.mult).then_inc(qs_ready, 1)
                    dve.wait_ge(exps, EXPS * u + 3)
                    dve.scalar_tensor_tensor(q2[:, u], e_mid[:, u], scale, q, ALU.mult, ALU.mult).then_inc(q2_ready, 1)
                    dve.tensor_tensor(k2[:, u], e_neg[:, u], k, ALU.mult).then_inc(k2_ready, 1)
                    if not samples:
                        dve.wait_ge(exps, EXPS * u + 5)
                        step(dve.tensor_tensor(x3[0:CHUNK, u], e_x[0:CHUNK, u], k[0:CHUNK], ALU.mult))
                        dve.scalar_tensor_tensor(x3[CHUNK:P, u], e_x[CHUNK:P, u], scale, q[CHUNK:P], ALU.mult, ALU.mult).then_inc(x3_ready, 1)
                for u in BL:
                    dve.wait_ge(scores, u + 1)
                    if samples:
                        dve.tensor_tensor(pT[:, u], sq4(b2[u]), masks["inside"].unsqueeze(1).broadcast_to([C, GH, C]), ALU.mult).then_inc(masked, 1)
                    else:
                        step(dve.tensor_tensor(pT[:, u], sq4(b2[u]), masks["inside"].unsqueeze(1).broadcast_to([C, GH, C]), ALU.mult))
                        dve.tensor_copy(pT[0:CHUNK, u, :, CHUNK:P], sq4(b3[u])[0:CHUNK, :, 0:CHUNK]).then_inc(masked, 1)
                if samples:
                    dve.wait_ge(x_ready, 1)
                    dve.wait_ge(exps, EXPS)
                    for b in range(NS):
                        step(dve.tensor_tensor(S[:, b], S[:, b], e_last[:, 0, :, b:b + 1].broadcast_to([GK, GH, GV]), ALU.mult))

                def normed(u):
                    step(dve.tensor_copy(o[:, u], wide(b0[u])))
                    step(dve.tensor_tensor(sq[:, u], o[:, u], o[:, u], ALU.mult))
                    dve.tensor_reduce(ss[:, u], sq[:, u], AX, ALU.add).then_inc(sum_ready, 1)
                for u in BL:
                    dve.wait_ge(o_ready, u + 1)
                    if not samples:
                        step(dve.tensor_tensor(S[:], S[:], e_last[:, u, :, 0:1].broadcast_to([GK, GH, GV]), ALU.mult))
                        dve.wait_ge(kv_ready, u + 1)
                        dve.tensor_tensor(S[:], S[:], wide(b1[u], GK), ALU.add).then_inc(s_out, 1)
                        dve.wait_ge(s_out, u + 1)
                    normed(u)
                if samples:
                    for b in range(NS):
                        dve.wait_ge(kv_ready, b + 1)
                        dve.tensor_tensor(S[:, b], S[:, b], wide((b1, b2)[b % 2][0], GK), ALU.add).then_inc(s_out, 1)
                for u in BL:
                    dve.wait_ge(er_ready, u + 1)
                    dve.wait_ge(ln_ready, u + 1)
                    step(dve.tensor_tensor(o[:, u], o[:, u], ss[:, u].unsqueeze(2).broadcast_to([C, GH, GV]), ALU.mult))
                    dve.tensor_tensor(o[:, u], o[:, u], er[:, u], ALU.mult).then_inc(done, 1)


def gla(nc, A, O, c, proj, log_a, mixed):
    STEP = 2 * P

    def sources(rows):
        by_block = lambda x, p: x.rearrange("(u p) n -> p u n", p=p)
        p = SROWS if isinstance(rows, slice) and rows.start == SEQ else P
        return by_block(proj[rows, 0:1536], p), by_block(log_a[rows, :], p)
    for samples in (False, True):
        with ExitStack() as ctx:
            sb = lambda n, s: ctx.enter_context(nc.sbuf_tensor(f"{n}_{nc.next_id()}", s, F32))
            C, U = (SROWS, 1) if samples else (P, 2)
            gnorm = sb("gla_norm", [C, GV])
            held = sb("gla_rows", [C, U, 1536]), sb("gla_la", [C, U, GH * GK])
            names = {"tri": "tri_s", "strict": "strict_s", "mid": "mid_s", "inside": "tri_s", "seq": "seq_mask"} if samples else {
                "tri": "tri_p", "strict": "strict_p", "mid": "mid_p", "inside": "inside_p", "border": "border_p"}
            tiles = {k: sb("m_" + k, list(A["c_" + n].shape)) for k, n in names.items()}
            first = slice(SEQ, T) if samples else slice(0, STEP)
            load_all(nc, [(tiles[k][:], A["c_" + n]) for k, n in names.items()] + [(gnorm[:], A["ab_gla_norm"][0].partition_broadcast(C))]
                     + [(buf[:], src) for buf, src in zip(held, sources(first))])
            masks = {k: x[:] for k, x in tiles.items()}
            if samples:
                S = sb("gla_states", [GK, NS, GH, GV])
                gla_block(nc, c, masks, gnorm, held, [mixed[SEQ:T, 0:512]], S, state_in=A["state_gla"][0], state_out=O["s_gla"][0])
                continue
            masks["seq"] = c["ones"][:, 0:1]
            S = sb("gla_state", [GK, GH, GV])
            with phase(nc, "cleared") as (block, cleared):
                @block.vector
                def _(dve):
                    dve.memset(S[:], 0.0).then_inc(cleared, 1)
            with nc.Fori(0, SEQ // STEP - 1) as i:
                gla_block(nc, c, masks, gnorm, held, [mixed[bass.ds(i * STEP + u * P, P), 0:512] for u in range(2)], S,
                          next_src=sources(bass.ds(i * STEP + STEP, STEP)))
            gla_block(nc, c, masks, gnorm, held, [mixed[SEQ - STEP + u * P:SEQ - STEP + (u + 1) * P, 0:512] for u in range(2)], S)
            with phase(nc, "stored") as (block, stored):
                @block.sync
                def _(sp):
                    sp.dma_start(O["p_gla"][0, 0].rearrange("h k v -> k h v"), S[:]).then_inc(stored, 16)
                    sp.wait_ge(stored, 16)


def project_in(nc, A, hT, proj):
    gemm_rows(nc, lambda m, k: hT[:, k, m * P:m * P + ROWS[m]], ROWS, KD, A["ab_w_in"][0],
              lambda m, cols: proj[m * P:m * P + ROWS[m], cols], 476, 6, tag="ab")


def channel_tables(nc, A, c, chan):
    CT = NCH // P
    with ExitStack() as ctx:
        rows = ctx.enter_context(nc.sbuf_tensor("conv_rows", [4 + 3 * NS, NCH], F32))
        pt = [banks(ctx, nc, f"ch{i}", [P, CT // 2, 4 + 3 * NS]) for i in range(2)]
        with phase(nc, "loaded", "turned", "copied") as (block, loaded, turned, copied):
            @block.sync
            def _(sp):
                sp.dma_start(rows[0:4, :], A["c_conv_w"][0]).then_inc(loaded, 16)
                sp.dma_start(rows[4:, :], A["state_gdn_conv"][0].rearrange("b j n -> (b j) n")).then_inc(loaded, 16)

            @block.tensor
            def _(pe):
                pe.wait_ge(loaded, 32)
                n = 4 + 3 * NS
                for t in range(CT):
                    last = pe.transpose(pt[t // (CT // 2)][:, t % (CT // 2), :], rows[:, t * P:(t + 1) * P], c["ident"][0:n, 0:n])
                last.then_inc(turned, 1)

            @block.vector
            def _(dve):
                dve.wait_ge(turned, 1)
                for i in range(2):
                    dve.tensor_copy(chan[:, i * (CT // 2):(i + 1) * (CT // 2), :], pt[i]).then_inc(copied, 1)


def project_convolved(nc, A, O, c, hT, chan, qkv, first, count, normed):
    wr = A["c_w_in"][0].rearrange("(k p) n -> p k n", p=P)
    chunks = [(0, 512), (512, 512), (SEQ, SROWS)]
    HIST = 3 * NS
    with ExitStack() as ctx:
        sb = lambda n, s: ctx.enter_context(nc.sbuf_tensor(f"{n}_{nc.next_id()}", s, F32))
        ws = [sb("w_conv", [P, KD, P]) for _ in range(2)]
        cur = [sb("cur", [P, 4 + HIST]) for _ in range(2)]
        xp, xs = [sb("xp", [P, 3 + SEQ]) for _ in range(2)], [sb("xs", [P, NS, 3 + TS]) for _ in range(2)]
        y = [sb("y_conv", [P, T]) for _ in range(2)]
        last_rows = [sb("last_rows", [P, 3 + HIST]) for _ in range(2)]
        sq, ss, eps = sb("sq", [P, TILES, P]), sb("ss", [P, TILES]), sb("eps", [P, 1])
        stage, stage_last = sb("stage", [P, TILES, P]), sb("stage_last", [3 + HIST, P])
        ps = [banks(ctx, nc, f"pc{j}", [P, 512]) for j in range(3)]
        pt = banks(ctx, nc, "pt", [P, TILES + 1, P])
        parts = [(P, slice(0, MT)), (SROWS, slice(MT, TILES))]
        with phase(nc, "w0", "w1", "w_free0", "w_free1", "filled", "cur_ready", "product", "raw_out", "last_ready", "conv_done",
                   "silu_done", "turned", "turned_free", "squared", "sums", "rs_ready", "staged", "stored", "pre_steps", "post_steps", "act_steps") as (
                block, w0, w1, w_free0, w_free1, filled, cur_ready, product, raw_out, last_ready, conv_done,
                silu_done, turned, turned_free, squared, sums, rs_ready, staged, stored, pre_steps, post_steps, act_steps):
            w_loaded, w_free = [w0, w1], [w_free0, w_free1]

            tile_at = lambda t: bass.ds(t + first, 1)

            @block.sync
            def _(sp):
                for slot in range(2):
                    sp.dma_start(ws[slot][:], wr[:, :, (first + slot) * P:(first + slot + 1) * P]).then_inc(w_loaded[slot], 16)
                with sp.Fori(0, count // 2 - 1) as i:
                    for slot in range(2):
                        sp.wait_ge(w_free[slot], i + 1)
                        sp.dma_start(ws[slot][:], wr[:, :, bass.ds(i * (2 * P) + (first + 2 + slot) * P, P)]).then_inc(w_loaded[slot], 16)

            @block.tensor
            def _(pe):
                pe.sem_inc(turned, 2)

                def pre(t, s):
                    pe.wait_ge(w_loaded[s], t * 8 + (16 - 8 * s))
                    for j, (t0, n) in enumerate(chunks):
                        pe.wait_ge(raw_out, t * 3 + j + 1)
                        for k in range(KD):
                            last = pe.matmul(ps[j][:, 0:n], ws[s][:, k, :], hT[:, k, t0:t0 + n], start=(k == 0), stop=(k == KD - 1))
                        last.then_inc(product, 1)
                    pe.wait_ge(product, t * 3 + 3)
                    pe.sem_inc(w_free[s], 1)

                def post(t, s):
                    pe.wait_ge(silu_done, t + 1)
                    pe.wait_ge(last_ready, t * 2 + 2)
                    pe.wait_ge(turned_free, t + 1)
                    for m in range(TILES):
                        pe.transpose(pt[0:ROWS[m], m, :], y[s][:, m * P:m * P + ROWS[m]], c["ident"][:])
                    pe.transpose(pt[0:3 + HIST, TILES, :], last_rows[s][:], c["ident"][:]).then_inc(turned, 1)
                pipelined(pe, count, pre, post)

            @block.scalar
            def _(act):
                act.sem_inc(raw_out, 3)
                act.sem_inc(stored, 64)

                def pre(t, s):
                    for j, (t0, n) in enumerate(chunks):
                        act.wait_ge(product, t * 3 + j + 1)
                        if j < 2:
                            act.copy(xp[s][:, 3 + t0:3 + t0 + n], ps[j]).then_inc(raw_out, 1)
                        else:
                            act.copy(xs[s][:, :, 3:], ps[j][:, 0:n].rearrange("p (b t) -> p b t", t=TS)).then_inc(raw_out, 1)
                    act.wait_ge(raw_out, t * 3 + 6)
                    act.wait_ge(turned, t + 1)
                    act.copy(last_rows[s][:, 0:3], xp[s][:, SEQ:SEQ + 3]).then_inc(last_ready, 1)
                    act.copy(last_rows[s][:, 3:].rearrange("p (b j) -> p b j", j=3), xs[s][:, :, TS:TS + 3]).then_inc(last_ready, 1)
                    act.wait_ge(conv_done, t + 1)
                    act.activation(y[s][:], y[s][:], ACT.Silu).then_inc(silu_done, 1)

                def post(t, s):
                    if normed:
                        act.wait_ge(turned, t + 3)
                        for r, tiles in parts:
                            act.activation(sq[0:r, tiles, :], pt[0:r, tiles, :], ACT.Square).then_inc(squared, 1)
                        act.wait_ge(sums, t + 1)
                        act.activation(ss[:], ss[:], ACT.Ln, bias=eps[:, 0:1]).then_inc(act_steps, 1)
                        act.wait_ge(act_steps, t + 1)
                        act.activation(ss[:], ss[:], ACT.Exp, scale=-0.5).then_inc(rs_ready, 1)
                    act.wait_ge(staged, t + 1)
                    cols = bass.ds(t * P + first * P, P)
                    act.dma_start(qkv[0:SEQ, cols].rearrange("(m p) n -> p m n", p=P), stage[:, 0:MT, :]).then_inc(stored, 16)
                    act.dma_start(qkv[SEQ:T, cols], stage[0:SROWS, MT, :]).then_inc(stored, 16)
                    act.dma_start(O["p_conv"][0, 0, :, cols], stage_last[0:3, :]).then_inc(stored, 16)
                    act.dma_start(O["s_conv"][0].rearrange("b j n -> (b j) n")[:, cols], stage_last[3:, :]).then_inc(stored, 16)
                pipelined(act, count, pre, post)
                act.wait_ge(stored, 64 * (count + 1))

            @block.gpsimd
            def _(pool):
                for s in range(2):
                    pool.memset(xp[s][:, 0:3], 0.0).then_inc(filled, 1)
                pool.memset(eps[:], L2_EPS).then_inc(filled, 1)

            @block.vector
            def _(dve):
                PRE, POST = 9, 3 if normed else 2

                def in_order(sem, before):
                    done = [0]

                    def step(ins):
                        done[0] += 1
                        ins.then_inc(sem, 1)
                        dve.wait_ge(sem, before + done[0])
                    return step
                dve.memset(ss[:], 1.0).then_inc(filled, 1)
                dve.wait_ge(filled, 4)
                dve.sem_inc(turned_free, 1)

                def pre(t, s):
                    step = in_order(pre_steps, t * PRE)
                    step(dve.tensor_copy(cur[s][:], chan[:, tile_at(t), :].rearrange("p a n -> p (a n)")))
                    step(dve.tensor_copy(xs[s][:, :, 0:3], cur[s][:, 4:].rearrange("p (b j) -> p b j", j=3)))
                    tap = lambda j: cur[s][:, j:j + 1]
                    by_seq = y[s][:, SEQ:T].rearrange("p (b t) -> p b t", t=TS)
                    dve.wait_ge(raw_out, t * 3 + 6)
                    dve.wait_ge(turned, t + 1)
                    step(dve.tensor_scalar(y[s][:, 0:SEQ], xp[s][:, 0:SEQ], tap(0), None, ALU.mult))
                    step(dve.tensor_scalar(by_seq, xs[s][:, :, 0:TS], tap(0), None, ALU.mult))
                    for j in range(1, 4):
                        step(dve.scalar_tensor_tensor(y[s][:, 0:SEQ], xp[s][:, j:j + SEQ], tap(j), y[s][:, 0:SEQ], ALU.mult, ALU.add))
                        last = dve.scalar_tensor_tensor(by_seq, xs[s][:, :, j:j + TS], tap(j), by_seq, ALU.mult, ALU.add)
                        if j < 3:
                            step(last)
                    last.then_inc(conv_done, 1)

                def post(t, s):
                    step = in_order(post_steps, t * POST)
                    dve.wait_ge(turned, t + 3)
                    if normed:
                        dve.wait_ge(squared, t * 2 + 2)
                        step(dve.tensor_reduce(ss[:, 0:MT], sq[:, 0:MT, :], AX, ALU.add))
                        dve.tensor_reduce(ss[0:SROWS, MT:], sq[0:SROWS, MT:, :], AX, ALU.add).then_inc(sums, 1)
                        dve.wait_ge(rs_ready, t + 1)
                    dve.wait_ge(stored, t * 64 + 64)
                    for r, tiles in parts:
                        if normed:
                            scale = ss[0:r, tiles].unsqueeze(2).broadcast_to([r, tiles.stop - tiles.start, P])
                            step(dve.tensor_tensor(stage[0:r, tiles, :], pt[0:r, tiles, :], scale, ALU.mult))
                        else:
                            step(dve.tensor_copy(stage[0:r, tiles, :], pt[0:r, tiles, :]))
                    dve.tensor_copy(stage_last[:], pt[0:3 + HIST, TILES, :]).then_inc(staged, 1)
                    dve.wait_ge(staged, t + 1)
                    dve.sem_inc(turned_free, 1)
                pipelined(dve, count, pre, post)


def gdn_gates(nc, A, ba, gb):
    with ExitStack() as ctx:
        sb = lambda n, s: ctx.enter_context(nc.sbuf_tensor(f"{n}_{nc.next_id()}", s, F32))
        x, e, y = sb("ba", [P, TILES, 2, DH]), sb("ba_e", [P, TILES, 2, DH]), sb("gb", [P, TILES, 2, DH])
        al, dt = sb("a_log", [P, DH]), sb("dt_bias", [P, DH])
        with phase(nc, "zeroed", "loaded", "dve_steps", "abs_ready", "exp_ready", "act_steps", "ln_ready", "done", "stored") as (
                block, zeroed, loaded, dve_steps, abs_ready, exp_ready, act_steps, ln_ready, done, stored):
            @block.sync
            def _(sp):
                sp.wait_ge(zeroed, 1)
                sp.dma_start(x[:, 0:MT], ba[0:SEQ].rearrange("(m p) (c h) -> p m c h", p=P, c=2)).then_inc(loaded, 16)
                sp.dma_start(x[0:SROWS, MT], ba[SEQ:T].rearrange("p (c h) -> p c h", c=2)).then_inc(loaded, 16)
                sp.dma_start(al[:], A["c_a_log"][0].partition_broadcast(P)).then_inc(loaded, 16)
                sp.dma_start(dt[:], A["c_dt_bias"][0].partition_broadcast(P)).then_inc(loaded, 16)
                sp.wait_ge(done, 1)
                sp.dma_start(gb[0:SEQ].rearrange("(m p) (c h) -> p m c h", p=P, c=2), y[:, 0:MT]).then_inc(stored, 16)
                sp.dma_start(gb[SEQ:T].rearrange("p (c h) -> p c h", c=2), y[0:SROWS, MT]).then_inc(stored, 16)
                sp.wait_ge(stored, 32)

            @block.vector
            def _(dve):
                step = InOrder(dve, dve_steps)
                dve.memset(x[:], 0.0).then_inc(zeroed, 1)
                dve.wait_ge(loaded, 64)
                b, a = x[:, :, 0, :], x[:, :, 1, :]
                step(dve.tensor_tensor(a, a, dt[:].unsqueeze(1).broadcast_to([P, TILES, DH]), ALU.add))
                step(dve.scalar_tensor_tensor(e[:, :, 1, :], a, -1.0, a, ALU.mult, ALU.min))
                dve.tensor_scalar(e[:, :, 0, :], b, -1.0, None, ALU.mult).then_inc(abs_ready, 1)
                dve.wait_ge(exp_ready, 2)
                step(dve.tensor_scalar(e[:, :, 0, :], e[:, :, 0, :], 1.0, None, ALU.add))
                step(dve.reciprocal(y[:, :, 1, :], e[:, :, 0, :]))
                dve.wait_ge(ln_ready, 1)
                step(dve.scalar_tensor_tensor(y[:, :, 0, :], a, 0.0, e[:, :, 1, :], ALU.max, ALU.add))
                step(dve.tensor_scalar(y[:, :, 0, :], y[:, :, 0, :], -1.0, None, ALU.mult))
                dve.tensor_tensor(y[:, :, 0, :], y[:, :, 0, :], al[:].unsqueeze(1).broadcast_to([P, TILES, DH]), ALU.mult).then_inc(done, 1)

            @block.scalar
            def _(act):
                step = InOrder(act, act_steps)
                act.wait_ge(loaded, 64)
                act.activation(al[:], al[:], ACT.Exp).then_inc(exp_ready, 1)
                act.wait_ge(abs_ready, 1)
                act.activation(e[:], e[:], ACT.Exp).then_inc(exp_ready, 1)
                act.wait_ge(exp_ready, 2)
                act.activation(e[:, :, 1, :], e[:, :, 1, :], ACT.Ln, bias=1.0).then_inc(ln_ready, 1)


def gdn_block(nc, c, masks, cnorm, held, dst, S, next_src=None, state_in=None, state_out=None):
    samples = state_in is not None
    C, D2 = (SROWS, 2) if samples else (P, 5)
    G, H = range(2), range(4)
    HC = [C, DH, C]
    row, z, gb = held
    tri, strict, ident = masks["tri"], masks["strict"], c["ident"][0:C, 0:C]
    ones = c["ones"]
    with ExitStack() as ctx:
        sb = lambda n, s: ctx.enter_context(nc.sbuf_tensor(f"{n}_{nc.next_id()}", s, F32))
        gm, bm = sb("gm", HC), sb("bm", HC)
        E, MTr, M, Z, PT = sb("E", HC), sb("MT", HC), sb("M", HC), sb("ZT", HC), sb("PT", HC)
        NB = NS if samples else 1
        ed, eend, elast, bd = sb("ed", [C, DH]), sb("eend", [C, DH]), sb("elast", [P, NB, DH]), sb("bd", [C, DH])
        kT, wq = sb("kT", [P, DH, C]), sb("wq", [P, DH, 2, C])
        wT, qT = wq[:, :, 0, :], wq[:, :, 1, :]
        vb, kbd, kl, vn, o, zs = [sb(n, [C, DH, P]) for n in ("vb", "kbd", "kl", "vn", "o", "zs")]
        ss, eps = sb("ss", [C, DH]), sb("eps", [C, 1])
        if samples:
            gs, klm, XT = sb("gs", [C, NS, DH]), sb("klm", [C, NS, DH, P]), sb("XT", [P, DH, 2, C])
        b_m, b_t, b_z, b_x = [[banks(ctx, nc, n, [P, 512]) for _ in G] for n in ("b_m", "b_t", "b_z", "b_x")]
        sq = lambda b: b[0:C, 0:4 * C].rearrange("p (h i) -> p h i", h=4)
        tall = lambda b: b[:, 0:4 * C].rearrange("p (h i) -> p h i", h=4)
        wide = lambda b, r=C: b[0:r, :].rearrange("p (h v) -> p h v", h=4)
        heads = lambda x, g: x[:, 4 * g:4 * g + 4]
        with phase(nc, "loaded", "state_loaded", "gs_ready", "gm_ready", "bm_ready", "sums", "turned", "turned_out", "exps", "kk",
                   "kq", "at_ready", "z_init", "pt_ready", "a_turned", "m_out", "mt_out", "stage", "z_out", "joins", "zn_out",
                   "r_out", "bd_ready", "vb_ready", "kbd_ready", "kl_ready", "klm_ready", "wt_ready", "wt_out", "x_ready", "x_out", "vn_ready",
                   "vn_out", "o_in", "s_ready", "s_out", "sum_ready", "ln_ready", "zs_ready", "zn_ready", "done",
                   "stored", "dve_steps", "act_steps") as (
                block, loaded, state_loaded, gs_ready, gm_ready, bm_ready, sums, turned, turned_out, exps, kk,
                kq, at_ready, z_init, pt_ready, a_turned, m_out, mt_out, stage, z_out, joins, zn_out,
                r_out, bd_ready, vb_ready, kbd_ready, kl_ready, klm_ready, wt_ready, wt_out, x_ready, x_out, vn_ready,
                vn_out, o_in, s_ready, s_out, sum_ready, ln_ready, zs_ready, zn_ready, done,
                stored, dve_steps, act_steps):
            @block.sync
            def _(sp):
                if samples:
                    for b in range(NS):
                        sp.dma_start(S[:, b], state_in[b].rearrange("h k v -> k h v")).then_inc(state_loaded, 16)
                if next_src is not None:
                    sp.wait_ge(turned, 2)
                    sp.wait_ge(vb_ready, 1)
                    sp.wait_ge(kbd_ready, 1)
                    sp.wait_ge(kl_ready, 1)
                    sp.wait_ge(bd_ready, 1)
                    sp.wait_ge(zs_ready, 1)
                    for buf, src in zip(held, next_src):
                        sp.dma_start(buf[:], src).then_inc(loaded, 16)
                if samples:
                    for b in range(NS):
                        sp.wait_ge(s_out, 2 * b + 2)
                        sp.dma_start(state_out[b].rearrange("h k v -> k h v"), S[:, b]).then_inc(stored, 16)
                for g in G:
                    sp.wait_ge(done, g + 1)
                    sp.dma_start(heads(dst, g), heads(o, g)).then_inc(stored, 16)
                sp.wait_ge(stored, 16 * (2 + (NS if samples else 0)))
                if next_src is not None:
                    sp.wait_ge(loaded, 48)

            @block.tensor
            def _(pe):
                pe.matmul(b_z[0][0:C, 0:DH], tri, gb[:, 0, :], start=True, stop=True)
                pe.matmul(b_z[0][0:C, DH:2 * DH], strict, gb[:, 0, :], start=True, stop=True)
                if samples:
                    pe.wait_ge(gs_ready, 1)
                    pe.matmul(b_z[0][:, 2 * DH:(2 + NS) * DH], ones[0:C, :], gs[:].rearrange("p b h -> p (b h)"), start=True, stop=True).then_inc(sums, 1)
                else:
                    pe.matmul(b_z[0][:, 2 * DH:3 * DH], ones[:], gb[:, 0, :], start=True, stop=True).then_inc(sums, 1)
                for g in G:
                    for h in H:
                        pe.transpose(tall(b_m[g])[:, h, :], row[:, 0, 4 * g + h, :], ident)
                    for h in H:
                        last = pe.transpose(tall(b_t[g])[:, h, :], row[:, 1, 4 * g + h, :], ident)
                    last.then_inc(turned, 1)
                pe.wait_ge(gm_ready, 1)
                for g in G:
                    pe.matmul(sq(b_x[g]), strict, heads(gm, g), start=True, stop=True).then_inc(sums, 1)
                pe.wait_ge(bm_ready, 1)
                pe.wait_ge(exps, 3)
                for g in G:
                    pe.matmul(sq(b_z[g]), strict, heads(bm, g), start=True, stop=True).then_inc(sums, 1)
                for g in G:
                    pe.wait_ge(turned_out, 2 * g + 2)
                    for h in H:
                        last = pe.matmul(sq(b_m[g])[:, h, :], kT[:, 4 * g + h, :], kT[:, 4 * g + h, :], start=True, stop=True)
                    last.then_inc(kk, 1)
                    pe.wait_ge(exps, 4 + g)
                    for h in H:
                        last = pe.matmul(sq(b_x[g])[:, h, :], kT[:, 4 * g + h, :], qT[:, 4 * g + h, :], start=True, stop=True)
                    last.then_inc(kq, 1)
                for g in G:
                    pe.wait_ge(at_ready, g + 1)
                    for h in H:
                        last = pe.transpose(sq(b_z[g])[:, h, :], MTr[:, 4 * g + h, :], ident)
                    last.then_inc(a_turned, 1)
                for s in range(D2 + 1):
                    for g in G:
                        pe.wait_ge(m_out, 2 * s + g + 1)
                        if 1 <= s < D2:
                            pe.wait_ge(mt_out, 2 * (s - 1) + g + 1)
                        if s == 1:
                            pe.wait_ge(z_init, g + 1)
                        if s >= 2:
                            pe.wait_ge(z_out, 2 * (s - 2) + g + 1)
                        for h in H:
                            n = 4 * g + h
                            if s < D2:
                                last = pe.matmul(sq(b_m[g])[:, h, :], MTr[:, n, :], M[:, n, :], start=True, stop=True)
                            if s < D2 - 1:
                                last = pe.matmul(sq(b_t[g])[:, h, :], M[:, n, :], MTr[:, n, :], start=True, stop=True)
                            if s >= 1:
                                last = pe.matmul(sq(b_z[g])[:, h, :], M[:, n, :], Z[:, n, :], start=True, stop=True)
                        last.then_inc(stage, 1)
                if not samples:
                    for g in G:
                        pe.wait_ge(z_out, 2 * (D2 - 1) + g + 1)
                        for h in H:
                            last = pe.transpose(sq(b_m[g])[:, h, :], Z[:, 4 * g + h, :], ident)
                        last.then_inc(joins, 1)
                    for g in G:
                        pe.wait_ge(zn_out, g + 1)
                        for h in H:
                            last = pe.matmul(sq(b_t[g])[:, h, :], masks["between"][:, 4 * g + h, :], M[:, 4 * g + h, :], start=True, stop=True)
                        last.then_inc(joins, 1)
                    for g in G:
                        pe.wait_ge(r_out, g + 1)
                        for h in H:
                            last = pe.matmul(sq(b_z[g])[:, h, :], MTr[:, 4 * g + h, :], Z[:, 4 * g + h, :], start=True, stop=True)
                        last.then_inc(joins, 1)
                z_last = 2 * D2 if samples else 2 * D2 + 2
                pe.wait_ge(kbd_ready, 1)
                for g in G:
                    pe.wait_ge(z_out, z_last - 1 + g)
                    for h in H:
                        last = pe.matmul(tall(b_m[g])[:, h, :], kbd[:, 4 * g + h, :], Z[:, 4 * g + h, :], start=True, stop=True)
                    last.then_inc(wt_ready, 1)
                pe.wait_ge(vb_ready, 1)
                pe.wait_ge(kl_ready, 1)
                pe.wait_ge(pt_ready, 2)
                if samples:
                    pe.wait_ge(state_loaded, 16 * NS)
                    for g in G:
                        pe.wait_ge(wt_out, g + 1)
                        out = b_t[g][:, 0:8 * C].rearrange("p (h two i) -> p h two i", h=4, two=2)
                        for h in H:
                            for b in range(NS):
                                t = slice(b * TS, (b + 1) * TS)
                                last = pe.matmul(out[:, h, :, t], S[:, b, 4 * g + h, :], wq[:, 4 * g + h, :, t], start=True, stop=True)
                        last.then_inc(x_ready, 1)
                for g in G:
                    pe.wait_ge(x_out if samples else wt_out, g + 1)
                    b_vn = b_m if samples else b_t
                    for h in H:
                        n = 4 * g + h
                        pe.matmul(wide(b_vn[g])[:, h, :], Z[:, n, :], vb[:, n, :], start=True, stop=False)
                        if samples:
                            last = pe.matmul(wide(b_vn[g])[:, h, :], XT[:, n, 0, :], c["ident"][:], start=False, stop=True)
                        else:
                            last = pe.matmul(wide(b_vn[g])[:, h, :], wT[:, n, :], S[:, n, :], start=False, stop=True)
                    last.then_inc(vn_ready, 1)
                for g in G:
                    for h in H:
                        n = 4 * g + h
                        if samples:
                            last = pe.matmul(wide(b_x[g])[:, h, :], XT[:, n, 1, :], c["ident"][:], start=True, stop=True)
                        else:
                            last = pe.matmul(wide(b_x[g])[:, h, :], qT[:, n, :], S[:, n, :], start=True, stop=True)
                    last.then_inc(o_in, 1)
                for g in G:
                    pe.wait_ge(vn_out, g + 1)
                    b_o = b_t if samples else b_m
                    for h in H:
                        last = pe.matmul(wide(b_o[g])[:, h, :], PT[:, 4 * g + h, :], vn[:, 4 * g + h, :], start=True, stop=True)
                    last.then_inc(o_in, 1)
                    if not samples:
                        for h in H:
                            last = pe.matmul(wide(b_z[g], P)[:, h, :], kl[:, 4 * g + h, :], vn[:, 4 * g + h, :], start=True, stop=True)
                        last.then_inc(s_ready, 1)
                if samples:
                    pe.wait_ge(klm_ready, 1)
                    for b in range(NS):
                        for g in G:
                            out = (b_z, b_m)[b % 2][g]
                            if b >= 2:
                                pe.wait_ge(s_out, 2 * (b - 2) + g + 1)
                            for h in H:
                                last = pe.matmul(wide(out, P)[:, h, :], klm[:, b, 4 * g + h, :], vn[:, 4 * g + h, :], start=True, stop=True)
                            last.then_inc(s_ready, 1)

            @block.scalar
            def _(act):
                step = InOrder(act, act_steps)
                act.activation(zs[:], z[:], ACT.Silu).then_inc(zs_ready, 1)
                act.preload_act_table_set("natural_log_exp_and_others")
                act.wait_ge(sums, 1)
                act.activation(ed[:], b_z[0][0:C, 0:DH], ACT.Exp).then_inc(exps, 1)
                act.activation(eend[:], b_z[0][0:C, DH:2 * DH], ACT.Exp).then_inc(exps, 1)
                act.activation(elast[:].rearrange("p b h -> p (b h)"), b_z[0][:, 2 * DH:(2 + NB) * DH], ACT.Exp).then_inc(exps, 1)
                for g in G:
                    act.wait_ge(turned, g + 1)
                    act.activation(heads(qT, g), tall(b_m[g]), ACT.Copy, scale=P ** -0.5).then_inc(turned_out, 1)
                    act.copy(heads(kT, g), tall(b_t[g])).then_inc(turned_out, 1)
                for g in G:
                    act.wait_ge(sums, 2 + g)
                    act.activation(heads(E, g), sq(b_x[g]), ACT.Exp).then_inc(exps, 1)
                for g in G:
                    act.wait_ge(a_turned, g + 1)
                    act.copy(heads(M, g), sq(b_z[g])).then_inc(m_out, 1)
                for s in range(D2):
                    for g in G:
                        act.wait_ge(stage, 2 * s + g + 1)
                        act.copy(heads(M, g), sq(b_m[g])).then_inc(m_out, 1)
                        if s < D2 - 1:
                            if s == 0:
                                act.wait_ge(z_init, g + 1)
                            act.copy(heads(MTr, g), sq(b_t[g])).then_inc(mt_out, 1)
                if not samples:
                    for g in G:
                        act.wait_ge(joins, g + 1)
                        act.copy(heads(M, g), sq(b_m[g])).then_inc(zn_out, 1)
                    for g in G:
                        act.wait_ge(joins, 3 + g)
                        act.copy(heads(MTr, g), sq(b_t[g])).then_inc(r_out, 1)
                for g in G:
                    act.wait_ge(wt_ready, g + 1)
                    act.copy(heads(wT, g), tall(b_m[g])).then_inc(wt_out, 1)
                if samples:
                    for g in G:
                        act.wait_ge(x_ready, g + 1)
                        act.copy(heads(XT, g), b_t[g][:, 0:8 * C].rearrange("p (h two i) -> p h two i", h=4, two=2)).then_inc(x_out, 1)
                for g in G:
                    act.wait_ge(vn_ready, g + 1)
                    act.copy(heads(vn, g), wide((b_m if samples else b_t)[g])).then_inc(vn_out, 1)
                for g in G:
                    act.wait_ge(sum_ready, g + 1)
                    step(act.activation(heads(ss, g), heads(ss, g), ACT.Ln, scale=1.0 / P, bias=eps[:, 0:1]))
                    act.activation(heads(ss, g), heads(ss, g), ACT.Exp, scale=-0.5).then_inc(ln_ready, 1)

            over_i = lambda x: x.unsqueeze(2).broadcast_to([x.shape[0], x.shape[1], C])
            over_v = lambda x: x.unsqueeze(2).broadcast_to([x.shape[0], x.shape[1], P])
            over_h = lambda x, n=4: x.unsqueeze(1).broadcast_to([C, n, x.shape[1]])

            @block.gpsimd
            def _(pool):
                beta = gb[:, 1, :]
                pool.tensor_tensor(bm[:], over_i(beta), over_h(ident, DH), ALU.mult).then_inc(bm_ready, 1)
                pool.wait_ge(exps, 2)
                pool.tensor_tensor(kl[:], row[:, 1], over_v(eend[:]), ALU.mult).then_inc(kl_ready, 1)
                pool.tensor_tensor(vb[:], row[:, 2], over_v(beta), ALU.mult).then_inc(vb_ready, 1)
                pool.wait_ge(bd_ready, 1)
                pool.tensor_tensor(kbd[:], row[:, 1], over_v(bd[:]), ALU.mult).then_inc(kbd_ready, 1)
                pool.wait_ge(zs_ready, 1)
                pool.tensor_tensor(zs[:], zs[:], over_h(cnorm[0:C, :], DH), ALU.mult).then_inc(zn_ready, 1)
                if samples:
                    flat = lambda x: x.rearrange("p h v -> p (h v)").unsqueeze(1).broadcast_to([C, NS, D])
                    pool.wait_ge(kl_ready, 1)
                    pool.tensor_tensor(klm[:].rearrange("p b h v -> p b (h v)"), flat(kl[:]), masks["seq"].unsqueeze(2).broadcast_to([C, NS, D]),
                                       ALU.mult).then_inc(klm_ready, 1)

            @block.vector
            def _(dve):
                step = InOrder(dve, dve_steps)
                g_, beta = gb[:, 0, :], gb[:, 1, :]
                if samples:
                    dve.tensor_tensor(gs[:], g_.unsqueeze(1).broadcast_to([C, NS, DH]), masks["seq"].unsqueeze(2).broadcast_to([C, NS, DH]),
                                      ALU.mult).then_inc(gs_ready, 1)
                dve.tensor_tensor(gm[:], over_i(g_), over_h(tri, DH), ALU.mult).then_inc(gm_ready, 1)
                step(dve.memset(eps[:], RMS_EPS))
                dve.wait_ge(exps, 1)
                dve.scalar_tensor_tensor(bd[:], ed[:], -1.0, beta, ALU.mult, ALU.mult).then_inc(bd_ready, 1)
                for g in G:
                    dve.wait_ge(exps, 4 + g)
                    step(dve.tensor_tensor(heads(E, g), heads(E, g), over_h(tri), ALU.mult))
                for g in G:
                    dve.wait_ge(kk, g + 1)
                    step(dve.tensor_tensor(heads(MTr, g), sq(b_m[g]), heads(E, g), ALU.mult))
                    dve.wait_ge(sums, 4 + g)
                    if samples:
                        dve.tensor_tensor(heads(MTr, g), heads(MTr, g), sq(b_z[g]), ALU.mult).then_inc(at_ready, 1)
                    else:
                        step(dve.tensor_tensor(heads(MTr, g), heads(MTr, g), sq(b_z[g]), ALU.mult))
                        off = heads(MTr, g)[0:CHUNK, :, CHUNK:P]
                        step(dve.tensor_copy(heads(masks["between"], g)[0:CHUNK, :, CHUNK:P], off))
                        dve.memset(off, 0.0).then_inc(at_ready, 1)
                    dve.wait_ge(at_ready, g + 1)
                    dve.tensor_tensor(heads(Z, g), over_h(ident), heads(MTr, g), ALU.subtract).then_inc(z_init, 1)
                for g in G:
                    dve.wait_ge(kq, g + 1)
                    dve.tensor_tensor(heads(PT, g), sq(b_x[g]), heads(E, g), ALU.mult).then_inc(pt_ready, 1)
                dve.wait_ge(z_init, 2)
                for s in range(1, D2 + 1):
                    for g in G:
                        dve.wait_ge(stage, 2 * s + g + 1)
                        if s > 1:
                            dve.wait_ge(z_out, 2 * (s - 2) + g + 1)
                        dve.tensor_tensor(heads(Z, g), heads(Z, g), sq(b_z[g]), ALU.add).then_inc(z_out, 1)
                if not samples:
                    for g in G:
                        dve.wait_ge(joins, 5 + g)
                        dve.wait_ge(z_out, 2 * (D2 - 1) + g + 1)
                        dve.tensor_tensor(heads(Z, g), heads(Z, g), sq(b_z[g]), ALU.subtract).then_inc(z_out, 1)
                for g in G:
                    dve.wait_ge(o_in, g + 1)
                    step(dve.tensor_tensor(heads(o, g), wide(b_x[g]), over_v(heads(ed, g)), ALU.mult))
                if samples:
                    dve.wait_ge(x_ready, 2)
                    for b in range(NS):
                        step(dve.tensor_tensor(S[:, b], S[:, b], over_v(elast[:, b]), ALU.mult))
                else:
                    step(dve.tensor_tensor(S[:], S[:], over_v(elast[:, 0]), ALU.mult))
                for g in G:
                    dve.wait_ge(o_in, 3 + g)
                    step(dve.tensor_tensor(heads(o, g), heads(o, g), wide((b_t if samples else b_m)[g]), ALU.add))
                    step(dve.tensor_tensor(heads(vb, g), heads(o, g), heads(o, g), ALU.mult))
                    dve.tensor_reduce(heads(ss, g), heads(vb, g), AX, ALU.add).then_inc(sum_ready, 1)
                if not samples:
                    for g in G:
                        dve.wait_ge(s_ready, g + 1)
                        dve.tensor_tensor(heads(S, g), heads(S, g), wide(b_z[g], P), ALU.add).then_inc(s_out, 1)
                dve.wait_ge(zn_ready, 1)
                for g in G:
                    dve.wait_ge(ln_ready, g + 1)
                    step(dve.tensor_tensor(heads(o, g), heads(o, g), over_v(heads(ss, g)), ALU.mult))
                    dve.tensor_tensor(heads(o, g), heads(o, g), heads(zs, g), ALU.mult).then_inc(done, 1)
                if samples:
                    for b in range(NS):
                        for g in G:
                            dve.wait_ge(s_ready, 2 * b + g + 1)
                            dve.tensor_tensor(heads(S[:, b], g), heads(S[:, b], g), wide((b_z, b_m)[b % 2][g], P), ALU.add).then_inc(s_out, 1)


def gdn(nc, A, O, c, z, ba, qkv, gb, mixed):
    with ExitStack() as ctx:
        sb = lambda n, s: ctx.enter_context(nc.sbuf_tensor(f"{n}_{nc.next_id()}", s, F32))
        gdn_gates(nc, A, ba, gb)
        cnorm = sb("c_norm", [P, P])
        load_all(nc, [(cnorm[:], A["c_norm"][0].partition_broadcast(P))])

        def sources(rows):
            return (qkv[rows].rearrange("t (n h k) -> t n h k", n=3, h=DH), z[rows].rearrange("t (h k) -> t h k", h=DH),
                    gb[rows].rearrange("t (n h) -> t n h", n=2))
        with ExitStack() as inner:
            sb = lambda n, s: inner.enter_context(nc.sbuf_tensor(f"{n}_{nc.next_id()}", s, F32))
            S, between = sb("gdn_state", [P, DH, P]), sb("between", [P, DH, P])
            held = sb("qkv", [P, 3, DH, P]), sb("z", [P, DH, P]), sb("gbc", [P, 2, DH])
            tri, strict = sb("tri_p", [P, P]), sb("strict_p", [P, P])
            load_all(nc, [(tri[:], A["c_tri_p"]), (strict[:], A["c_strict_p"])] + [(buf[:], src) for buf, src in zip(held, sources(slice(0, P)))])
            with phase(nc, "cleared") as (block, cleared):
                @block.vector
                def _(dve):
                    dve.memset(S[:], 0.0).then_inc(cleared, 1)
                    dve.memset(between[:], 0.0).then_inc(cleared, 1)
            masks = {"tri": tri[:], "strict": strict[:], "between": between[:]}
            out_rows = lambda rows: mixed[rows].rearrange("t (h k) -> t h k", h=DH)
            with nc.Fori(0, MT - 1) as i:
                gdn_block(nc, c, masks, cnorm, held, out_rows(bass.ds(i * P, P)), S, next_src=sources(bass.ds(i * P + P, P)))
            gdn_block(nc, c, masks, cnorm, held, out_rows(slice(SEQ - P, SEQ)), S)
            with phase(nc, "stored") as (block, stored):
                @block.sync
                def _(sp):
                    sp.dma_start(O["p_gdn"][0, 0].rearrange("h k v -> k h v"), S[:]).then_inc(stored, 16)
                    sp.wait_ge(stored, 16)
        with ExitStack() as inner:
            sb = lambda n, s: inner.enter_context(nc.sbuf_tensor(f"{n}_{nc.next_id()}", s, F32))
            S = sb("gdn_states", [P, NS, DH, P])
            held = sb("qkv", [SROWS, 3, DH, P]), sb("z", [SROWS, DH, P]), sb("gbc", [SROWS, 2, DH])
            tri, strict, seq = sb("tri_s", [SROWS, SROWS]), sb("strict_s", [SROWS, SROWS]), sb("seq_mask", [SROWS, NS])
            load_all(nc, [(tri[:], A["c_tri_s"]), (strict[:], A["c_strict_s"]), (seq[:], A["c_seq_mask"])]
                     + [(buf[:], src) for buf, src in zip(held, sources(slice(SEQ, T)))])
            gdn_block(nc, c, {"tri": tri[:], "strict": strict[:], "seq": seq[:]}, cnorm, held, out_rows(slice(SEQ, T)), S,
                      state_in=A["state_gdn"][0], state_out=O["s_gdn"][0])


def cache_rows(nc, A, O, proj):
    pairs = []
    for name, col in (("cmp_k", K_CMP), ("cmp_v", V_CMP), ("sel_k", K_SEL), ("sel_v", V_SEL)):
        pairs.append((O["p_" + name][0, 0].rearrange("t g d -> t (g d)"), proj[0:SEQ, col:col + P]))
        pairs.append((O["s_" + name][0].rearrange("b t g d -> (b t) (g d)"), proj[SEQ:T, col:col + P]))
    for name, col in (("win_k", K_WIN), ("win_v", V_WIN)):
        pairs.append((O["p_" + name][0, 0].rearrange("t g d -> t (g d)"), proj[SEQ - WIN:SEQ, col:col + P]))
        flat = O["s_" + name][0].rearrange("b t g d -> b t (g d)")
        pairs.append((flat[:, 0:WIN - TS], A["state_" + name][0, :, TS:WIN].rearrange("b t g d -> b t (g d)")))
        pairs.append((flat[:, WIN - TS:WIN], proj[SEQ:T, col:col + P].rearrange("(b t) c -> b t c", t=TS)))
    with phase(nc, "stored_sp", "stored_act") as (block, stored_sp, stored_act):
        @block.sync
        def _(sp):
            for dst, src in pairs[::2]:
                sp.dma_start(dst, src).then_inc(stored_sp, 16)
            sp.wait_ge(stored_sp, 16 * len(pairs[::2]))

        @block.scalar
        def _(act):
            for dst, src in pairs[1::2]:
                act.dma_start(dst, src).then_inc(stored_act, 16)
            act.wait_ge(stored_act, 16 * len(pairs[1::2]))


def turn_queries(nc, c, proj, qk_turned):
    with ExitStack() as ctx:
        rows = ctx.enter_context(nc.sbuf_tensor("qk_rows", [P, MT, D], F32))
        qkT = ctx.enter_context(nc.sbuf_tensor("qkT", [P, KD, SEQ], F32))
        tok = lambda col, n: proj[0:SEQ, col:col + n].rearrange("(m p) c -> p m c", p=P)
        loads = [(rows[:, :, 0:512], tok(Q_B, 512))]
        for j, col in enumerate((K_SEL, K_SEL + HD, K_WIN, K_WIN + HD)):
            for half in range(2):
                at = 512 + j * P + half * HD
                loads.append((rows[:, :, at:at + HD], tok(col, HD)))
        transpose_rows(nc, rows, qkT, c["ident"], tiles=MT, loads=loads)
        with phase(nc, "stored") as (block, stored):
            @block.sync
            def _(sp):
                sp.dma_start(qk_turned.rearrange("n p t -> p n t"), qkT[:]).then_inc(stored, 16)
                sp.wait_ge(stored, 16)


def turn_sample(nc, c, proj, q_diag, k_new):
    with ExitStack() as ctx:
        sb = lambda n, s: ctx.enter_context(nc.sbuf_tensor(f"{n}_{nc.next_id()}", s, F32))
        rows, kn = sb("s_rows", [SROWS, 6, P]), sb("k_new_sb", [P, NS, 2, TS])
        pt = [banks(ctx, nc, f"qs{i}", [P, 4, SROWS]) for i in range(2)]
        with phase(nc, "loaded", "turned", "zeroed", "copied", "stored") as (block, loaded, turned, zeroed, copied, stored):
            @block.sync
            def _(sp):
                q = proj[SEQ:T, Q_B:Q_B + 512].rearrange("r (g h d) -> r g h d", g=2, h=4)
                for g in range(2):
                    sp.dma_start(rows[:, 0:4, g * HD:(g + 1) * HD], q[:, g]).then_inc(loaded, 16)
                sp.dma_start(rows[:, 4, :], proj[SEQ:T, K_SEL:K_SEL + P]).then_inc(loaded, 16)
                sp.dma_start(rows[:, 5, :], proj[SEQ:T, K_WIN:K_WIN + P]).then_inc(loaded, 16)
                sp.wait_ge(copied, 10)
                sp.dma_start(k_new.rearrange("b p n t -> p b n t"), kn[:]).then_inc(stored, 16)
                sp.wait_ge(stored, 16)

            @block.tensor
            def _(pe):
                pe.wait_ge(loaded, 64)
                for n in range(6):
                    last = pe.transpose(pt[n // 4][:, n % 4, :], rows[:, n, :], c["ident"][0:SROWS, 0:SROWS])
                last.then_inc(turned, 1)

            @block.vector
            def _(dve):
                dve.memset(q_diag[:], 0.0).then_inc(zeroed, 1)
                dve.wait_ge(zeroed, 1)
                dve.wait_ge(turned, 1)
                by_seq = lambda x: x.rearrange("p (b t) -> p b t", t=TS)
                for g in range(2):
                    lo = g * HD
                    for h in range(4):
                        at = (g * 4 + h) * TS
                        dve.tensor_copy(q_diag[lo:lo + HD, :, at:at + TS], by_seq(pt[0][lo:lo + HD, h, :])).then_inc(copied, 1)
                for n in range(2):
                    dve.tensor_copy(kn[:, :, n, :], by_seq(pt[1][:, n, :])).then_inc(copied, 1)


def compress_weights(nc, A, n, W1, W2, pe_bias):
    with ExitStack() as ctx:
        pe_sb = ctx.enter_context(nc.sbuf_tensor(f"cmp_pe_sb{n}", [BLK, HD], F32))
        pb = banks(ctx, nc, f"pe{n}", [P, 1])
        with phase(nc, "loaded", "zeroed", "summed", "copied") as (block, loaded, zeroed, summed, copied):
            @block.sync
            def _(sp):
                for half in range(2):
                    sp.dma_start(W1[half * 64:half * 64 + 64, :, half, :],
                                 A["ab_cmp_w1"][0, n].rearrange("(t d) h -> t d h", d=HD)).then_inc(loaded, 16)
                sp.dma_start(W2[:], A["ab_cmp_w2"][0, n]).then_inc(loaded, 16)
                sp.dma_start(pe_sb[:], A["ab_cmp_pe"][0, n]).then_inc(loaded, 16)

            @block.tensor
            def _(pe):
                pe.wait_ge(loaded, 16 * 4)
                for d in range(HD):
                    last = pe.matmul(pb, W1[0:64, d, 0, :], pe_sb[:, d:d + 1], start=(d == 0), stop=(d == HD - 1))
                last.then_inc(summed, 1)

            @block.gpsimd
            def _(pool):
                pool.memset(W1[0:64, :, 1, :], 0.0).then_inc(zeroed, 1)

            @block.vector
            def _(dve):
                dve.memset(W1[64:P, :, 0, :], 0.0).then_inc(zeroed, 1)
                dve.wait_ge(summed, 1)
                dve.tensor_copy(pe_bias[:], pb).then_inc(copied, 1)


def hidden_products(pe, pages, W1, out):
    x = pages.rearrange("p m (g d) -> p (m g) d", d=HD)
    for half in range(2):
        for d in range(HD):
            last = pe.matmul(out[half], W1[:, d, half, :], x[:, :, d], start=(d == 0), stop=(d == HD - 1))
    return last


def compress_prompt(nc, n, proj, W1, W2, pe_bias, out):
    NB = SEQ // BLK
    with ExitStack() as ctx:
        sb = lambda name, s: ctx.enter_context(nc.sbuf_tensor(f"{name}_{nc.next_id()}", s, F32))
        src, hid = sb("cmp_src", [P, MT, P]), sb("cmp_hid", [P, 2, MT, 2])
        ph = [banks(ctx, nc, f"ph{half}", [P, MT * 2]) for half in range(2)]
        r, w = (P, NB) if n == 0 else (NB, HD)
        res, pk = sb("cmp_res", [r, 2, w]), banks(ctx, nc, "pk", [r, 2, w])
        with phase(nc, "loaded", "hidden", "silu_done", "product", "copied", "stored") as (
                block, loaded, hidden, silu_done, product, copied, stored):
            @block.sync
            def _(sp):
                col = (K_CMP, V_CMP)[n]
                sp.dma_start(src[:], proj[0:SEQ, col:col + P].rearrange("(m p) c -> p m c", p=P)).then_inc(loaded, 16)
                sp.wait_ge(copied, 1)
                sp.dma_start(out.rearrange("g p n -> p g n"), res[:]).then_inc(stored, 16)
                sp.wait_ge(stored, 16)

            @block.tensor
            def _(pe):
                pe.wait_ge(loaded, 16)
                hidden_products(pe, src[:], W1, ph).then_inc(hidden, 1)
                pe.wait_ge(silu_done, 2)
                for g in range(2):
                    flat = hid[:, g].rearrange("p m two -> p (m two)")
                    if n == 0:
                        for half in range(2):
                            last = pe.matmul(pk[half * 64:half * 64 + 64, g, :], W2[:], flat, start=True, stop=True)
                    else:
                        last = pe.matmul(pk[:, g, :], flat, W2[:], start=True, stop=True)
                last.then_inc(product, 1)

            @block.scalar
            def _(act):
                act.wait_ge(hidden, 1)
                for half in range(2):
                    act.activation(hid[:, :, :, half], ph[half].rearrange("p (m g) -> p g m", g=2), ACT.Silu,
                                   bias=pe_bias[:, 0:1]).then_inc(silu_done, 1)

            @block.vector
            def _(dve):
                dve.wait_ge(product, 1)
                dve.tensor_copy(res[:], pk).then_inc(copied, 1)


def prompt_attention(nc, c, A, proj, qk_turned, kc_turned, vc_rows, mixed):
    HP = 2
    units = [(m, h) for m in range(MT) for h in range(HP)]
    NB = SEQ // BLK
    NP = MT + WIN // P + 1 + 1
    with ExitStack() as ctx:
        sb = lambda n, s: ctx.enter_context(nc.sbuf_tensor(f"{n}_{nc.next_id()}", s, F32))
        qT, ks, kw, kc = sb("qT", [P, SEQ]), sb("ks", [P, SEQ]), sb("kw", [P, SEQ]), sb("kc", [P, NB])
        v, vc = sb("v", [P, MT, 2, HD]), sb("vc", [NB, HD])
        gates, slopes = sb("gates", [P, MT, HP, 3]), sb("slopes", [P, HP])
        dist_sel, dist_win = sb("dist_sel", [P, 1024]), sb("dist_win", [P, 640])
        dist_cmp, seen = sb("dist_cmp", [P, MT, NB]), sb("seen", [P, MT, NB])
        s_sel, s_win, s_cmp = [[sb(n, [P, w]) for _ in range(2)] for n, w in (("s_sel", 1024), ("s_win", 640), ("s_cmp", NB))]
        top, neg, den, wgt = [[sb(n, [P, 3]) for _ in range(2)] for n in ("top", "neg", "den", "wgt")]
        pT = [sb("pT", [P, NP, P]) for _ in range(2)]
        o = sb("o_pair", [P, MT, HP, HD])
        p_sel, p_win = banks(ctx, nc, "p_sel", [P, 1024]), banks(ctx, nc, "p_win", [P, 1024])
        p_tr = [banks(ctx, nc, f"p_tr{i}", [P, 4, P]) for i in range(2)]
        p_o = [banks(ctx, nc, f"p_o{i}", [P, 3, P]) for i in range(2)]
        load_all(nc, [(dist_sel[:], A["c_dist_sel"]), (dist_win[:], A["c_dist_win"]), (dist_cmp[:], A["c_dist_cmp"]), (seen[:], A["c_seen_cmp"])])
        tok = lambda col, n: proj[0:SEQ, col].rearrange("(m p) c -> p m c", p=P)

        def key_tiles(m):
            n_sel, w0 = m + 1, max(0, m - 4)
            slots = [("s", k) for k in range(n_sel)] + [("w", k) for k in range(w0, m + 1)] + [("c", 0)]
            return n_sel, w0, [slots[i:i + 4] for i in range(0, len(slots), 4)]
        groups_before = [0]
        for m, h in units:
            groups_before.append(groups_before[-1] + len(key_tiles(m)[2]))

        def pair_phase(g, pair):
            with phase(nc, "loaded", "gates_ready", "scores", "scores_out", "neg_ready", "probs", "cmp_masked", "turned", "turned_out",
                       "values", "o_ready", "act_steps", "dve_steps", "stored") as (
                    block, loaded, gates_ready, scores, scores_out, neg_ready, probs, cmp_masked, turned, turned_out,
                    values, o_ready, act_steps, dve_steps, stored):
                @block.sync
                def _(sp):
                    lone = lambda x: x.rearrange("a p t -> p (a t)")
                    sp.dma_start(qT[:], lone(qk_turned[bass.ds(pair, 1)])).then_inc(loaded, 16)
                    sp.dma_start(ks[:], lone(qk_turned[bass.ds(g + 4, 1)])).then_inc(loaded, 16)
                    sp.dma_start(kw[:], lone(qk_turned[bass.ds(g + 6, 1)])).then_inc(loaded, 16)
                    sp.dma_start(kc[:], lone(kc_turned[bass.ds(g, 1)])).then_inc(loaded, 16)
                    sp.dma_start(vc[:], lone(vc_rows[bass.ds(g, 1)])).then_inc(loaded, 16)
                    sp.dma_start(v[:, :, 0, :], tok(bass.ds(g * HD + V_SEL, HD), HD)).then_inc(loaded, 16)
                    sp.dma_start(v[:, :, 1, :], tok(bass.ds(g * HD + V_WIN, HD), HD)).then_inc(loaded, 16)
                    sp.dma_start(gates[:].rearrange("p m h b -> p m (h b)"), tok(bass.ds(pair * 6 + GATE_B, 6), 6)).then_inc(loaded, 16)
                    sp.dma_start(slopes[:], lone(A["c_slopes8"][bass.ds(pair, 1)])).then_inc(loaded, 16)
                    sp.wait_ge(o_ready, len(units))
                    sp.dma_start(mixed[0:SEQ, bass.ds(pair * P + 512, P)].rearrange("(m p) c -> p m c", p=P),
                                 o[:].rearrange("p m h d -> p m (h d)")).then_inc(stored, 16)
                    sp.wait_ge(stored, 16)

                @block.tensor
                def _(pe):
                    def score(u):
                        m, h = units[u]
                        n_sel, w0, _ = key_tiles(m)
                        q = qT[h * HD:(h + 1) * HD, m * P:(m + 1) * P]
                        lo = slice(h * HD, (h + 1) * HD)
                        if u:
                            pe.wait_ge(scores_out, u)
                        for a in range(0, n_sel * P, 512):
                            b = min(a + 512, n_sel * P)
                            pe.matmul(p_sel[:, a:b], q, ks[lo, a:b], start=True, stop=True)
                        nw = (m + 1 - w0) * P
                        for a in range(0, nw, 512):
                            b = min(a + 512, nw)
                            pe.matmul(p_win[:, a:b], q, kw[lo, w0 * P + a:w0 * P + b], start=True, stop=True)
                        pe.matmul(p_win[:, 1024 - NB:1024], q, kc[lo, :], start=True, stop=True).then_inc(scores, 1)

                    pe.wait_ge(loaded, 16 * 9)
                    score(0)
                    for u, (m, h) in enumerate(units):
                        if u + 1 < len(units):
                            score(u + 1)
                        n_sel, w0, groups = key_tiles(m)
                        for n, group in enumerate(groups):
                            done = groups_before[u] + n
                            if done >= 2:
                                pe.wait_ge(turned_out, done - 1)
                            if n == 0:
                                pe.wait_ge(probs, u + 1)
                                pe.wait_ge(cmp_masked, u + 1)
                            for j, (kind, k) in enumerate(group):
                                if kind == "s":
                                    last = pe.transpose(p_tr[done % 2][:, j, :], s_sel[u % 2][:, k * P:(k + 1) * P], c["ident"][:])
                                elif kind == "w":
                                    last = pe.transpose(p_tr[done % 2][:, j, :], s_win[u % 2][:, (k - w0) * P:(k - w0 + 1) * P], c["ident"][:])
                                else:
                                    last = pe.transpose(p_tr[done % 2][0:NB, j, :], s_cmp[u % 2][:], c["ident"][:])
                            last.then_inc(turned, 1)
                        pe.wait_ge(turned_out, groups_before[u + 1])
                        if u >= 2:
                            pe.wait_ge(o_ready, u - 1)
                        slot = 0
                        for k in range(n_sel):
                            pe.matmul(p_o[u % 2][:, 1, :], pT[u % 2][:, slot, :], v[:, k].rearrange("p n d -> p (n d)"), start=(k == 0), stop=(k == n_sel - 1))
                            slot += 1
                        for k in range(w0, m + 1):
                            pe.matmul(p_o[u % 2][:, 2, :], pT[u % 2][:, slot, :], v[:, k].rearrange("p n d -> p (n d)"), start=(k == w0), stop=(k == m))
                            slot += 1
                        pe.matmul(p_o[u % 2][:, 0, 0:HD], pT[u % 2][0:NB, slot, :], vc[:], start=True, stop=True).then_inc(values, 1)

                @block.scalar
                def _(act):
                    act.wait_ge(loaded, 16 * 9)
                    act.activation(gates[:], gates[:], ACT.Exp, scale=-1.0).then_inc(gates_ready, 1)

                    def probabilities(u):
                        m, h = units[u]
                        n_sel, w0, _ = key_tiles(m)
                        act.wait_ge(neg_ready, u + 1)
                        for n, (s, w) in enumerate(((s_cmp[u % 2], NB), (s_sel[u % 2], n_sel * P), (s_win[u % 2], (m + 1 - w0) * P))):
                            ins = act.activation(s[:, 0:w], s[:, 0:w], ACT.Exp, bias=neg[u % 2][:, n:n + 1], scale=HD ** -0.5,
                                                 accum_out=den[u % 2][:, n:n + 1])
                        ins.then_inc(probs, 1)
                    probabilities(0)
                    for u, (m, h) in enumerate(units):
                        _, _, groups = key_tiles(m)
                        slot = 0
                        if u >= 2:
                            act.wait_ge(values, u - 1)
                        for n, group in enumerate(groups):
                            done = groups_before[u] + n
                            act.wait_ge(turned, done + 1)
                            full = len(group) - (group[-1][0] == "c")
                            ins = None
                            if full:
                                ins = act.copy(pT[u % 2][:, slot:slot + full, :], p_tr[done % 2][:, 0:full, :])
                            if full < len(group):
                                ins = act.copy(pT[u % 2][0:NB, slot + full, :], p_tr[done % 2][0:NB, full, :])
                            ins.then_inc(turned_out, 1)
                            slot += len(group)
                        if u + 1 < len(units):
                            probabilities(u + 1)

                @block.vector
                def _(dve):
                    step = InOrder(dve, dve_steps)
                    dve.wait_ge(gates_ready, 1)
                    step(dve.tensor_scalar(gates[:], gates[:], 1.0, None, ALU.add))
                    step(dve.reciprocal(gates[:], gates[:]))

                    def finish_scores(u):
                        m, h = units[u]
                        n_sel, w0, _ = key_tiles(m)
                        b, nw = u % 2, (m + 1 - w0) * P
                        dve.wait_ge(scores, u + 1)
                        if u >= 2:
                            dve.wait_ge(values, u - 1)
                        slope = slopes[:, h:h + 1]
                        add = lambda out, dist, ps: dve.scalar_tensor_tensor(out, dist, slope, ps, ALU.mult, ALU.add)
                        add(s_sel[b][:, 0:n_sel * P], dist_sel[:, 896 - m * P:1024], p_sel[:, 0:n_sel * P])
                        add(s_win[b][:, 0:nw], dist_win[:, 640 - nw:640], p_win[:, 0:nw])
                        step(add(s_cmp[b][:], dist_cmp[:, m, :], p_win[:, 1024 - NB:1024]))
                        dve.sem_inc(scores_out, 1)
                        dve.reduce_max(top[b][:, 0:1], s_cmp[b][:], AX)
                        dve.reduce_max(top[b][:, 1:2], s_sel[b][:, 0:n_sel * P], AX)
                        step(dve.reduce_max(top[b][:, 2:3], s_win[b][:, 0:nw], AX))
                        dve.tensor_scalar(neg[b][:], top[b][:], -(HD ** -0.5), None, ALU.mult).then_inc(neg_ready, 1)
                    finish_scores(0)
                    for u, (m, h) in enumerate(units):
                        b = u % 2
                        dve.wait_ge(probs, u + 1)
                        dve.tensor_tensor(s_cmp[b][:], s_cmp[b][:], seen[:, m, :], ALU.mult).then_inc(cmp_masked, 1)
                        if u + 1 < len(units):
                            finish_scores(u + 1)
                        dve.wait_ge(cmp_masked, u + 1)
                        step(dve.reduce_sum(den[b][:, 0:1], s_cmp[b][:], AX))
                        step(dve.tensor_scalar(den[b][:], den[b][:], 1e-30, None, ALU.max))
                        step(dve.reciprocal(wgt[b][:], den[b][:]))
                        step(dve.tensor_tensor(wgt[b][:], wgt[b][:], gates[:, m, h, :], ALU.mult))
                        dve.wait_ge(values, u + 1)
                        out = o[:, m, h, :]
                        step(dve.tensor_scalar(out, p_o[b][:, 0, 0:HD], wgt[b][:, 0:1], None, ALU.mult))
                        step(dve.scalar_tensor_tensor(out, p_o[b][:, 1, 0:HD], wgt[b][:, 1:2], out, ALU.mult, ALU.add))
                        dve.scalar_tensor_tensor(out, p_o[b][:, 2, HD:P], wgt[b][:, 2:3], out, ALU.mult, ALU.add).then_inc(o_ready, 1)

        with nc.Fori(0, 2) as g:
            with nc.Fori(0, 2) as pr:
                pair_phase(g, g * 2 + pr)


HW_PAGES = 32


def load_pages(eng, pool, ids, seq, some, pages, loaded, taken):
    eng.sem_inc(taken, 1)
    for p in some:
        page = eng.value_load(ids[0:1, bass.ds(seq * PAGES + p, 1)], min_val=0, max_val=NPOOL - 1)
        eng.dma_start(pages[:, p, :], pool[0, bass.ds(page, 1)].rearrange("a t g d -> t (a g d)")).then_inc(loaded, 16)


def sample_hidden(nc, pool_rows, ids, W1, pe_bias, hid, software, turn):
    with ExitStack() as ctx:
        pages = [ctx.enter_context(nc.sbuf_tensor(f"pages{i}_{nc.next_id()}", [P, PAGES, P], F32)) for i in range(2)]
        ph = [[banks(ctx, nc, f"ph{i}{half}", [P, PAGES * 2]) for half in range(2)] for i in range(2)]
        with phase(nc, "hw0", "hw1", "free0", "free1", "hidden", "psum_free", "silu_done", "taken", "taken_sw", "taken_act") as (
                block, hw0, hw1, free0, free1, hidden, psum_free, silu_done, taken, taken_sw, taken_act):
            hw, sw, free = [hw0, hw1], software, [free0, free1]
            to_sp, to_act = 24, 44
            sw_pages = PAGES - to_act
            sw_before = turn * (NS // 2) * 16 * sw_pages

            @block.sync
            def _(sp):
                with sp.Fori(0, NS // 2) as i:
                    for j in range(2):
                        sp.wait_ge(free[j], i * 2 + 2)
                        load_pages(sp, pool_rows, ids, i * 2 + j, range(to_sp), pages[j], hw[j], taken)

            @block.gpsimd
            def _(pool):
                with pool.Fori(0, NS // 2) as i:
                    for j in range(2):
                        pool.wait_ge(free[j], i * 2 + 2)
                        load_pages(pool, pool_rows, ids, i * 2 + j, range(to_act, PAGES), pages[j], sw[j], taken_sw)

            @block.tensor
            def _(pe):
                pe.sem_inc(free0, 2)
                pe.sem_inc(free1, 2)
                with pe.Fori(0, NS // 2) as i:
                    for j in range(2):
                        pe.wait_ge(hw[j], i * (16 * to_act) + 16 * to_act)
                        pe.wait_ge(sw[j], i * (16 * sw_pages) + (sw_before + 16 * sw_pages))
                        pe.wait_ge(psum_free, i * 2 + j + 1)
                        hidden_products(pe, pages[j][:], W1, ph[j]).then_inc(hidden, 1)
                        pe.wait_ge(hidden, i * 2 + j + 1)
                        pe.sem_inc(free[j], 2)

            @block.scalar
            def _(act):
                act.sem_inc(psum_free, 2)

                def load(t, j):
                    act.wait_ge(free[j], t + (2 - j))
                    load_pages(act, pool_rows, ids, t, range(to_sp, to_act), pages[j], hw[j], taken_act)

                def silu(t, j):
                    act.wait_ge(hidden, t + 1)
                    for half in range(2):
                        out = hid[:, bass.ds(t, 1), :, :, half].rearrange("p b g m -> p (b g) m")
                        act.activation(out, ph[j][half].rearrange("p (m g) -> p g m", g=2), ACT.Silu,
                                       bias=pe_bias[:, 0:1]).then_inc(silu_done, 1)
                    act.wait_ge(silu_done, t * 2 + 2)
                    act.sem_inc(psum_free, 1)
                pipelined(act, NS, load, silu)


def sample_importance(nc, c, A, hid, W2, q_diag, p_turned, importance):
    with ExitStack() as ctx:
        sb = lambda n, s, d=F32: ctx.enter_context(nc.sbuf_tensor(f"{n}_{nc.next_id()}", s, d))
        alibi, hsum = sb("alibi_cmp", [64, P]), sb("hsum", [64, NS, P])
        kc, s, top, den = sb("kc_s", [P, NS, P]), sb("s_c", [64, NS, P]), sb("top_c", [64, NS]), sb("den_c", [64, NS])
        pk, ps = banks(ctx, nc, "pk", [P, NS, P]), banks(ctx, nc, "ps", [64, NS, P])
        pt, pi = banks(ctx, nc, "pt", [P, NS, 64]), banks(ctx, nc, "pi", [P, P])
        with phase(nc, "loaded", "keys", "keys_out", "scores", "shifted", "probs", "p_ready", "turned", "sums", "dve_steps", "done") as (
                block, loaded, keys, keys_out, scores, shifted, probs, p_ready, turned, sums, dve_steps, done):
            @block.sync
            def _(sp):
                sp.dma_start(alibi[:], A["c_alibi_cmp"]).then_inc(loaded, 16)
                sp.dma_start(hsum[:].rearrange("p b r -> p (b r)"), A["c_head_sum"]).then_inc(loaded, 16)

            @block.tensor
            def _(pe):
                for b in range(NS):
                    for g in range(2):
                        last = pe.matmul(pk[g * 64:g * 64 + 64, b, :], W2[:], hid[:, b, g].rearrange("p m two -> p (m two)"),
                                         start=True, stop=True)
                last.then_inc(keys, 1)
                pe.wait_ge(keys_out, 1)
                for b in range(NS):
                    last = pe.matmul(ps[:, b, :], q_diag[:, b, :], kc[:, b, :], start=True, stop=True)
                last.then_inc(scores, 1)
                pe.wait_ge(loaded, 32)
                pe.wait_ge(p_ready, 1)
                for b in range(NS):
                    last = pe.transpose(pt[:, b, :], s[:, b, :], c["ident"][0:64, 0:64])
                last.then_inc(turned, 1)
                for b in range(NS):
                    last = pe.matmul(pi, hsum[:, b, :], s[:, b, :], start=(b == 0), stop=(b == NS - 1))
                last.then_inc(sums, 1)

            @block.scalar
            def _(act):
                act.wait_ge(shifted, 1)
                act.activation(s[:], s[:], ACT.Exp).then_inc(probs, 1)

            @block.vector
            def _(dve):
                step = InOrder(dve, dve_steps)
                over = lambda x: x.unsqueeze(2).broadcast_to([64, NS, P])
                dve.wait_ge(keys, 1)
                dve.tensor_copy(kc[:], pk).then_inc(keys_out, 1)
                dve.wait_ge(loaded, 32)
                dve.wait_ge(scores, 1)
                step(dve.scalar_tensor_tensor(s[:], ps, HD ** -0.5, alibi[:].unsqueeze(1).broadcast_to([64, NS, P]), ALU.mult, ALU.add))
                step(dve.reduce_max(top[:], s[:], AX))
                dve.tensor_tensor(s[:], s[:], over(top[:]), ALU.subtract).then_inc(shifted, 1)
                dve.wait_ge(probs, 1)
                step(dve.reduce_sum(den[:], s[:], AX))
                step(dve.tensor_scalar(den[:], den[:], 1e-30, None, ALU.max))
                step(dve.reciprocal(den[:], den[:]))
                dve.tensor_tensor(s[:], s[:], over(den[:]), ALU.mult).then_inc(p_ready, 1)
                dve.wait_ge(turned, 1)
                dve.tensor_copy(p_turned[:], pt).then_inc(done, 1)
                dve.wait_ge(sums, 1)
                dve.tensor_copy(importance[:], pi).then_inc(done, 1)


def sample_compressed_values(nc, hid, W2, p_turned, o_cmp):
    with ExitStack() as ctx:
        vc = ctx.enter_context(nc.sbuf_tensor("vc_s", [P, NS, P], F32))
        pv, po = banks(ctx, nc, "pv", [P, NS, P]), banks(ctx, nc, "po", [64, NS, P])
        with phase(nc, "rows_ready", "rows_out", "values", "done") as (block, rows_ready, rows_out, values, done):
            @block.tensor
            def _(pe):
                for b in range(NS):
                    for g in range(2):
                        last = pe.matmul(pv[:, b, g * HD:(g + 1) * HD], hid[:, b, g].rearrange("p m two -> p (m two)"), W2[:],
                                         start=True, stop=True)
                last.then_inc(rows_ready, 1)
                pe.wait_ge(rows_out, 1)
                for b in range(NS):
                    last = pe.matmul(po[:, b, :], p_turned[:, b, :], vc[:, b, :], start=True, stop=True)
                last.then_inc(values, 1)

            @block.vector
            def _(dve):
                dve.wait_ge(rows_ready, 1)
                dve.tensor_copy(vc[:], pv).then_inc(rows_out, 1)
                dve.wait_ge(values, 1)
                for g in range(2):
                    r = slice(g * 32, g * 32 + 32)
                    dve.tensor_copy(o_cmp[r, :, :], po[r, :, g * HD:(g + 1) * HD]).then_inc(done, 1)


def choose_blocks(nc, importance, block_mask):
    TAKEN = -2.0
    with ExitStack() as ctx:
        sb = lambda n, s: ctx.enter_context(nc.sbuf_tensor(f"{n}_{nc.next_id()}", s, F32))
        left, rest, top, mask = sb("left", [P, P]), sb("rest", [P, P]), sb("top8", [P, 8]), sb("mask", [P, 2, PAGES])
        with phase(nc, "dve_steps", "done", "stored") as (block, dve_steps, done, stored):
            @block.vector
            def _(dve):
                step = InOrder(dve, dve_steps)
                step(dve.memset(importance[:, 0:1], 1000.0))
                step(dve.memset(importance[:, P - 1:P], 1000.0))
                step(dve.max(top[:], importance[:]))
                step(dve.match_replace(left[:], top[:], importance[:], TAKEN))
                step(dve.max(top[:], left[:]))
                step(dve.memset(top[:, 7:8], TAKEN))
                step(dve.match_replace(rest[:], top[:], left[:], TAKEN))
                dve.tensor_scalar(mask[:], rest[:].rearrange("p (m two) -> p two m", two=2), TAKEN, NEG,
                                  ALU.not_equal, ALU.mult).then_inc(done, 1)

            @block.sync
            def _(sp):
                sp.wait_ge(done, 1)
                for b in range(NS):
                    sp.dma_start(block_mask[b].rearrange("two c m -> c two m"), mask[b * 16:(b + 1) * 16]).then_inc(stored, 16)
                sp.wait_ge(stored, 16 * NS)


def sample_selected(nc, c, A, proj, ids, q_diag, k_new, block_mask, o_cmp, mixed, k_sw, v_sw):
    COLS = 64
    branches = [(0, PAGES), (1, 4)]
    with ExitStack() as ctx:
        sb = lambda n, s, d=F32: ctx.enter_context(nc.sbuf_tensor(f"{n}_{nc.next_id()}", s, d))
        kp, vp = sb("k_pages", [P, PAGES, P]), sb("v_pages", [P, PAGES, P])
        kw, vw = sb("k_win", [P, 4, P]), sb("v_win", [P, 4, P])
        kn, vn = sb("k_new", [P, 2, TS]), sb("v_new", [TS, 2, P])
        E = [sb("e_sel", [P, PAGES + 1, COLS]), sb("e_win", [P, 5, COLS])]
        alibi = [sb("alibi_page", [P, PAGES, COLS]), sb("alibi_win", [P, 4, COLS])]
        alibi_new = sb("alibi_new", [TS, COLS])
        kT = [sb("kT", [P, 4, P]) for _ in range(2)]
        half, mask = sb("half", [2, P]), sb("mask_b", [2, 16, PAGES])
        cm, diag, mB = sb("cm", [P, 2, COLS]), sb("diag", [P, P]), sb("mB", [P, 2, COLS])
        mcol = sb("mcol", [P, 1])
        rs, gates, o = sb("rs", [P, 2, COLS]), sb("gates_s", [COLS, NS, 3]), sb("o_s", [COLS, NS, HD])
        w = sb("w_s", [COLS, 2])
        p_tr = [banks(ctx, nc, f"st{i}", [P, 4, P]) for i in range(2)]
        p_s = [banks(ctx, nc, f"ss{i}", [P, 8, COLS]) for i in range(2)]
        p_mask = banks(ctx, nc, "smask", [P, 16, PAGES])
        p_a, p_o = banks(ctx, nc, "sa", [P, P]), banks(ctx, nc, "so", [COLS, 4, P])
        g_rows = [(gates[h * TS:(h + 1) * TS], proj[SEQ:T, GATE_B + 3 * h:GATE_B + 3 * h + 3].rearrange("(b t) c -> t b c", t=TS)) for h in range(NH)]
        load_all(nc, [(alibi[0][:].rearrange("p m c -> p (m c)"), A["c_alibi_page"]), (alibi[1][:].rearrange("p m c -> p (m c)"), A["c_alibi_win"]),
                      (alibi_new[:], A["c_alibi_new"]), (half[:], A["c_half"])] + g_rows)
        SG = PAGES // 4 + 1
        SMALL = 5
        STEPS = 2 + SG + 2 + 2 + 1 + 1 + 3 + 4
        with phase(nc, "k_hw", "v_hw", "taken", "taken_sw", "taken_act", "k_free", "v_free", "small", "small_free", "turned", "kT_out", "scores",
                   "scores_out", "masks", "max_ready", "max_turned", "diag_ready", "max_spread", "shifted", "probs", "summed",
                   "values", "dve_steps", "gates_exp", "gates_done", "o_ready", "stored") as (
                block, k_hw, v_hw, taken, taken_sw, taken_act, k_free, v_free, small, small_free, turned, kT_out, scores,
                scores_out, masks, max_ready, max_turned, diag_ready, max_spread, shifted, probs, summed,
                values, dve_steps, gates_exp, gates_done, o_ready, stored):
            lone = lambda x: x.rearrange("a p n t -> p (a n) t")
            K_SP, K_ACT = 22, 42
            K_SW, V_SW = PAGES - K_ACT, PAGES - HW_PAGES

            @block.sync
            def _(sp):
                with sp.Fori(0, NS) as b:
                    sp.wait_ge(k_free, b + 1)
                    load_pages(sp, A["cache_sel_k"], ids, b, range(K_SP), kp, k_hw, taken)
                    sp.wait_ge(small_free, b + 1)
                    sp.dma_start(kw[:], A["state_win_k"][0, bass.ds(b, 1)].rearrange("a (m p) g d -> p (a m) (g d)", p=P)).then_inc(small, 16)
                    sp.dma_start(vw[:], A["state_win_v"][0, bass.ds(b, 1)].rearrange("a (m p) g d -> p (a m) (g d)", p=P)).then_inc(small, 16)
                    sp.dma_start(mask[:], block_mask[bass.ds(b, 1)].rearrange("a two c m -> two (a c) m")).then_inc(small, 16)
                    sp.dma_start(kn[:], lone(k_new[bass.ds(b, 1)])).then_inc(small, 16)
                    sp.dma_start(vn[:], proj[bass.ds(b * TS + SEQ, TS), V_SEL:V_SEL + 3 * P].rearrange("t (n c) -> t n c", c=P)[:, 0:3:2, :]).then_inc(small, 16)
                    sp.wait_ge(v_free, b + 1)
                    load_pages(sp, A["cache_sel_v"], ids, b, range(HW_PAGES), vp, v_hw, taken)
                sp.wait_ge(o_ready, NS)
                for h in range(NH):
                    sp.dma_start(mixed[SEQ:T, 512 + h * HD:512 + (h + 1) * HD].rearrange("(b t) d -> t b d", t=TS), o[h * TS:(h + 1) * TS]).then_inc(stored, 16)
                sp.wait_ge(stored, 16 * NH)

            @block.gpsimd
            def _(pool):
                with pool.Fori(0, NS) as b:
                    pool.wait_ge(k_free, b + 1)
                    load_pages(pool, A["cache_sel_k"], ids, b, range(K_ACT, PAGES), kp, k_sw, taken_sw)
                    pool.wait_ge(v_free, b + 1)
                    load_pages(pool, A["cache_sel_v"], ids, b, range(HW_PAGES, PAGES), vp, v_sw, taken_sw)

            @block.tensor
            def _(pe):
                pe.sem_inc(k_free, 1)
                pe.sem_inc(v_free, 1)
                with pe.Fori(0, NS) as b:
                    q = q_diag[:, bass.ds(b, 1), :].rearrange("p b c -> p (b c)")
                    pe.wait_ge(k_hw, b * (16 * K_ACT) + 16 * K_ACT)
                    pe.wait_ge(k_sw, b * (16 * K_SW) + 16 * K_SW)
                    for n in range(SG + 1):
                        if n < SG:
                            pe.wait_ge(kT_out, b * SG + n + 1)
                            if n == SG - 1:
                                pe.wait_ge(small, b * (16 * SMALL) + 16 * SMALL)
                            for j in range(4):
                                page = kw[:, j, :] if n == SG - 1 else kp[:, 4 * n + j, :]
                                last = pe.transpose(p_tr[n % 2][:, j, :], page, c["ident"][:])
                            last.then_inc(turned, 1)
                            if n == SG - 2:
                                pe.wait_ge(turned, b * SG + n + 1)
                                pe.sem_inc(k_free, 1)
                        if n >= 1:
                            s = n - 1
                            pe.wait_ge(kT_out, b * SG + s + 3)
                            pe.wait_ge(scores_out, b * SG + s + 1)
                            for j in range(4):
                                last = pe.matmul(p_s[s % 2][:, j, :], kT[s % 2][:, j, :], q, start=True, stop=True)
                            if s == SG - 1:
                                for k in range(2):
                                    last = pe.matmul(p_s[s % 2][0:TS, 4 + k, :], kn[:, k, :], q_diag[:, bass.ds(b, 1), :].rearrange("p b c -> p (b c)"), start=True, stop=True)
                            last.then_inc(scores, 1)
                    for n in range(2):
                        last = pe.matmul(p_mask[:, n * 8:(n + 1) * 8, :], half[:], mask[:, n * 8:(n + 1) * 8, :], start=True, stop=True)
                    last.then_inc(masks, 1)
                    pe.wait_ge(max_ready, b + 1)
                    pe.transpose(p_a, cm[:].rearrange("p n c -> p (n c)"), c["ident"][:]).then_inc(max_turned, 1)
                    pe.wait_ge(diag_ready, b + 1)
                    pe.matmul(p_a, c["ones"][:], diag[:], start=True, stop=True).then_inc(max_spread, 1)
                    pe.wait_ge(v_hw, b * (16 * HW_PAGES) + 16 * HW_PAGES)
                    pe.wait_ge(v_sw, b * (16 * V_SW) + 16 * V_SW)
                    for n, count in branches:
                        pe.wait_ge(probs, b * 2 + n + 1)
                        for k in range(count):
                            pe.matmul(p_o[:, n, :], E[n][:, k, :], (vp if n == 0 else vw)[:, k, :], start=(k == 0), stop=False)
                        pe.matmul(p_o[:, n, :], E[n][0:TS, count, :], vn[:, n, :], start=False, stop=True)
                    pe.wait_ge(summed, b * 2 + 2)
                    for n in range(2):
                        last = pe.matmul(p_o[:, 2, n:n + 1], rs[:, n, :], c["ones"][:, 0:1], start=True, stop=True)
                    last.then_inc(values, 1)
                    pe.wait_ge(values, b + 1)
                    pe.sem_inc(v_free, 1)

            @block.scalar
            def _(act):
                act.activation(gates[:], gates[:], ACT.Exp, scale=-1.0).then_inc(gates_exp, 1)
                act.sem_inc(kT_out, 2)

                def load_keys(b):
                    act.wait_ge(k_free, b + 1)
                    load_pages(act, A["cache_sel_k"], ids, b, range(K_SP, K_ACT), kp, k_hw, taken_act)

                def sequence(b, more):
                    for n in range(SG):
                        act.wait_ge(turned, b * SG + n + 1)
                        if n >= 2:
                            act.wait_ge(scores, b * SG + n - 1)
                        act.copy(kT[n % 2][:], p_tr[n % 2]).then_inc(kT_out, 1)
                    if more:
                        load_keys(b + 1)
                    for n in range(2):
                        act.wait_ge(shifted, b * 2 + n + 1)
                        act.activation(E[n][:], E[n][:], ACT.Exp).then_inc(probs, 1)
                load_keys(0)
                with act.Fori(0, NS - 1) as b:
                    sequence(b, True)
                sequence(NS - 1, False)

            @block.vector
            def _(dve):
                dve.wait_ge(gates_exp, 1)
                dve.tensor_scalar(gates[:], gates[:], 1.0, None, ALU.add).then_inc(gates_done, 1)
                dve.wait_ge(gates_done, 1)
                dve.reciprocal(gates[:], gates[:]).then_inc(gates_done, 1)
                dve.wait_ge(gates_done, 2)
                dve.tensor_tensor(o[:], o_cmp[:], gates[:, :, 0:1].broadcast_to([COLS, NS, HD]), ALU.mult).then_inc(gates_done, 1)
                dve.wait_ge(gates_done, 3)
                dve.sem_inc(small_free, 1)
                dve.sem_inc(scores_out, 2)
                with dve.Fori(0, NS) as b:
                    done = [0]

                    def step(ins):
                        done[0] += 1
                        ins.then_inc(dve_steps, 1)
                        dve.wait_ge(dve_steps, b * STEPS + done[0])
                    for n, count in branches:
                        step(dve.memset(E[n][:, count, :], NEG))
                    for s in range(SG):
                        dve.wait_ge(scores, b * SG + s + 1)
                        ps = p_s[s % 2]
                        if s == SG - 1:
                            for n, count in branches:
                                dve.scalar_tensor_tensor(E[n][0:TS, count, :], ps[0:TS, 4 + n, :], HD ** -0.5, alibi_new[:], ALU.mult, ALU.add)
                            out, al = E[1][:, 0:4, :], alibi[1][:]
                        else:
                            out, al = E[0][:, 4 * s:4 * s + 4, :], alibi[0][:, 4 * s:4 * s + 4, :]
                        step(dve.scalar_tensor_tensor(out, ps[:, 0:4, :], HD ** -0.5, al, ALU.mult, ALU.add))
                        dve.sem_inc(scores_out, 1)
                    dve.wait_ge(masks, b + 1)
                    for g in range(2):
                        v = E[0][:, 0:PAGES, g * 32:(g + 1) * 32].rearrange("p m (h t) -> p h t m", h=4)
                        step(dve.tensor_tensor(v, v, p_mask[:, g * 8:(g + 1) * 8, :].unsqueeze(1).broadcast_to([P, 4, TS, PAGES]), ALU.add))
                    for n, count in branches:
                        step(dve.reduce_max(cm[:, n, :], E[n][:].rearrange("p m c -> p c m"), AX))
                    dve.sem_inc(max_ready, 1)
                    dve.wait_ge(max_turned, b + 1)
                    step(dve.reduce_max(mcol[:], p_a, AX))
                    dve.tensor_scalar(diag[:], c["ident"][:], mcol[:, 0:1], None, ALU.mult).then_inc(diag_ready, 1)
                    dve.wait_ge(max_spread, b + 1)
                    step(dve.tensor_copy(mB[:].rearrange("p n c -> p (n c)"), p_a))
                    for n, count in branches:
                        dve.tensor_tensor(E[n][:], E[n][:], mB[:, n, :].unsqueeze(1).broadcast_to([P, count + 1, COLS]), ALU.subtract).then_inc(shifted, 1)
                    for n, count in branches:
                        dve.wait_ge(probs, b * 2 + n + 1)
                        dve.reduce_sum(rs[:, n, :], E[n][:].rearrange("p m c -> p c m"), AX).then_inc(summed, 1)
                    dve.wait_ge(values, b + 1)
                    g_b = gates[:, bass.ds(b, 1), 1:3].rearrange("p b n -> p (b n)")
                    step(dve.tensor_scalar(w[:], p_o[:, 2, 0:2], 1e-30, None, ALU.max))
                    step(dve.reciprocal(w[:], w[:]))
                    step(dve.tensor_tensor(w[:], w[:], g_b, ALU.mult))
                    for n in range(2):
                        for g in range(2):
                            r = slice(g * 32, g * 32 + 32)
                            ob = o[r, bass.ds(b, 1), :].rearrange("p b d -> p (b d)")
                            step(dve.scalar_tensor_tensor(ob, p_o[r, n, g * HD:(g + 1) * HD], w[r, n:n + 1], ob, ALU.mult, ALU.add))
                    dve.sem_inc(o_ready, 1)
                    dve.sem_inc(small_free, 1)
                    assert done[0] == STEPS


def sample_nsa_cache(nc, c, A, proj, kc_turned, vc_rows, ids, q_diag, importance, o_cmp, software):
    with ExitStack() as ctx:
        sb = lambda n, s: ctx.enter_context(nc.sbuf_tensor(n, s, F32))
        W1, W2, pe_bias = sb("cmp_w1", [P, HD, 2, P]), sb("cmp_w2", [P, HD]), sb("pe_bias", [P, 1])
        p_turned = sb("p_turned", [P, NS, 64])
        for n in range(2):
            compress_weights(nc, A, n, W1, W2, pe_bias)
            compress_prompt(nc, n, proj, W1, W2, pe_bias, (kc_turned, vc_rows)[n])
            with nc.sbuf_tensor(f"cmp_hid_all{n}", [P, NS, 2, PAGES, 2], F32) as hid:
                sample_hidden(nc, A[("cache_cmp_k", "cache_cmp_v")[n]], ids, W1, pe_bias, hid, software, n)
                if n == 0:
                    sample_importance(nc, c, A, hid, W2, q_diag, p_turned, importance)
                else:
                    sample_compressed_values(nc, hid, W2, p_turned, o_cmp)


BASE = ("ident", "ones", "sel_mod_p", "sel_mod_s")


def hybrid_decoder(nc, A, O):
    scratch = lambda n, s: nc.dram_tensor("scratch_" + n, s, F32, kind="Internal").ap()
    mod_rows = scratch("mod_rows", [MODS, 2, 6 * D])
    y, mixed = scratch("y", [T, D]), scratch("mixed", [T, D])
    software = [nc.alloc_semaphore(f"software_dma{i}") for i in range(4)]
    row_tile = lambda x, m, cols: x[m * P:m * P + ROWS[m], cols]
    with ExitStack() as top:
        sb = lambda n, s, st=top: st.enter_context(nc.sbuf_tensor(n, s, F32))
        c = {k: sb("c_" + k, list(A["c_" + k].shape)) for k in BASE}
        X, modT = sb("X", [P, TILES, D]), sb("modT", [P, 2, 4, KD, MODS])
        load_all(nc, [(c[k][:], A["c_" + k]) for k in BASE]
                 + [(X[:, 0:MT, :], A["x_prompt"][0].rearrange("(m p) d -> p m d", p=P)),
                    (X[0:SROWS, MT, :], A["x_sample"].rearrange("b t d -> (b t) d"))])
        adaln_mods(nc, A, c, modT, mod_rows)

        def mix_in(w, layer):
            with ExitStack() as ctx:
                hT = ctx.enter_context(nc.sbuf_tensor(f"mT_{nc.next_id()}", [P, KD, T], F32))
                with nc.sbuf_tensor(f"mrows_{nc.next_id()}", [P, TILES, D], F32) as rows:
                    loads = [(rows[:, 0:MT, :], mixed[0:SEQ].rearrange("(m p) d -> p m d", p=P)), (rows[0:SROWS, MT, :], mixed[SEQ:T])]
                    transpose_rows(nc, rows, hT, c["ident"], loads=loads)
                project_norm(nc, X, hT, w, mod_rows[:, layer, 2 * D:3 * D], A["ln_g"][layer, 0], A["ln_b"][layer, 0], c)

        proj = scratch("proj", [T, AB_IN])
        with nc.sbuf_tensor("hT_ab", [P, KD, T], F32) as hT:
            transpose_rows(nc, X, hT, c["ident"], (modT[:, 0, 0], modT[:, 0, 1]))
            project_in(nc, A, hT, proj)
        cache_rows(nc, A, O, proj)
        log_a = scratch("log_a", [T, GH * GK])
        gla_gates(nc, A, c, proj, log_a)
        gla(nc, A, O, c, proj, log_a, mixed)
        qk_turned, k_new = scratch("qk", [8, P, SEQ]), scratch("k_new", [NS, P, 2, TS])
        kc_turned, vc_rows = scratch("kc", [2, P, SEQ // BLK]), scratch("vc", [2, SEQ // BLK, HD])
        block_mask = scratch("block_mask", [NS, 2, 16, PAGES])
        turn_queries(nc, c, proj, qk_turned)
        with ExitStack() as ctx:
            importance, q_diag, o_cmp = sb("importance", [P, P], ctx), sb("q_diag", [P, NS, 64], ctx), sb("o_cmp", [64, NS, HD], ctx)
            ids = ctx.enter_context(nc.sbuf_tensor("page_ids", [1, NS * PAGES], I32))
            load_all(nc, [(ids[:], A["page_table"].rearrange("b p -> (b p)").unsqueeze(0))])
            turn_sample(nc, c, proj, q_diag, k_new)
            sample_nsa_cache(nc, c, A, proj, kc_turned, vc_rows, ids, q_diag, importance, o_cmp, software[0:2])
            choose_blocks(nc, importance, block_mask)
            sample_selected(nc, c, A, proj, ids, q_diag, k_new, block_mask, o_cmp, mixed, *software[2:4])
        prompt_attention(nc, c, A, proj, qk_turned, kc_turned, vc_rows, mixed)
        mix_in(A["ab_w_out"][0], 0)
        ffn(nc, A, c, X, 0, modT, mod_rows, y)

        z, ba, qkv, gb = scratch("z", [T, D]), scratch("ba", [T, 16]), scratch("qkv", [T, NCH]), scratch("gb", [T, 16])
        with ExitStack() as ctx:
            hT, chan = sb("hT_c", [P, KD, T], ctx), sb("chan", [P, NCH // P, 4 + 3 * NS], ctx)
            transpose_rows(nc, X, hT, c["ident"], (modT[:, 1, 0], modT[:, 1, 1]))
            lhsT = lambda m, k: hT[:, k, m * P:m * P + ROWS[m]]
            w = A["c_w_in"][0]
            channel_tables(nc, A, c, chan)
            project_convolved(nc, A, O, c, hT, chan, qkv, 0, 2 * DH, True)
            project_convolved(nc, A, O, c, hT, chan, qkv, 2 * DH, DH, False)
            gemm_rows(nc, lhsT, ROWS, KD, w[:, C_BA:C_Z], lambda m, cols: row_tile(ba, m, cols), 16, 1, tag="cb")
            gemm_rows(nc, lhsT, ROWS, KD, w[:, C_Z:C_IN], lambda m, cols: row_tile(z, m, cols), 512, 2, tag="cz")
        gdn(nc, A, O, c, z, ba, qkv, gb, mixed)
        mix_in(A["c_w_out"][0], 1)
        ffn(nc, A, c, X, 1, modT, mod_rows, y, (O["y_prompt"][0], O["y_sample"].rearrange("b t d -> (b t) d")))
    nc.all_engine_barrier(sems_to_clear=range(software[0].num, software[-1].num + 1))


_INS = ["x_prompt", "x_sample", "c_prompt", "c_sample", "page_table", "cache_cmp_k", "cache_cmp_v", "cache_sel_k", "cache_sel_v",
        "state_win_k", "state_win_v", "state_gla", "state_gdn", "state_gdn_conv", "w_ada", "b_ada", "ln_g", "ln_b", "w_ffn_in",
        "w_ffn_out", "ab_w_in", "ab_w_gk2", "ab_b_gk", "ab_gla_norm", "ab_cmp_pe", "ab_cmp_w1", "ab_cmp_w2", "ab_w_out", "c_w_in",
        "c_conv_w", "c_a_log", "c_dt_bias", "c_norm", "c_w_out"]
_ROWS_P, _ROWS_S = (1, 1, SEQ, 2, HD), (1, NS, TS, 2, HD)
_OUTS = {"y_prompt": (1, SEQ, D), "y_sample": (NS, TS, D),
         "p_cmp_k": _ROWS_P, "p_cmp_v": _ROWS_P, "p_sel_k": _ROWS_P, "p_sel_v": _ROWS_P,
         "p_win_k": (1, 1, WIN, 2, HD), "p_win_v": (1, 1, WIN, 2, HD),
         "p_gla": (1, 1, GH, GK, GV), "p_gdn": (1, 1, DH, P, P), "p_conv": (1, 1, 3, NCH),
         "s_cmp_k": _ROWS_S, "s_cmp_v": _ROWS_S, "s_sel_k": _ROWS_S, "s_sel_v": _ROWS_S,
         "s_win_k": (1, NS, WIN, 2, HD), "s_win_v": (1, NS, WIN, 2, HD),
         "s_gla": (1, NS, GH, GK, GV), "s_gdn": (1, NS, DH, P, P), "s_conv": (1, NS, 3, NCH)}


def kernel(**inputs):
    import numpy as _np
    import concourse.bacc as _bacc
    from concourse import mybir as _mybir
    from concourse.bass_utils import run_bass_kernel_spmd as _run

    nc = _bacc.Bacc("TRN2", target_bir_lowering=False, num_devices=1)
    arrays, A, O = {}, {}, {}
    given = {name: inputs[name] for name in _INS}
    given.update({"c_" + name: a for name, a in shape_constants().items()})
    for name, a in given.items():
        a = _np.ascontiguousarray(a)
        arrays[f"in_{name}"] = a
        A[name] = nc.dram_tensor(f"in_{name}", a.shape, _mybir.dt.from_np(a.dtype), kind="ExternalInput").ap()
    for name, shape in _OUTS.items():
        O[name] = nc.dram_tensor(f"out_{name}", shape, _mybir.dt.float32, kind="ExternalOutput").ap()
    hybrid_decoder(nc, A, O)
    r = _run(nc, [arrays], core_ids=[0])
    return tuple(r.results[0][f"out_{name}"] for name in _OUTS)
```
